# Optimizing a Trainium2 kernel written in Bass

```python
import jax, jax.numpy as jnp
from jax import lax
import numpy as np

D_MODEL = 1024
BATCH = 1
SEQ = 256
DEPTH = 2

EPS = 1e-6
D_FF = 2816
CONV_WIDTH = 4
D_RG = D_MODEL // 2
RG_BLOCKS = 8
RG_C = 8.0
ML_HEADS = 4
D_ML = D_MODEL // 2
ML_HEAD_DIM = D_ML // ML_HEADS
ML_CHUNK = 128
D_AB_IN = 2 * D_RG + 4 * D_ML + 2 * ML_HEADS
NSA_HEADS = 16
NSA_GROUPS = 4
NSA_HEAD_DIM = 64
NSA_KV = NSA_GROUPS * NSA_HEAD_DIM
NSA_WIDTH = NSA_HEADS * NSA_HEAD_DIM
CMP_BLOCK = 32
CMP_STRIDE = 16
CMP_HIDDEN = 256
SEL_BLOCK = 64
SEL_TOPN = 8
WINDOW = 256
NSA_QBLOCK = 64
NSA_BRANCHES = 3
D_NSA_IN = NSA_WIDTH + 6 * NSA_KV + NSA_BRANCHES * NSA_HEADS
FORCED_SCORE = 1e6
N_EVEN = (DEPTH + 1) // 2
N_ODD = DEPTH // 2


def rmsnorm(x, g):
    xf = x.astype(jnp.float32)
    y = xf * lax.rsqrt(jnp.mean(xf * xf, axis=-1, keepdims=True) + EPS)
    return (y * g.astype(jnp.float32)).astype(x.dtype)

def swiglu_ffn(x, w_gu, w_down):
    gate, up = jnp.split(x @ w_gu, 2, axis=-1)
    return (jax.nn.silu(gate) * up) @ w_down

def causal_dwconv(x, w, b):
    k, c = w.shape
    y = lax.conv_general_dilated(x, w[:, None, :], window_strides=(1,), padding=[(k - 1, 0)],
                                 dimension_numbers=('NWC', 'WIO', 'NWC'), feature_group_count=c)
    return y + b

def masked_softmax(s, mask):
    s = jnp.where(mask, s.astype(jnp.float32), -1e30)
    return jax.nn.softmax(s, axis=-1) * mask

def rglru(x, w_r, b_r, w_i, b_i, lam):
    bsz, s, c = x.shape
    xb = x.reshape(bsz, s, RG_BLOCKS, c // RG_BLOCKS)
    r = jax.nn.sigmoid(jnp.einsum('bsnc,ncd->bsnd', xb, w_r).reshape(bsz, s, c) + b_r)
    ig = jax.nn.sigmoid(jnp.einsum('bsnc,ncd->bsnd', xb, w_i).reshape(bsz, s, c) + b_i)
    log_a = -RG_C * r.astype(jnp.float32) * jax.nn.softplus(-lam.astype(jnp.float32))
    a = jnp.exp(log_a)
    u = jnp.sqrt(-jnp.expm1(2.0 * log_a)) * (ig * x).astype(jnp.float32)

    def combine(left, right):
        a1, b1 = left
        a2, b2 = right
        return a1 * a2, a2 * b1 + b2

    _, h = lax.associative_scan(combine, (a, u), axis=1)
    return h.astype(x.dtype)

def mlstm_chunkwise(q, k, v, log_i, log_f):
    bsz, nh, s, dh = q.shape
    nc = s // ML_CHUNK
    q = q.reshape(bsz, nh, nc, ML_CHUNK, dh) * (dh ** -0.5)
    k = k.reshape(bsz, nh, nc, ML_CHUNK, dh)
    v = v.reshape(bsz, nh, nc, ML_CHUNK, dh)
    log_i = log_i.reshape(bsz, nh, nc, ML_CHUNK)
    b = jnp.cumsum(log_f.reshape(bsz, nh, nc, ML_CHUNK), axis=-1)
    g = b[..., -1]
    w = g[..., None] - b + log_i
    m_loc = jnp.max(w, axis=-1)
    wk = jnp.exp(w - m_loc[..., None])
    c_loc = jnp.einsum('bhcl,bhclv,bhclk->bhcvk', wk, v, k)
    n_loc = jnp.einsum('bhcl,bhclk->bhck', wk, k)

    def step(carry, xs):
        c_st, n_st, m_st = carry
        c_l, n_l, m_l, g_c = xs
        m_new = jnp.maximum(g_c + m_st, m_l)
        sa = jnp.exp(g_c + m_st - m_new)
        sb = jnp.exp(m_l - m_new)
        new = (sa[..., None, None] * c_st + sb[..., None, None] * c_l,
               sa[..., None] * n_st + sb[..., None] * n_l, m_new)
        return new, carry

    init = (jnp.zeros((bsz, nh, dh, dh), jnp.float32), jnp.zeros((bsz, nh, dh), jnp.float32),
            jnp.full((bsz, nh), -1e30, jnp.float32))
    xs = (jnp.moveaxis(c_loc, 2, 0), jnp.moveaxis(n_loc, 2, 0),
          jnp.moveaxis(m_loc, 2, 0), jnp.moveaxis(g, 2, 0))
    _, (c0, n0, m0) = lax.scan(step, init, xs)
    c0 = jnp.moveaxis(c0, 0, 2)
    n0 = jnp.moveaxis(n0, 0, 2)
    m0 = jnp.moveaxis(m0, 0, 2)
    causal = jnp.tril(jnp.ones((ML_CHUNK, ML_CHUNK), bool))
    d = jnp.where(causal, b[..., :, None] - b[..., None, :] + log_i[..., None, :], -jnp.inf)
    m_inter = b + m0[..., None]
    m = jnp.maximum(m_inter, jnp.max(d, axis=-1))
    p = jnp.exp(d - m[..., None]) * jnp.einsum('bhcjd,bhckd->bhcjk', q, k)
    sc = jnp.exp(m_inter - m)
    num = sc[..., None] * jnp.einsum('bhcvk,bhcjk->bhcjv', c0, q) + jnp.einsum('bhcjk,bhckv->bhcjv', p, v)
    den = sc * jnp.einsum('bhck,bhcjk->bhcj', n0, q) + jnp.sum(p, axis=-1)
    h = num / jnp.maximum(jnp.abs(den), jnp.exp(-m))[..., None]
    return h.reshape(bsz, nh, s, dh)

def mlstm_block(qk, v, o, i_pre, f_pre, conv_w, conv_b, b_i, b_f, norm_g):
    bsz, s, _ = v.shape
    qk = jax.nn.silu(causal_dwconv(qk, conv_w, conv_b))
    q, k = jnp.split(qk, 2, axis=-1)
    heads = lambda t: t.reshape(bsz, s, ML_HEADS, ML_HEAD_DIM).transpose(0, 2, 1, 3).astype(jnp.float32)
    log_i = (i_pre + b_i).astype(jnp.float32).transpose(0, 2, 1)
    log_f = jax.nn.log_sigmoid((f_pre + b_f).astype(jnp.float32)).transpose(0, 2, 1)
    h = mlstm_chunkwise(heads(q), heads(k), heads(v), log_i, log_f)
    h = h * lax.rsqrt(jnp.mean(h * h, axis=-1, keepdims=True) + EPS)
    h = h.transpose(0, 2, 1, 3).reshape(bsz, s, D_ML) * norm_g.astype(jnp.float32)
    return (jax.nn.sigmoid(o.astype(jnp.float32)) * h).astype(v.dtype)

def ab_mixer(xn, w_in, rg_conv_w, rg_conv_b, rg_w_r, rg_b_r, rg_w_i, rg_b_i, rg_lambda,
             ml_conv_w, ml_conv_b, ml_b_i, ml_b_f, ml_norm, w_out):
    proj = xn @ w_in
    cuts = [D_RG, 2 * D_RG, 2 * D_RG + 2 * D_ML, 2 * D_RG + 3 * D_ML, 2 * D_RG + 4 * D_ML,
            2 * D_RG + 4 * D_ML + ML_HEADS]
    xa, ga, qk, v, o, i_pre, f_pre = jnp.split(proj, cuts, axis=-1)
    ya = jax.nn.gelu(ga) * rglru(causal_dwconv(xa, rg_conv_w, rg_conv_b),
                                 rg_w_r, rg_b_r, rg_w_i, rg_b_i, rg_lambda)
    yb = mlstm_block(qk, v, o, i_pre, f_pre, ml_conv_w, ml_conv_b, ml_b_i, ml_b_f, ml_norm)
    return jnp.concatenate([ya, yb], axis=-1) @ w_out

def compress_blocks(kv, pe, w1, b1, w2):
    bsz, s, g, dk = kv.shape
    nb = (s - CMP_BLOCK) // CMP_STRIDE + 1
    idx = np.arange(nb)[:, None] * CMP_STRIDE + np.arange(CMP_BLOCK)[None, :]
    blk = kv[:, idx] + pe[:, None, :]
    blk = blk.transpose(0, 1, 3, 2, 4).reshape(bsz, nb, g, CMP_BLOCK * dk)
    return jax.nn.gelu(blk @ w1 + b1) @ w2

def cmp_to_sel_matrix(n_cmp, n_sel):
    cs = np.arange(n_cmp)[:, None] * CMP_STRIDE
    ss = np.arange(n_sel)[None, :] * SEL_BLOCK
    ov = np.clip(np.minimum(cs + CMP_BLOCK, ss + SEL_BLOCK) - np.maximum(cs, ss), 0, None)
    return jnp.asarray(ov / CMP_BLOCK, dtype=jnp.float32)

def nsa_mixer(xn, w_in, pe_k, k_w1, k_b1, k_w2, pe_v, v_w1, v_b1, v_w2, b_gate, w_out):
    bsz, s, _ = xn.shape
    g, r, dk = NSA_GROUPS, NSA_HEADS // NSA_GROUPS, NSA_HEAD_DIM
    proj = xn @ w_in
    cuts = list(np.cumsum([NSA_WIDTH] + [NSA_KV] * 6))
    q, kc, vc, ks, vs, kw, vw, gates = jnp.split(proj, cuts, axis=-1)
    q = q.reshape(bsz, s, g, r, dk) * (dk ** -0.5)
    kvh = lambda t: t.reshape(bsz, s, g, dk)
    kc = compress_blocks(kvh(kc), pe_k, k_w1, k_b1, k_w2)
    vc = compress_blocks(kvh(vc), pe_v, v_w1, v_b1, v_w2)
    n_cmp = kc.shape[1]
    n_sel = s // SEL_BLOCK
    top_n = min(SEL_TOPN, n_sel)
    m_sel = cmp_to_sel_matrix(n_cmp, n_sel)
    cmp_end = jnp.arange(n_cmp) * CMP_STRIDE + CMP_BLOCK - 1
    sel_blk = jnp.arange(n_sel)
    ks = kvh(ks).transpose(0, 2, 1, 3)
    vs = kvh(vs).transpose(0, 2, 1, 3)
    pad = jnp.zeros((bsz, WINDOW, g, dk), xn.dtype)
    kw = jnp.concatenate([pad, kvh(kw)], axis=1)
    vw = jnp.concatenate([pad, kvh(vw)], axis=1)
    gates = jax.nn.sigmoid(gates.reshape(bsz, s, g, r, NSA_BRANCHES) + b_gate.reshape(g, r, NSA_BRANCHES))

    def query_block(s0):
        t = s0 + jnp.arange(NSA_QBLOCK)
        qb = lax.dynamic_slice_in_dim(q, s0, NSA_QBLOCK, axis=1)
        gb = lax.dynamic_slice_in_dim(gates, s0, NSA_QBLOCK, axis=1)
        sc = jnp.einsum('bqgrd,bngd->bgrqn', qb, kc)
        p_cmp = masked_softmax(sc, cmp_end[None, :] <= t[:, None])
        o_cmp = jnp.einsum('bgrqn,bngd->bqgrd', p_cmp.astype(vc.dtype), vc)
        score = jnp.einsum('bgqn,nj->bgqj', jnp.sum(p_cmp, axis=2), m_sel)
        cur = (t // SEL_BLOCK)[:, None]
        valid = sel_blk[None, :] * SEL_BLOCK <= t[:, None]
        forced = (sel_blk[None, :] == 0) | (sel_blk[None, :] == cur) | (sel_blk[None, :] == cur - 1)
        score = jnp.where(forced & valid, FORCED_SCORE, jnp.where(valid, score, -1.0))
        _, idx = lax.top_k(score, top_n)
        key_idx = (idx[..., None] * SEL_BLOCK + jnp.arange(SEL_BLOCK)).reshape(bsz, g, -1)
        n_keys = top_n * SEL_BLOCK
        k_sel = jnp.take_along_axis(ks, key_idx[..., None], axis=2).reshape(bsz, g, NSA_QBLOCK, n_keys, dk)
        v_sel = jnp.take_along_axis(vs, key_idx[..., None], axis=2).reshape(bsz, g, NSA_QBLOCK, n_keys, dk)
        ss = jnp.einsum('bqgrd,bgqkd->bgrqk', qb, k_sel)
        sel_mask = key_idx.reshape(bsz, g, 1, NSA_QBLOCK, n_keys) <= t[:, None]
        p_slc = masked_softmax(ss, sel_mask)
        o_slc = jnp.einsum('bgrqk,bgqkd->bqgrd', p_slc.astype(v_sel.dtype), v_sel)
        k_win = lax.dynamic_slice_in_dim(kw, s0, WINDOW + NSA_QBLOCK, axis=1)
        v_win = lax.dynamic_slice_in_dim(vw, s0, WINDOW + NSA_QBLOCK, axis=1)
        pos = s0 - WINDOW + jnp.arange(WINDOW + NSA_QBLOCK)
        win_mask = (pos[None, :] <= t[:, None]) & (pos[None, :] > t[:, None] - WINDOW) & (pos[None, :] >= 0)
        sw = jnp.einsum('bqgrd,bkgd->bgrqk', qb, k_win)
        p_win = masked_softmax(sw, win_mask)
        o_win = jnp.einsum('bgrqk,bkgd->bqgrd', p_win.astype(v_win.dtype), v_win)
        out = gb[..., 0:1] * o_cmp + gb[..., 1:2] * o_slc + gb[..., 2:3] * o_win
        return out.reshape(bsz, NSA_QBLOCK, NSA_WIDTH)

    starts = jnp.arange(s // NSA_QBLOCK) * NSA_QBLOCK
    out = lax.map(query_block, starts)
    out = out.transpose(1, 0, 2, 3).reshape(bsz, s, NSA_WIDTH)
    return out @ w_out

def first_inputs(seed: int = 0) -> dict:
    key = jax.random.key(seed)
    keys = iter(jax.random.split(key, 40))
    nrm = lambda shape, scale: scale * jax.random.normal(next(keys), shape, jnp.float32)
    gain = lambda shape: 1.0 + 0.05 * jax.random.normal(next(keys), shape, jnp.float32)
    a8 = jax.random.uniform(next(keys), (N_EVEN, D_RG), jnp.float32, 0.9, 0.999)
    a0 = a8 ** (1.0 / RG_C)
    rg_lambda = jnp.log(a0) - jnp.log1p(-a0)
    ml_b_f = jnp.linspace(3.0, 6.0, ML_HEADS, dtype=jnp.float32)[None, :] + nrm((N_EVEN, ML_HEADS), 0.1)
    flat = CMP_BLOCK * NSA_HEAD_DIM
    return {
        "x": nrm((BATCH, SEQ, D_MODEL), 1.0),
        "ffn1_norm": gain((DEPTH, D_MODEL)),
        "ffn1_w_gu": nrm((DEPTH, D_MODEL, 2 * D_FF), D_MODEL ** -0.5),
        "ffn1_w_down": nrm((DEPTH, D_FF, D_MODEL), D_FF ** -0.5),
        "mix_norm": gain((DEPTH, D_MODEL)),
        "ffn2_norm": gain((DEPTH, D_MODEL)),
        "ffn2_w_gu": nrm((DEPTH, D_MODEL, 2 * D_FF), D_MODEL ** -0.5),
        "ffn2_w_down": nrm((DEPTH, D_FF, D_MODEL), D_FF ** -0.5),
        "ab_w_in": nrm((N_EVEN, D_MODEL, D_AB_IN), D_MODEL ** -0.5),
        "rg_conv_w": nrm((N_EVEN, CONV_WIDTH, D_RG), CONV_WIDTH ** -0.5),
        "rg_conv_b": nrm((N_EVEN, D_RG), 0.02),
        "rg_w_r": nrm((N_EVEN, RG_BLOCKS, D_RG // RG_BLOCKS, D_RG // RG_BLOCKS), (D_RG // RG_BLOCKS) ** -0.5),
        "rg_b_r": nrm((N_EVEN, D_RG), 0.02),
        "rg_w_i": nrm((N_EVEN, RG_BLOCKS, D_RG // RG_BLOCKS, D_RG // RG_BLOCKS), (D_RG // RG_BLOCKS) ** -0.5),
        "rg_b_i": nrm((N_EVEN, D_RG), 0.02),
        "rg_lambda": rg_lambda,
        "ml_conv_w": nrm((N_EVEN, CONV_WIDTH, 2 * D_ML), CONV_WIDTH ** -0.5),
        "ml_conv_b": nrm((N_EVEN, 2 * D_ML), 0.02),
        "ml_b_i": nrm((N_EVEN, ML_HEADS), 0.1),
        "ml_b_f": ml_b_f,
        "ml_norm": gain((N_EVEN, D_ML)),
        "ab_w_out": nrm((N_EVEN, D_RG + D_ML, D_MODEL), (D_RG + D_ML) ** -0.5),
        "nsa_w_in": nrm((N_ODD, D_MODEL, D_NSA_IN), D_MODEL ** -0.5),
        "nsa_pe_k": nrm((N_ODD, CMP_BLOCK, NSA_HEAD_DIM), 0.1),
        "nsa_k_w1": nrm((N_ODD, flat, CMP_HIDDEN), flat ** -0.5),
        "nsa_k_b1": nrm((N_ODD, CMP_HIDDEN), 0.02),
        "nsa_k_w2": nrm((N_ODD, CMP_HIDDEN, NSA_HEAD_DIM), CMP_HIDDEN ** -0.5),
        "nsa_pe_v": nrm((N_ODD, CMP_BLOCK, NSA_HEAD_DIM), 0.1),
        "nsa_v_w1": nrm((N_ODD, flat, CMP_HIDDEN), flat ** -0.5),
        "nsa_v_b1": nrm((N_ODD, CMP_HIDDEN), 0.02),
        "nsa_v_w2": nrm((N_ODD, CMP_HIDDEN, NSA_HEAD_DIM), CMP_HIDDEN ** -0.5),
        "nsa_b_gate": nrm((N_ODD, NSA_BRANCHES * NSA_HEADS), 0.1),
        "nsa_w_out": nrm((N_ODD, NSA_WIDTH, D_MODEL), NSA_WIDTH ** -0.5),
        "final_norm": gain((D_MODEL,)),
    }

def first_block(x, ffn1_norm, ffn1_w_gu, ffn1_w_down, mix_norm, ffn2_norm, ffn2_w_gu, ffn2_w_down,
              ab_w_in, rg_conv_w, rg_conv_b, rg_w_r, rg_b_r, rg_w_i, rg_b_i, rg_lambda,
              ml_conv_w, ml_conv_b, ml_b_i, ml_b_f, ml_norm, ab_w_out,
              nsa_w_in, nsa_pe_k, nsa_k_w1, nsa_k_b1, nsa_k_w2, nsa_pe_v, nsa_v_w1, nsa_v_b1, nsa_v_w2,
              nsa_b_gate, nsa_w_out, final_norm):
    for i in range(DEPTH):
        j = i // 2
        x = x + 0.5 * swiglu_ffn(rmsnorm(x, ffn1_norm[i]), ffn1_w_gu[i], ffn1_w_down[i])
        xn = rmsnorm(x, mix_norm[i])
        if i % 2 == 0:
            x = x + ab_mixer(xn, ab_w_in[j], rg_conv_w[j], rg_conv_b[j], rg_w_r[j], rg_b_r[j],
                             rg_w_i[j], rg_b_i[j], rg_lambda[j], ml_conv_w[j], ml_conv_b[j],
                             ml_b_i[j], ml_b_f[j], ml_norm[j], ab_w_out[j])
        else:
            x = x + nsa_mixer(xn, nsa_w_in[j], nsa_pe_k[j], nsa_k_w1[j], nsa_k_b1[j], nsa_k_w2[j],
                              nsa_pe_v[j], nsa_v_w1[j], nsa_v_b1[j], nsa_v_w2[j], nsa_b_gate[j], nsa_w_out[j])
        x = x + 0.5 * swiglu_ffn(rmsnorm(x, ffn2_norm[i]), ffn2_w_gu[i], ffn2_w_down[i])
    return rmsnorm(x, final_norm)


DEPTH_2 = 1

CTX_LEN = 256
GRID_W = 64

POOL_WINDOWS = (2, 4, 8, 16)
POOL_WIDTH = D_MODEL // 2
POOL_GROUP = POOL_WIDTH // len(POOL_WINDOWS)

RET_HEADS = 4
RET_DK = 128
RET_DV = 256
RET_CHUNK = 128
ROPE_BASE = 10000.0
QK_WIDTH = RET_HEADS * RET_DK
V_WIDTH = RET_HEADS * RET_DV

OFF_POOL = 0
OFF_Q = OFF_POOL + POOL_WIDTH
OFF_K = OFF_Q + QK_WIDTH
OFF_V = OFF_K + QK_WIDTH
OFF_G = OFF_V + V_WIDTH
OFF_MERGE = OFF_G + V_WIDTH
IN_WIDTH = OFF_MERGE + 2 * D_MODEL

PEER_HEADS = 8
PEER_NKEYS = 128
PEER_EXPERTS = PEER_NKEYS * PEER_NKEYS
PEER_TOPK = 16
PEER_DQ = 256
PEER_BLOCK = 128


def rmsnorm_2(x, g):
    xf = x.astype(jnp.float32)
    y = xf * lax.rsqrt(jnp.mean(xf * xf, axis=-1, keepdims=True) + EPS)
    return (y * g.astype(jnp.float32)).astype(x.dtype)

def modulate(h, shift, scale):
    return h * (1.0 + scale) + shift

def heads(a, d):
    b, l, _ = a.shape
    return a.reshape(b, l, -1, d).transpose(0, 2, 1, 3)

def axial_rope(a, row, col):
    quarter = a.shape[-1] // 4
    inv = ROPE_BASE ** (-jnp.arange(quarter, dtype=jnp.float32) / quarter)
    ang = jnp.concatenate([row[:, None] * inv, col[:, None] * inv], axis=-1)
    cos, sin = jnp.cos(ang), jnp.sin(ang)
    a1, a2 = jnp.split(a, 2, axis=-1)
    return jnp.concatenate([a1 * cos - a2 * sin, a1 * sin + a2 * cos], axis=-1).astype(a.dtype)

def multiscale_pool(p, pool_w, pool_scale):
    L = p.shape[1]
    pf = p.astype(jnp.float32)
    cs = jnp.pad(jnp.cumsum(pf, axis=1), ((0, 0), (1, 0), (0, 0)))
    t = jnp.arange(L)
    groups = []
    for gi, w in enumerate(POOL_WINDOWS):
        lo = jnp.clip(t - w // 2, 0, L)
        hi = jnp.clip(t + w - w // 2, 0, L)
        sl = slice(gi * POOL_GROUP, (gi + 1) * POOL_GROUP)
        win_sum = cs[:, hi, sl] - cs[:, lo, sl]
        cnt = (hi - lo).astype(jnp.float32)[None, :, None]
        groups.append(win_sum / cnt - pf[:, :, sl])
    d = jnp.stack(groups, axis=2).astype(p.dtype)
    mixed = jnp.einsum('blgc,gcd->blgd', d, pool_w).reshape(p.shape)
    return mixed * pool_scale

def retention_scan(q, k, v, log_gamma, s0, strict):
    b, h, L, _ = q.shape
    dv = v.shape[-1]
    C = RET_CHUNK
    n = L // C

    def chunks(a):
        return a.reshape(b, h, n, C, a.shape[-1]).transpose(2, 0, 1, 3, 4)

    idx = jnp.arange(C, dtype=jnp.float32)
    rel = idx[:, None] - idx[None, :]
    mask = (rel > 0) if strict else (rel >= 0)
    lg = log_gamma[:, None, None]
    intra = jnp.where(mask, jnp.exp(lg * jnp.where(mask, rel, 0.0)), 0.0)
    q_dec = jnp.exp(log_gamma[:, None] * (idx + 1.0))[..., None]
    k_dec = jnp.exp(log_gamma[:, None] * (C - 1.0 - idx))[..., None]
    blk_dec = jnp.exp(log_gamma * C)[:, None, None]

    def step(s, qkv):
        qi, ki, vi = qkv
        scores = jnp.einsum('bhnd,bhmd->bhnm', qi, ki) * intra
        y = (jnp.einsum('bhnm,bhme->bhne', scores, vi)
             + jnp.einsum('bhnd,bhde->bhne', qi * q_dec, s))
        s = s * blk_dec + jnp.einsum('bhmd,bhme->bhde', ki * k_dec, vi)
        return s, y

    _, ys = lax.scan(step, s0, (chunks(q), chunks(k), chunks(v)))
    return ys.transpose(1, 2, 0, 3, 4).reshape(b, h, L, dv)

def context_states(kc, vc, lg):
    Lc = kc.shape[2]
    m = jnp.arange(Lc, dtype=jnp.float32)
    w_f = jnp.exp(lg[0][:, None] * (Lc - 1.0 - m))
    w_b = jnp.exp(lg[1][:, None] * m)
    kf = kc.astype(jnp.float32)
    vf = vc.astype(jnp.float32)
    s_f = jnp.einsum('hm,bhmd,bhme->bhde', w_f, kf, vf)
    s_b = jnp.einsum('hm,bhmd,bhme->bhde', w_b, kf, vf)
    return s_f, s_b

def bidir_retention(q, k, v, lg, s_f, s_b):
    y_f = retention_scan(q, k, v, lg[0], s_f, False)
    y_b = retention_scan(jnp.flip(q, 2), jnp.flip(k, 2), jnp.flip(v, 2), lg[1], s_b, True)
    return y_f + jnp.flip(y_b, 2)

def retention_out(y, gate, norm_g, w_o):
    b, h, L, dv = y.shape
    yf = y.astype(jnp.float32)
    mu = jnp.mean(yf, axis=-1, keepdims=True)
    var = jnp.mean(jnp.square(yf - mu), axis=-1, keepdims=True)
    yn = ((yf - mu) * lax.rsqrt(var + EPS)).transpose(0, 2, 1, 3).reshape(b, L, h * dv)
    yn = (yn * norm_g.astype(jnp.float32)).astype(gate.dtype)
    return (yn * jax.nn.silu(gate)) @ w_o

def mix_tokens(proj, y_ret, lp):
    pool = multiscale_pool(proj[..., OFF_POOL:OFF_Q], lp['pool_w'], lp['pool_scale']) @ lp['pool_out']
    ret = retention_out(y_ret, proj[..., OFF_G:OFF_MERGE], lp['ret_norm_g'], lp['ret_out'])
    g_pool, g_ret = jnp.split(proj[..., OFF_MERGE:], 2, axis=-1)
    merged = jax.nn.sigmoid(g_pool) * pool + jax.nn.sigmoid(g_ret) * ret
    return merged @ lp['w_out']

def peer_ffn(h, wq, keys, u, v):
    b, L, d = h.shape
    blocks = h.reshape(-1, PEER_BLOCK, d)

    def one_block(hb):
        t = hb.shape[0]
        q = (hb @ wq).reshape(t, PEER_HEADS, 2, PEER_DQ // 2)
        s = jnp.einsum('thpd,hpkd->thpk', q, keys).astype(jnp.float32)
        s1, i1 = lax.top_k(s[:, :, 0], PEER_TOPK)
        s2, i2 = lax.top_k(s[:, :, 1], PEER_TOPK)
        cand = (s1[..., :, None] + s2[..., None, :]).reshape(t, PEER_HEADS, PEER_TOPK * PEER_TOPK)
        cidx = (i1[..., :, None] * PEER_NKEYS + i2[..., None, :]).reshape(t, PEER_HEADS, PEER_TOPK * PEER_TOPK)
        best, pos = lax.top_k(cand, PEER_TOPK)
        eidx = jnp.take_along_axis(cidx, pos, axis=-1)
        g = jax.nn.softmax(best, axis=-1)
        act = jax.nn.gelu(jnp.einsum('thkd,td->thk', u[eidx], hb).astype(jnp.float32), approximate=False)
        return jnp.einsum('thk,thkd->td', (g * act).astype(hb.dtype), v[eidx])

    return lax.map(one_block, blocks).reshape(b, L, d)

def trunk_layer(x, ctx, c, c_ctx, lp, update_ctx):
    b, L, d = x.shape
    mod = jax.nn.silu(c) @ lp['ada_w'] + lp['ada_b']
    mod_c = jax.nn.silu(c_ctx) @ lp['ada_w'] + lp['ada_b']
    sh1, sc1, g1, sh2, sc2, g2 = jnp.split(mod[:, None, :], 6, axis=-1)
    csh1, csc1, cg1, csh2, csc2, cg2 = jnp.split(mod_c, 6, axis=-1)
    lg = jax.nn.log_sigmoid(lp['ret_decay'].astype(jnp.float32))
    k_scale = RET_DK ** -0.5

    rows = L // GRID_W
    row = jnp.repeat(jnp.arange(rows, dtype=jnp.float32), GRID_W)
    col = jnp.tile(jnp.arange(GRID_W, dtype=jnp.float32), rows)

    hc = modulate(rmsnorm_2(ctx, lp['norm_mix_g']), csh1, csc1)
    if update_ctx:
        projc = hc @ lp['w_in']
        kv_c = projc[..., OFF_K:OFF_G]
    else:
        kv_c = hc @ lp['w_in'][:, OFF_K:OFF_G]
    kc = heads(kv_c[..., :QK_WIDTH], RET_DK) * k_scale
    vc = heads(kv_c[..., QK_WIDTH:], RET_DV)
    s_f, s_b = context_states(kc, vc, lg)

    h = modulate(rmsnorm_2(x, lp['norm_mix_g']), sh1, sc1)
    proj = h @ lp['w_in']
    q = axial_rope(heads(proj[..., OFF_Q:OFF_K], RET_DK), row, col)
    k = axial_rope(heads(proj[..., OFF_K:OFF_V], RET_DK), row, col) * k_scale
    v = heads(proj[..., OFF_V:OFF_G], RET_DV)
    y = bidir_retention(q, k, v, lg, s_f, s_b)
    x = x + g1 * mix_tokens(proj, y, lp)

    hf = modulate(rmsnorm_2(x, lp['norm_ffn_g']), sh2, sc2)
    x = x + g2 * peer_ffn(hf, lp['peer_wq'], lp['peer_keys'], lp['peer_u'], lp['peer_v'])

    if update_ctx:
        qc = heads(projc[..., OFF_Q:OFF_K], RET_DK)
        zero = jnp.zeros_like(s_f)
        yc = bidir_retention(qc, kc, vc, lg, zero, zero)
        ctx = ctx + cg1 * mix_tokens(projc, yc, lp)
        hcf = modulate(rmsnorm_2(ctx, lp['norm_ffn_g']), csh2, csc2)
        ctx = ctx + cg2 * peer_ffn(hcf, lp['peer_wq'], lp['peer_keys'], lp['peer_u'], lp['peer_v'])
    return x, ctx

def second_inputs(seed: int = 0) -> dict:
    key = jax.random.key(seed)
    ks = jax.random.split(key, 24)
    f32 = jnp.float32
    D = D_MODEL

    def nrm(k, shape, s):
        return jax.random.normal(k, shape, f32) * s

    base_logit = jnp.log(2.0 ** (5.0 + jnp.arange(RET_HEADS, dtype=f32)) - 1.0)
    return {
        'x': nrm(ks[0], (BATCH, SEQ, D), 1.0),
        'c': nrm(ks[1], (BATCH, D), 1.0),
        'ctx': nrm(ks[2], (BATCH, CTX_LEN, D), 1.0),
        'c_ctx': nrm(ks[3], (D,), 1.0),
        'ada_w': nrm(ks[4], (DEPTH_2, D, 6 * D), 0.5 * D ** -0.5),
        'ada_b': nrm(ks[5], (DEPTH_2, 6 * D), 0.02),
        'norm_mix_g': 1.0 + nrm(ks[6], (DEPTH_2, D), 0.02),
        'norm_ffn_g': 1.0 + nrm(ks[7], (DEPTH_2, D), 0.02),
        'w_in': nrm(ks[8], (DEPTH_2, D, IN_WIDTH), D ** -0.5),
        'pool_w': nrm(ks[9], (DEPTH_2, len(POOL_WINDOWS), POOL_GROUP, POOL_GROUP), POOL_GROUP ** -0.5),
        'pool_scale': 1.0 + nrm(ks[10], (DEPTH_2, POOL_WIDTH), 0.1),
        'pool_out': nrm(ks[11], (DEPTH_2, POOL_WIDTH, D), POOL_WIDTH ** -0.5),
        'ret_decay': base_logit[None, None, :] + nrm(ks[12], (DEPTH_2, 2, RET_HEADS), 0.1),
        'ret_norm_g': 1.0 + nrm(ks[13], (DEPTH_2, V_WIDTH), 0.02),
        'ret_out': nrm(ks[14], (DEPTH_2, V_WIDTH, D), V_WIDTH ** -0.5),
        'w_out': nrm(ks[15], (DEPTH_2, D, D), D ** -0.5),
        'peer_wq': nrm(ks[16], (DEPTH_2, D, PEER_HEADS * PEER_DQ), D ** -0.5),
        'peer_keys': nrm(ks[17], (DEPTH_2, PEER_HEADS, 2, PEER_NKEYS, PEER_DQ // 2), (PEER_DQ // 2) ** -0.5),
        'peer_u': nrm(ks[18], (DEPTH_2, PEER_EXPERTS, D), D ** -0.5),
        'peer_v': nrm(ks[19], (DEPTH_2, PEER_EXPERTS, D), 0.5),
        'final_g': 1.0 + nrm(ks[20], (D,), 0.02),
    }

def second_block(x, c, ctx, c_ctx, ada_w, ada_b, norm_mix_g, norm_ffn_g, w_in, pool_w,
              pool_scale, pool_out, ret_decay, ret_norm_g, ret_out, w_out, peer_wq,
              peer_keys, peer_u, peer_v, final_g):
    for layer in range(DEPTH_2):
        lp = {
            'ada_w': ada_w[layer], 'ada_b': ada_b[layer],
            'norm_mix_g': norm_mix_g[layer], 'norm_ffn_g': norm_ffn_g[layer],
            'w_in': w_in[layer], 'pool_w': pool_w[layer], 'pool_scale': pool_scale[layer],
            'pool_out': pool_out[layer], 'ret_decay': ret_decay[layer],
            'ret_norm_g': ret_norm_g[layer], 'ret_out': ret_out[layer], 'w_out': w_out[layer],
            'peer_wq': peer_wq[layer], 'peer_keys': peer_keys[layer],
            'peer_u': peer_u[layer], 'peer_v': peer_v[layer],
        }
        x, ctx = trunk_layer(x, ctx, c, c_ctx, lp, layer + 1 < DEPTH_2)
    return rmsnorm_2(x, final_g)


def setup_inputs(seed=0):
    out = dict(first_inputs(seed))
    for name, value in second_inputs(seed + 1).items():
        if name != "x":
            out[name + "_2"] = value
    return out


def reference(
    x, ffn1_norm, ffn1_w_gu, ffn1_w_down, mix_norm, ffn2_norm, ffn2_w_gu, ffn2_w_down, ab_w_in,
    rg_conv_w, rg_conv_b, rg_w_r, rg_b_r, rg_w_i, rg_b_i, rg_lambda, ml_conv_w, ml_conv_b,
    ml_b_i, ml_b_f, ml_norm, ab_w_out, nsa_w_in, nsa_pe_k, nsa_k_w1, nsa_k_b1, nsa_k_w2,
    nsa_pe_v, nsa_v_w1, nsa_v_b1, nsa_v_w2, nsa_b_gate, nsa_w_out, final_norm, c_2, ctx_2,
    c_ctx_2, ada_w_2, ada_b_2, norm_mix_g_2, norm_ffn_g_2, w_in_2, pool_w_2, pool_scale_2,
    pool_out_2, ret_decay_2, ret_norm_g_2, ret_out_2, w_out_2, peer_wq_2, peer_keys_2, peer_u_2,
    peer_v_2, final_g_2,
):
    x = first_block(
        x, ffn1_norm, ffn1_w_gu, ffn1_w_down, mix_norm, ffn2_norm, ffn2_w_gu, ffn2_w_down,
        ab_w_in, rg_conv_w, rg_conv_b, rg_w_r, rg_b_r, rg_w_i, rg_b_i, rg_lambda, ml_conv_w,
        ml_conv_b, ml_b_i, ml_b_f, ml_norm, ab_w_out, nsa_w_in, nsa_pe_k, nsa_k_w1, nsa_k_b1,
        nsa_k_w2, nsa_pe_v, nsa_v_w1, nsa_v_b1, nsa_v_w2, nsa_b_gate, nsa_w_out, final_norm,
    )
    return second_block(
        x, c_2, ctx_2, c_ctx_2, ada_w_2, ada_b_2, norm_mix_g_2, norm_ffn_g_2, w_in_2, pool_w_2,
        pool_scale_2, pool_out_2, ret_decay_2, ret_norm_g_2, ret_out_2, w_out_2, peer_wq_2,
        peer_keys_2, peer_u_2, peer_v_2, final_g_2,
    )


_drawn_inputs = setup_inputs


def setup_inputs(seed=0):
    import zlib

    import numpy as np

    out = dict(_drawn_inputs(seed))
    spreads = {}
    factors = {'rg_b_r': 27.541,
     'rg_b_i': 8.0,
     'ml_conv_b': 5.144,
     'ml_b_i': 64.0,
     'nsa_pe_k': 8.0,
     'nsa_k_b1': 39.263,
     'nsa_v_b1': 7.943,
     'nsa_b_gate': 4.309,
     'norm_mix_g_2': 7.103,
     'norm_ffn_g_2': 36.376,
     'pool_scale_2': 3.134,
     'ret_norm_g_2': 24.036,
     'final_g_2': 7.757}
    for name, (base, spread) in spreads.items():
        noise = np.random.default_rng([zlib.crc32(name.encode()), seed]).standard_normal(out[name].shape)
        drawn = base * np.exp(spread * noise) if base else spread * noise
        out[name] = __import__('jax').numpy.asarray(drawn.astype(out[name].dtype))
    for name, factor in factors.items():
        out[name] = (out[name] * factor).astype(out[name].dtype)
    return out
```

```python
import concourse.bass as bass
from concourse import mybir
import numpy as np
from contextlib import ExitStack

F32 = mybir.dt.float32
U32 = mybir.dt.uint32
ALU = mybir.AluOpType
ACT = mybir.ActivationFunctionType
AX = mybir.AxisListType

P = 128
T = 256
TT = T // P
D = 1024
KD = D // P
EPS = 1e-6
NEG = -1e30
D_FF = 2816
FFN_GROUPS = D_FF // 256
TILE = 2048
GROUP = 3 * TILE
RING = 4
RG_CHUNKS = 4
CONV = 4
ML_HEADS, ML_DH = 4, 128
NSA_HEADS, NSA_GROUPS, NSA_DH = 16, 4, 64
CMP_BLOCK, CMP_STRIDE = 32, 16
N_CMP = (T - CMP_BLOCK) // CMP_STRIDE + 1
RET_HEADS, RET_DK, RET_DV = 4, 128, 256
PEER_HEADS, PEER_KEYS, PEER_TOPK = 8, 128, 16
XSLOTS = 4

G_FFN1A = 0
G_AB = G_FFN1A + FFN_GROUPS
G_FFN2A = G_AB + 6
G_FFN1B = G_FFN2A + FFN_GROUPS
G_NSA = G_FFN1B + FFN_GROUPS
G_FFN2B = G_NSA + 7
G_SECOND = G_FFN2B + FFN_GROUPS
G_PEER = G_SECOND + 19
N_GROUPS = G_SECOND + 22


class Signal:

    def __init__(self, sem):
        self.sem, self.base = sem, 0

    def at(self, n):
        return self.sem, n + self.base


class Chain:

    def __init__(self, eng, signal):
        self.eng, self.counter = eng, signal

    def __call__(self, ins):
        self.counter.base += 1
        ins.then_inc(self.counter.sem, 1)
        self.eng.wait_ge(self.counter.sem, self.counter.base)


class Arena:

    def __init__(self, nc, tag, start, end):
        self.nc, self.tag, self.at, self.end = nc, tag, start, end

    def __call__(self, name, cols, parts=P, dt=F32):
        size = (cols * 4 + 31) // 32 * 32
        t = self.nc.alloc_sbuf_tensor_at(f"{self.tag}_{name}", [parts, cols], dt, offset=self.at)
        self.at += size
        assert self.at <= self.end, (self.tag, name, self.at, self.end)
        return t[:, :]


def sbuf_plan(nc):
    base = (nc.sbuf_base + 31) // 32 * 32
    end = nc.sbuf_usable_end // 32 * 32
    ring_end = base + RING * GROUP * 4
    keep = end - (2 * 8192 + 3200)
    return base, ring_end, keep, end


class Kernel:
    def __init__(self, nc, dram, out, stages):
        self.nc, self.dram, self.out, self.stages = nc, dram, out, stages
        self.ctx = ExitStack()
        self.base, self.ring_end, self.keep, self.end = sbuf_plan(nc)
        ring = nc.alloc_sbuf_tensor_at("ring", [P, RING * GROUP], F32, offset=self.base)
        self.ring = ring[:, :]
        keep = Arena(nc, "keep", self.keep, self.end)
        self.x = keep("x", TT * D).rearrange("p (t d) -> p t d", t=TT)
        self.xT = keep("xT", KD * T).rearrange("p (k t) -> p k t", k=KD)
        self.ident = keep("ident", P)
        self.gains = keep("gains", 8 * KD).rearrange("p (n k) -> p n k", n=8)
        self.stat = keep("stat", 64)
        self.modT = keep("modT", 48 * 2).rearrange("p (c s) -> p c s", s=2)
        self.gA = keep("gA", 4 * KD).rearrange("p (n k) -> p n k", n=4)
        self.psum = [self.ctx.enter_context(nc.psum_tensor(f"bank{i}", [P, 512], F32)) for i in range(8)]
        self.sems, self.own, self.keeping = {}, [], True
        self.next_load = 0
        self.groups = 0
        self.first_group = 0
        self.loaded = [self.counter(f"ring_loaded{s}") for s in range(RING)]
        self.released = self.counter("ring_released")
        self.act_chain = self.counter("act_chain")
        self.dve_chain = self.counter("dve_chain")
        self.keeping = False

    def counter(self, name):
        if name not in self.sems:
            if self.keeping or name.startswith(("nrm_", "ffn_", "add_", "fn_")):
                sem = self.ctx.enter_context(self.nc.semaphore(name))
            else:
                sem = self.nc.alloc_semaphore(name)
                self.own.append((name, sem))
            self.sems[name] = Signal(sem)
        return self.sems[name]

    def end_stage(self):
        for name, _ in self.own:
            self.sems.pop(name)
        self.nc.clear_and_free_semaphores([sem for _, sem in self.own])
        self.nc.all_engine_barrier()
        self.own = []

    def counters(self, *names):
        return [self.counter(n) for n in names]

    def arena(self, tag):
        return Arena(self.nc, tag, self.ring_end, self.keep)

    def slot_of(self, g):
        return (g - self.first_group) % RING

    def ring_part(self, g, j):
        at = self.slot_of(g) * GROUP + j * TILE
        return self.ring[:, at:at + TILE]

    def wait_group(self, pe, g, loop=0):
        n = g - self.first_group
        pe.wait_ge(self.loaded[n % RING].sem, 16 * (n // RING + 1) + loop)

    def sync_loads(self, sp, used_end):
        end = min(used_end + RING, self.first_group + self.groups)
        stream = self.dram["stream"]

        def load(g, value, index):
            slot = self.slot_of(g)
            if value is not None:
                sp.wait_ge(self.released.sem, value)
            sp.dma_start(self.ring[:, slot * GROUP:(slot + 1) * GROUP],
                         stream[bass.ds(index, 1)].rearrange("a p n -> p (a n)")
                         ).then_inc(self.loaded[slot].sem, 16)

        g = self.next_load
        while g < end:
            n = g - self.first_group
            turns = (end - g) // RING
            if n >= RING and turns >= 2:
                with sp.Fori(0, turns) as turn:
                    for s in range(RING):
                        load(g + s, turn * RING + (n + s - RING + 1), turn * RING + (g + s))
                g += turns * RING
            else:
                load(g, n - RING + 1 if n >= RING else None, g)
                g += 1
        self.next_load = end

    def norm_parts(self, src, outT, scale, bias, tag, work):
        nc, stat, ps = self.nc, self.stat, self.psum
        ss, rstd = stat[:, 0:TT], stat[:, TT:2 * TT]
        xs = work
        squared, mean, root, scaled, turned, evac = self.counters(
            "nrm_squared", "nrm_mean", "nrm_root", "nrm_scaled", "nrm_turned", "nrm_evac")

        def on_act(act):
            for t in range(TT):
                nc.scalar.activation(xs[:, t, :], src[:, t, :], ACT.Square,
                                     accum_out=ss[:, t:t + 1]).then_inc(squared.sem, 1)
            act.wait_ge(*mean.at(1))
            nc.scalar.activation(rstd, ss, ACT.Sqrt).then_inc(root.sem, 1)
            for k in (2, 3, 6, 7):
                act.wait_ge(*turned.at(k // 2 + 1))
                nc.scalar.activation(outT[:, k, :], ps[k // 2][:, (k % 2) * T:(k % 2 + 1) * T], ACT.Identity,
                                     scale=scale[:, k:k + 1],
                                     bias=bias[:, k:k + 1] if bias is not None else 0.0).then_inc(evac.sem, 1)

        def on_dve(dve):
            link = Chain(dve, self.dve_chain)
            dve.wait_ge(*squared.at(TT))
            nc.vector.tensor_scalar(ss, ss, 1.0 / D, EPS, ALU.mult, ALU.add).then_inc(mean.sem, 1)
            dve.wait_ge(*root.at(1))
            link(nc.vector.reciprocal(rstd, rstd))
            for t in range(TT):
                nc.vector.tensor_scalar(xs[:, t, :], src[:, t, :], rstd[:, t:t + 1], None,
                                        ALU.mult).then_inc(scaled.sem, 1)
            for k in (0, 1, 4, 5):
                dve.wait_ge(*turned.at(k // 2 + 1))
                if bias is not None:
                    nc.vector.tensor_scalar(outT[:, k, :], ps[k // 2][:, (k % 2) * T:(k % 2 + 1) * T], scale[:, k:k + 1],
                                            bias[:, k:k + 1], ALU.mult, ALU.add).then_inc(evac.sem, 1)
                else:
                    nc.vector.tensor_scalar(outT[:, k, :], ps[k // 2][:, (k % 2) * T:(k % 2 + 1) * T], scale[:, k:k + 1],
                                            None, ALU.mult).then_inc(evac.sem, 1)

        def on_pe(pe):
            pe.wait_ge(*scaled.at(TT))
            for b in range(KD // 2):
                for k in (2 * b, 2 * b + 1):
                    for t in range(TT):
                        last = nc.tensor.transpose(ps[b][:, (k % 2) * T + t * P:(k % 2) * T + (t + 1) * P],
                                                   xs[:, t, k * P:(k + 1) * P], self.ident)
                last.then_inc(turned.sem, 1)
            pe.wait_ge(*evac.at(KD))

        def end():
            squared.base += TT
            mean.base += 1
            root.base += 1
            scaled.base += TT
            turned.base += KD // 2
            evac.base += KD
        return on_act, on_dve, on_pe, end

    def start(self):
        nc = self.nc
        (here,) = self.counters("start_loaded")
        with nc.Block() as block:
            @block.sync
            def _(sp):
                sp.dma_start(self.x, self.dram["x"].rearrange("(t p) d -> p t d", p=P)).then_inc(here.sem, 16)
                sp.dma_start(self.ident, self.dram["ident"]).then_inc(here.sem, 16)
                sp.dma_start(self.gains, self.dram["gains"].rearrange("p (n k) -> p n k", k=KD)).then_inc(here.sem, 16)
                self.sync_loads(sp, self.first_group)
                sp.wait_ge(*here.at(48))
        here.base += 48

    def ffn(self, g0, gain):
        nc, ps = self.nc, self.psum
        work = self.arena(f"ffn{g0}")
        xs = work("xs", TT * D).rearrange("p (t d) -> p t d", t=TT)
        sg = [work(f"silu{t}", 256) for t in range(TT)]
        h = [work(f"h{t}", 256) for t in range(TT)]
        hT = [work(f"hT{t}", 256).rearrange("p (f t) -> p f t", f=2) for t in range(TT)]
        norm_act, norm_dve, norm_pe, norm_end = self.norm_parts(
            self.x, self.xT, self.gains[:, gain, :], None, f"ffn{g0}", xs)
        gu = self.counters("ffn_gu0", "ffn_gu1")
        silu = self.counters("ffn_silu0", "ffn_silu1")
        made = self.counters("ffn_h0", "ffn_h1")
        turned = self.counters("ffn_turned0", "ffn_turned1")
        hready = self.counters("ffn_hT0", "ffn_hT1")
        down0, acc = self.counters("ffn_down0", "ffn_acc")
        N = FFN_GROUPS
        rel0 = g0 - self.first_group

        with nc.Block() as block:
            @block.sync
            def _(sp):
                self.sync_loads(sp, g0 + N)

            @block.tensor
            def _(pe):
                norm_pe(pe)

                def gate_up(g, i, t, lo, hi):
                    for k in range(lo, hi):
                        w = self.ring_part(g, k // 4)[:, (k % 4) * 512:(k % 4 + 1) * 512]
                        last = nc.tensor.matmul(ps[t][:, :], self.xT[:, k, t * P:(t + 1) * P], w,
                                                start=k == 0, stop=k == KD - 1)
                    if hi == KD:
                        last.then_inc(gu[t].sem, 1)

                def turn(i, t, first=False):
                    pe.wait_ge(*made[t].at(i + 1))
                    if not first:
                        pe.wait_ge(*hready[t].at(i))
                    for f in range(2):
                        last = nc.tensor.transpose(ps[2 + t][:, f * P:(f + 1) * P],
                                                   h[t][:, f * P:(f + 1) * P], self.ident)
                    last.then_inc(turned[t].sem, 1)

                def down(g, i, t, start, stop):
                    pe.wait_ge(*hready[t].at(i + 1))
                    for f in range(2):
                        for half in range(2):
                            w = self.ring_part(g, 2)[:, f * 1024 + half * 512:f * 1024 + (half + 1) * 512]
                            last = nc.tensor.matmul(ps[4 + 2 * t + half][:, :], hT[t][:, f, :], w,
                                                    start=start and f == 0, stop=stop and f == 1)
                    if t == 0:
                        last.then_inc(down0.sem, 1)
                    else:
                        last.then_inc(self.released.sem, 1)

                def group(g, i, loaded, first=False, second=False, last=False):
                    self.wait_group(pe, g, loaded)
                    if not first:
                        pe.wait_ge(*made[0].at(i))
                    gate_up(g, i, 0, 0, 6)
                    if not first:
                        turn(i - 1, 1, first=second)
                    gate_up(g, i, 0, 6, KD)
                    if not first:
                        down(g - 1, i - 1, 1, second, False)
                    gate_up(g, i, 1, 0, 6)
                    turn(i, 0, first=first)
                    gate_up(g, i, 1, 6, KD)
                    down(g, i, 0, first, last)

                group(g0, 0, 0, first=True)
                group(g0 + 1, 1, 0, second=True)
                with pe.Fori(0, (N - 3) // RING) as turn_:
                    for s in range(RING):
                        group(g0 + 2 + s, turn_ * RING + (2 + s), turn_ * 16)
                group(g0 + N - 1, N - 1, 0, last=True)
                turn(N - 1, 1)
                down(g0 + N - 1, N - 1, 1, False, True)

            @block.scalar
            def _(act):
                norm_act(act)

                def step(i, first=False):
                    for t in range(TT):
                        act.wait_ge(*gu[t].at(i + 1))
                        if not first:
                            act.wait_ge(*made[t].at(i))
                        nc.scalar.activation(sg[t], ps[t][:, 0:256], ACT.Silu).then_inc(silu[t].sem, 1)

                step(0, first=True)
                with act.Fori(1, N) as i:
                    step(i)

            @block.vector
            def _(dve):
                norm_dve(dve)

                def step(i, first=False):
                    for t in range(TT):
                        dve.wait_ge(*silu[t].at(i + 1))
                        if not first:
                            dve.wait_ge(*turned[t].at(i))
                        nc.vector.tensor_tensor(h[t], sg[t], ps[t][:, 256:512], ALU.mult
                                                ).then_inc(made[t].sem, 1)
                        dve.wait_ge(*turned[t].at(i + 1))
                        if not first:
                            if t == 0:
                                dve.wait_ge(*down0.at(i))
                            else:
                                dve.wait_ge(self.released.sem, i + rel0)
                        nc.vector.tensor_copy(hT[t].rearrange("p f t -> p (f t)"), ps[2 + t][:, 0:256]
                                              ).then_inc(hready[t].sem, 1)

                step(0, first=True)
                with dve.Fori(1, N) as i:
                    step(i)
                dve.wait_ge(*down0.at(N))
                dve.wait_ge(self.released.sem, N + rel0)
                for t in range(TT):
                    for half in range(2):
                        xv = self.x[:, t, half * 512:(half + 1) * 512]
                        last = nc.vector.scalar_tensor_tensor(xv, ps[4 + 2 * t + half][:, :], 0.5, xv,
                                                              ALU.mult, ALU.add)
                last.then_inc(acc.sem, 1)
                dve.wait_ge(*acc.at(1))
        norm_end()
        for s in gu + silu + made + turned + hready + [down0]:
            s.base += N
        acc.base += 1

    def store(self, src):
        nc = self.nc
        (stored,) = self.counters("stored")
        with nc.Block() as block:
            @block.sync
            def _(sp):
                sp.dma_start(self.out[0].rearrange("(t p) d -> p t d", p=P), src).then_inc(stored.sem, 16)
                sp.wait_ge(*stored.at(16))
        stored.base += 16

    def ring_tile(self, pe, g0, t):
        g = g0 + t // 3
        if g not in self.waited:
            self.waited.add(g)
            self.wait_group(pe, g)
        return self.ring_part(g, t % 3)

    def mm(self, out, lhsT, rhs, start, stop):
        ins = self.nc.tensor.matmul(out, lhsT, rhs, start=start, stop=stop)
        if self.owed:
            self.owed -= 1
            ins.then_inc(self.released.sem, 1)
        return ins

    def give_back(self, t):
        if t % 3 == 2:
            self.owed += 1

    def flush(self, pe, done):
        pe.wait_ge(*done)
        while self.owed:
            self.owed -= 1
            pe.sem_inc(self.released.sem, 1)

    def stationary_cols(self, out, w, c, actT):
        for k in range(KD):
            last = self.mm(out, w[:, k * 256 + c * P:k * 256 + (c + 1) * P], actT[:, k, :], k == 0, k == KD - 1)
        return last

    def moving_cols(self, pe, out, g0, tile, actT, t):
        for k in range(KD):
            w = self.ring_tile(pe, g0, tile + k // 4)[:, (k % 4) * 512:(k % 4 + 1) * 512]
            last = self.mm(out, actT[:, k, t * P:(t + 1) * P], w, k == 0, k == KD - 1)
        return last

    def rows_product(self, pe, g0, tile, actT, kn, banks, done):
        for k in range(kn):
            w = self.ring_tile(pe, g0, tile + k // 2)
            for t in range(TT):
                for half in range(2):
                    at = (k % 2) * D + half * 512
                    last = self.mm(self.psum[banks[2 * t + half]][:, :], actT[:, k, t * P:(t + 1) * P],
                                   w[:, at:at + 512], k == 0, k == kn - 1)
            if k % 2 == 1:
                self.give_back(tile + k // 2)
        last.then_inc(done.sem, 1)

    def begin_stage(self):
        self.waited, self.owed = set(), 0

    def ab(self):
        nc, ps, G = self.nc, self.psum, G_AB
        v_, s_ = nc.vector, nc.scalar
        self.begin_stage()
        work = self.arena("ab")
        taps = work("taps", 60).rearrange("p (m k) -> p m k", k=5)
        cols = work("cols", 16).rearrange("p (n c) -> p n c", c=4)
        wif = work("wif", 64).rearrange("p (k f) -> p k f", f=8)
        bif = work("bif", 2, parts=4)
        mask = work("mask", 384)
        sel = work("sel", 512, parts=4)
        xs = work("xs", TT * D).rearrange("p (t d) -> p t d", t=TT)
        xa = work("xa", 4 * (T + 3)).rearrange("p (c t) -> p c t", c=4)
        qk = work("qk", 8 * (T + 3)).rearrange("p (c t) -> p c t", c=8)
        ga = work("ga", 4 * T).rearrange("p (c t) -> p c t", c=4)
        v1 = work("v1", TT * 4 * 129).rearrange("p (t h d) -> p t h d", t=TT, h=4)
        so = work("so", TT * 512).rearrange("p (t d) -> p t d", t=TT)
        xc = work("xc", 4 * T).rearrange("p (c t) -> p c t", c=4)
        qc = work("qc", 8 * T).rearrange("p (c t) -> p c t", c=8)
        r = work("r", 4 * T).rearrange("p (c t) -> p c t", c=4)
        ig = work("ig", 4 * T).rearrange("p (c t) -> p c t", c=4)
        a = work("a", 4 * T).rearrange("p (c t) -> p c t", c=4)
        u = work("u", 4 * T).rearrange("p (c t) -> p c t", c=4)
        row = [work(f"row{i}", T, parts=4) for i in range(7)]
        ir, fr, mn, ex, cumf, al, ones = row
        big = work("E", 4 * 384).rearrange("p (h n) -> p h n", h=4)
        tiny = work("tiny", 96)
        Hn = work("Hn", TT * 4 * 129).rearrange("p (t h d) -> p t h d", t=TT, h=4)
        yT = self.xT
        small, done, freed, conv, z = self.counters("ab_small", "ab_done", "ab_freed", "ab_conv", "ab_padded")
        norm_act, norm_dve, norm_pe, norm_end = self.norm_parts(
            self.x, self.xT, self.gains[:, 1, :], None, "ab", xs)

        with nc.Block() as block:
            @block.sync
            def _(sp):
                for dst, name in ((taps.rearrange("p m k -> p (m k)"), "ab_taps"), (cols.rearrange("p n c -> p (n c)"), "ab_cols"),
                                  (wif.rearrange("p k f -> p (k f)"), "ab_if"), (bif, "ab_b"),
                                  (mask, "ab_mask"), (sel, "ab_sel")):
                    sp.dma_start(dst, self.dram[name]).then_inc(small.sem, 16)
                self.sync_loads(sp, G + 4)

            @block.gpsimd
            def _(pool):
                nc.gpsimd.memset(xa[:, :, 0:3], 0.0).then_inc(z.sem, 1)
                nc.gpsimd.memset(qk[:, :, 0:3], 0.0).then_inc(z.sem, 1)
                nc.gpsimd.memset(v1[:, :, :, 128:129], 1.0).then_inc(z.sem, 1)
                nc.gpsimd.memset(ones, 1.0).then_inc(z.sem, 1)

            @block.tensor
            def _(pe):
                norm_pe(pe)
                for n in range(16):
                    if n >= 4:
                        pe.wait_ge(*freed.at(n - 3))
                    w = self.ring_tile(pe, G, n // 2)
                    self.stationary_cols(ps[n % 4][:, 0:T], w, n % 2, self.xT).then_inc(done.sem, 1)
                    if n % 2:
                        self.give_back(n // 2)
                for n in range(16, 20):
                    pe.wait_ge(*freed.at(n - 3))
                    tile = 8 + 2 * ((n - 16) // 2)
                    self.moving_cols(pe, ps[n % 4][:, :], G, tile, self.xT, n % 2).then_inc(done.sem, 1)
                    if n % 2:
                        self.give_back(tile)
                        self.give_back(tile + 1)
                pe.wait_ge(*freed.at(17))
                pe.wait_ge(*small.at(96))
                for f in range(2):
                    for k in range(KD):
                        last = self.mm(ps[0][0:4, f * T:(f + 1) * T], wif[:, k, 4 * f:4 * f + 4],
                                       self.xT[:, k, :], k == 0, k == KD - 1)
                last.then_inc(done.sem, 1)

            @block.scalar
            def _(act):
                norm_act(act)
                for n in range(20):
                    act.wait_ge(*done.at(n + 1))
                    src = ps[n % 4]
                    if n < 4:
                        ins = s_.activation(xa[:, n, 3:], src[:, 0:T], ACT.Copy)
                    elif n < 8:
                        ins = s_.activation(ga[:, n - 4, :], src[:, 0:T], ACT.Gelu_apprx_tanh)
                    elif n < 16:
                        ins = s_.activation(qk[:, n - 8, 3:], src[:, 0:T], ACT.Copy)
                    elif n < 18:
                        ins = s_.activation(v1[:, n - 16, :, 0:128], src[:, :].rearrange("p (h d) -> p h d", h=4), ACT.Copy)
                    else:
                        ins = s_.activation(so[:, n - 18, :], src[:, :], ACT.Sigmoid)
                    ins.then_inc(freed.sem, 1)
                act.wait_ge(*done.at(21))
                act.wait_ge(*small.at(96))
                s_.activation(ir, ps[0][0:4, 0:T], ACT.Identity, bias=bif[:, 0:1]).then_inc(freed.sem, 1)
                s_.activation(fr, ps[0][0:4, T:2 * T], ACT.Identity, bias=bif[:, 1:2]).then_inc(freed.sem, 1)
                for c in range(8):
                    act.wait_ge(*conv.at(5 + c))
                    s_.activation(qc[:, c, :], qc[:, c, :], ACT.Silu).then_inc(freed.sem, 1)

            @block.vector
            def _(dve):
                norm_dve(dve)
                link = Chain(dve, self.dve_chain)
                dve.wait_ge(*small.at(96))
                dve.wait_ge(*z.at(4))
                for m in range(12):
                    src, dst = (xa[:, m, :], xc[:, m, :]) if m < 4 else (qk[:, m - 4, :], qc[:, m - 4, :])
                    dve.wait_ge(*freed.at(m + 1 if m < 4 else m + 5))
                    link(v_.tensor_scalar(dst, src[:, 0:T], taps[:, m, 0:1], taps[:, m, 4:5], ALU.mult, ALU.add))
                    for j in range(1, CONV):
                        ins = v_.scalar_tensor_tensor(dst, src[:, j:j + T], taps[:, m, j:j + 1], dst, ALU.mult, ALU.add)
                        if j < CONV - 1:
                            link(ins)
                    ins.then_inc(conv.sem, 1)
        norm_end()
        done.base += 21
        freed.base += 30
        conv.base += 12
        z.base += 4

        lam = tiny[:, 0:4]
        y, s1, s2, q_, negc, posc, mx = (tiny[:, 4 * i:4 * i + 4] for i in range(1, 8))
        aCol = tiny[:, 32:40]
        em = tiny[:, 40:48]
        dn, rc, ss, rt = (tiny[:, 48 + 8 * i:56 + 8 * i] for i in range(4))
        gates, sig, lamy, lamc, decays, u2, root, hs, ydone = self.counters(
            "ab_gates", "ab_sig", "ab_lamy", "ab_lamc", "ab_decays", "ab_u2", "ab_root", "ab_hs", "ab_y")
        r1, r3, r4, turned, colsr, mrow, sdone, e1, e2, pready, pv, hn, n1, n2, n3, turn2, yb = self.counters(
            "ml_arg", "ml_ln", "ml_rows", "ml_turned", "ml_cols", "ml_bcast", "ml_scores", "ml_e1",
            "ml_e2", "ml_p", "ml_pv", "ml_hn", "ml_ss", "ml_rt", "ml_yb", "ml_turn2", "ml_yT")
        ln_ = row[3]
        with nc.Block() as block:
            @block.sync
            def _(sp):
                self.sync_loads(sp, G + 4)

            @block.tensor
            def _(pe):
                w = self.ring_tile(pe, G, 12)
                for m in range(2):
                    for c in range(4):
                        last = self.mm(ps[2 * m + c // 2][:, (c % 2) * T:(c % 2 + 1) * T],
                                       w[:, (4 * m + c) * P:(4 * m + c + 1) * P], xc[:, c, :], True, True)
                    last.then_inc(gates.sem, 1)
                pe.wait_ge(*sig.at(4))
                def scores(h):
                    b = ps[6 + h % 2]
                    nc.tensor.matmul(b[:, 0:256], qc[:, 4 + h, 0:P], qc[:, h, :], start=True, stop=True)
                    nc.tensor.matmul(b[:, 256:384], qc[:, 4 + h, P:T], qc[:, h, P:T], start=True, stop=True
                                     ).then_inc(sdone.sem, 1)
                scores(0)
                scores(1)
                pe.wait_ge(*r4.at(1))
                for n, rw in enumerate((al, mn)):
                    for t in range(TT):
                        last = nc.tensor.transpose(ps[3][:, 8 * n + 4 * t:8 * n + 4 * t + 4],
                                                   rw[:, t * P:(t + 1) * P], self.ident[0:4, 0:4])
                last.then_inc(turned.sem, 1)
                for h in range(4):
                    last = nc.tensor.matmul(ps[4 + h // 2][:, (h % 2) * T:(h % 2 + 1) * T],
                                            sel[:, h * P:(h + 1) * P], ex, start=True, stop=True)
                last.then_inc(mrow.sem, 1)
                for h in range(4):
                    pe.wait_ge(*pready.at(h + 1))
                    if h < 2:
                        scores(h + 2)
                    else:
                        pe.wait_ge(*hn.at(h - 1))
                    b = ps[h % 2]
                    nc.tensor.matmul(b[:, 0:129], big[:, h, 0:P], v1[:, 0, h, :], start=True, stop=True)
                    nc.tensor.matmul(b[:, 256:385], big[:, h, P:T], v1[:, 0, h, :], start=True, stop=False)
                    nc.tensor.matmul(b[:, 256:385], big[:, h, T:T + P], v1[:, 1, h, :], start=False, stop=True
                                     ).then_inc(pv.sem, 1)
                pe.wait_ge(*n3.at(1))
                for c in range(4):
                    for t in range(TT):
                        last = nc.tensor.transpose(ps[4 + c // 2][:, (c % 2) * T + t * P:(c % 2) * T + (t + 1) * P],
                                                   xs[:, t, c * P:(c + 1) * P], self.ident)
                last.then_inc(turn2.sem, 1)

            @block.scalar
            def _(act):
                link = Chain(act, self.act_chain)
                act.wait_ge(*r1.at(1))
                s_.activation(y, y, ACT.Exp).then_inc(lamy.sem, 1)
                link(s_.activation(ex, ex, ACT.Exp))
                s_.activation(ln_, ex, ACT.Ln, bias=1.0).then_inc(r3.sem, 1)
                act.wait_ge(*gates.at(2))
                for m, dst in enumerate((r, ig)):
                    for c in range(4):
                        ins = s_.activation(dst[:, c, :], ps[2 * m + c // 2][:, (c % 2) * T:(c % 2 + 1) * T],
                                            ACT.Sigmoid, bias=cols[:, m, c:c + 1])
                        if c % 2:
                            ins.then_inc(sig.sem, 1)
                act.wait_ge(*sig.at(4))
                act.wait_ge(*lamc.at(1))
                for c in range(4):
                    s_.activation(a[:, c, :], r[:, c, :], ACT.Exp, scale=negc[:, c:c + 1])
                    s_.activation(u[:, c, :], r[:, c, :], ACT.Tanh, scale=posc[:, c:c + 1]).then_inc(decays.sem, 1)
                act.wait_ge(*turned.at(1))
                link(s_.activation(aCol, ps[3][:, 0:8], ACT.Copy))
                s_.activation(em, ps[3][:, 8:16], ACT.Exp, scale=-1.0).then_inc(colsr.sem, 1)
                for h in range(4):
                    act.wait_ge(*e1.at(h + 1))
                    s_.activation(big[:, h, :], big[:, h, :], ACT.Exp).then_inc(e2.sem, 1)
                act.wait_ge(*u2.at(1))
                s_.activation(u.rearrange("p c t -> p (c t)"), u.rearrange("p c t -> p (c t)"), ACT.Sqrt
                              ).then_inc(root.sem, 1)
                for h in range(4):
                    act.wait_ge(*pv.at(h + 1))
                    s_.activation(Hn[:, :, h, :], ps[h % 2][:, :].rearrange("p (t n) -> p t n", t=2)[:, :, 0:129],
                                  ACT.Copy).then_inc(hn.sem, 1)
                act.wait_ge(*n1.at(1))
                s_.activation(rt, ss, ACT.Sqrt).then_inc(n2.sem, 1)

            @block.vector
            def _(dve):
                link = Chain(dve, self.dve_chain)
                lam_ = cols[:, 2, :]
                link(v_.tensor_scalar(mx, lam_, -1.0, 0.0, ALU.mult, ALU.max))
                link(v_.tensor_scalar(s1, lam_, 0.0, None, ALU.max))
                link(v_.scalar_tensor_tensor(y, s1, -1.0, mx, ALU.mult, ALU.subtract))
                link(v_.tensor_scalar(mn, fr, 0.0, None, ALU.min))
                v_.scalar_tensor_tensor(ex, mn, 2.0, fr, ALU.mult, ALU.subtract).then_inc(r1.sem, 1)
                dve.wait_ge(*lamy.at(1))
                link(v_.tensor_scalar(s1, y, 2.0, None, ALU.add))
                link(v_.reciprocal(s1, s1))
                link(v_.tensor_tensor(s1, s1, y, ALU.mult))
                link(v_.tensor_tensor(s2, s1, s1, ALU.mult))
                link(v_.tensor_scalar(q_, s2, 1.0 / 15, None, ALU.mult))
                for o in (13, 11, 9, 7, 5, 3):
                    link(v_.scalar_tensor_tensor(q_, q_, 1.0 / o, s2, ALU.add, ALU.mult))
                link(v_.scalar_tensor_tensor(q_, q_, 1.0, s1, ALU.add, ALU.mult))
                link(v_.scalar_tensor_tensor(q_, q_, 2.0, mx, ALU.mult, ALU.add))
                link(v_.tensor_scalar(posc, q_, 8.0, None, ALU.mult))
                v_.tensor_scalar(negc, q_, -8.0, None, ALU.mult).then_inc(lamc.sem, 1)
                dve.wait_ge(*r3.at(1))
                link(v_.tensor_tensor(fr, mn, ln_, ALU.subtract))
                link(v_.tensor_tensor_scan(cumf, ones, fr, 0.0, ALU.mult, ALU.add))
                link(v_.tensor_tensor(al, ir, cumf, ALU.subtract))
                link(v_.tensor_tensor_scan(fr, al, al, NEG, ALU.max, ALU.max))
                link(v_.tensor_scalar(ex, fr, -1.0, None, ALU.mult))
                v_.tensor_tensor(mn, fr, cumf, ALU.add).then_inc(r4.sem, 1)
                dve.wait_ge(*colsr.at(1))
                dve.wait_ge(*mrow.at(1))
                for h in range(4):
                    mb = ps[4 + h // 2][:, (h % 2) * T:(h % 2 + 1) * T]
                    v_.tensor_scalar(big[:, h, 0:T], mb, aCol[:, h:h + 1], 0.0, ALU.add, ALU.min)
                    v_.tensor_scalar(big[:, h, T:], mb[:, P:T], aCol[:, 4 + h:5 + h], 0.0, ALU.add, ALU.min
                                     ).then_inc(e1.sem, 1)
                dve.wait_ge(*decays.at(4))
                link(v_.tensor_tensor(r, a, a, ALU.mult))
                v_.scalar_tensor_tensor(u.rearrange("p c t -> p (c t)"), r.rearrange("p c t -> p (c t)"), 1.0,
                                        u.rearrange("p c t -> p (c t)"), ALU.add, ALU.mult).then_inc(u2.sem, 1)
                for h in range(4):
                    dve.wait_ge(*e2.at(h + 1))
                    link(v_.tensor_tensor(big[:, h, :], big[:, h, :], mask, ALU.mult))
                    dve.wait_ge(*sdone.at(h + 1))
                    v_.tensor_tensor(big[:, h, :], big[:, h, :], ps[6 + h % 2][:, 0:384], ALU.mult
                                     ).then_inc(pready.sem, 1)
                link(v_.tensor_tensor(ig, ig, xc, ALU.mult))
                dve.wait_ge(*root.at(1))
                link(v_.tensor_tensor(u, u, ig, ALU.mult))
                for c in range(4):
                    v_.tensor_tensor_scan(r[:, c, :], a[:, c, :], u[:, c, :], 0.0, ALU.mult, ALU.add).then_inc(hs.sem, 1)
                dve.wait_ge(*hs.at(4))
                v_.tensor_tensor(yT[:, 0:4, :], ga, r, ALU.mult).then_inc(ydone.sem, 1)
                dve.wait_ge(*hn.at(4))
                heads = Hn.rearrange("p t h d -> p (t h) d")
                link(v_.tensor_copy(rc.unsqueeze(2), heads[:, :, 128:129]))
                link(v_.scalar_tensor_tensor(dn, rc, -1.0, rc, ALU.mult, ALU.max))
                link(v_.tensor_tensor(dn, dn, em, ALU.max))
                link(v_.reciprocal(rc, dn))
                link(v_.tensor_tensor(heads[:, :, 0:128], heads[:, :, 0:128],
                                      rc.unsqueeze(2).to_broadcast([P, 8, 128]), ALU.mult))
                sq = xs.rearrange("p t (h d) -> p (t h) d", d=128)[:, 0:8, :]
                link(v_.tensor_tensor(sq, heads[:, :, 0:128], heads[:, :, 0:128], ALU.mult))
                link(v_.tensor_reduce(ss, sq, AX.X, ALU.add))
                v_.tensor_scalar(ss, ss, 1.0 / ML_DH, EPS, ALU.mult, ALU.add).then_inc(n1.sem, 1)
                dve.wait_ge(*n2.at(1))
                link(v_.reciprocal(rt, rt))
                link(v_.tensor_tensor(heads[:, :, 0:128], heads[:, :, 0:128],
                                      rt.unsqueeze(2).to_broadcast([P, 8, 128]), ALU.mult))
                for t in range(TT):
                    ins = v_.tensor_tensor(xs[:, t, 0:512].rearrange("p (h d) -> p h d", h=4), Hn[:, t, :, 0:128],
                                           so[:, t, :].rearrange("p (h d) -> p h d", h=4), ALU.mult)
                    if t == 0:
                        link(ins)
                ins.then_inc(n3.sem, 1)
                dve.wait_ge(*turn2.at(1))
                for c in range(4):
                    v_.tensor_scalar(yT[:, 4 + c, :], ps[4 + c // 2][:, (c % 2) * T:(c % 2 + 1) * T],
                                     cols[:, 3, c:c + 1], None, ALU.mult).then_inc(yb.sem, 1)
        for s, n in ((gates, 2), (sig, 4), (lamy, 1), (lamc, 1), (decays, 4), (u2, 1), (root, 1), (hs, 4), (ydone, 1),
                     (r1, 1), (r3, 1), (r4, 1), (turned, 1), (colsr, 1), (mrow, 1), (sdone, 4), (e1, 4), (e2, 4),
                     (pready, 4), (pv, 4), (hn, 4), (n1, 1), (n2, 1), (n3, 1), (turn2, 1), (yb, 4)):
            s.base += n
        small.base += 96
        self.add_rows_product(G, 13, yT, KD, G + 6)

    def add_rows_product(self, g0, tile, actT, kn, end, scale=None):
        nc, ps = self.nc, self.psum
        done, added = self.counters("add_done", "add_added")
        with nc.Block() as block:
            @block.sync
            def _(sp):
                self.sync_loads(sp, end)

            @block.tensor
            def _(pe):
                self.rows_product(pe, g0, tile, actT, kn, (0, 1, 2, 3), done)
                if (tile + kn // 2) % 3:
                    self.owed += 1
                self.flush(pe, done.at(1))

            @block.vector
            def _(dve):
                dve.wait_ge(*done.at(1))
                for t in range(TT):
                    for half in range(2):
                        xv = self.x[:, t, half * 512:(half + 1) * 512]
                        if scale is None:
                            nc.vector.tensor_tensor(xv, ps[2 * t + half][:, :], xv, ALU.add).then_inc(added.sem, 1)
                dve.wait_ge(*added.at(4))
        done.base += 1
        added.base += 4

    def final_norm(self, name):
        nc = self.nc
        work = self.arena(name)
        gain = work("gain", D)
        sq = work("sq", TT * D).rearrange("p (t d) -> p t d", t=TT)
        ss = self.stat[:, 0:2]
        here, a_, b_, c_, d_ = self.counters("fn_here", "fn_sq", "fn_mean", "fn_root", "fn_x")
        with nc.Block() as block:
            @block.sync
            def _(sp):
                sp.dma_start(gain, self.dram[name].partition_broadcast(P).rearrange("p a d -> p (a d)")).then_inc(here.sem, 16)

            @block.scalar
            def _(act):
                for t in range(TT):
                    nc.scalar.activation(sq[:, t, :], self.x[:, t, :], ACT.Square, accum_out=ss[:, t:t + 1]).then_inc(a_.sem, 1)
                act.wait_ge(*b_.at(1))
                nc.scalar.activation(ss, ss, ACT.Sqrt).then_inc(c_.sem, 1)

            @block.vector
            def _(dve):
                link = Chain(dve, self.dve_chain)
                dve.wait_ge(*a_.at(2))
                nc.vector.tensor_scalar(ss, ss, 1.0 / D, EPS, ALU.mult, ALU.add).then_inc(b_.sem, 1)
                dve.wait_ge(*c_.at(1))
                link(nc.vector.reciprocal(ss, ss))
                dve.wait_ge(*here.at(16))
                for t in range(TT):
                    nc.vector.scalar_tensor_tensor(self.x[:, t, :], self.x[:, t, :], ss[:, t:t + 1], gain,
                                                   ALU.mult, ALU.mult).then_inc(d_.sem, 1)
                dve.wait_ge(*d_.at(2))
        here.base += 16
        a_.base += 2
        b_.base += 1
        c_.base += 1
        d_.base += 2

    def nsa(self):
        nc, ps, G = self.nc, self.psum, G_NSA
        v_, s_ = nc.vector, nc.scalar
        self.begin_stage()
        SC = NSA_DH ** -0.5
        work = self.arena("nsa")
        w2 = work("w2", 384).rearrange("p (k n) -> p k n", k=2)
        pe_ = work("pe", 32)
        b1 = work("b1", 4)
        gw = work("gw", 384).rearrange("p (k n) -> p k n", k=KD)
        gb = work("gb", 48)
        causal = work("causal", 384)
        cm = work("cm", 32).rearrange("p (t n) -> p t n", t=TT)
        cneg = work("cneg", 32).rearrange("p (t n) -> p t n", t=TT)
        blocks = work("blocks", 8)
        xs = work("xs", TT * D).rearrange("p (t d) -> p t d", t=TT)
        qT = work("qT", 8 * T).rearrange("p (c t) -> p c t", c=8)
        kT = [work(f"kT{i}", 2 * T).rearrange("p (c t) -> p c t", c=2) for i in range(2)]
        X = [work(f"cmpX{i}", 5 * T).rearrange("p (g t) -> p g t", g=5) for i in range(2)]
        vv = work("vv", TT * 512).rearrange("p (t n) -> p t n", t=TT)
        gates = work("gates", TT * 48).rearrange("p (t h b) -> p t h b", t=TT, b=3)
        hid = [work(f"hid{i}", 2 * 64).rearrange("p (c g n) -> p c g n", c=2, g=4) for i in range(2)]
        bcol = work("bcol", 4)
        hidR = work("hidR", 4 * P).rearrange("p (a c n) -> p a c n", a=2, c=2)
        kcT = work("kcT", 64)
        R = work("R", 128).rearrange("p (a d) -> p a d", a=2)
        Vbd = work("Vbd", 2 * 512).rearrange("p (a h d) -> p a h d", a=2, h=8)
        Sc = work("Sc", TT * 256).rearrange("p (t h n) -> p t h n", t=TT, h=16)
        cs = work("cs", 96)
        cPT = work("cPT", 512)
        SB = [work(f"SB{i}", 384) for i in range(4)]
        PT = [work(f"PT{i}", 384) for i in range(4)]
        m3 = [work(f"m3_{i}", 4) for i in range(4)]
        nm = [work(f"nm{i}", 2) for i in range(4)]
        sums = [work(f"sums{i}", 2) for i in range(4)]
        coef = [work(f"coef{i}", 2) for i in range(4)]
        small, done, fa, fd, z, gsum = self.counters("nsa_small", "nsa_done", "nsa_freed_act", "nsa_freed_dve",
                                                    "nsa_zero", "nsa_gates")
        norm_act, norm_dve, norm_pe, norm_end = self.norm_parts(
            self.x, self.xT, self.gains[:, 4, :], None, "nsa", xs)
        UNITS = 23

        with nc.Block() as block:
            @block.sync
            def _(sp):
                for dst, name in ((w2.rearrange("p k n -> p (k n)"), "nsa_w2"), (pe_, "nsa_pe"), (b1, "nsa_b1"),
                                  (gw.rearrange("p k n -> p (k n)"), "nsa_gw"), (causal[:, 0:P], "nsa_causal"),
                                  (causal[:, T:], "nsa_causal"), (cm.rearrange("p t n -> p (t n)"), "nsa_cmp"),
                                  (blocks, "nsa_blocks")):
                    sp.dma_start(dst, self.dram[name]).then_inc(small.sem, 16)
                sp.dma_start(gb, self.dram["nsa_gb"].partition_broadcast(P).rearrange("p a d -> p (a d)")).then_inc(small.sem, 16)
                self.sync_loads(sp, G + 4)

            @block.gpsimd
            def _(pool):
                g_ = nc.gpsimd
                g_.memset(causal[:, P:T], 0.0).then_inc(z.sem, 1)
                for i in range(2):
                    g_.memset(X[i][:, 4, :], 0.0).then_inc(z.sem, 1)
                    g_.memset(hid[i].rearrange("p c g n -> p (c g n)"), 0.0).then_inc(z.sem, 1)
                g_.memset(kcT, 0.0).then_inc(z.sem, 1)

            @block.tensor
            def _(pe):
                norm_pe(pe)
                for n in range(UNITS):
                    if n >= 4:
                        pe.wait_ge(*(fd if n % 2 else fa).at((n - 4) // 2 + 1))
                    b = ps[n % 4]
                    if n < 20:
                        w = self.ring_tile(pe, G, n // 2)
                        self.stationary_cols(b[:, 0:T], w, n % 2, self.xT).then_inc(done.sem, 1)
                        if n % 2:
                            self.give_back(n // 2)
                    elif n < 22:
                        self.moving_cols(pe, b[:, :], G, 10, self.xT, n % 2).then_inc(done.sem, 1)
                        if n % 2:
                            self.give_back(10)
                            self.give_back(11)
                    else:
                        pe.wait_ge(*small.at(16 * 9))
                        for t in range(TT):
                            for k in range(KD):
                                last = self.mm(b[:, t * 48:(t + 1) * 48], self.xT[:, k, t * P:(t + 1) * P],
                                               gw[:, k, :], k == 0, k == KD - 1)
                        last.then_inc(done.sem, 1)
                self.flush(pe, done.at(UNITS))

            def unit(n, copy):
                b = ps[n % 4]
                if n < 8:
                    return [copy(qT[:, n, :], b[:, 0:T])]
                if n < 12:
                    return [copy(kT[(n - 8) // 2][:, n % 2, :], b[:, 0:T])]
                if n < 20:
                    x_, g = X[(n - 12) // 4], n % 4
                    return [copy(x_[0:64, g, :], b[0:64, 0:T]), copy(x_[64:P, g, 0:T - 1], b[64:P, 1:T])]
                if n < 22:
                    return [copy(vv[:, n - 20, :], b[:, :])]

            @block.scalar
            def _(act):
                norm_act(act)
                for n in range(0, 22, 2):
                    act.wait_ge(*done.at(n + 1))
                    unit(n, lambda o, i: s_.activation(o, i, ACT.Copy))[-1].then_inc(fa.sem, 1)
                act.wait_ge(*gsum.at(1))
                g2 = gates.rearrange("p t h b -> p (t h b)")
                s_.activation(g2, g2, ACT.Sigmoid).then_inc(fa.sem, 1)

            @block.vector
            def _(dve):
                norm_dve(dve)
                for n in range(1, 22, 2):
                    dve.wait_ge(*done.at(n + 1))
                    unit(n, lambda o, i: v_.tensor_copy(o, i))[-1].then_inc(fd.sem, 1)
                dve.wait_ge(*small.at(16 * 9))
                dve.wait_ge(*done.at(23))
                v_.tensor_tensor(gates.rearrange("p t h b -> p t (h b)"),
                                 ps[2][:, 0:96].rearrange("p (t n) -> p t n", t=TT),
                                 gb.unsqueeze(1).to_broadcast([P, TT, 48]), ALU.add).then_inc(gsum.sem, 1)
                dve.wait_ge(*z.at(6))
                for i in range(2):
                    v_.tensor_copy(X[i][:, 4, 0:32].rearrange("p (j s) -> p j s", s=2)[:, :, 0],
                                   pe_[:, 16 * i:16 * i + 16]).then_inc(fd.sem, 1)
                v_.tensor_scalar(cneg, cm, -1.0, -NEG, ALU.add, ALU.mult).then_inc(fd.sem, 1)
        norm_end()
        done.base += UNITS
        fa.base += 12
        fd.base += 14
        z.base += 6
        gsum.base += 1
        small.base += 16 * 9

        (hdone, hb, hready, c2, kready, repl, c4, rready, vbd, cscore, cexp, cpt, cpte, cdone, mxs, csum) = self.counters(
            "cm_hidden", "cm_bias", "cm_gelu", "cm_k2", "cm_kT", "cm_repl", "cm_R", "cm_Rs", "cm_vbd",
            "cm_scores", "cm_exp", "cm_turned", "cm_PT", "cm_out", "cm_max", "cm_scaled")
        with nc.Block() as block:
            @block.sync
            def _(sp):
                self.sync_loads(sp, G + 5)

            @block.tensor
            def _(pe):
                for i in range(2):
                    for hc in range(2):
                        for jj in range(16):
                            w = self.ring_tile(pe, G, 12 + 2 * i + jj // 8)
                            at = (jj % 8) * 256 + hc * P
                            rhs = X[i][:, :, 2 * jj:2 * jj + 225].rearrange("p g t -> p g t")[:, :, 0:225:16]
                            last = self.mm(ps[4 + i][:, 128 * hc:128 * hc + 75], w[:, at:at + P], rhs, jj == 0, jj == 15)
                    last.then_inc(hdone.sem, 1)
                    self.give_back(12 + 2 * i)
                    self.give_back(13 + 2 * i)
                pe.wait_ge(*hready.at(1))
                for hc in range(2):
                    last = self.mm(ps[6][:, 0:64], w2[:, hc, 0:128], hid[0][:, hc, :, :].rearrange("p g n -> p (g n)"),
                                   hc == 0, hc == 1)
                last.then_inc(c2.sem, 1)
                pe.wait_ge(*repl.at(1))
                for a in range(2):
                    for hc in range(2):
                        last = self.mm(ps[7][:, a * 64:(a + 1) * 64], hidR[:, a, hc, :], w2[:, hc, 128:192], hc == 0, hc == 1)
                last.then_inc(c4.sem, 1)
                pe.wait_ge(*kready.at(1))
                for t in range(TT):
                    for g in range(4):
                        b = ps[4 + g % 2]
                        lo = 64 * (g % 2)
                        for r in range(4):
                            at = t * P + (g // 2) * 64 + r * 16
                            last = self.mm(b[:, at:at + 16], qT[lo:lo + 64, 4 * (g // 2) + r, t * P:(t + 1) * P],
                                           kcT[lo:lo + 64, g * 16:(g + 1) * 16], True, True)
                last.then_inc(cscore.sem, 1)
                pe.wait_ge(*csum.at(1))
                for t in range(TT):
                    for a in range(2):
                        n = 2 * t + a
                        last = nc.tensor.transpose(ps[6][:, n * P:(n + 1) * P],
                                                   Sc[:, t, 8 * a:8 * a + 8, :].rearrange("p h n -> p (h n)"), self.ident)
                last.then_inc(cpt.sem, 1)
                pe.wait_ge(*cpte.at(1))
                pe.wait_ge(*vbd.at(2))
                for t in range(TT):
                    for a in range(2):
                        n = 2 * t + a
                        last = self.mm(ps[n][:, :], cPT[:, n * P:(n + 1) * P], Vbd[:, a, :, :].rearrange("p h d -> p (h d)"),
                                       True, True)
                last.then_inc(cdone.sem, 1)
                self.flush(pe, cdone.at(1))

            @block.scalar
            def _(act):
                for i in range(2):
                    act.wait_ge(*hb.at(i + 1))
                    for hc in range(2):
                        ins = s_.activation(hid[i][:, hc, :, 0:N_CMP],
                                            ps[4 + i][:, 128 * hc:128 * hc + 60].rearrange("p (g n) -> p g n", g=4),
                                            ACT.Gelu_apprx_tanh, bias=bcol[:, 2 * i + hc:2 * i + hc + 1])
                    ins.then_inc(hready.sem, 1)
                act.wait_ge(*c2.at(1))
                s_.activation(kcT, ps[6][:, 0:64], ACT.Copy).then_inc(kready.sem, 1)
                act.wait_ge(*c4.at(1))
                s_.activation(R.rearrange("p a d -> p (a d)"), ps[7][:, 0:128], ACT.Copy).then_inc(rready.sem, 1)
                act.wait_ge(*mxs.at(1))
                s2 = Sc.rearrange("p t h n -> p (t h n)")
                s_.activation(s2, s2, ACT.Exp, scale=SC).then_inc(cexp.sem, 1)
                act.wait_ge(*cpt.at(1))
                s_.activation(cPT, ps[6][:, :], ACT.Copy).then_inc(cpte.sem, 1)

            @block.vector
            def _(dve):
                link = Chain(dve, self.dve_chain)
                for i in range(2):
                    dve.wait_ge(*hdone.at(i + 1))
                    v_.tensor_tensor(bcol[:, 2 * i:2 * i + 2].unsqueeze(2),
                                     ps[4 + i][:, 0:256].rearrange("p (c n) -> p c n", c=2)[:, :, 60:61],
                                     b1[:, 2 * i:2 * i + 2].unsqueeze(2), ALU.add).then_inc(hb.sem, 1)
                dve.wait_ge(*hready.at(2))
                for a in range(2):
                    for hc in range(2):
                        for g in range(2):
                            last = v_.tensor_copy(hidR[:, a, hc, g * 64:(g + 1) * 64].rearrange("p (r n) -> p r n", r=4),
                                                  hid[1][:, hc, 2 * a + g, :].unsqueeze(1).to_broadcast([P, 4, 16]))
                last.then_inc(repl.sem, 1)
                dve.wait_ge(*rready.at(1))
                for a in range(2):
                    v_.tensor_tensor(Vbd[:, a, :, :], R[:, a, :].unsqueeze(1).to_broadcast([P, 8, 64]),
                                     blocks.unsqueeze(2).to_broadcast([P, 8, 64]), ALU.mult).then_inc(vbd.sem, 1)
                dve.wait_ge(*cscore.at(1))
                mx, sm, co = cs[:, 0:32], cs[:, 32:64], cs[:, 64:96]
                for t in range(TT):
                    for b in range(2):
                        o = Sc[:, t, :, :].rearrange("p (a b r) n -> p a b r n", a=2, b=2)[:, :, b, :, :]
                        i_ = ps[4 + b][:, t * P:(t + 1) * P].rearrange("p (a r n) -> p a r n", a=2, r=4)
                        for a in range(2):
                            last = v_.tensor_tensor(o[:, a], i_[:, a], cm[:, t, :].unsqueeze(1).to_broadcast([P, 4, 16]), ALU.mult)
                link(last)
                for t in range(TT):
                    last = v_.tensor_tensor(Sc[:, t, :, :], Sc[:, t, :, :],
                                            cneg[:, t, :].unsqueeze(1).to_broadcast([P, 16, 16]), ALU.add)
                link(last)
                flat = Sc.rearrange("p t h n -> p (t h) n")
                link(v_.tensor_reduce(mx, flat, AX.X, ALU.max))
                v_.tensor_tensor(flat, flat, mx.unsqueeze(2).to_broadcast([P, 32, 16]), ALU.subtract).then_inc(mxs.sem, 1)
                dve.wait_ge(*cexp.at(1))
                link(v_.tensor_reduce(sm, flat, AX.X, ALU.add))
                link(v_.reciprocal(sm, sm))
                link(v_.tensor_tensor(co.rearrange("p (t h) -> p t h", t=TT), sm.rearrange("p (t h) -> p t h", t=TT),
                                      gates[:, :, :, 0], ALU.mult))
                for t in range(TT):
                    last = v_.tensor_tensor(Sc[:, t, :, :], Sc[:, t, :, :],
                                            cm[:, t, :].unsqueeze(1).to_broadcast([P, 16, 16]), ALU.mult)
                link(last)
                v_.tensor_tensor(flat, flat, co.unsqueeze(2).to_broadcast([P, 32, 16]), ALU.mult).then_inc(csum.sem, 1)
        for s, n in ((hdone, 2), (hb, 2), (hready, 2), (c2, 1), (kready, 1), (repl, 1), (c4, 1), (rready, 1), (vbd, 2),
                     (cscore, 1), (cexp, 1), (cpt, 1), (cpte, 1), (cdone, 1), (mxs, 1), (csum, 1)):
            s.base += n

        units = [(c, br, b) for c in range(8) for br in range(2) for b in range(2)]
        NU = len(units)
        head = lambda c, b: 4 * (2 * (c // 4) + b) + c % 4
        sco, sadd, smax, sexp, scoef, sscale, stn, spt, spv, ofin = self.counters(
            "at_scores", "at_masked", "at_max", "at_exp", "at_coef", "at_scaled", "at_turned", "at_PT", "at_pv", "at_o")
        oT_done, oT_ev = self.counters("at_oT", "at_oTs")
        with nc.Block() as block:
            @block.sync
            def _(sp):
                self.sync_loads(sp, G + 5)

            @block.tensor
            def _(pe):
                def scores(n):
                    c, br, b = units[n]
                    if n >= 2:
                        pe.wait_ge(*sadd.at(n - 1))
                    lo = 64 * b
                    q, k, o = qT[lo:lo + 64, c, :], kT[br][lo:lo + 64, c // 4, :], ps[4 + b]
                    nc.tensor.matmul(o[:, 0:P], q[:, 0:P], k[:, 0:P], start=True, stop=True)
                    nc.tensor.matmul(o[:, P:384], q[:, P:T], k, start=True, stop=True).then_inc(sco.sem, 1)

                def turn(n):
                    b = units[n][2]
                    pe.wait_ge(*sscale.at(n + 1))
                    if n >= 2:
                        pe.wait_ge(*spt.at(n - 1))
                    for j in range(3):
                        last = nc.tensor.transpose(ps[6 + b][:, j * P:(j + 1) * P], SB[n % 4][:, j * P:(j + 1) * P], self.ident)
                    last.then_inc(stn.sem, 1)

                def values(n):
                    c, br, b = units[n]
                    h = head(c, b)
                    g, a, at = h // 4, h // 8, (h % 8) * 64
                    pe.wait_ge(*spt.at(n + 1))
                    col = br * 256 + g * 64
                    w = PT[n % 4]
                    nc.tensor.matmul(ps[a][:, at:at + 64], w[:, 0:P], vv[:, 0, col:col + 64], start=False, stop=True,
                                     skip_group_check=True)
                    nc.tensor.matmul(ps[2 + a][:, at:at + 64], w[:, P:T], vv[:, 0, col:col + 64], start=False, stop=True,
                                     skip_group_check=True)
                    nc.tensor.matmul(ps[2 + a][:, at:at + 64], w[:, T:384], vv[:, 1, col:col + 64], start=False, stop=True,
                                     skip_group_check=True).then_inc(spv.sem, 1)

                for n in range(NU + 3):
                    if n < NU:
                        scores(n)
                    if 2 <= n < NU + 2:
                        turn(n - 2)
                    if n >= 3:
                        values(n - 3)
                pe.wait_ge(*ofin.at(4))
                for k in range(KD):
                    for t in range(TT):
                        last = nc.tensor.transpose(ps[4 + k // 2][:, (k % 2) * T + t * P:(k % 2) * T + (t + 1) * P],
                                                   xs[:, t, k * P:(k + 1) * P], self.ident)
                    if k % 2:
                        last.then_inc(oT_done.sem, 1)

            @block.scalar
            def _(act):
                def pt(n):
                    act.wait_ge(*stn.at(n + 1))
                    if n >= 4:
                        act.wait_ge(*spv.at(n - 3))
                    s_.activation(PT[n % 4], ps[6 + units[n][2]][:, 0:384], ACT.Copy).then_inc(spt.sem, 1)

                for n in range(NU + 1):
                    if n < NU:
                        act.wait_ge(*smax.at(n + 1))
                        if n >= 4:
                            act.wait_ge(*scoef.at(n - 3))
                        for t in range(TT):
                            w = SB[n % 4][:, t * P:(2 * t + 1) * P + t * 0] if t == 0 else SB[n % 4][:, P:384]
                            s_.activation(w, w, ACT.Exp, scale=SC, bias=nm[n % 4][:, t:t + 1],
                                          accum_out=sums[n % 4][:, t:t + 1]).then_inc(sexp.sem, 1)
                    if n >= 1:
                        pt(n - 1)
                for k in (2, 3, 6, 7):
                    act.wait_ge(*oT_done.at(k // 2 + 1))
                    s_.activation(self.xT[:, k, :], ps[4 + k // 2][:, (k % 2) * T:(k % 2 + 1) * T], ACT.Copy).then_inc(oT_ev.sem, 1)

            @block.vector
            def _(dve):
                link = Chain(dve, self.dve_chain)

                def coefs(n):
                    c, br, b = units[n]
                    dve.wait_ge(*sexp.at(2 * n + 2))
                    if n >= 4:
                        dve.wait_ge(*sscale.at(n - 3))
                    link(v_.reciprocal(coef[n % 4], sums[n % 4]))
                    v_.tensor_tensor(coef[n % 4], coef[n % 4], gates[:, :, head(c, b), 1 + br], ALU.mult).then_inc(scoef.sem, 1)

                for n in range(NU + 1):
                    if n < NU:
                        dve.wait_ge(*sco.at(n + 1))
                        if n >= 4:
                            dve.wait_ge(*stn.at(n - 3))
                            dve.wait_ge(*sexp.at(2 * n - 6))
                        v_.tensor_tensor(SB[n % 4], ps[4 + units[n][2]][:, 0:384], causal, ALU.add).then_inc(sadd.sem, 1)
                        dve.wait_ge(*sadd.at(n + 1))
                        link(v_.tensor_reduce(m3[n % 4][:, 0:3], SB[n % 4].rearrange("p (j k) -> p j k", j=3), AX.X, ALU.max))
                        link(v_.tensor_tensor(m3[n % 4][:, 1:2], m3[n % 4][:, 1:2], m3[n % 4][:, 2:3], ALU.max))
                        v_.tensor_scalar(nm[n % 4], m3[n % 4][:, 0:2], -SC, None, ALU.mult).then_inc(smax.sem, 1)
                    if n >= 1:
                        coefs(n - 1)
                dve.wait_ge(*spv.at(NU))
                for t in range(TT):
                    for a in range(2):
                        v_.tensor_copy(xs[:, t, a * 512:(a + 1) * 512], ps[2 * t + a][:, :]).then_inc(ofin.sem, 1)
                for k in (0, 1, 4, 5):
                    dve.wait_ge(*oT_done.at(k // 2 + 1))
                    v_.tensor_copy(self.xT[:, k, :], ps[4 + k // 2][:, (k % 2) * T:(k % 2 + 1) * T]).then_inc(oT_ev.sem, 1)

            @block.gpsimd
            def _(pool):
                for n in range(NU):
                    pool.wait_ge(*scoef.at(n + 1))
                    nc.gpsimd.tensor_scalar(SB[n % 4][:, 0:P], SB[n % 4][:, 0:P], coef[n % 4][:, 0:1], 1.0, ALU.mult, ALU.mult)
                    nc.gpsimd.tensor_scalar(SB[n % 4][:, P:384], SB[n % 4][:, P:384], coef[n % 4][:, 1:2], 1.0,
                                            ALU.mult, ALU.mult).then_inc(sscale.sem, 1)
        for s, n in ((sco, NU), (sadd, NU), (smax, NU), (sexp, 2 * NU), (scoef, NU), (sscale, NU), (stn, NU), (spt, NU),
                     (spv, NU), (ofin, 4), (oT_done, 4), (oT_ev, 8)):
            s.base += n
        self.add_rows_product(G, 16, self.xT, KD, G + 7)

    def softplus_tail(self, link, y, mx, s1, s2, q_):
        v_ = self.nc.vector
        link(v_.tensor_scalar(s1, y, 2.0, None, ALU.add))
        link(v_.reciprocal(s1, s1))
        link(v_.tensor_tensor(s1, s1, y, ALU.mult))
        link(v_.tensor_tensor(s2, s1, s1, ALU.mult))
        link(v_.tensor_scalar(q_, s2, 1.0 / 15, None, ALU.mult))
        for o in (13, 11, 9, 7, 5, 3):
            link(v_.scalar_tensor_tensor(q_, q_, 1.0 / o, s2, ALU.add, ALU.mult))
        link(v_.scalar_tensor_tensor(q_, q_, 1.0, s1, ALU.add, ALU.mult))
        link(v_.scalar_tensor_tensor(q_, q_, 2.0, mx, ALU.mult, ALU.add))

    def gate_row(self, part, banks):
        for k in range(KD):
            last = self.nc.tensor.matmul(self.psum[banks[k // 4]][:, (k % 4) * P:(k % 4 + 1) * P],
                                         self.modT[:, 8 * part + k, 0:1].to_broadcast([P, P]), self.ident,
                                         start=True, stop=True)
        return last

    def second(self):
        nc, ps, G = self.nc, self.psum, G_SECOND
        v_, s_ = nc.vector, nc.scalar
        self.begin_stage()
        KS = RET_DK ** -0.5
        work = self.arena("mix2")
        R0, R1, R2, Rh = (work(f"R{i}", 2048) for i in range(4))
        qkn = work("qkn", TT * 1024).rearrange("p (t n) -> p t n", t=TT)
        vn = work("vn", TT * 1024).rearrange("p (t n) -> p t n", t=TT)
        gn = work("gn", TT * 1024).rearrange("p (t n) -> p t n", t=TT)
        gp = work("gp", TT * 1024).rearrange("p (t n) -> p t n", t=TT)
        gr = work("gr", TT * 1024).rearrange("p (t n) -> p t n", t=TT)
        vc = work("vc", TT * 1024).rearrange("p (t n) -> p t n", t=TT)
        kc = work("kc", TT * 512).rearrange("p (t n) -> p t n", t=TT)
        pn = work("pn", TT * 512).rearrange("p (t n) -> p t n", t=TT)
        cond = work("cond", 16).rearrange("p (k s) -> p k s", s=2)
        adab = work("adab", 48)
        rope = work("rope", 256).rearrange("p (s t n) -> p s t n", s=2, t=TT)
        pscale = work("pscale", 4)
        rnorm = work("rnorm", 8)
        rcol = work("rcol", 4).rearrange("p (t s) -> p t s", s=2)
        lg = work("lg", 8)
        tiny = work("tiny", 5 * 8)
        wfb = work("wfb", 16).rearrange("p (s h t) -> p s h t", s=2, h=4)
        small, silu, ada, mods, sfirst, slast = self.counters("s2_small", "s2_silu", "s2_ada", "s2_mods", "s2_lgy", "s2_lg")
        ctx_in = R0.rearrange("p (t d) -> p t d", t=TT)
        hcT = Rh.rearrange("p (k t) -> p k t", k=KD)

        with nc.Block() as block:
            @block.sync
            def _(sp):
                for dst, name in ((cond.rearrange("p k s -> p (k s)"), "cond"), (adab, "ada_b"),
                                  (rope.rearrange("p s t n -> p (s t n)"), "rope"), (pscale, "pool_scale"),
                                  (rnorm, "ret_norm"), (rcol.rearrange("p t s -> p (t s)"), "ret_col")):
                    sp.dma_start(dst, self.dram[name]).then_inc(small.sem, 16)
                sp.dma_start(lg, self.dram["decay"].partition_broadcast(P).rearrange("p a d -> p (a d)")).then_inc(small.sem, 16)
                sp.dma_start(ctx_in, self.dram["ctx"].rearrange("(t p) d -> p t d", p=P)).then_inc(small.sem, 16)
                self.sync_loads(sp, G + 8)

            @block.scalar
            def _(act):
                act.wait_ge(*small.at(16 * 8))
                c2 = cond.rearrange("p k s -> p (k s)")
                s_.activation(c2, c2, ACT.Silu).then_inc(silu.sem, 1)
                act.wait_ge(*sfirst.at(1))
                s_.activation(tiny[:, 0:8], tiny[:, 0:8], ACT.Exp).then_inc(slast.sem, 1)

            @block.tensor
            def _(pe):
                pe.wait_ge(*silu.at(1))
                for c in range(48):
                    w = self.ring_tile(pe, G, c // 2)
                    for k in range(KD):
                        last = self.mm(ps[0][:, 2 * c:2 * c + 2], w[:, k * 256 + (c % 2) * P:k * 256 + (c % 2 + 1) * P],
                                       cond[:, k, :], k == 0, k == KD - 1)
                    if c % 2:
                        self.give_back(c // 2)
                last.then_inc(ada.sem, 1)
                self.flush(pe, ada.at(1))

            @block.vector
            def _(dve):
                link = Chain(dve, self.dve_chain)
                dve.wait_ge(*small.at(16 * 8))
                y, mx, s1, s2, q_ = (tiny[:, 8 * i:8 * i + 8] for i in range(5))
                link(v_.tensor_scalar(mx, lg, -1.0, 0.0, ALU.mult, ALU.max))
                link(v_.tensor_scalar(s1, lg, 0.0, None, ALU.max))
                v_.scalar_tensor_tensor(y, s1, -1.0, mx, ALU.mult, ALU.subtract).then_inc(sfirst.sem, 1)
                dve.wait_ge(*slast.at(1))
                self.softplus_tail(link, y, mx, s1, s2, q_)
                link(v_.tensor_scalar(lg, q_, -1.0, None, ALU.mult))
                dve.wait_ge(*ada.at(1))
                link(v_.tensor_tensor(self.modT, ps[0][:, 0:96].rearrange("p (c s) -> p c s", s=2),
                                      adab.unsqueeze(2).to_broadcast([P, 48, 2]), ALU.add))
                for n, (part, s, g) in enumerate(((1, 0, 6), (1, 1, 6), (4, 0, 7))):
                    v_.scalar_tensor_tensor(self.gA[:, n, :], self.modT[:, 8 * part:8 * part + 8, s], 1.0,
                                            self.gains[:, g, :], ALU.add, ALU.mult).then_inc(mods.sem, 1)
        for s, n in ((silu, 1), (ada, 1), (mods, 3), (sfirst, 1), (slast, 1), (small, 16 * 8)):
            s.base += n

        nact, ndve, npe, nend = self.norm_parts(ctx_in, hcT, self.gA[:, 1, :], self.modT[:, 0:8, 1], "ctx",
                                                R1.rearrange("p (t d) -> p t d", t=TT))
        with nc.Block() as block:
            block.sync(lambda sp: self.sync_loads(sp, G + 8))
            block.scalar(nact)
            block.vector(ndve)
            block.tensor(npe)
        nend()

        nact, ndve, npe, nend = self.norm_parts(self.x, self.xT, self.gA[:, 0, :], self.modT[:, 0:8, 0], "mixx",
                                                R2.rearrange("p (t d) -> p t d", t=TT))
        units = [(b, c, t) for b in range(11) for c in ((0, 1) if b in (2, 3, 4) else (0,)) for t in range(TT)]
        NU = len(units)
        done, freed = self.counters("s2_done", "s2_freed")
        with nc.Block() as block:
            @block.sync
            def _(sp):
                self.sync_loads(sp, G + 15)

            @block.tensor
            def _(pe):
                npe(pe)
                for n, (b, c, t) in enumerate(units):
                    if n >= 4:
                        pe.wait_ge(*freed.at(n - 3))
                    self.moving_cols(pe, ps[n % 4][:, :], G, 24 + 2 * b, hcT if c else self.xT, t).then_inc(done.sem, 1)
                    if n + 1 == NU or units[n + 1][0] != b:
                        self.give_back(24 + 2 * b)
                        self.give_back(25 + 2 * b)
                self.flush(pe, done.at(NU))

            @block.scalar
            def _(act):
                nact(act)
                for n, (b, c, t) in enumerate(units):
                    act.wait_ge(*done.at(n + 1))
                    src, half = ps[n % 4][:, :], slice(((b + 1) % 2) * 512, ((b + 1) % 2) * 512 + 512)
                    if b == 0:
                        ins = s_.activation(pn[:, t, :], src, ACT.Copy)
                    elif b == 1:
                        ins = s_.activation(qkn[:, t, 0:512], src, ACT.Copy)
                    elif b == 2:
                        ins = s_.activation(kc[:, t, :] if c else qkn[:, t, 512:], src, ACT.Copy, scale=KS)
                    elif b < 5:
                        ins = s_.activation((vc if c else vn)[:, t, half], src, ACT.Copy)
                    elif b < 7:
                        ins = s_.activation(gn[:, t, half], src, ACT.Silu)
                    elif b < 9:
                        ins = s_.activation(gp[:, t, half], src, ACT.Sigmoid)
                    else:
                        ins = s_.activation(gr[:, t, half], src, ACT.Sigmoid)
                    ins.then_inc(freed.sem, 1)

            @block.vector
            def _(dve):
                ndve(dve)
        nend()
        done.base += NU
        freed.base += NU

        band = R0.rearrange("p (g s t) -> p g s t", g=4, s=TT)
        dT, mT = R1[:, 0:1024].rearrange("p (g t) -> p g t", g=4), R1[:, 1024:2048].rearrange("p (g t) -> p g t", g=4)
        here, p1, p2, p3, p4, p5 = self.counters("pl_here", "pl_d", "pl_ds", "pl_m", "pl_ms", "pl_out")
        qk5 = qkn.rearrange("p t (h s n) -> p t h s n", h=8, s=2)
        ra = R2[:, 0:512].rearrange("p (h n) -> p h n", h=8)
        rb = R2[:, 512:1024].rearrange("p (h n) -> p h n", h=8)
        rc_ = R2[:, 1024:1536].rearrange("p (h n) -> p h n", h=8)
        rd_ = R2[:, 1536:2048].rearrange("p (h n) -> p h n", h=8)
        with nc.Block() as block:
            @block.sync
            def _(sp):
                sp.dma_start(R0, self.dram["band"]).then_inc(here.sem, 16)
                self.sync_loads(sp, G + 16)

            @block.tensor
            def _(pe):
                pe.wait_ge(*here.at(16))
                for g in range(4):
                    for s in range(TT):
                        last = self.mm(ps[g // 2][:, (g % 2) * T:(g % 2 + 1) * T], pn[:, s, g * P:(g + 1) * P],
                                       band[:, g, s, :], s == 0, s == 1)
                last.then_inc(p1.sem, 1)
                w = self.ring_tile(pe, G, 46)
                pe.wait_ge(*p2.at(1))
                for g in range(4):
                    last = self.mm(ps[2 + g // 2][:, (g % 2) * T:(g % 2 + 1) * T], w[:, g * P:(g + 1) * P], dT[:, g, :], True, True)
                last.then_inc(p3.sem, 1)
                self.give_back(46)
                pe.wait_ge(*p4.at(4))
                self.rows_product(pe, G, 47, mT, 4, (4, 5, 6, 7), p5)
                self.flush(pe, p5.at(1))

            @block.scalar
            def _(act):
                act.wait_ge(*p1.at(1))
                for b in range(2):
                    ins = s_.activation(dT[:, 2 * b:2 * b + 2, :], ps[b][:, :].rearrange("p (g t) -> p g t", g=2), ACT.Copy)
                ins.then_inc(p2.sem, 1)
                act.wait_ge(*p3.at(1))
                for g in range(4):
                    s_.activation(mT[:, g, :], ps[2 + g // 2][:, (g % 2) * T:(g % 2 + 1) * T], ACT.Copy,
                                  scale=pscale[:, g:g + 1]).then_inc(p4.sem, 1)

            @block.vector
            def _(dve):
                link = Chain(dve, self.dve_chain)
                for t in range(TT):
                    cos, sin = (rope[:, s, t, :].unsqueeze(1).to_broadcast([P, 8, 64]) for s in range(2))
                    lo, hi = qk5[:, t, :, 0, :], qk5[:, t, :, 1, :]
                    v_.tensor_tensor(ra, lo, cos, ALU.mult)
                    v_.tensor_tensor(rb, hi, sin, ALU.mult)
                    v_.tensor_tensor(rc_, lo, sin, ALU.mult)
                    link(v_.tensor_tensor(rd_, hi, cos, ALU.mult))
                    v_.tensor_tensor(lo, ra, rb, ALU.subtract)
                    link(v_.tensor_tensor(hi, rc_, rd_, ALU.add))
                dve.wait_ge(*p5.at(1))
                for t in range(TT):
                    for half in range(2):
                        o = gp[:, t, half * 512:(half + 1) * 512]
                        link(v_.tensor_tensor(o, o, ps[4 + 2 * t + half][:, :], ALU.mult))
        for s, n in ((here, 16), (p1, 1), (p2, 1), (p3, 1), (p4, 4), (p5, 1)):
            s.base += n

        qkT = Rh.rearrange("p (h t) -> p h t", h=8)
        kcw = R0.rearrange("p (s h t n) -> p s h t n", s=2, h=4, t=TT)
        S = R1.rearrange("p (s h e) -> p s h e", s=2, h=4)
        Dm = R2.rearrange("p (h m n) -> p h m n", h=4, m=TT)
        c1, c2_, c3_, c4_, c5_, c6_ = self.counters("cx_w", "cx_kw", "cx_S", "cx_Ss", "cx_turned", "cx_qk")
        with nc.Block() as block:
            block.sync(lambda sp: self.sync_loads(sp, G + 16))

            @block.scalar
            def _(act):
                for s in range(2):
                    for h in range(4):
                        s_.activation(wfb[:, s, h, :], rcol[:, :, s], ACT.Exp, scale=lg[:, 4 * s + h:4 * s + h + 1]
                                      ).then_inc(c1.sem, 1)
                for n in range(2):
                    act.wait_ge(*c5_.at(n + 1))
                    for b in range(2):
                        s_.activation(qkT[:, 4 * n + 2 * b:4 * n + 2 * b + 2, :],
                                      ps[4 + 2 * n + b][:, :].rearrange("p (h t) -> p h t", h=2), ACT.Copy).then_inc(c6_.sem, 1)
                act.wait_ge(*c3_.at(1))
                for b in range(4):
                    s_.activation(S[:, b // 2, 2 * (b % 2):2 * (b % 2) + 2, :], ps[b][:, :].rearrange("p (h e) -> p h e", h=2),
                                  ACT.Copy).then_inc(c4_.sem, 1)

            @block.vector
            def _(dve):
                dve.wait_ge(*c1.at(8))
                for s in range(2):
                    for h in range(4):
                        for t in range(TT):
                            v_.tensor_scalar(kcw[:, s, h, t, :], kc[:, t, h * P:(h + 1) * P], wfb[:, s, h, t:t + 1], None,
                                             ALU.mult).then_inc(c2_.sem, 1)

            @block.tensor
            def _(pe):
                for n in range(2):
                    for h in range(4):
                        for t in range(TT):
                            last = nc.tensor.transpose(ps[4 + 2 * n + h // 2][:, (h % 2) * T + t * P:(h % 2) * T + (t + 1) * P],
                                                       qkn[:, t, n * 512 + h * P:n * 512 + (h + 1) * P], self.ident)
                    last.then_inc(c5_.sem, 1)
                for s in range(2):
                    for h in range(4):
                        pe.wait_ge(*c2_.at(8 * s + 2 * h + 2))
                        for t in range(TT):
                            last = nc.tensor.matmul(ps[2 * s + h // 2][:, (h % 2) * T:(h % 2 + 1) * T], kcw[:, s, h, t, :],
                                                    vc[:, t, h * 256:(h + 1) * 256], start=t == 0, stop=t == 1)
                last.then_inc(c3_.sem, 1)
        for s, n in ((c1, 8), (c2_, 16), (c3_, 1), (c4_, 4), (c5_, 2), (c6_, 4)):
            s.base += n

        rel = kc.rearrange("p t n -> p (t n)").rearrange("p (s n) -> p s n", s=2)
        qd = qkn.rearrange("p t n -> p (t n)").rearrange("p (s h t) -> p s h t", s=2, h=4)
        PTb = pn.rearrange("p t n -> p (t n)").rearrange("p (b m n) -> p b m n", b=2, m=TT)
        yv = vc.rearrange("p t (h e) -> p t h e", h=4)
        rows_ = R0[:, 0:512].rearrange("p (s t) -> p s t", s=2)
        bn = R0[:, 512:512 + 48].rearrange("p (n s) -> p n s", n=8)
        mv = R0[:, 576:592].rearrange("p (n s) -> p n s", n=8)
        d1, d2, d3, d4, sc_, pt_, y_, ye, v1_, v2_, tn, te = self.counters(
            "rt_exp", "rt_D", "rt_dec", "rt_qd", "rt_scores", "rt_P", "rt_y", "rt_ys", "rt_var", "rt_root", "rt_turned", "rt_rT")
        here2, yn = self.counters("rt_here", "rt_yn")
        rT = self.xT
        with nc.Block() as block:
            @block.sync
            def _(sp):
                sp.dma_start(rel.rearrange("p s n -> p (s n)"), self.dram["ret"][:, 0:1024]).then_inc(here2.sem, 16)
                sp.dma_start(R0[:, 0:512], self.dram["ret_row"]).then_inc(here2.sem, 16)
                self.sync_loads(sp, G + 16)

            @block.scalar
            def _(act):
                act.wait_ge(*here2.at(32))
                for s in range(2):
                    for h in range(4):
                        s_.activation(qd[:, s, h, :], rows_[:, s, :], ACT.Exp, scale=lg[:, 4 * s + h:4 * s + h + 1]).then_inc(d3.sem, 1)
                for h in range(4):
                    act.wait_ge(*d1.at(h + 1))
                    o = Dm[:, h, :, :].rearrange("p m n -> p (m n)")
                    s_.activation(o, o, ACT.Exp).then_inc(d2.sem, 1)
                for h in range(4):
                    act.wait_ge(*y_.at(h + 1))
                    s_.activation(yv[:, :, h, :], ps[2 + h % 2][:, :].rearrange("p (t e) -> p t e", t=TT), ACT.Copy).then_inc(ye.sem, 1)
                act.wait_ge(*v1_.at(1))
                s_.activation(mv[:, :, 1], mv[:, :, 1], ACT.Sqrt).then_inc(v2_.sem, 1)
                for k in (2, 3, 6, 7):
                    act.wait_ge(*tn.at(k // 2 + 1))
                    s_.activation(rT[:, k, :], ps[4 + k // 2][:, (k % 2) * T:(k % 2 + 1) * T], ACT.Copy,
                                  scale=rnorm[:, k:k + 1]).then_inc(te.sem, 1)

            @block.vector
            def _(dve):
                link = Chain(dve, self.dve_chain)
                dve.wait_ge(*here2.at(32))
                for h in range(4):
                    o = Dm[:, h, :, :].rearrange("p m n -> p (m n)")
                    link(v_.tensor_scalar(o, rel[:, 0, :], lg[:, h:h + 1], None, ALU.mult))
                    v_.scalar_tensor_tensor(o, rel[:, 1, :], lg[:, 4 + h:5 + h], o, ALU.mult, ALU.add).then_inc(d1.sem, 1)
                dve.wait_ge(*d3.at(8))
                for s in range(2):
                    v_.tensor_tensor(qd[:, s, :, :], qd[:, s, :, :], qkT[:, 0:4, :], ALU.mult).then_inc(d4.sem, 1)
                for h in range(4):
                    dve.wait_ge(*sc_.at(h + 1))
                    dve.wait_ge(*d2.at(h + 1))
                    if h >= 2:
                        dve.wait_ge(*y_.at(h - 1))
                    v_.tensor_tensor(PTb[:, h % 2, :, :], ps[h % 2][:, :].rearrange("p (m n) -> p m n", m=TT), Dm[:, h, :, :],
                                     ALU.mult).then_inc(pt_.sem, 1)
                for h in range(4):
                    dve.wait_ge(*ye.at(h + 1))
                    for t in range(TT):
                        link(v_.bn_stats(bn[:, 4 * t + h, :], yv[:, t, h, :]))
                        link(v_.bn_aggr(mv[:, 4 * t + h, :], bn[:, 4 * t + h, :]))
                v_.tensor_scalar(mv[:, :, 1], mv[:, :, 1], EPS, None, ALU.add).then_inc(v1_.sem, 1)
                dve.wait_ge(*v2_.at(1))
                link(v_.reciprocal(mv[:, :, 1], mv[:, :, 1]))
                for t in range(TT):
                    for h in range(4):
                        n = 4 * t + h
                        last = v_.tensor_scalar(yv[:, t, h, :], yv[:, t, h, :], mv[:, n, 0:1], mv[:, n, 1:2], ALU.subtract, ALU.mult)
                link(last)
                for t in range(TT):
                    v_.tensor_tensor(vc[:, t, :], vc[:, t, :], gn[:, t, :], ALU.mult).then_inc(yn.sem, 1)
                for k in (0, 1, 4, 5):
                    dve.wait_ge(*tn.at(k // 2 + 1))
                    v_.tensor_scalar(rT[:, k, :], ps[4 + k // 2][:, (k % 2) * T:(k % 2 + 1) * T], rnorm[:, k:k + 1], None,
                                     ALU.mult).then_inc(te.sem, 1)

            @block.tensor
            def _(pe):
                def scores(h):
                    for m in range(TT):
                        last = nc.tensor.matmul(ps[h % 2][:, m * T:(m + 1) * T], qkT[:, 4 + h, m * P:(m + 1) * P], qkT[:, h, :],
                                                start=True, stop=True)
                    last.then_inc(sc_.sem, 1)
                scores(0)
                scores(1)
                pe.wait_ge(*d4.at(2))
                for h in range(4):
                    pe.wait_ge(*pt_.at(h + 1))
                    if h < 2:
                        scores(h + 2)
                    else:
                        pe.wait_ge(*ye.at(h - 1))
                    for t in range(TT):
                        o = ps[2 + h % 2][:, t * T:(t + 1) * T]
                        for m in range(TT):
                            nc.tensor.matmul(o, PTb[:, h % 2, m, t * P:(t + 1) * P], vn[:, m, h * 256:(h + 1) * 256],
                                             start=m == 0, stop=False)
                        for s in range(2):
                            last = nc.tensor.matmul(o, qd[:, s, h, t * P:(t + 1) * P], S[:, s, h, :], start=False, stop=s == 1)
                    last.then_inc(y_.sem, 1)
                pe.wait_ge(*yn.at(2))
                for k in range(KD):
                    for t in range(TT):
                        last = nc.tensor.transpose(ps[4 + k // 2][:, (k % 2) * T + t * P:(k % 2) * T + (t + 1) * P],
                                                   vc[:, t, k * P:(k + 1) * P], self.ident)
                    if k % 2:
                        last.then_inc(tn.sem, 1)
        for s, n in ((d1, 4), (d2, 4), (d3, 8), (d4, 2), (sc_, 4), (pt_, 4), (y_, 4), (ye, 4), (v1_, 1), (v2_, 1), (tn, 4),
                     (te, 8), (here2, 32), (yn, 2)):
            s.base += n

        o1, o2, o3, o4, o5, o6, o7 = self.counters("mo_ret", "mo_merged", "mo_turned", "mo_mT", "mo_g1", "mo_g1s", "mo_out")
        g1 = R0[:, 0:1024]
        mgT = Rh.rearrange("p (k t) -> p k t", k=KD)
        with nc.Block() as block:
            block.sync(lambda sp: self.sync_loads(sp, G + 19))

            @block.tensor
            def _(pe):
                self.gate_row(2, (4, 5)).then_inc(o5.sem, 1)
                self.rows_product(pe, G, 49, rT, KD, (0, 1, 2, 3), o1)
                pe.wait_ge(*o2.at(4))
                pe.wait_ge(*o6.at(2))
                for k in range(KD):
                    for t in range(TT):
                        last = nc.tensor.transpose(ps[4 + k // 2][:, (k % 2) * T + t * P:(k % 2) * T + (t + 1) * P],
                                                   gp[:, t, k * P:(k + 1) * P], self.ident)
                    if k % 2:
                        last.then_inc(o3.sem, 1)
                pe.wait_ge(*o4.at(8))
                self.rows_product(pe, G, 53, mgT, KD, (0, 1, 2, 3), o7)
                self.flush(pe, o7.at(1))

            @block.scalar
            def _(act):
                act.wait_ge(*o5.at(1))
                for b in range(2):
                    s_.activation(g1[:, b * 512:(b + 1) * 512], ps[4 + b][:, :], ACT.Copy).then_inc(o6.sem, 1)
                for k in (2, 3, 6, 7):
                    act.wait_ge(*o3.at(k // 2 + 1))
                    s_.activation(mgT[:, k, :], ps[4 + k // 2][:, (k % 2) * T:(k % 2 + 1) * T], ACT.Copy).then_inc(o4.sem, 1)

            @block.vector
            def _(dve):
                link = Chain(dve, self.dve_chain)
                dve.wait_ge(*o1.at(1))
                for t in range(TT):
                    for half in range(2):
                        sl = slice(half * 512, (half + 1) * 512)
                        link(v_.tensor_tensor(gr[:, t, sl], gr[:, t, sl], ps[2 * t + half][:, :], ALU.mult))
                        v_.tensor_tensor(gp[:, t, sl], gp[:, t, sl], gr[:, t, sl], ALU.add).then_inc(o2.sem, 1)
                for k in (0, 1, 4, 5):
                    dve.wait_ge(*o3.at(k // 2 + 1))
                    v_.tensor_copy(mgT[:, k, :], ps[4 + k // 2][:, (k % 2) * T:(k % 2 + 1) * T]).then_inc(o4.sem, 1)
                dve.wait_ge(*o7.at(1))
                for t in range(TT):
                    for half in range(2):
                        sl = slice(half * 512, (half + 1) * 512)
                        link(v_.tensor_tensor(gr[:, t, sl], ps[2 * t + half][:, :], g1[:, sl], ALU.mult))
                        link(v_.tensor_tensor(self.x[:, t, sl], self.x[:, t, sl], gr[:, t, sl], ALU.add))
        for s, n in ((o1, 1), (o2, 4), (o3, 4), (o4, 8), (o5, 1), (o6, 2), (o7, 1)):
            s.base += n

    def peer(self):
        nc, ps, G = self.nc, self.psum, G_SECOND
        v_, s_, g_ = nc.vector, nc.scalar, nc.gpsimd
        self.begin_stage()
        XSLOT = 2 * D
        w_at = self.base + XSLOTS * XSLOT * 4
        p_at = w_at + P * T * 4
        Wt = Arena(nc, "peerW", w_at, p_at)("W", P * T).rearrange("p (t i) -> p t i", t=T)
        xring = Arena(nc, "peerX", self.base, w_at)("ring", XSLOTS * XSLOT).rearrange("p (s n) -> p s n", s=XSLOTS)
        stay = Arena(nc, "peerP", p_at, self.keep)
        iota = stay("iota", P)
        GT, I1T, I2T = (stay(n, T) for n in ("GT", "I1T", "I2T"))
        O1 = stay("O1", 8 * P).rearrange("p (q n) -> p q n", q=8)
        O2 = stay("O2", 8 * P).rearrange("p (q n) -> p q n", q=8)
        Ab = stay("Ab", 2 * T).rearrange("p (b t) -> p b t", b=2)
        GA = stay("GA", 2 * T).rearrange("p (b t) -> p b t", b=2)
        g2 = stay("g2", D)
        tmp = Arena(nc, "peerT", self.ring_end, p_at)
        xs = tmp("xs", TT * D).rearrange("p (t d) -> p t d", t=TT)
        qT = tmp("qT", 16 * T).rearrange("p (c t) -> p c t", c=16)
        sc = tmp("sc", 32 * P).rearrange("p (r n) -> p r n", r=32)
        val = tmp("val", 512).rearrange("p (r k) -> p r k", r=32)
        idx = tmp("idx", 512, dt=U32).rearrange("p (r k) -> p r k", r=32)
        best = tmp("best", 256).rearrange("p (r k) -> p r k", r=16)
        pos = tmp("pos", 256, dt=U32).rearrange("p (r k) -> p r k", r=16)
        posh = tmp("posh", 256, dt=U32).rearrange("p (r k) -> p r k", r=16)
        sm = tmp("sm", 16)

        done, freed, here, sdone, sfree = self.counters("pr_done", "pr_freed", "pr_here", "pr_scores", "pr_sfreed")
        nact, ndve, npe, nend = self.norm_parts(self.x, self.xT, self.gA[:, 2, :], self.modT[:, 24:32, 0], "peer", xs)
        with nc.Block() as block:
            @block.sync
            def _(sp):
                sp.dma_start(iota, self.dram["iota"]).then_inc(here.sem, 16)
                self.sync_loads(sp, G + 22)
                sp.wait_ge(*here.at(16))

            @block.tensor
            def _(pe):
                npe(pe)
                for n in range(16):
                    if n >= 4:
                        pe.wait_ge(*freed.at(n - 3))
                    self.stationary_cols(ps[n % 4][:, 0:T], self.ring_tile(pe, G, 57 + n // 2), n % 2, self.xT
                                         ).then_inc(done.sem, 1)
                    if n % 2:
                        self.give_back(57 + n // 2)
                pe.wait_ge(*freed.at(16))
                keys = self.ring_tile(pe, G, 65)
                for t in range(TT):
                    for b in range(4):
                        if t:
                            pe.wait_ge(*sfree.at(b + 1))
                        for j in range(4):
                            c = 4 * b + j
                            last = self.mm(ps[4 + b][:, j * P:(j + 1) * P], qT[:, c, t * P:(t + 1) * P],
                                           keys[:, c * P:(c + 1) * P], True, True)
                        last.then_inc(sdone.sem, 1)
                self.give_back(65)
                self.flush(pe, sdone.at(8))
                self.gate_row(5, (0, 1)).then_inc(done.sem, 1)

            @block.scalar
            def _(act):
                nact(act)
                for n in range(16):
                    act.wait_ge(*done.at(n + 1))
                    s_.activation(qT[:, n, :], ps[n % 4][:, 0:T], ACT.Copy).then_inc(freed.sem, 1)
                for t in range(TT):
                    for b in range(4):
                        act.wait_ge(*sdone.at(4 * t + b + 1))
                        s_.activation(sc[:, 16 * t + 4 * b:16 * t + 4 * b + 4, :], ps[4 + b][:, :].rearrange("p (r n) -> p r n", r=4),
                                      ACT.Copy).then_inc(sfree.sem, 1)
                act.wait_ge(*done.at(17))
                for b in range(2):
                    s_.activation(g2[:, b * 512:(b + 1) * 512], ps[b][:, :], ACT.Copy).then_inc(freed.sem, 1)

            @block.vector
            def _(dve):
                ndve(dve)
        nend()
        for s, n in ((done, 17), (freed, 18), (here, 16), (sdone, 8), (sfree, 8)):
            s.base += n

        xloaded = [self.counter(f"experts_loaded{s}") for s in range(XSLOTS)]
        xreleased = self.counter("experts_released")
        experts = self.dram["experts"]
        tk1, tk2, tk3, tk4 = self.counters("tk_sub", "tk_exp", "tk_ready", "tk_turned")
        (tk5,) = self.counters("tk_T")
        sw = qT.rearrange("p c t -> p (c t)").rearrange("p (r n) -> p r n", r=32)
        cand = sc.rearrange("p r n -> p (r n)").rearrange("p (r n) -> p r n", r=16)
        cw = sw.rearrange("p r n -> p (r n)").rearrange("p (r n) -> p r n", r=16)
        with nc.Block() as block:
            @block.sync
            def _(sp):
                for s in range(XSLOTS):
                    sp.dma_start(xring[:, s, :], experts[s]).then_inc(xloaded[s].sem, 16)

            @block.vector
            def _(dve):
                link = Chain(dve, self.dve_chain)

                def top16(rows, src, spare, values, index):
                    for r in range(rows):
                        last = v_.max(values[:, r, 0:8], src[:, r, :])
                    link(last)
                    for r in range(rows):
                        last = v_.max_index(index[:, r, 0:8], values[:, r, 0:8], src[:, r, :])
                    for r in range(rows):
                        last = v_.match_replace(spare[:, r, :], values[:, r, 0:8], src[:, r, :], -3.0e38)
                    link(last)
                    for r in range(rows):
                        last = v_.max(values[:, r, 8:16], spare[:, r, :])
                    link(last)
                    for r in range(rows):
                        last = v_.max_index(index[:, r, 8:16], values[:, r, 8:16], spare[:, r, :])
                    link(last)

                top16(32, sc, sw, val, idx)
                v4 = val.rearrange("p (t h s) k -> p t h s k", t=TT, s=2)
                c4 = cand.rearrange("p (t h) n -> p t h n", t=TT)
                for t in range(TT):
                    last = v_.tensor_tensor(c4[:, t].rearrange("p h (a b) -> p h a b", a=16),
                                            v4[:, t, :, 0, :].unsqueeze(3).to_broadcast([P, 8, 16, 16]),
                                            v4[:, t, :, 1, :].unsqueeze(2).to_broadcast([P, 8, 16, 16]), ALU.add)
                link(last)
                top16(16, cand, cw, best, pos)
                link(v_.tensor_tensor(val[:, 0:16, :], best, best[:, :, 0:1].to_broadcast([P, 16, 16]), ALU.subtract))
                v_.tensor_scalar(posh, pos, 4, None, ALU.logical_shift_right).then_inc(tk1.sem, 1)
                dve.wait_ge(*tk1.at(1))
                link(v_.tensor_scalar(pos, pos, 15, None, ALU.bitwise_and))
                idf = sw.rearrange("p r n -> p (r n)")[:, 0:512].rearrange("p (r k) -> p r k", r=32)
                hf_, lf_ = (sw.rearrange("p r n -> p (r n)")[:, 512 + 256 * i:768 + 256 * i].rearrange("p (r k) -> p r k", r=16) for i in range(2))
                v_.tensor_copy(idf, idx)
                v_.tensor_copy(hf_, posh)
                link(v_.tensor_copy(lf_, pos))
                eq = sc.rearrange("p r n -> p (r n)").rearrange("p (r k j) -> p r k j", r=16, k=16)
                id2 = idf.rearrange("p (r s) k -> p r s k", s=2)
                jot = iota[:, 0:16].unsqueeze(1).unsqueeze(1).to_broadcast([P, 16, 16, 16])
                for part, (which, out) in enumerate(((hf_, xs[:, 0, 0:256]), (lf_, xs[:, 0, 256:512]))):
                    link(v_.tensor_tensor(eq, which.unsqueeze(3).to_broadcast([P, 16, 16, 16]), jot, ALU.is_equal))
                    link(v_.tensor_tensor(eq, eq, id2[:, :, part, :].unsqueeze(2).to_broadcast([P, 16, 16, 16]), ALU.mult))
                    link(v_.tensor_reduce(out.rearrange("p (r k) -> p r k", r=16), eq, AX.X, ALU.add))
                dve.wait_ge(*tk2.at(1))
                link(v_.tensor_reduce(sm, val[:, 0:16, :], AX.X, ALU.add))
                link(v_.reciprocal(sm, sm))
                v_.tensor_tensor(val[:, 0:16, :], val[:, 0:16, :], sm.unsqueeze(2).to_broadcast([P, 16, 16]), ALU.mult
                                 ).then_inc(tk3.sem, 1)
                dve.wait_ge(*tk4.at(1))
                for b, dst in enumerate((GT, I1T, I2T)):
                    v_.tensor_copy(dst, ps[b][:, 0:T]).then_inc(tk5.sem, 1)
                dve.wait_ge(*tk5.at(3))

            @block.scalar
            def _(act):
                act.wait_ge(*tk1.at(1))
                s_.activation(val[:, 0:16, :], val[:, 0:16, :], ACT.Exp).then_inc(tk2.sem, 1)

            @block.tensor
            def _(pe):
                pe.wait_ge(*tk3.at(1))
                v3 = val.rearrange("p r k -> p (r k)")
                for t in range(TT):
                    for b, src in enumerate((v3[:, t * P:(t + 1) * P], xs[:, 0, t * P:(t + 1) * P],
                                             xs[:, 0, 256 + t * P:256 + (t + 1) * P])):
                        last = nc.tensor.transpose(ps[b][:, t * P:(t + 1) * P], src, self.ident)
                last.then_inc(tk4.sem, 1)
        for s, n in ((tk1, 1), (tk2, 1), (tk3, 1), (tk4, 1), (tk5, 3)):
            s.base += n

        wo1, wo2, wmm, wev = self.counters("w_rows1", "w_rows2", "w_product", "w_written")
        QUADS = T // 4
        with nc.Block() as block:
            @block.vector
            def _(dve):
                def quad(q, b, first=False):
                    if not first:
                        dve.wait_ge(*wmm.at(q - 1))
                    for j in range(4):
                        t = q * 4 + j
                        last = v_.tensor_scalar(O1[:, 4 * b + j, :], iota, I1T[:, bass.ds(t, 1)], GT[:, bass.ds(t, 1)],
                                                ALU.is_equal, ALU.mult)
                    last.then_inc(wo1.sem, 1)
                quad(0, 0, True)
                quad(1, 1, True)
                with dve.Fori(1, QUADS // 2) as turn:
                    for b in range(2):
                        quad(turn * 2 + b, b)

            @block.gpsimd
            def _(pool):
                def quad(q, b, first=False):
                    if not first:
                        pool.wait_ge(*wmm.at(q - 1))
                    for j in range(4):
                        t = q * 4 + j
                        last = g_.tensor_scalar(O2[:, 4 * b + j, :], iota, I2T[:, bass.ds(t, 1)], None, ALU.is_equal)
                    last.then_inc(wo2.sem, 1)
                for q in range(QUADS):
                    quad(q, q % 2, q < 2)

            @block.tensor
            def _(pe):
                def quad(q, b, first=False):
                    pe.wait_ge(*wo1.at(q + 1))
                    pe.wait_ge(*wo2.at(q + 1))
                    if not first:
                        pe.wait_ge(*wev.at(q - 1))
                    for j in range(4):
                        last = nc.tensor.matmul(ps[b][:, j * P:(j + 1) * P], O1[:, 4 * b + j, :], O2[:, 4 * b + j, :],
                                                start=True, stop=True)
                    last.then_inc(wmm.sem, 1)
                quad(0, 0, True)
                quad(1, 1, True)
                with pe.Fori(1, QUADS // 2) as turn:
                    for b in range(2):
                        quad(turn * 2 + b, b)

            @block.scalar
            def _(act):
                with act.Fori(0, QUADS // 2) as turn:
                    for b in range(2):
                        act.wait_ge(*wmm.at(turn * 2 + (b + 1)))
                        s_.activation(Wt[:, bass.ds((turn * 2 + b) * 4, 4), :], ps[b][:, :].rearrange("p (t i) -> p t i", t=4),
                                      ACT.Copy).then_inc(wev.sem, 1)
        for s, n in ((wo1, QUADS), (wo2, QUADS), (wmm, QUADS), (wev, QUADS)):
            s.base += n

        xu, xa, xg = self.counters("ex_u", "ex_gelu", "ex_weighted")
        N = PEER_KEYS
        TURNS = N // XSLOTS
        with nc.Block() as block:
            @block.sync
            def _(sp):
                with sp.Fori(1, TURNS) as turn:
                    for s in range(XSLOTS):
                        sp.wait_ge(*xreleased.at(turn * XSLOTS + (s - XSLOTS + 1)))
                        sp.dma_start(xring[:, s, :], experts[bass.ds(turn * XSLOTS + s, 1)].rearrange("a p n -> p (a n)")
                                     ).then_inc(xloaded[s].sem, 16)

            @block.tensor
            def _(pe):
                def up(n, s, loaded, first=False):
                    pe.wait_ge(*xloaded[s].at(loaded))
                    if not first:
                        pe.wait_ge(*xa.at(n - 1))
                    for k in range(KD):
                        last = nc.tensor.matmul(ps[s % 2][:, 0:T], xring[:, s, k * P:(k + 1) * P], self.xT[:, k, :],
                                                start=k == 0, stop=k == KD - 1)
                    last.then_inc(xu.sem, 1)

                def down(n, s, start, stop):
                    pe.wait_ge(*xg.at(n + 1))
                    for t in range(TT):
                        for half in range(2):
                            last = nc.tensor.matmul(ps[4 + 2 * t + half][:, :], GA[:, s % 2, t * P:(t + 1) * P],
                                                    xring[:, s, D + half * 512:D + (half + 1) * 512], start=start, stop=stop)
                    last.then_inc(xreleased.sem, 1)

                for n in range(XSLOTS):
                    up(n, n, 16, first=n < 2)
                    if n:
                        down(n - 1, n - 1, n == 1, False)
                with pe.Fori(1, TURNS) as turn:
                    for s in range(XSLOTS):
                        up(turn * XSLOTS + s, s, turn * 16 + 16)
                        down(turn * XSLOTS + (s - 1), (s - 1) % XSLOTS, False, False)
                down(N - 1, XSLOTS - 1, False, True)

            @block.scalar
            def _(act):
                def step(n, b, first=False):
                    act.wait_ge(*xu.at(n + 1))
                    if not first:
                        act.wait_ge(*xg.at(n - 1))
                    s_.activation(Ab[:, b, :], ps[b][:, 0:T], ACT.Gelu).then_inc(xa.sem, 1)
                step(0, 0, True)
                step(1, 1, True)
                with act.Fori(1, N // 2) as turn:
                    for b in range(2):
                        step(turn * 2 + b, b)

            @block.vector
            def _(dve):
                def step(n, b, first=False):
                    dve.wait_ge(*xa.at(n + 1))
                    if not first:
                        dve.wait_ge(*xreleased.at(n - 1))
                    v_.tensor_tensor(GA[:, b, :].unsqueeze(2), Ab[:, b, :].unsqueeze(2), Wt[:, :, bass.ds(n, 1)], ALU.mult
                                     ).then_inc(xg.sem, 1)
                step(0, 0, True)
                step(1, 1, True)
                with dve.Fori(1, N // 2) as turn:
                    for b in range(2):
                        step(turn * 2 + b, b)
                dve.wait_ge(*xreleased.at(N))
                link = Chain(dve, self.dve_chain)
                for t in range(TT):
                    for half in range(2):
                        sl = slice(half * 512, (half + 1) * 512)
                        o = O1.rearrange("p q n -> p (q n)")[:, sl]
                        link(v_.tensor_tensor(o, ps[4 + 2 * t + half][:, :], g2[:, sl], ALU.mult))
                        link(v_.tensor_tensor(self.x[:, t, sl], self.x[:, t, sl], o, ALU.add))
        for s in (xu, xa, xg, xreleased):
            s.base += N
        for s in xloaded:
            s.base += 16 * TURNS


def build(nc, dram, out, stages=None, first_group=0, groups=N_GROUPS):
    k = Kernel(nc, dram, out, stages)
    k.first_group, k.next_load, k.groups = first_group, first_group, groups
    steps = [("ffn1a", lambda: k.ffn(G_FFN1A, 0)), ("ab", lambda: k.ab()),
             ("ffn2a", lambda: k.ffn(G_FFN2A, 2)), ("ffn1b", lambda: k.ffn(G_FFN1B, 3)),
             ("nsa", lambda: k.nsa()), ("ffn2b", lambda: k.ffn(G_FFN2B, 5)),
             ("final1", lambda: k.final_norm("final_norm")), ("mixed", lambda: k.second()),
             ("pre_final", lambda: k.peer()), ("out", lambda: k.final_norm("final_g"))]
    with k.ctx:
        k.start()
        k.end_stage()
        for name, step in steps:
            if stages is None or name in stages:
                step()
                k.end_stage()
        k.store(k.x)
        k.end_stage()


def cols_block(w, c0, n):
    return w[:, c0:c0 + n].reshape(KD, P, n).transpose(1, 0, 2).reshape(P, KD * n)


def rows_tiles(w):
    r = w.shape[0] // 256
    return [w[256 * i:256 * (i + 1)].reshape(2, P, D).transpose(1, 0, 2).reshape(P, TILE) for i in range(r)]


def tiles_of(block):
    return [block[:, i:i + TILE] for i in range(0, block.shape[1], TILE)]


def columns(v):
    return v.reshape(-1, P).T


def ffn_tiles(w_gu, w_down):
    tiles = []
    downs = rows_tiles(w_down)
    for i in range(FFN_GROUPS):
        both = np.concatenate([w_gu[:, 256 * i:256 * (i + 1)], w_gu[:, D_FF + 256 * i:D_FF + 256 * (i + 1)]], 1)
        tiles += tiles_of(cols_block(both, 0, 512)) + [downs[i]]
    return tiles


def rg_tile(w_r, w_i):
    out = np.zeros((P, 16, P), np.float32)
    for m, w in enumerate((w_r, w_i)):
        for c in range(RG_CHUNKS):
            for b in range(2):
                out[64 * b:64 * b + 64, 4 * m + c, 64 * b:64 * b + 64] = w[2 * c + b]
    return out.reshape(P, TILE)


def pad_tiles(tiles):
    return tiles + [np.zeros((P, TILE), np.float32)] * (-len(tiles) % 3)


def nsa_q_order():
    order = []
    for c in range(8):
        for g in (2 * (c // 4), 2 * (c // 4) + 1):
            head = 4 * g + c % 4
            order += list(range(head * NSA_DH, (head + 1) * NSA_DH))
    return order


def layout(x, ffn1_norm, ffn1_w_gu, ffn1_w_down, mix_norm, ffn2_norm, ffn2_w_gu, ffn2_w_down, ab_w_in,
           rg_conv_w, rg_conv_b, rg_w_r, rg_b_r, rg_w_i, rg_b_i, rg_lambda, ml_conv_w, ml_conv_b,
           ml_b_i, ml_b_f, ml_norm, ab_w_out, nsa_w_in, nsa_pe_k, nsa_k_w1, nsa_k_b1, nsa_k_w2,
           nsa_pe_v, nsa_v_w1, nsa_v_b1, nsa_v_w2, nsa_b_gate, nsa_w_out, final_norm, c_2, ctx_2,
           c_ctx_2, ada_w_2, ada_b_2, norm_mix_g_2, norm_ffn_g_2, w_in_2, pool_w_2, pool_scale_2,
           pool_out_2, ret_decay_2, ret_norm_g_2, ret_out_2, w_out_2, peer_wq_2, peer_keys_2, peer_u_2,
           peer_v_2, final_g_2):
    tiles = ffn_tiles(ffn1_w_gu[0], ffn1_w_down[0])
    ab = ab_w_in[0]
    for c in range(0, 3072, 256):
        if c < 2048:
            tiles.append(cols_block(ab, c, 256))
        elif c % 512 == 0:
            tiles += tiles_of(cols_block(ab, c, 512))
    tiles += pad_tiles([rg_tile(rg_w_r[0], rg_w_i[0])] + rows_tiles(ab_w_out[0]))
    tiles += ffn_tiles(ffn2_w_gu[0], ffn2_w_down[0])
    tiles += ffn_tiles(ffn1_w_gu[1], ffn1_w_down[1])
    nsa = nsa_w_in[0]
    part = lambda i: nsa[:, 1024 + 256 * i:1024 + 256 * (i + 1)]
    q = nsa[:, :1024][:, nsa_q_order()]
    n_tiles = [cols_block(q, c, 256) for c in range(0, 1024, 256)]
    n_tiles += [cols_block(part(2), 0, 256), cols_block(part(4), 0, 256)]
    for kv in (0, 1):
        w = part(kv).reshape(D, NSA_GROUPS, 1, NSA_DH)
        w = np.concatenate([w, w], 2).reshape(D, 512)
        n_tiles += [cols_block(w, 0, 256), cols_block(w, 256, 256)]
    n_tiles += tiles_of(cols_block(np.concatenate([part(3), part(5)], 1), 0, 512))
    for w1 in (nsa_k_w1[0], nsa_v_w1[0]):
        n_tiles += tiles_of(w1.reshape(16, P, 256).transpose(1, 0, 2).reshape(P, 4096))
    n_tiles += rows_tiles(nsa_w_out[0])
    tiles += pad_tiles(n_tiles)
    tiles += ffn_tiles(ffn2_w_gu[1], ffn2_w_down[1])
    w = w_in_2[0]
    s_tiles = [cols_block(ada_w_2[0], c, 256) for c in range(0, 6144, 256)]
    for c in range(0, 5632, 512):
        s_tiles += tiles_of(cols_block(w, c, 512))
    pw = np.zeros((P, TILE), np.float32)
    pw[:, :512] = pool_w_2[0].transpose(1, 0, 2).reshape(P, 512)
    s_tiles.append(pw)
    s_tiles += rows_tiles(pool_out_2[0]) + rows_tiles(ret_out_2[0]) + rows_tiles(w_out_2[0])
    s_tiles += [cols_block(peer_wq_2[0], c, 256) for c in range(0, 2048, 256)]
    s_tiles.append(peer_keys_2[0].transpose(3, 0, 1, 2).reshape(P, TILE))
    tiles += pad_tiles(s_tiles)
    stream = np.stack(tiles).reshape(-1, 3, P, TILE).transpose(0, 2, 1, 3).reshape(-1, P, GROUP)
    assert stream.shape[0] == N_GROUPS, stream.shape

    u = peer_u_2[0].reshape(P, P, KD, P)
    v = peer_v_2[0].reshape(P, P, D)
    experts = np.concatenate([u.transpose(1, 3, 2, 0).reshape(P, P, D), v.transpose(1, 0, 2)], 2)

    gains = np.concatenate([columns(a) for a in (
        ffn1_norm[0], mix_norm[0], ffn2_norm[0], ffn1_norm[1], mix_norm[1], ffn2_norm[1],
        norm_mix_g_2[0], norm_ffn_g_2[0])], 1)
    conv_w = np.concatenate([rg_conv_w[0], ml_conv_w[0]], 1)
    conv_b = np.concatenate([rg_conv_b[0], ml_conv_b[0]], 0)
    taps = np.stack([columns(a) for a in [*conv_w, conv_b]], 2).reshape(P, 60)
    rgb = np.concatenate([columns(rg_b_r[0]), columns(rg_b_i[0]), columns(rg_lambda[0]), columns(ml_norm[0])], 1)
    ml_if = cols_block(ab, 3072, 8)
    ml_b = np.stack([ml_b_i[0], ml_b_f[0]], 1)
    j = np.arange(P)
    causal = (j[None, :] >= j[:, None]).astype(np.float32)
    ones = np.ones((P, P), np.float32)
    ml_mask = np.concatenate([causal, ones, causal], 1) * np.float32(ML_DH ** -0.5)
    ml_sel = np.repeat(np.eye(4, dtype=np.float32), P, 1)
    nsa_small = dict(
        w2=np.concatenate([nsa_k_w2[0].reshape(2, P, 64), nsa_k_w2[0].reshape(2, P, 64), nsa_v_w2[0].reshape(2, P, 64)], 2
                          ).transpose(1, 0, 2).reshape(P, 384),
        pe=np.concatenate([nsa_pe_k[0].reshape(16, P).T, nsa_pe_v[0].reshape(16, P).T], 1),
        b1=np.concatenate([columns(nsa_k_b1[0]), columns(nsa_v_b1[0])], 1),
        gw=cols_block(nsa, 2560, 48), gb=nsa_b_gate[0][None])
    t = np.arange(T)
    n = np.arange(16)
    cmask = ((n[None, :] * CMP_STRIDE + CMP_BLOCK - 1 <= t[:, None]) & (n[None, :] < N_CMP)).astype(np.float32)
    head_blocks = np.repeat(np.eye(8, dtype=np.float32), 16, 0)
    nmask = dict(causal_add=np.where(causal.T > 0, np.float32(0), np.float32(NEG)).astype(np.float32),
                 cmp=cmask.reshape(2, P, 16).transpose(1, 0, 2).reshape(P, 32), blocks=head_blocks)
    rows = T // 64
    row, col = np.repeat(np.arange(rows, dtype=np.float32), 64), np.tile(np.arange(64, dtype=np.float32), rows)
    inv = np.float32(10000.0) ** (-np.arange(32, dtype=np.float32) / 32)
    ang = np.concatenate([row[:, None] * inv, col[:, None] * inv], 1).astype(np.float32)
    rope = np.stack([np.cos(ang), np.sin(ang)], 0).astype(np.float32)
    rope = rope.reshape(2, 2, P, 64).transpose(2, 0, 1, 3).reshape(P, 256)
    band = np.zeros((4, T, T), np.float32)
    for g, wd in enumerate((2, 4, 8, 16)):
        lo, hi = np.clip(t - wd // 2, 0, T), np.clip(t + wd - wd // 2, 0, T)
        inside = (t[:, None] >= lo[None]) & (t[:, None] < hi[None])
        band[g] = inside / (hi - lo)[None].astype(np.float32) - np.eye(T, dtype=np.float32)
    band = band.reshape(4, 2, P, T).transpose(2, 0, 1, 3).reshape(P, 2048)
    rel = (t[None, :] - t[:, None]).astype(np.float32)
    ret = np.stack([np.maximum(rel, 0), np.maximum(-rel, 0), (rel >= 0).astype(np.float32), (rel < 0).astype(np.float32)])
    ret = ret.reshape(4, 2, P, T).transpose(2, 0, 1, 3).reshape(P, 2048)
    ret_row = np.concatenate([np.tile(t + 1, (P, 1)), np.tile(T - t, (P, 1))], 1).astype(np.float32)
    ret_col = np.stack([T - 1 - t, t], 1).reshape(2, P, 2).transpose(1, 0, 2).reshape(P, 4).astype(np.float32)
    iota = np.tile(np.arange(P, dtype=np.float32), (P, 1))
    return dict(
        x=x[0], stream=stream, experts=experts, ident=np.eye(P, dtype=np.float32), gains=gains,
        ab_taps=taps, ab_cols=rgb, ab_if=ml_if, ab_b=ml_b, ab_mask=ml_mask, ab_sel=ml_sel,
        nsa_w2=nsa_small["w2"], nsa_pe=nsa_small["pe"], nsa_b1=nsa_small["b1"], nsa_gw=nsa_small["gw"],
        nsa_gb=nsa_small["gb"], nsa_causal=nmask["causal_add"], nsa_cmp=nmask["cmp"], nsa_blocks=nmask["blocks"],
        final_norm=final_norm[None], final_g=final_g_2[None], ctx=ctx_2[0],
        cond=np.stack([columns(c_2[0]), columns(c_ctx_2)], 2).reshape(P, 16), ada_b=columns(ada_b_2[0]),
        rope=rope, band=band, pool_scale=columns(pool_scale_2[0]), decay=ret_decay_2[0].reshape(1, 8),
        ret=ret, ret_row=ret_row, ret_col=ret_col, ret_norm=columns(ret_norm_g_2[0]), iota=iota)


OUT_SHAPE = (1, T, D)


def kernel(**inputs):
    import concourse.bacc as bacc
    from concourse.bass_utils import run_bass_kernel_spmd
    arrays = layout(**{k: np.asarray(v) for k, v in inputs.items()})
    nc = bacc.Bacc("TRN2", target_bir_lowering=False, num_devices=1)
    dram, given = {}, {}
    for name, a in arrays.items():
        a = np.ascontiguousarray(a)
        given[f"in_{name}"] = a
        dram[name] = nc.dram_tensor(f"in_{name}", a.shape, mybir.dt.from_np(a.dtype), kind="ExternalInput").ap()
    out = nc.dram_tensor("out_0", OUT_SHAPE, F32, kind="ExternalOutput").ap()
    build(nc, dram, out)
    result = run_bass_kernel_spmd(nc, [given], core_ids=[0])
    return result.results[0]["out_0"]
```

```python
import concourse.bass as bass
from concourse import mybir
import numpy as np
from contextlib import ExitStack

F32 = mybir.dt.float32
F32R = mybir.dt.float32r
U32 = mybir.dt.uint32
ALU = mybir.AluOpType
ACT = mybir.ActivationFunctionType
AX = mybir.AxisListType

P = 128
T = 256
TT = T // P
D = 1024
KD = D // P
EPS = 1e-6
NEG = -1e30
D_FF = 2816
FFN_GROUPS = D_FF // 256
TILE = 2048
RAW, SPLIT = 6, 3
RG_CHUNKS = 4
CONV = 4
ML_HEADS, ML_DH = 4, 128
NSA_HEADS, NSA_GROUPS, NSA_DH = 16, 4, 64
CMP_BLOCK, CMP_STRIDE = 32, 16
N_CMP = (T - CMP_BLOCK) // CMP_STRIDE + 1
RET_HEADS, RET_DK, RET_DV = 4, 128, 256
PEER_HEADS, PEER_KEYS, PEER_TOPK = 8, 128, 16

FFN_TILES = 3 * FFN_GROUPS
G_FFN1A = 0
G_AB = G_FFN1A + FFN_TILES
G_FFN2A = G_AB + 17
G_FFN1B = G_FFN2A + FFN_TILES
G_NSA = G_FFN1B + FFN_TILES
G_FFN2B = G_NSA + 20
G_SECOND = G_FFN2B + FFN_TILES
G_PEER = G_SECOND + 57
N_TILES = G_SECOND + 66
WHOLE = {*range(G_AB, G_FFN2A), *range(G_NSA, G_FFN2B), *range(G_SECOND, N_TILES)}


class Signal:

    def __init__(self, sem):
        self.sem, self.base = sem, 0

    def at(self, n):
        return self.sem, n + self.base


class Chain:

    def __init__(self, eng, signal):
        self.eng, self.counter = eng, signal

    def __call__(self, ins):
        self.counter.base += 1
        ins.then_inc(self.counter.sem, 1)
        self.eng.wait_ge(self.counter.sem, self.counter.base)


class Arena:

    def __init__(self, nc, tag, start, end):
        self.nc, self.tag, self.at, self.end = nc, tag, start, end

    def __call__(self, name, cols, parts=P, dt=F32):
        size = (cols * 4 + 31) // 32 * 32
        t = self.nc.alloc_sbuf_tensor_at(f"{self.tag}_{name}", [parts, cols], dt, offset=self.at)
        self.at += size
        assert self.at <= self.end, (self.tag, name, self.at, self.end)
        return t[:, :]


def sbuf_plan(nc):
    base = (nc.sbuf_base + 31) // 32 * 32
    end = nc.sbuf_usable_end // 32 * 32
    ring_end = base + (RAW + 2 * SPLIT) * TILE * 4
    keep = end - (3 * 8192 + 3200)
    return base, ring_end, keep, end


class Kernel:
    def __init__(self, nc, dram, out, stages):
        self.nc, self.dram, self.out, self.stages = nc, dram, out, stages
        self.ctx = ExitStack()
        self.base, self.ring_end, self.keep, self.end = sbuf_plan(nc)
        rings = Arena(nc, "ring", self.base, self.ring_end)
        self.raw = rings("raw", RAW * TILE)
        self.high = rings("high", SPLIT * TILE, dt=F32R)
        self.low = rings("low", SPLIT * TILE, dt=F32R)
        keep = Arena(nc, "keep", self.keep, self.end)
        self.x = keep("x", TT * D).rearrange("p (t d) -> p t d", t=TT)
        self.xw = Arena(nc, "alias", keep.at, keep.at + 8192)("xT", KD * T).rearrange("p (k t) -> p k t", k=KD)
        self.spare_at = keep.at + 8192
        self.xT = tuple(keep(f"xT{n}", KD * T, dt=F32R).rearrange("p (k t) -> p k t", k=KD) for n in ("high", "low"))
        self.ident = keep("ident", P)
        self.gains = keep("gains", 8 * KD).rearrange("p (n k) -> p n k", n=8)
        self.stat = keep("stat", 64)
        self.modT = keep("modT", 48 * 2).rearrange("p (c s) -> p c s", s=2)
        self.gA = keep("gA", 4 * KD).rearrange("p (n k) -> p n k", n=4)
        self.psum = [self.ctx.enter_context(nc.psum_tensor(f"bank{i}", [P, 512], F32)) for i in range(8)]
        self.sems, self.own, self.keeping = {}, [], True
        self.next_load = self.next_high = self.next_low = 0
        self.first, self.tiles = 0, 0
        self.loaded = [self.counter(f"raw_loaded{s}") for s in range(RAW)]
        self.high_done, self.low_done, self.released = self.counters("high_made", "low_made", "tile_released")
        self.act_chain = self.counter("act_chain")
        self.dve_chain = self.counter("dve_chain")
        self.keeping = False

    def counter(self, name):
        if name not in self.sems:
            if self.keeping or name.startswith(("nrm_", "ffn_", "add_", "fn_")):
                sem = self.ctx.enter_context(self.nc.semaphore(name))
            else:
                sem = self.nc.alloc_semaphore(name)
                self.own.append((name, sem))
            self.sems[name] = Signal(sem)
        return self.sems[name]

    def end_stage(self):
        for name, _ in self.own:
            self.sems.pop(name)
        self.nc.clear_and_free_semaphores([sem for _, sem in self.own])
        self.nc.all_engine_barrier()
        self.own = []

    def counters(self, *names):
        return [self.counter(n) for n in names]

    def arena(self, tag, whole=False):
        return Arena(self.nc, tag, self.base + RAW * TILE * 4 if whole else self.ring_end, self.keep)

    def raw_slot(self, n):
        at = (n - self.first) % RAW * TILE
        return self.raw[:, at:at + TILE]

    def parts(self, n):
        at = (n - self.first) % SPLIT * TILE
        return self.high[:, at:at + TILE], self.low[:, at:at + TILE]

    def highs(self, n):
        return sum(i not in WHOLE for i in range(self.first, n + 1))

    def released_at(self, n, loop=0):
        return self.released.sem, loop + (n - self.first + 1)

    def need(self, pe, n, loop=0):
        i = n - self.first
        if n in WHOLE:
            pe.wait_ge(self.loaded[i % RAW].sem, 16 * (i // RAW + 1))
        else:
            pe.wait_ge(self.low_done.sem, loop + (i + 1))

    def make_high(self, act, n, loop=0):
        i = n - self.first
        if n in WHOLE or i >= self.tiles:
            return
        act.wait_ge(self.loaded[i % RAW].sem, (loop * 16) + 16 * (i // RAW + 1))
        if i >= SPLIT:
            act.wait_ge(self.released.sem, loop * RAW + (i - SPLIT + 1))
        self.nc.scalar.activation(self.parts(n)[0], self.raw_slot(n), ACT.Copy).then_inc(self.high_done.sem, 1)

    def make_lows(self, pool, used_end):
        end = min(used_end + SPLIT, self.first + self.tiles)

        def low(n, loop=0):
            high, low_ = self.parts(n)
            if n in WHOLE:
                if n > self.first and n - 1 not in WHOLE:
                    pool.wait_ge(self.low_done.sem, n - self.first)
                pool.sem_inc(self.low_done.sem, 1)
                return
            pool.wait_ge(self.high_done.sem, loop + self.highs(n))
            self.nc.gpsimd.tensor_tensor(low_, self.raw_slot(n), high.bitcast(F32), ALU.subtract
                                         ).then_inc(self.low_done.sem, 1)

        n = self.next_low
        while n < end:
            turns = (end - n) // RAW
            if turns >= 2 and not any(n <= i < n + turns * RAW for i in WHOLE):
                with pool.Fori(0, turns) as turn:
                    for s in range(RAW):
                        low(n + s, turn * RAW)
                n += turns * RAW
            else:
                low(n)
                n += 1
        self.next_low = end

    def loads(self, sp, used_end):
        end = min([used_end + SPLIT + RAW, self.first + self.tiles] + [w + RAW for w in WHOLE if w >= used_end])
        stream = self.dram["stream"]

        def load(n, index, loop=0):
            i = n - self.first
            if i >= RAW:
                sp.wait_ge(self.low_done.sem, loop + (i - RAW + 1))
                if n - RAW in WHOLE:
                    sp.wait_ge(*self.released_at(n - RAW))
            sp.dma_start(self.raw_slot(n), stream[bass.ds(index, 1)].rearrange("a p n -> p (a n)")
                         ).then_inc(self.loaded[i % RAW].sem, 16)

        n = self.next_load
        while n < end:
            turns = (end - n) // RAW
            if n - self.first >= RAW and turns >= 2 and not any(n - RAW <= i < n + turns * RAW for i in WHOLE):
                with sp.Fori(0, turns) as turn:
                    for s in range(RAW):
                        load(n + s, turn * RAW + (n + s), turn * RAW)
                n += turns * RAW
            else:
                load(n, n)
                n += 1
        self.next_load = max(end, self.next_load)

    def product(self, out, stationary, moving, start, stop):
        (sh, sl), (mh, ml) = stationary, moving
        mm = self.nc.tensor.matmul
        mm(out, sh, mh, start=start, stop=False)
        mm(out, sh, ml, start=False, stop=False)
        return mm(out, sl, mh, start=False, stop=stop)

    def highs_from_psum(self, act, b0, out, filled, made, scale=None, bias=None):
        s_ = self.nc.scalar
        for b in range(KD // 2):
            act.wait_ge(*filled.at(b + 1))
            for k in (2 * b, 2 * b + 1):
                v = self.psum[b0 + b][:, (k % 2) * T:(k % 2 + 1) * T]
                if bias is not None:
                    s_.activation(v, v, ACT.Identity, scale=scale[:, k:k + 1], bias=bias[:, k:k + 1]).then_inc(made.sem, 1)
            if bias is not None:
                act.wait_ge(*made.at(4 * b + 2))
            for k in (2 * b, 2 * b + 1):
                v = self.psum[b0 + b][:, (k % 2) * T:(k % 2 + 1) * T]
                if bias is None and scale is not None:
                    ins = s_.activation(out[0][:, k, :], v, ACT.Copy, scale=scale[:, k:k + 1])
                else:
                    ins = s_.activation(out[0][:, k, :], v, ACT.Copy)
                ins.then_inc(made.sem, 1)

    def lows_from_psum(self, dve, b0, out, made, low, scale=None, bias=None):
        v_ = self.nc.vector
        step = 2 if bias is None else 4
        for b in range(KD // 2):
            dve.wait_ge(*made.at(step * (b + 1)))
            for k in (2 * b, 2 * b + 1):
                v = self.psum[b0 + b][:, (k % 2) * T:(k % 2 + 1) * T]
                h = out[0][:, k, :].bitcast(F32)
                if bias is None and scale is not None:
                    ins = v_.scalar_tensor_tensor(out[1][:, k, :], v, scale[:, k:k + 1], h, ALU.mult, ALU.subtract)
                else:
                    ins = v_.tensor_tensor(out[1][:, k, :], v, h, ALU.subtract)
                ins.then_inc(low.sem, 1)

    def norm_parts(self, src, outT, scale, bias, tag, work):
        nc, stat, ps = self.nc, self.stat, self.psum
        ss, rstd = stat[:, 0:TT], stat[:, TT:2 * TT]
        xs, split = work, isinstance(outT, tuple)
        squared, mean, root, scaled, turned, high, evac = self.counters(
            "nrm_squared", "nrm_mean", "nrm_root", "nrm_scaled", "nrm_turned", "nrm_high", "nrm_low")

        def on_act(act):
            for t in range(TT):
                nc.scalar.activation(xs[:, t, :], src[:, t, :], ACT.Square,
                                     accum_out=ss[:, t:t + 1]).then_inc(squared.sem, 1)
            act.wait_ge(*mean.at(1))
            nc.scalar.activation(rstd, ss, ACT.Sqrt).then_inc(root.sem, 1)
            if split:
                self.highs_from_psum(act, 0, outT, turned, high, scale, bias)
                return
            for k in (2, 3, 6, 7):
                act.wait_ge(*turned.at(k // 2 + 1))
                nc.scalar.activation(outT[:, k, :], ps[k // 2][:, (k % 2) * T:(k % 2 + 1) * T], ACT.Identity,
                                     scale=scale[:, k:k + 1],
                                     bias=bias[:, k:k + 1] if bias is not None else 0.0).then_inc(evac.sem, 1)


        def on_dve(dve):
            link = Chain(dve, self.dve_chain)
            dve.wait_ge(*squared.at(TT))
            nc.vector.tensor_scalar(ss, ss, 1.0 / D, EPS, ALU.mult, ALU.add).then_inc(mean.sem, 1)
            dve.wait_ge(*root.at(1))
            link(nc.vector.reciprocal(rstd, rstd))
            for t in range(TT):
                nc.vector.tensor_scalar(xs[:, t, :], src[:, t, :], rstd[:, t:t + 1], None,
                                        ALU.mult).then_inc(scaled.sem, 1)
            if split:
                self.lows_from_psum(dve, 0, outT, high, evac, scale, bias)
                return
            for k in (0, 1, 4, 5):
                dve.wait_ge(*turned.at(k // 2 + 1))
                if bias is not None:
                    nc.vector.tensor_scalar(outT[:, k, :], ps[k // 2][:, (k % 2) * T:(k % 2 + 1) * T], scale[:, k:k + 1],
                                            bias[:, k:k + 1], ALU.mult, ALU.add).then_inc(evac.sem, 1)
                else:
                    nc.vector.tensor_scalar(outT[:, k, :], ps[k // 2][:, (k % 2) * T:(k % 2 + 1) * T], scale[:, k:k + 1],
                                            None, ALU.mult).then_inc(evac.sem, 1)


        def on_pe(pe):
            pe.wait_ge(*scaled.at(TT))
            for b in range(KD // 2):
                for k in (2 * b, 2 * b + 1):
                    for t in range(TT):
                        last = nc.tensor.transpose(ps[b][:, (k % 2) * T + t * P:(k % 2) * T + (t + 1) * P],
                                                   xs[:, t, k * P:(k + 1) * P], self.ident)
                last.then_inc(turned.sem, 1)
            pe.wait_ge(*evac.at(KD))

        def end():
            squared.base += TT
            mean.base += 1
            root.base += 1
            scaled.base += TT
            turned.base += KD // 2
            evac.base += KD
            if split:
                high.base += KD if bias is None else 2 * KD
        return on_act, on_dve, on_pe, end

    def start(self):
        nc = self.nc
        (here,) = self.counters("start_loaded")
        with nc.Block() as block:
            @block.sync
            def _(sp):
                sp.dma_start(self.x, self.dram["x"].rearrange("(t p) d -> p t d", p=P)).then_inc(here.sem, 16)
                sp.dma_start(self.ident, self.dram["ident"]).then_inc(here.sem, 16)
                sp.dma_start(self.gains, self.dram["gains"].rearrange("p (n k) -> p n k", k=KD)).then_inc(here.sem, 16)
                self.loads(sp, self.first)
                sp.wait_ge(*here.at(48))

            @block.scalar
            def _(act):
                for n in range(SPLIT):
                    self.make_high(act, self.first + n)

            @block.gpsimd
            def _(pool):
                self.make_lows(pool, self.first)
        here.base += 48

    def ffn(self, g0, gain):
        nc, ps = self.nc, self.psum
        work = self.arena(f"ffn{g0}")
        xs = work("xs", TT * D).rearrange("p (t d) -> p t d", t=TT)
        sg = [work(f"silu{t}", 256) for t in range(TT)]
        h = [work(f"h{t}", 256) for t in range(TT)]
        hT = [[work(f"hT{t}{n}", 256, dt=F32R) for n in range(2)] for t in range(TT)]
        norm_act, norm_dve, norm_pe, norm_end = self.norm_parts(
            self.x, self.xT, self.gains[:, gain, :], None, f"ffn{g0}", xs)
        silu = self.counters("ffn_silu0", "ffn_silu1")
        made = self.counters("ffn_h0", "ffn_h1")
        turned = self.counters("ffn_turned0", "ffn_turned1")
        hready = self.counters("ffn_hT0", "ffn_hT1")
        hhigh, acc = self.counters("ffn_hThigh", "ffn_acc")
        N = FFN_GROUPS
        TURNS = (N - 3) // 2
        tile_a = lambda i: g0 + (3 * i - 1 if i else 0)
        tile_b = lambda i: tile_a(i) + 1
        tile_d = lambda i: g0 + 3 * i + 4 if i < N - 1 else g0 + 3 * N - 1
        bank = lambda i, t: ps[2 * (i % 2) + t]

        with nc.Block() as block:
            @block.sync
            def _(sp):
                self.loads(sp, g0 + FFN_TILES)

            @block.gpsimd
            def _(pool):
                self.make_lows(pool, g0 + FFN_TILES)

            @block.tensor
            def _(pe):
                norm_pe(pe)

                def gate_up(i, second, loop):
                    n = tile_b(i) if second else tile_a(i)
                    self.need(pe, n, 3 * loop)
                    high, low = self.parts(n)
                    for k in range(4):
                        cut = slice(k * 512, (k + 1) * 512)
                        for t in range(TT):
                            kk = k + 4 * second
                            last = self.product(bank(i, t)[:, :], [x[:, kk, t * P:(t + 1) * P] for x in self.xT],
                                                (high[:, cut], low[:, cut]), kk == 0, kk == KD - 1)
                    last.then_inc(self.released.sem, 1)

                def turn(i, loop):
                    for t in range(TT):
                        pe.wait_ge(*made[t].at(loop + (i + 1)))
                        for f in range(2):
                            last = nc.tensor.transpose(bank(i, t)[:, f * P:(f + 1) * P],
                                                       h[t][:, f * P:(f + 1) * P], self.ident)
                        last.then_inc(turned[t].sem, 1)

                def down(i, loop, start, stop):
                    n = tile_d(i)
                    self.need(pe, n, 3 * loop)
                    high, low = self.parts(n)
                    for t in range(TT):
                        pe.wait_ge(*hready[t].at(loop + (i + 1)))
                        for f in range(2):
                            for half in range(2):
                                cut = slice(f * 1024 + half * 512, f * 1024 + (half + 1) * 512)
                                last = self.product(ps[4 + 2 * t + half][:, :], [x[:, f * P:(f + 1) * P] for x in hT[t]],
                                                    (high[:, cut], low[:, cut]), start and f == 0, stop and f == 1)
                    last.then_inc(self.released.sem, 1)

                def group(i, loop=0):
                    if i >= 2:
                        for t in range(TT):
                            pe.wait_ge(*hready[t].at(loop + (i - 1)))
                    gate_up(i, 0, loop)
                    if i:
                        turn(i - 1, loop)
                    gate_up(i, 1, loop)
                    if i:
                        down(i - 1, loop, i == 1, False)

                group(0)
                group(1)
                with pe.Fori(0, TURNS) as turns:
                    for i in (2, 3):
                        group(i, turns * 2)
                group(N - 1)
                turn(N - 1, 0)
                down(N - 1, 0, False, True)

            @block.scalar
            def _(act):
                norm_act(act)

                def step(i, loop=0, tiles=0):
                    if i:
                        self.make_high(act, tile_a(i) + SPLIT, loop)
                    else:
                        self.make_high(act, g0 + SPLIT)
                    act.wait_ge(*self.released_at(tile_b(i), loop * RAW))
                    for t in range(TT):
                        if i:
                            act.wait_ge(*made[t].at(loop * 2 + i))
                        nc.scalar.activation(sg[t], bank(i, t)[:, 0:256], ACT.Silu).then_inc(silu[t].sem, 1)
                    self.make_high(act, tile_b(i) + SPLIT, loop)
                    if i:
                        self.make_high(act, tile_b(i) + 1 + SPLIT, loop)

                step(0)
                step(1)
                with act.Fori(0, TURNS) as turns:
                    for i in (2, 3):
                        step(i, turns)
                step(N - 1)
                self.make_high(act, g0 + FFN_TILES - 1 + SPLIT)

            @block.vector
            def _(dve):
                norm_dve(dve)

                def step(i, loop=0):
                    for t in range(TT):
                        dve.wait_ge(*silu[t].at(loop + (i + 1)))
                        if i:
                            dve.wait_ge(*turned[t].at(loop + i))
                        nc.vector.tensor_tensor(h[t], sg[t], bank(i, t)[:, 256:512], ALU.mult
                                                ).then_inc(made[t].sem, 1)
                    if i:
                        dve.wait_ge(*self.released_at(tile_d(i - 1), loop * 3))
                    for t in range(TT):
                        dve.wait_ge(*turned[t].at(loop + (i + 1)))
                        v = bank(i, t)[:, 0:256]
                        nc.vector.tensor_copy(hT[t][0], v).then_inc(hhigh.sem, 1)
                        dve.wait_ge(*hhigh.at(loop * 2 + (2 * i + t + 1)))
                        nc.vector.tensor_tensor(hT[t][1], v, hT[t][0].bitcast(F32), ALU.subtract
                                                ).then_inc(hready[t].sem, 1)

                step(0)
                step(1)
                with dve.Fori(0, TURNS) as turns:
                    for i in (2, 3):
                        step(i, turns * 2)
                step(N - 1)
                dve.wait_ge(*self.released_at(tile_d(N - 1)))
                for t in range(TT):
                    for half in range(2):
                        xv = self.x[:, t, half * 512:(half + 1) * 512]
                        last = nc.vector.scalar_tensor_tensor(xv, ps[4 + 2 * t + half][:, :], 0.5, xv,
                                                              ALU.mult, ALU.add)
                last.then_inc(acc.sem, 1)
                dve.wait_ge(*acc.at(1))
        norm_end()
        for s in silu + made + turned + hready:
            s.base += N
        hhigh.base += 2 * N
        acc.base += 1

    def store(self, src):
        nc = self.nc
        (stored,) = self.counters("stored")
        with nc.Block() as block:
            @block.sync
            def _(sp):
                sp.dma_start(self.out[0].rearrange("(t p) d -> p t d", p=P), src).then_inc(stored.sem, 16)
                sp.wait_ge(*stored.at(16))
        stored.base += 16

    def ring_tile(self, pe, g0, t):
        if g0 + t not in self.waited:
            self.waited.add(g0 + t)
            self.need(pe, g0 + t)
        return self.raw_slot(g0 + t)

    def mm(self, out, lhsT, rhs, start, stop):
        ins = self.nc.tensor.matmul(out, lhsT, rhs, start=start, stop=stop)
        if self.owed:
            self.owed -= 1
            ins.then_inc(self.released.sem, 1)
        return ins

    def give_back(self, t):
        self.owed += 1

    def flush(self, pe, done):
        pe.wait_ge(*done)
        while self.owed:
            self.owed -= 1
            pe.sem_inc(self.released.sem, 1)

    def stationary_cols(self, out, w, c, actT):
        for k in range(KD):
            last = self.mm(out, w[:, k * 256 + c * P:k * 256 + (c + 1) * P], actT[:, k, :], k == 0, k == KD - 1)
        return last

    def moving_cols(self, pe, out, g0, tile, actT, t):
        for k in range(KD):
            w = self.ring_tile(pe, g0, tile + k // 4)[:, (k % 4) * 512:(k % 4 + 1) * 512]
            last = self.mm(out, actT[:, k, t * P:(t + 1) * P], w, k == 0, k == KD - 1)
        return last

    def rows_product(self, pe, g0, tile, actT, kn, banks, done):
        for k in range(kn):
            w = self.ring_tile(pe, g0, tile + k // 2)
            for t in range(TT):
                for half in range(2):
                    at = (k % 2) * D + half * 512
                    last = self.mm(self.psum[banks[2 * t + half]][:, :], actT[:, k, t * P:(t + 1) * P],
                                   w[:, at:at + 512], k == 0, k == kn - 1)
            if k % 2 == 1:
                self.give_back(tile + k // 2)
        last.then_inc(done.sem, 1)

    def begin_stage(self):
        self.waited, self.owed = set(), 0

    def ab(self):
        nc, ps, G = self.nc, self.psum, G_AB
        v_, s_ = nc.vector, nc.scalar
        self.begin_stage()
        work = self.arena("ab", whole=True)
        taps = work("taps", 60).rearrange("p (m k) -> p m k", k=5)
        cols = work("cols", 16).rearrange("p (n c) -> p n c", c=4)
        wif = work("wif", 64).rearrange("p (k f) -> p k f", f=8)
        bif = work("bif", 2, parts=4)
        mask = work("mask", 384)
        sel = work("sel", 512, parts=4)
        xs = work("xs", TT * D).rearrange("p (t d) -> p t d", t=TT)
        xa = work("xa", 4 * (T + 3)).rearrange("p (c t) -> p c t", c=4)
        qk = work("qk", 8 * (T + 3)).rearrange("p (c t) -> p c t", c=8)
        ga = work("ga", 4 * T).rearrange("p (c t) -> p c t", c=4)
        v1 = work("v1", TT * 4 * 129).rearrange("p (t h d) -> p t h d", t=TT, h=4)
        so = work("so", TT * 512).rearrange("p (t d) -> p t d", t=TT)
        xc = work("xc", 4 * T).rearrange("p (c t) -> p c t", c=4)
        qc = work("qc", 8 * T).rearrange("p (c t) -> p c t", c=8)
        r = work("r", 4 * T).rearrange("p (c t) -> p c t", c=4)
        ig = work("ig", 4 * T).rearrange("p (c t) -> p c t", c=4)
        a = work("a", 4 * T).rearrange("p (c t) -> p c t", c=4)
        u = work("u", 4 * T).rearrange("p (c t) -> p c t", c=4)
        row = [work(f"row{i}", T, parts=4) for i in range(7)]
        ir, fr, mn, ex, cumf, al, ones = row
        big = work("E", 4 * 384).rearrange("p (h n) -> p h n", h=4)
        tiny = work("tiny", 96)
        Hn = work("Hn", TT * 4 * 129).rearrange("p (t h d) -> p t h d", t=TT, h=4)
        yT = self.xw
        small, done, freed, conv, z = self.counters("ab_small", "ab_done", "ab_freed", "ab_conv", "ab_padded")
        norm_act, norm_dve, norm_pe, norm_end = self.norm_parts(
            self.x, self.xw, self.gains[:, 1, :], None, "ab", xs)

        with nc.Block() as block:
            @block.sync
            def _(sp):
                for dst, name in ((taps.rearrange("p m k -> p (m k)"), "ab_taps"), (cols.rearrange("p n c -> p (n c)"), "ab_cols"),
                                  (wif.rearrange("p k f -> p (k f)"), "ab_if"), (bif, "ab_b"),
                                  (mask, "ab_mask"), (sel, "ab_sel")):
                    sp.dma_start(dst, self.dram[name]).then_inc(small.sem, 16)
                self.loads(sp, G + 12)

            @block.gpsimd
            def _(pool):
                self.make_lows(pool, G + 12)
                nc.gpsimd.memset(xa[:, :, 0:3], 0.0).then_inc(z.sem, 1)
                nc.gpsimd.memset(qk[:, :, 0:3], 0.0).then_inc(z.sem, 1)
                nc.gpsimd.memset(v1[:, :, :, 128:129], 1.0).then_inc(z.sem, 1)
                nc.gpsimd.memset(ones, 1.0).then_inc(z.sem, 1)

            @block.tensor
            def _(pe):
                norm_pe(pe)
                for n in range(16):
                    if n >= 4:
                        pe.wait_ge(*freed.at(n - 3))
                    w = self.ring_tile(pe, G, n // 2)
                    self.stationary_cols(ps[n % 4][:, 0:T], w, n % 2, self.xw).then_inc(done.sem, 1)
                    if n % 2:
                        self.give_back(n // 2)
                for n in range(16, 20):
                    pe.wait_ge(*freed.at(n - 3))
                    tile = 8 + 2 * ((n - 16) // 2)
                    self.moving_cols(pe, ps[n % 4][:, :], G, tile, self.xw, n % 2).then_inc(done.sem, 1)
                    if n % 2:
                        self.give_back(tile)
                        self.give_back(tile + 1)
                pe.wait_ge(*freed.at(17))
                pe.wait_ge(*small.at(96))
                for f in range(2):
                    for k in range(KD):
                        last = self.mm(ps[0][0:4, f * T:(f + 1) * T], wif[:, k, 4 * f:4 * f + 4],
                                       self.xw[:, k, :], k == 0, k == KD - 1)
                last.then_inc(done.sem, 1)

            @block.scalar
            def _(act):
                norm_act(act)
                for n in range(20):
                    act.wait_ge(*done.at(n + 1))
                    src = ps[n % 4]
                    if n < 4:
                        ins = s_.activation(xa[:, n, 3:], src[:, 0:T], ACT.Copy)
                    elif n < 8:
                        ins = s_.activation(ga[:, n - 4, :], src[:, 0:T], ACT.Gelu_apprx_tanh)
                    elif n < 16:
                        ins = s_.activation(qk[:, n - 8, 3:], src[:, 0:T], ACT.Copy)
                    elif n < 18:
                        ins = s_.activation(v1[:, n - 16, :, 0:128], src[:, :].rearrange("p (h d) -> p h d", h=4), ACT.Copy)
                    else:
                        ins = s_.activation(so[:, n - 18, :], src[:, :], ACT.Sigmoid)
                    ins.then_inc(freed.sem, 1)
                act.wait_ge(*done.at(21))
                act.wait_ge(*small.at(96))
                s_.activation(ir, ps[0][0:4, 0:T], ACT.Identity, bias=bif[:, 0:1]).then_inc(freed.sem, 1)
                s_.activation(fr, ps[0][0:4, T:2 * T], ACT.Identity, bias=bif[:, 1:2]).then_inc(freed.sem, 1)
                for c in range(8):
                    act.wait_ge(*conv.at(5 + c))
                    s_.activation(qc[:, c, :], qc[:, c, :], ACT.Silu).then_inc(freed.sem, 1)

            @block.vector
            def _(dve):
                norm_dve(dve)
                link = Chain(dve, self.dve_chain)
                dve.wait_ge(*small.at(96))
                dve.wait_ge(*z.at(4))
                for m in range(12):
                    src, dst = (xa[:, m, :], xc[:, m, :]) if m < 4 else (qk[:, m - 4, :], qc[:, m - 4, :])
                    dve.wait_ge(*freed.at(m + 1 if m < 4 else m + 5))
                    link(v_.tensor_scalar(dst, src[:, 0:T], taps[:, m, 0:1], taps[:, m, 4:5], ALU.mult, ALU.add))
                    for j in range(1, CONV):
                        ins = v_.scalar_tensor_tensor(dst, src[:, j:j + T], taps[:, m, j:j + 1], dst, ALU.mult, ALU.add)
                        if j < CONV - 1:
                            link(ins)
                    ins.then_inc(conv.sem, 1)
        norm_end()
        done.base += 21
        freed.base += 30
        conv.base += 12
        z.base += 4

        lam = tiny[:, 0:4]
        y, s1, s2, q_, negc, posc, mx = (tiny[:, 4 * i:4 * i + 4] for i in range(1, 8))
        aCol = tiny[:, 32:40]
        em = tiny[:, 40:48]
        dn, rc, ss, rt = (tiny[:, 48 + 8 * i:56 + 8 * i] for i in range(4))
        gates, sig, lamy, lamc, decays, u2, root, hs, ydone = self.counters(
            "ab_gates", "ab_sig", "ab_lamy", "ab_lamc", "ab_decays", "ab_u2", "ab_root", "ab_hs", "ab_y")
        r1, r3, r4, turned, colsr, mrow, sdone, e1, e2, pready, pv, hn, n1, n2, n3, turn2, yb = self.counters(
            "ml_arg", "ml_ln", "ml_rows", "ml_turned", "ml_cols", "ml_bcast", "ml_scores", "ml_e1",
            "ml_e2", "ml_p", "ml_pv", "ml_hn", "ml_ss", "ml_rt", "ml_yb", "ml_turn2", "ml_yT")
        ln_ = row[3]
        with nc.Block() as block:
            @block.sync
            def _(sp):
                self.loads(sp, G + 13)

            @block.gpsimd
            def _(pool):
                self.make_lows(pool, G + 13)

            @block.tensor
            def _(pe):
                w = self.ring_tile(pe, G, 12)
                for m in range(2):
                    for c in range(4):
                        last = self.mm(ps[2 * m + c // 2][:, (c % 2) * T:(c % 2 + 1) * T],
                                       w[:, (4 * m + c) * P:(4 * m + c + 1) * P], xc[:, c, :], True, True)
                    last.then_inc(gates.sem, 1)
                self.give_back(12)
                self.flush(pe, gates.at(2))
                pe.wait_ge(*sig.at(4))
                def scores(h):
                    b = ps[6 + h % 2]
                    nc.tensor.matmul(b[:, 0:256], qc[:, 4 + h, 0:P], qc[:, h, :], start=True, stop=True)
                    nc.tensor.matmul(b[:, 256:384], qc[:, 4 + h, P:T], qc[:, h, P:T], start=True, stop=True
                                     ).then_inc(sdone.sem, 1)
                scores(0)
                scores(1)
                pe.wait_ge(*r4.at(1))
                for n, rw in enumerate((al, mn)):
                    for t in range(TT):
                        last = nc.tensor.transpose(ps[3][:, 8 * n + 4 * t:8 * n + 4 * t + 4],
                                                   rw[:, t * P:(t + 1) * P], self.ident[0:4, 0:4])
                last.then_inc(turned.sem, 1)
                for h in range(4):
                    last = nc.tensor.matmul(ps[4 + h // 2][:, (h % 2) * T:(h % 2 + 1) * T],
                                            sel[:, h * P:(h + 1) * P], ex, start=True, stop=True)
                last.then_inc(mrow.sem, 1)
                for h in range(4):
                    pe.wait_ge(*pready.at(h + 1))
                    if h < 2:
                        scores(h + 2)
                    else:
                        pe.wait_ge(*hn.at(h - 1))
                    b = ps[h % 2]
                    nc.tensor.matmul(b[:, 0:129], big[:, h, 0:P], v1[:, 0, h, :], start=True, stop=True)
                    nc.tensor.matmul(b[:, 256:385], big[:, h, P:T], v1[:, 0, h, :], start=True, stop=False)
                    nc.tensor.matmul(b[:, 256:385], big[:, h, T:T + P], v1[:, 1, h, :], start=False, stop=True
                                     ).then_inc(pv.sem, 1)
                pe.wait_ge(*n3.at(1))
                for c in range(4):
                    for t in range(TT):
                        last = nc.tensor.transpose(ps[4 + c // 2][:, (c % 2) * T + t * P:(c % 2) * T + (t + 1) * P],
                                                   xs[:, t, c * P:(c + 1) * P], self.ident)
                last.then_inc(turn2.sem, 1)

            @block.scalar
            def _(act):
                link = Chain(act, self.act_chain)
                act.wait_ge(*r1.at(1))
                s_.activation(y, y, ACT.Exp).then_inc(lamy.sem, 1)
                link(s_.activation(ex, ex, ACT.Exp))
                s_.activation(ln_, ex, ACT.Ln, bias=1.0).then_inc(r3.sem, 1)
                act.wait_ge(*gates.at(2))
                for m, dst in enumerate((r, ig)):
                    for c in range(4):
                        ins = s_.activation(dst[:, c, :], ps[2 * m + c // 2][:, (c % 2) * T:(c % 2 + 1) * T],
                                            ACT.Sigmoid, bias=cols[:, m, c:c + 1])
                        if c % 2:
                            ins.then_inc(sig.sem, 1)
                act.wait_ge(*sig.at(4))
                act.wait_ge(*lamc.at(1))
                for c in range(4):
                    s_.activation(a[:, c, :], r[:, c, :], ACT.Exp, scale=negc[:, c:c + 1])
                    s_.activation(u[:, c, :], r[:, c, :], ACT.Tanh, scale=posc[:, c:c + 1]).then_inc(decays.sem, 1)
                act.wait_ge(*turned.at(1))
                link(s_.activation(aCol, ps[3][:, 0:8], ACT.Copy))
                s_.activation(em, ps[3][:, 8:16], ACT.Exp, scale=-1.0).then_inc(colsr.sem, 1)
                for h in range(4):
                    act.wait_ge(*e1.at(h + 1))
                    s_.activation(big[:, h, :], big[:, h, :], ACT.Exp).then_inc(e2.sem, 1)
                act.wait_ge(*u2.at(1))
                s_.activation(u.rearrange("p c t -> p (c t)"), u.rearrange("p c t -> p (c t)"), ACT.Sqrt
                              ).then_inc(root.sem, 1)
                for h in range(4):
                    act.wait_ge(*pv.at(h + 1))
                    s_.activation(Hn[:, :, h, :], ps[h % 2][:, :].rearrange("p (t n) -> p t n", t=2)[:, :, 0:129],
                                  ACT.Copy).then_inc(hn.sem, 1)
                act.wait_ge(*n1.at(1))
                s_.activation(rt, ss, ACT.Sqrt).then_inc(n2.sem, 1)

            @block.vector
            def _(dve):
                link = Chain(dve, self.dve_chain)
                lam_ = cols[:, 2, :]
                link(v_.tensor_scalar(mx, lam_, -1.0, 0.0, ALU.mult, ALU.max))
                link(v_.tensor_scalar(s1, lam_, 0.0, None, ALU.max))
                link(v_.scalar_tensor_tensor(y, s1, -1.0, mx, ALU.mult, ALU.subtract))
                link(v_.tensor_scalar(mn, fr, 0.0, None, ALU.min))
                v_.scalar_tensor_tensor(ex, mn, 2.0, fr, ALU.mult, ALU.subtract).then_inc(r1.sem, 1)
                dve.wait_ge(*lamy.at(1))
                link(v_.tensor_scalar(s1, y, 2.0, None, ALU.add))
                link(v_.reciprocal(s1, s1))
                link(v_.tensor_tensor(s1, s1, y, ALU.mult))
                link(v_.tensor_tensor(s2, s1, s1, ALU.mult))
                link(v_.tensor_scalar(q_, s2, 1.0 / 15, None, ALU.mult))
                for o in (13, 11, 9, 7, 5, 3):
                    link(v_.scalar_tensor_tensor(q_, q_, 1.0 / o, s2, ALU.add, ALU.mult))
                link(v_.scalar_tensor_tensor(q_, q_, 1.0, s1, ALU.add, ALU.mult))
                link(v_.scalar_tensor_tensor(q_, q_, 2.0, mx, ALU.mult, ALU.add))
                link(v_.tensor_scalar(posc, q_, 8.0, None, ALU.mult))
                v_.tensor_scalar(negc, q_, -8.0, None, ALU.mult).then_inc(lamc.sem, 1)
                dve.wait_ge(*r3.at(1))
                link(v_.tensor_tensor(fr, mn, ln_, ALU.subtract))
                link(v_.tensor_tensor_scan(cumf, ones, fr, 0.0, ALU.mult, ALU.add))
                link(v_.tensor_tensor(al, ir, cumf, ALU.subtract))
                link(v_.tensor_tensor_scan(fr, al, al, NEG, ALU.max, ALU.max))
                link(v_.tensor_scalar(ex, fr, -1.0, None, ALU.mult))
                v_.tensor_tensor(mn, fr, cumf, ALU.add).then_inc(r4.sem, 1)
                dve.wait_ge(*colsr.at(1))
                dve.wait_ge(*mrow.at(1))
                for h in range(4):
                    mb = ps[4 + h // 2][:, (h % 2) * T:(h % 2 + 1) * T]
                    v_.tensor_scalar(big[:, h, 0:T], mb, aCol[:, h:h + 1], 0.0, ALU.add, ALU.min)
                    v_.tensor_scalar(big[:, h, T:], mb[:, P:T], aCol[:, 4 + h:5 + h], 0.0, ALU.add, ALU.min
                                     ).then_inc(e1.sem, 1)
                dve.wait_ge(*decays.at(4))
                link(v_.tensor_tensor(r, a, a, ALU.mult))
                v_.scalar_tensor_tensor(u.rearrange("p c t -> p (c t)"), r.rearrange("p c t -> p (c t)"), 1.0,
                                        u.rearrange("p c t -> p (c t)"), ALU.add, ALU.mult).then_inc(u2.sem, 1)
                for h in range(4):
                    dve.wait_ge(*e2.at(h + 1))
                    link(v_.tensor_tensor(big[:, h, :], big[:, h, :], mask, ALU.mult))
                    dve.wait_ge(*sdone.at(h + 1))
                    v_.tensor_tensor(big[:, h, :], big[:, h, :], ps[6 + h % 2][:, 0:384], ALU.mult
                                     ).then_inc(pready.sem, 1)
                link(v_.tensor_tensor(ig, ig, xc, ALU.mult))
                dve.wait_ge(*root.at(1))
                link(v_.tensor_tensor(u, u, ig, ALU.mult))
                for c in range(4):
                    v_.tensor_tensor_scan(r[:, c, :], a[:, c, :], u[:, c, :], 0.0, ALU.mult, ALU.add).then_inc(hs.sem, 1)
                dve.wait_ge(*hs.at(4))
                v_.tensor_tensor(yT[:, 0:4, :], ga, r, ALU.mult).then_inc(ydone.sem, 1)
                dve.wait_ge(*hn.at(4))
                heads = Hn.rearrange("p t h d -> p (t h) d")
                link(v_.tensor_copy(rc.unsqueeze(2), heads[:, :, 128:129]))
                link(v_.scalar_tensor_tensor(dn, rc, -1.0, rc, ALU.mult, ALU.max))
                link(v_.tensor_tensor(dn, dn, em, ALU.max))
                link(v_.reciprocal(rc, dn))
                link(v_.tensor_tensor(heads[:, :, 0:128], heads[:, :, 0:128],
                                      rc.unsqueeze(2).to_broadcast([P, 8, 128]), ALU.mult))
                sq = xs.rearrange("p t (h d) -> p (t h) d", d=128)[:, 0:8, :]
                link(v_.tensor_tensor(sq, heads[:, :, 0:128], heads[:, :, 0:128], ALU.mult))
                link(v_.tensor_reduce(ss, sq, AX.X, ALU.add))
                v_.tensor_scalar(ss, ss, 1.0 / ML_DH, EPS, ALU.mult, ALU.add).then_inc(n1.sem, 1)
                dve.wait_ge(*n2.at(1))
                link(v_.reciprocal(rt, rt))
                link(v_.tensor_tensor(heads[:, :, 0:128], heads[:, :, 0:128],
                                      rt.unsqueeze(2).to_broadcast([P, 8, 128]), ALU.mult))
                for t in range(TT):
                    ins = v_.tensor_tensor(xs[:, t, 0:512].rearrange("p (h d) -> p h d", h=4), Hn[:, t, :, 0:128],
                                           so[:, t, :].rearrange("p (h d) -> p h d", h=4), ALU.mult)
                    if t == 0:
                        link(ins)
                ins.then_inc(n3.sem, 1)
                dve.wait_ge(*turn2.at(1))
                for c in range(4):
                    v_.tensor_scalar(yT[:, 4 + c, :], ps[4 + c // 2][:, (c % 2) * T:(c % 2 + 1) * T],
                                     cols[:, 3, c:c + 1], None, ALU.mult).then_inc(yb.sem, 1)
        for s, n in ((gates, 2), (sig, 4), (lamy, 1), (lamc, 1), (decays, 4), (u2, 1), (root, 1), (hs, 4), (ydone, 1),
                     (r1, 1), (r3, 1), (r4, 1), (turned, 1), (colsr, 1), (mrow, 1), (sdone, 4), (e1, 4), (e2, 4),
                     (pready, 4), (pv, 4), (hn, 4), (n1, 1), (n2, 1), (n3, 1), (turn2, 1), (yb, 4)):
            s.base += n
        small.base += 96
        self.add_rows_product(G, 13, yT, KD, G + 17)

    def add_rows_product(self, g0, tile, actT, kn, end, scale=None):
        nc, ps = self.nc, self.psum
        done, added = self.counters("add_done", "add_added")
        with nc.Block() as block:
            @block.sync
            def _(sp):
                self.loads(sp, end)

            @block.tensor
            def _(pe):
                self.rows_product(pe, g0, tile, actT, kn, (0, 1, 2, 3), done)
                self.flush(pe, done.at(1))

            @block.scalar
            def _(act):
                for n in range(SPLIT):
                    self.make_high(act, end + n)

            @block.gpsimd
            def _(pool):
                self.make_lows(pool, end)

            @block.vector
            def _(dve):
                dve.wait_ge(*done.at(1))
                for t in range(TT):
                    for half in range(2):
                        xv = self.x[:, t, half * 512:(half + 1) * 512]
                        if scale is None:
                            nc.vector.tensor_tensor(xv, ps[2 * t + half][:, :], xv, ALU.add).then_inc(added.sem, 1)
                dve.wait_ge(*added.at(4))
        done.base += 1
        added.base += 4

    def final_norm(self, name):
        nc = self.nc
        work = self.arena(name)
        gain = work("gain", D)
        sq = work("sq", TT * D).rearrange("p (t d) -> p t d", t=TT)
        ss = self.stat[:, 0:2]
        here, a_, b_, c_, d_ = self.counters("fn_here", "fn_sq", "fn_mean", "fn_root", "fn_x")
        with nc.Block() as block:
            @block.sync
            def _(sp):
                sp.dma_start(gain, self.dram[name].partition_broadcast(P).rearrange("p a d -> p (a d)")).then_inc(here.sem, 16)

            @block.scalar
            def _(act):
                for t in range(TT):
                    nc.scalar.activation(sq[:, t, :], self.x[:, t, :], ACT.Square, accum_out=ss[:, t:t + 1]).then_inc(a_.sem, 1)
                act.wait_ge(*b_.at(1))
                nc.scalar.activation(ss, ss, ACT.Sqrt).then_inc(c_.sem, 1)

            @block.vector
            def _(dve):
                link = Chain(dve, self.dve_chain)
                dve.wait_ge(*a_.at(2))
                nc.vector.tensor_scalar(ss, ss, 1.0 / D, EPS, ALU.mult, ALU.add).then_inc(b_.sem, 1)
                dve.wait_ge(*c_.at(1))
                link(nc.vector.reciprocal(ss, ss))
                dve.wait_ge(*here.at(16))
                for t in range(TT):
                    nc.vector.scalar_tensor_tensor(self.x[:, t, :], self.x[:, t, :], ss[:, t:t + 1], gain,
                                                   ALU.mult, ALU.mult).then_inc(d_.sem, 1)
                dve.wait_ge(*d_.at(2))
        here.base += 16
        a_.base += 2
        b_.base += 1
        c_.base += 1
        d_.base += 2

    def nsa(self):
        nc, ps, G = self.nc, self.psum, G_NSA
        v_, s_ = nc.vector, nc.scalar
        self.begin_stage()
        SC = NSA_DH ** -0.5
        work = self.arena("nsa", whole=True)
        w2 = work("w2", 384).rearrange("p (k n) -> p k n", k=2)
        pe_ = work("pe", 32)
        b1 = work("b1", 4)
        gw = work("gw", 384).rearrange("p (k n) -> p k n", k=KD)
        gb = work("gb", 48)
        causal = work("causal", 384)
        cm = work("cm", 32).rearrange("p (t n) -> p t n", t=TT)
        cneg = work("cneg", 32).rearrange("p (t n) -> p t n", t=TT)
        blocks = work("blocks", 8)
        xs = work("xs", TT * D).rearrange("p (t d) -> p t d", t=TT)
        qT = work("qT", 8 * T).rearrange("p (c t) -> p c t", c=8)
        kT = [work(f"kT{i}", 2 * T).rearrange("p (c t) -> p c t", c=2) for i in range(2)]
        X = [work(f"cmpX{i}", 5 * T).rearrange("p (g t) -> p g t", g=5) for i in range(2)]
        vv = work("vv", TT * 512).rearrange("p (t n) -> p t n", t=TT)
        gates = work("gates", TT * 48).rearrange("p (t h b) -> p t h b", t=TT, b=3)
        hid = [work(f"hid{i}", 2 * 64).rearrange("p (c g n) -> p c g n", c=2, g=4) for i in range(2)]
        bcol = work("bcol", 4)
        hidR = work("hidR", 4 * P).rearrange("p (a c n) -> p a c n", a=2, c=2)
        kcT = work("kcT", 64)
        R = work("R", 128).rearrange("p (a d) -> p a d", a=2)
        Vbd = work("Vbd", 2 * 512).rearrange("p (a h d) -> p a h d", a=2, h=8)
        Sc = work("Sc", TT * 256).rearrange("p (t h n) -> p t h n", t=TT, h=16)
        cs = work("cs", 96)
        cPT = work("cPT", 512)
        SB = [work(f"SB{i}", 384) for i in range(4)]
        PT = [work(f"PT{i}", 384) for i in range(4)]
        m3 = [work(f"m3_{i}", 4) for i in range(4)]
        nm = [work(f"nm{i}", 2) for i in range(4)]
        sums = [work(f"sums{i}", 2) for i in range(4)]
        coef = [work(f"coef{i}", 2) for i in range(4)]
        small, done, fa, fd, z, gsum = self.counters("nsa_small", "nsa_done", "nsa_freed_act", "nsa_freed_dve",
                                                    "nsa_zero", "nsa_gates")
        norm_act, norm_dve, norm_pe, norm_end = self.norm_parts(
            self.x, self.xw, self.gains[:, 4, :], None, "nsa", xs)
        UNITS = 23

        with nc.Block() as block:
            @block.sync
            def _(sp):
                for dst, name in ((w2.rearrange("p k n -> p (k n)"), "nsa_w2"), (pe_, "nsa_pe"), (b1, "nsa_b1"),
                                  (gw.rearrange("p k n -> p (k n)"), "nsa_gw"), (causal[:, 0:P], "nsa_causal"),
                                  (causal[:, T:], "nsa_causal"), (cm.rearrange("p t n -> p (t n)"), "nsa_cmp"),
                                  (blocks, "nsa_blocks")):
                    sp.dma_start(dst, self.dram[name]).then_inc(small.sem, 16)
                sp.dma_start(gb, self.dram["nsa_gb"].partition_broadcast(P).rearrange("p a d -> p (a d)")).then_inc(small.sem, 16)
                self.loads(sp, G + 12)

            @block.gpsimd
            def _(pool):
                self.make_lows(pool, G + 12)
                g_ = nc.gpsimd
                g_.memset(causal[:, P:T], 0.0).then_inc(z.sem, 1)
                for i in range(2):
                    g_.memset(X[i][:, 4, :], 0.0).then_inc(z.sem, 1)
                    g_.memset(hid[i].rearrange("p c g n -> p (c g n)"), 0.0).then_inc(z.sem, 1)
                g_.memset(kcT, 0.0).then_inc(z.sem, 1)

            @block.tensor
            def _(pe):
                norm_pe(pe)
                for n in range(UNITS):
                    if n >= 4:
                        pe.wait_ge(*(fd if n % 2 else fa).at((n - 4) // 2 + 1))
                    b = ps[n % 4]
                    if n < 20:
                        w = self.ring_tile(pe, G, n // 2)
                        self.stationary_cols(b[:, 0:T], w, n % 2, self.xw).then_inc(done.sem, 1)
                        if n % 2:
                            self.give_back(n // 2)
                    elif n < 22:
                        self.moving_cols(pe, b[:, :], G, 10, self.xw, n % 2).then_inc(done.sem, 1)
                        if n % 2:
                            self.give_back(10)
                            self.give_back(11)
                    else:
                        pe.wait_ge(*small.at(16 * 9))
                        for t in range(TT):
                            for k in range(KD):
                                last = self.mm(b[:, t * 48:(t + 1) * 48], self.xw[:, k, t * P:(t + 1) * P],
                                               gw[:, k, :], k == 0, k == KD - 1)
                        last.then_inc(done.sem, 1)
                self.flush(pe, done.at(UNITS))

            def unit(n, copy):
                b = ps[n % 4]
                if n < 8:
                    return [copy(qT[:, n, :], b[:, 0:T])]
                if n < 12:
                    return [copy(kT[(n - 8) // 2][:, n % 2, :], b[:, 0:T])]
                if n < 20:
                    x_, g = X[(n - 12) // 4], n % 4
                    return [copy(x_[0:64, g, :], b[0:64, 0:T]), copy(x_[64:P, g, 0:T - 1], b[64:P, 1:T])]
                if n < 22:
                    return [copy(vv[:, n - 20, :], b[:, :])]

            @block.scalar
            def _(act):
                norm_act(act)
                for n in range(0, 22, 2):
                    act.wait_ge(*done.at(n + 1))
                    unit(n, lambda o, i: s_.activation(o, i, ACT.Copy))[-1].then_inc(fa.sem, 1)
                act.wait_ge(*gsum.at(1))
                g2 = gates.rearrange("p t h b -> p (t h b)")
                s_.activation(g2, g2, ACT.Sigmoid).then_inc(fa.sem, 1)

            @block.vector
            def _(dve):
                norm_dve(dve)
                for n in range(1, 22, 2):
                    dve.wait_ge(*done.at(n + 1))
                    unit(n, lambda o, i: v_.tensor_copy(o, i))[-1].then_inc(fd.sem, 1)
                dve.wait_ge(*small.at(16 * 9))
                dve.wait_ge(*done.at(23))
                v_.tensor_tensor(gates.rearrange("p t h b -> p t (h b)"),
                                 ps[2][:, 0:96].rearrange("p (t n) -> p t n", t=TT),
                                 gb.unsqueeze(1).to_broadcast([P, TT, 48]), ALU.add).then_inc(gsum.sem, 1)
                dve.wait_ge(*z.at(6))
                for i in range(2):
                    v_.tensor_copy(X[i][:, 4, 0:32].rearrange("p (j s) -> p j s", s=2)[:, :, 0],
                                   pe_[:, 16 * i:16 * i + 16]).then_inc(fd.sem, 1)
                v_.tensor_scalar(cneg, cm, -1.0, -NEG, ALU.add, ALU.mult).then_inc(fd.sem, 1)
        norm_end()
        done.base += UNITS
        fa.base += 12
        fd.base += 14
        z.base += 6
        gsum.base += 1
        small.base += 16 * 9

        (hdone, hb, hready, c2, kready, repl, c4, rready, vbd, cscore, cexp, cpt, cpte, cdone, mxs, csum) = self.counters(
            "cm_hidden", "cm_bias", "cm_gelu", "cm_k2", "cm_kT", "cm_repl", "cm_R", "cm_Rs", "cm_vbd",
            "cm_scores", "cm_exp", "cm_turned", "cm_PT", "cm_out", "cm_max", "cm_scaled")
        with nc.Block() as block:
            @block.sync
            def _(sp):
                self.loads(sp, G + 16)

            @block.gpsimd
            def _(pool):
                self.make_lows(pool, G + 16)

            @block.tensor
            def _(pe):
                for i in range(2):
                    for hc in range(2):
                        for jj in range(16):
                            w = self.ring_tile(pe, G, 12 + 2 * i + jj // 8)
                            at = (jj % 8) * 256 + hc * P
                            rhs = X[i][:, :, 2 * jj:2 * jj + 225].rearrange("p g t -> p g t")[:, :, 0:225:16]
                            last = self.mm(ps[4 + i][:, 128 * hc:128 * hc + 75], w[:, at:at + P], rhs, jj == 0, jj == 15)
                            if hc and jj == 7:
                                self.give_back(12 + 2 * i)
                    last.then_inc(hdone.sem, 1)
                    self.give_back(13 + 2 * i)
                pe.wait_ge(*hready.at(1))
                for hc in range(2):
                    last = self.mm(ps[6][:, 0:64], w2[:, hc, 0:128], hid[0][:, hc, :, :].rearrange("p g n -> p (g n)"),
                                   hc == 0, hc == 1)
                last.then_inc(c2.sem, 1)
                pe.wait_ge(*repl.at(1))
                for a in range(2):
                    for hc in range(2):
                        last = self.mm(ps[7][:, a * 64:(a + 1) * 64], hidR[:, a, hc, :], w2[:, hc, 128:192], hc == 0, hc == 1)
                last.then_inc(c4.sem, 1)
                pe.wait_ge(*kready.at(1))
                for t in range(TT):
                    for g in range(4):
                        b = ps[4 + g % 2]
                        lo = 64 * (g % 2)
                        for r in range(4):
                            at = t * P + (g // 2) * 64 + r * 16
                            last = self.mm(b[:, at:at + 16], qT[lo:lo + 64, 4 * (g // 2) + r, t * P:(t + 1) * P],
                                           kcT[lo:lo + 64, g * 16:(g + 1) * 16], True, True)
                last.then_inc(cscore.sem, 1)
                pe.wait_ge(*csum.at(1))
                for t in range(TT):
                    for a in range(2):
                        n = 2 * t + a
                        last = nc.tensor.transpose(ps[6][:, n * P:(n + 1) * P],
                                                   Sc[:, t, 8 * a:8 * a + 8, :].rearrange("p h n -> p (h n)"), self.ident)
                last.then_inc(cpt.sem, 1)
                pe.wait_ge(*cpte.at(1))
                pe.wait_ge(*vbd.at(2))
                for t in range(TT):
                    for a in range(2):
                        n = 2 * t + a
                        last = self.mm(ps[n][:, :], cPT[:, n * P:(n + 1) * P], Vbd[:, a, :, :].rearrange("p h d -> p (h d)"),
                                       True, True)
                last.then_inc(cdone.sem, 1)
                self.flush(pe, cdone.at(1))

            @block.scalar
            def _(act):
                for i in range(2):
                    act.wait_ge(*hb.at(i + 1))
                    for hc in range(2):
                        ins = s_.activation(hid[i][:, hc, :, 0:N_CMP],
                                            ps[4 + i][:, 128 * hc:128 * hc + 60].rearrange("p (g n) -> p g n", g=4),
                                            ACT.Gelu_apprx_tanh, bias=bcol[:, 2 * i + hc:2 * i + hc + 1])
                    ins.then_inc(hready.sem, 1)
                act.wait_ge(*c2.at(1))
                s_.activation(kcT, ps[6][:, 0:64], ACT.Copy).then_inc(kready.sem, 1)
                act.wait_ge(*c4.at(1))
                s_.activation(R.rearrange("p a d -> p (a d)"), ps[7][:, 0:128], ACT.Copy).then_inc(rready.sem, 1)
                act.wait_ge(*mxs.at(1))
                s2 = Sc.rearrange("p t h n -> p (t h n)")
                s_.activation(s2, s2, ACT.Exp, scale=SC).then_inc(cexp.sem, 1)
                act.wait_ge(*cpt.at(1))
                s_.activation(cPT, ps[6][:, :], ACT.Copy).then_inc(cpte.sem, 1)

            @block.vector
            def _(dve):
                link = Chain(dve, self.dve_chain)
                for i in range(2):
                    dve.wait_ge(*hdone.at(i + 1))
                    v_.tensor_tensor(bcol[:, 2 * i:2 * i + 2].unsqueeze(2),
                                     ps[4 + i][:, 0:256].rearrange("p (c n) -> p c n", c=2)[:, :, 60:61],
                                     b1[:, 2 * i:2 * i + 2].unsqueeze(2), ALU.add).then_inc(hb.sem, 1)
                dve.wait_ge(*hready.at(2))
                for a in range(2):
                    for hc in range(2):
                        for g in range(2):
                            last = v_.tensor_copy(hidR[:, a, hc, g * 64:(g + 1) * 64].rearrange("p (r n) -> p r n", r=4),
                                                  hid[1][:, hc, 2 * a + g, :].unsqueeze(1).to_broadcast([P, 4, 16]))
                last.then_inc(repl.sem, 1)
                dve.wait_ge(*rready.at(1))
                for a in range(2):
                    v_.tensor_tensor(Vbd[:, a, :, :], R[:, a, :].unsqueeze(1).to_broadcast([P, 8, 64]),
                                     blocks.unsqueeze(2).to_broadcast([P, 8, 64]), ALU.mult).then_inc(vbd.sem, 1)
                dve.wait_ge(*cscore.at(1))
                mx, sm, co = cs[:, 0:32], cs[:, 32:64], cs[:, 64:96]
                for t in range(TT):
                    for b in range(2):
                        o = Sc[:, t, :, :].rearrange("p (a b r) n -> p a b r n", a=2, b=2)[:, :, b, :, :]
                        i_ = ps[4 + b][:, t * P:(t + 1) * P].rearrange("p (a r n) -> p a r n", a=2, r=4)
                        for a in range(2):
                            last = v_.tensor_tensor(o[:, a], i_[:, a], cm[:, t, :].unsqueeze(1).to_broadcast([P, 4, 16]), ALU.mult)
                link(last)
                for t in range(TT):
                    last = v_.tensor_tensor(Sc[:, t, :, :], Sc[:, t, :, :],
                                            cneg[:, t, :].unsqueeze(1).to_broadcast([P, 16, 16]), ALU.add)
                link(last)
                flat = Sc.rearrange("p t h n -> p (t h) n")
                link(v_.tensor_reduce(mx, flat, AX.X, ALU.max))
                v_.tensor_tensor(flat, flat, mx.unsqueeze(2).to_broadcast([P, 32, 16]), ALU.subtract).then_inc(mxs.sem, 1)
                dve.wait_ge(*cexp.at(1))
                link(v_.tensor_reduce(sm, flat, AX.X, ALU.add))
                link(v_.reciprocal(sm, sm))
                link(v_.tensor_tensor(co.rearrange("p (t h) -> p t h", t=TT), sm.rearrange("p (t h) -> p t h", t=TT),
                                      gates[:, :, :, 0], ALU.mult))
                for t in range(TT):
                    last = v_.tensor_tensor(Sc[:, t, :, :], Sc[:, t, :, :],
                                            cm[:, t, :].unsqueeze(1).to_broadcast([P, 16, 16]), ALU.mult)
                link(last)
                v_.tensor_tensor(flat, flat, co.unsqueeze(2).to_broadcast([P, 32, 16]), ALU.mult).then_inc(csum.sem, 1)
        for s, n in ((hdone, 2), (hb, 2), (hready, 2), (c2, 1), (kready, 1), (repl, 1), (c4, 1), (rready, 1), (vbd, 2),
                     (cscore, 1), (cexp, 1), (cpt, 1), (cpte, 1), (cdone, 1), (mxs, 1), (csum, 1)):
            s.base += n

        units = [(c, br, b) for c in range(8) for br in range(2) for b in range(2)]
        NU = len(units)
        head = lambda c, b: 4 * (2 * (c // 4) + b) + c % 4
        sco, sadd, smax, sexp, scoef, sscale, stn, spt, spv, ofin = self.counters(
            "at_scores", "at_masked", "at_max", "at_exp", "at_coef", "at_scaled", "at_turned", "at_PT", "at_pv", "at_o")
        oT_done, oT_ev = self.counters("at_oT", "at_oTs")
        with nc.Block() as block:
            @block.sync
            def _(sp):
                self.loads(sp, G + 16)

            @block.tensor
            def _(pe):
                def scores(n):
                    c, br, b = units[n]
                    if n >= 2:
                        pe.wait_ge(*sadd.at(n - 1))
                    lo = 64 * b
                    q, k, o = qT[lo:lo + 64, c, :], kT[br][lo:lo + 64, c // 4, :], ps[4 + b]
                    nc.tensor.matmul(o[:, 0:P], q[:, 0:P], k[:, 0:P], start=True, stop=True)
                    nc.tensor.matmul(o[:, P:384], q[:, P:T], k, start=True, stop=True).then_inc(sco.sem, 1)

                def turn(n):
                    b = units[n][2]
                    pe.wait_ge(*sscale.at(n + 1))
                    if n >= 2:
                        pe.wait_ge(*spt.at(n - 1))
                    for j in range(3):
                        last = nc.tensor.transpose(ps[6 + b][:, j * P:(j + 1) * P], SB[n % 4][:, j * P:(j + 1) * P], self.ident)
                    last.then_inc(stn.sem, 1)

                def values(n):
                    c, br, b = units[n]
                    h = head(c, b)
                    g, a, at = h // 4, h // 8, (h % 8) * 64
                    pe.wait_ge(*spt.at(n + 1))
                    col = br * 256 + g * 64
                    w = PT[n % 4]
                    nc.tensor.matmul(ps[a][:, at:at + 64], w[:, 0:P], vv[:, 0, col:col + 64], start=False, stop=True,
                                     skip_group_check=True)
                    nc.tensor.matmul(ps[2 + a][:, at:at + 64], w[:, P:T], vv[:, 0, col:col + 64], start=False, stop=True,
                                     skip_group_check=True)
                    nc.tensor.matmul(ps[2 + a][:, at:at + 64], w[:, T:384], vv[:, 1, col:col + 64], start=False, stop=True,
                                     skip_group_check=True).then_inc(spv.sem, 1)

                for n in range(NU + 3):
                    if n < NU:
                        scores(n)
                    if 2 <= n < NU + 2:
                        turn(n - 2)
                    if n >= 3:
                        values(n - 3)
                pe.wait_ge(*ofin.at(4))
                for k in range(KD):
                    for t in range(TT):
                        last = nc.tensor.transpose(ps[4 + k // 2][:, (k % 2) * T + t * P:(k % 2) * T + (t + 1) * P],
                                                   xs[:, t, k * P:(k + 1) * P], self.ident)
                    if k % 2:
                        last.then_inc(oT_done.sem, 1)

            @block.scalar
            def _(act):
                def pt(n):
                    act.wait_ge(*stn.at(n + 1))
                    if n >= 4:
                        act.wait_ge(*spv.at(n - 3))
                    s_.activation(PT[n % 4], ps[6 + units[n][2]][:, 0:384], ACT.Copy).then_inc(spt.sem, 1)

                for n in range(NU + 1):
                    if n < NU:
                        act.wait_ge(*smax.at(n + 1))
                        if n >= 4:
                            act.wait_ge(*scoef.at(n - 3))
                        for t in range(TT):
                            w = SB[n % 4][:, t * P:(2 * t + 1) * P + t * 0] if t == 0 else SB[n % 4][:, P:384]
                            s_.activation(w, w, ACT.Exp, scale=SC, bias=nm[n % 4][:, t:t + 1],
                                          accum_out=sums[n % 4][:, t:t + 1]).then_inc(sexp.sem, 1)
                    if n >= 1:
                        pt(n - 1)
                for k in (2, 3, 6, 7):
                    act.wait_ge(*oT_done.at(k // 2 + 1))
                    s_.activation(self.xw[:, k, :], ps[4 + k // 2][:, (k % 2) * T:(k % 2 + 1) * T], ACT.Copy).then_inc(oT_ev.sem, 1)

            @block.vector
            def _(dve):
                link = Chain(dve, self.dve_chain)

                def coefs(n):
                    c, br, b = units[n]
                    dve.wait_ge(*sexp.at(2 * n + 2))
                    if n >= 4:
                        dve.wait_ge(*sscale.at(n - 3))
                    link(v_.reciprocal(coef[n % 4], sums[n % 4]))
                    v_.tensor_tensor(coef[n % 4], coef[n % 4], gates[:, :, head(c, b), 1 + br], ALU.mult).then_inc(scoef.sem, 1)

                for n in range(NU + 1):
                    if n < NU:
                        dve.wait_ge(*sco.at(n + 1))
                        if n >= 4:
                            dve.wait_ge(*stn.at(n - 3))
                            dve.wait_ge(*sexp.at(2 * n - 6))
                        v_.tensor_tensor(SB[n % 4], ps[4 + units[n][2]][:, 0:384], causal, ALU.add).then_inc(sadd.sem, 1)
                        dve.wait_ge(*sadd.at(n + 1))
                        link(v_.tensor_reduce(m3[n % 4][:, 0:3], SB[n % 4].rearrange("p (j k) -> p j k", j=3), AX.X, ALU.max))
                        link(v_.tensor_tensor(m3[n % 4][:, 1:2], m3[n % 4][:, 1:2], m3[n % 4][:, 2:3], ALU.max))
                        v_.tensor_scalar(nm[n % 4], m3[n % 4][:, 0:2], -SC, None, ALU.mult).then_inc(smax.sem, 1)
                    if n >= 1:
                        coefs(n - 1)
                dve.wait_ge(*spv.at(NU))
                for t in range(TT):
                    for a in range(2):
                        v_.tensor_copy(xs[:, t, a * 512:(a + 1) * 512], ps[2 * t + a][:, :]).then_inc(ofin.sem, 1)
                for k in (0, 1, 4, 5):
                    dve.wait_ge(*oT_done.at(k // 2 + 1))
                    v_.tensor_copy(self.xw[:, k, :], ps[4 + k // 2][:, (k % 2) * T:(k % 2 + 1) * T]).then_inc(oT_ev.sem, 1)

            @block.gpsimd
            def _(pool):
                self.make_lows(pool, G + 16)
                for n in range(NU):
                    pool.wait_ge(*scoef.at(n + 1))
                    nc.gpsimd.tensor_scalar(SB[n % 4][:, 0:P], SB[n % 4][:, 0:P], coef[n % 4][:, 0:1], 1.0, ALU.mult, ALU.mult)
                    nc.gpsimd.tensor_scalar(SB[n % 4][:, P:384], SB[n % 4][:, P:384], coef[n % 4][:, 1:2], 1.0,
                                            ALU.mult, ALU.mult).then_inc(sscale.sem, 1)
        for s, n in ((sco, NU), (sadd, NU), (smax, NU), (sexp, 2 * NU), (scoef, NU), (sscale, NU), (stn, NU), (spt, NU),
                     (spv, NU), (ofin, 4), (oT_done, 4), (oT_ev, 8)):
            s.base += n
        self.add_rows_product(G, 16, self.xw, KD, G + 20)

    def softplus_tail(self, link, y, mx, s1, s2, q_):
        v_ = self.nc.vector
        link(v_.tensor_scalar(s1, y, 2.0, None, ALU.add))
        link(v_.reciprocal(s1, s1))
        link(v_.tensor_tensor(s1, s1, y, ALU.mult))
        link(v_.tensor_tensor(s2, s1, s1, ALU.mult))
        link(v_.tensor_scalar(q_, s2, 1.0 / 15, None, ALU.mult))
        for o in (13, 11, 9, 7, 5, 3):
            link(v_.scalar_tensor_tensor(q_, q_, 1.0 / o, s2, ALU.add, ALU.mult))
        link(v_.scalar_tensor_tensor(q_, q_, 1.0, s1, ALU.add, ALU.mult))
        link(v_.scalar_tensor_tensor(q_, q_, 2.0, mx, ALU.mult, ALU.add))

    def gate_row(self, part, banks):
        for k in range(KD):
            last = self.nc.tensor.matmul(self.psum[banks[k // 4]][:, (k % 4) * P:(k % 4 + 1) * P],
                                         self.modT[:, 8 * part + k, 0:1].to_broadcast([P, P]), self.ident,
                                         start=True, stop=True)
        return last

    def second(self):
        nc, ps, G = self.nc, self.psum, G_SECOND
        v_, s_ = nc.vector, nc.scalar
        self.begin_stage()
        KS = RET_DK ** -0.5
        work = self.arena("mix2", whole=True)
        R0, R1, R2, Rh = (work(f"R{i}", 2048) for i in range(4))
        qkn = work("qkn", TT * 1024).rearrange("p (t n) -> p t n", t=TT)
        vn = work("vn", TT * 1024).rearrange("p (t n) -> p t n", t=TT)
        gn = work("gn", TT * 1024).rearrange("p (t n) -> p t n", t=TT)
        gp = work("gp", TT * 1024).rearrange("p (t n) -> p t n", t=TT)
        gr = work("gr", TT * 1024).rearrange("p (t n) -> p t n", t=TT)
        vc = work("vc", TT * 1024).rearrange("p (t n) -> p t n", t=TT)
        kc = work("kc", TT * 512).rearrange("p (t n) -> p t n", t=TT)
        pn = work("pn", TT * 512).rearrange("p (t n) -> p t n", t=TT)
        cond = work("cond", 16).rearrange("p (k s) -> p k s", s=2)
        adab = work("adab", 48)
        rope = work("rope", 256).rearrange("p (s t n) -> p s t n", s=2, t=TT)
        pscale = work("pscale", 4)
        rnorm = work("rnorm", 8)
        rcol = work("rcol", 4).rearrange("p (t s) -> p t s", s=2)
        lg = work("lg", 8)
        tiny = work("tiny", 5 * 8)
        wfb = work("wfb", 16).rearrange("p (s h t) -> p s h t", s=2, h=4)
        small, silu, ada, mods, sfirst, slast = self.counters("s2_small", "s2_silu", "s2_ada", "s2_mods", "s2_lgy", "s2_lg")
        ctx_in = R0.rearrange("p (t d) -> p t d", t=TT)
        hcT = Rh.rearrange("p (k t) -> p k t", k=KD)

        with nc.Block() as block:
            @block.sync
            def _(sp):
                for dst, name in ((cond.rearrange("p k s -> p (k s)"), "cond"), (adab, "ada_b"),
                                  (rope.rearrange("p s t n -> p (s t n)"), "rope"), (pscale, "pool_scale"),
                                  (rnorm, "ret_norm"), (rcol.rearrange("p t s -> p (t s)"), "ret_col")):
                    sp.dma_start(dst, self.dram[name]).then_inc(small.sem, 16)
                sp.dma_start(lg, self.dram["decay"].partition_broadcast(P).rearrange("p a d -> p (a d)")).then_inc(small.sem, 16)
                sp.dma_start(ctx_in, self.dram["ctx"].rearrange("(t p) d -> p t d", p=P)).then_inc(small.sem, 16)
                self.loads(sp, G + 24)

            @block.gpsimd
            def _(pool):
                self.make_lows(pool, G + 24)

            @block.scalar
            def _(act):
                act.wait_ge(*small.at(16 * 8))
                c2 = cond.rearrange("p k s -> p (k s)")
                s_.activation(c2, c2, ACT.Silu).then_inc(silu.sem, 1)
                act.wait_ge(*sfirst.at(1))
                s_.activation(tiny[:, 0:8], tiny[:, 0:8], ACT.Exp).then_inc(slast.sem, 1)

            @block.tensor
            def _(pe):
                pe.wait_ge(*silu.at(1))
                for c in range(48):
                    w = self.ring_tile(pe, G, c // 2)
                    for k in range(KD):
                        last = self.mm(ps[0][:, 2 * c:2 * c + 2], w[:, k * 256 + (c % 2) * P:k * 256 + (c % 2 + 1) * P],
                                       cond[:, k, :], k == 0, k == KD - 1)
                    if c % 2:
                        self.give_back(c // 2)
                last.then_inc(ada.sem, 1)
                self.flush(pe, ada.at(1))

            @block.vector
            def _(dve):
                link = Chain(dve, self.dve_chain)
                dve.wait_ge(*small.at(16 * 8))
                y, mx, s1, s2, q_ = (tiny[:, 8 * i:8 * i + 8] for i in range(5))
                link(v_.tensor_scalar(mx, lg, -1.0, 0.0, ALU.mult, ALU.max))
                link(v_.tensor_scalar(s1, lg, 0.0, None, ALU.max))
                v_.scalar_tensor_tensor(y, s1, -1.0, mx, ALU.mult, ALU.subtract).then_inc(sfirst.sem, 1)
                dve.wait_ge(*slast.at(1))
                self.softplus_tail(link, y, mx, s1, s2, q_)
                link(v_.tensor_scalar(lg, q_, -1.0, None, ALU.mult))
                dve.wait_ge(*ada.at(1))
                link(v_.tensor_tensor(self.modT, ps[0][:, 0:96].rearrange("p (c s) -> p c s", s=2),
                                      adab.unsqueeze(2).to_broadcast([P, 48, 2]), ALU.add))
                for n, (part, s, g) in enumerate(((1, 0, 6), (1, 1, 6), (4, 0, 7))):
                    v_.scalar_tensor_tensor(self.gA[:, n, :], self.modT[:, 8 * part:8 * part + 8, s], 1.0,
                                            self.gains[:, g, :], ALU.add, ALU.mult).then_inc(mods.sem, 1)
        for s, n in ((silu, 1), (ada, 1), (mods, 3), (sfirst, 1), (slast, 1), (small, 16 * 8)):
            s.base += n

        nact, ndve, npe, nend = self.norm_parts(ctx_in, hcT, self.gA[:, 1, :], self.modT[:, 0:8, 1], "ctx",
                                                R1.rearrange("p (t d) -> p t d", t=TT))
        with nc.Block() as block:
            block.sync(lambda sp: self.loads(sp, G + 24))
            block.gpsimd(lambda pool: self.make_lows(pool, G + 24))
            block.scalar(nact)
            block.vector(ndve)
            block.tensor(npe)
        nend()

        nact, ndve, npe, nend = self.norm_parts(self.x, self.xw, self.gA[:, 0, :], self.modT[:, 0:8, 0], "mixx",
                                                R2.rearrange("p (t d) -> p t d", t=TT))
        units = [(b, c, t) for b in range(11) for c in ((0, 1) if b in (2, 3, 4) else (0,)) for t in range(TT)]
        NU = len(units)
        done, freed = self.counters("s2_done", "s2_freed")
        with nc.Block() as block:
            @block.sync
            def _(sp):
                self.loads(sp, G + 46)

            @block.gpsimd
            def _(pool):
                self.make_lows(pool, G + 46)

            @block.tensor
            def _(pe):
                npe(pe)
                for n, (b, c, t) in enumerate(units):
                    if n >= 4:
                        pe.wait_ge(*freed.at(n - 3))
                    self.moving_cols(pe, ps[n % 4][:, :], G, 24 + 2 * b, hcT if c else self.xw, t).then_inc(done.sem, 1)
                    if n + 1 == NU or units[n + 1][0] != b:
                        self.give_back(24 + 2 * b)
                        self.give_back(25 + 2 * b)
                self.flush(pe, done.at(NU))

            @block.scalar
            def _(act):
                nact(act)
                for n, (b, c, t) in enumerate(units):
                    act.wait_ge(*done.at(n + 1))
                    src, half = ps[n % 4][:, :], slice(((b + 1) % 2) * 512, ((b + 1) % 2) * 512 + 512)
                    if b == 0:
                        ins = s_.activation(pn[:, t, :], src, ACT.Copy)
                    elif b == 1:
                        ins = s_.activation(qkn[:, t, 0:512], src, ACT.Copy)
                    elif b == 2:
                        ins = s_.activation(kc[:, t, :] if c else qkn[:, t, 512:], src, ACT.Copy, scale=KS)
                    elif b < 5:
                        ins = s_.activation((vc if c else vn)[:, t, half], src, ACT.Copy)
                    elif b < 7:
                        ins = s_.activation(gn[:, t, half], src, ACT.Silu)
                    elif b < 9:
                        ins = s_.activation(gp[:, t, half], src, ACT.Sigmoid)
                    else:
                        ins = s_.activation(gr[:, t, half], src, ACT.Sigmoid)
                    ins.then_inc(freed.sem, 1)

            @block.vector
            def _(dve):
                ndve(dve)
        nend()
        done.base += NU
        freed.base += NU

        band = R0.rearrange("p (g s t) -> p g s t", g=4, s=TT)
        dT, mT = R1[:, 0:1024].rearrange("p (g t) -> p g t", g=4), R1[:, 1024:2048].rearrange("p (g t) -> p g t", g=4)
        here, p1, p2, p3, p4, p5 = self.counters("pl_here", "pl_d", "pl_ds", "pl_m", "pl_ms", "pl_out")
        qk5 = qkn.rearrange("p t (h s n) -> p t h s n", h=8, s=2)
        ra = R2[:, 0:512].rearrange("p (h n) -> p h n", h=8)
        rb = R2[:, 512:1024].rearrange("p (h n) -> p h n", h=8)
        rc_ = R2[:, 1024:1536].rearrange("p (h n) -> p h n", h=8)
        rd_ = R2[:, 1536:2048].rearrange("p (h n) -> p h n", h=8)
        with nc.Block() as block:
            @block.sync
            def _(sp):
                sp.dma_start(R0, self.dram["band"]).then_inc(here.sem, 16)
                self.loads(sp, G + 49)

            @block.gpsimd
            def _(pool):
                self.make_lows(pool, G + 49)

            @block.tensor
            def _(pe):
                pe.wait_ge(*here.at(16))
                for g in range(4):
                    for s in range(TT):
                        last = self.mm(ps[g // 2][:, (g % 2) * T:(g % 2 + 1) * T], pn[:, s, g * P:(g + 1) * P],
                                       band[:, g, s, :], s == 0, s == 1)
                last.then_inc(p1.sem, 1)
                w = self.ring_tile(pe, G, 46)
                pe.wait_ge(*p2.at(1))
                for g in range(4):
                    last = self.mm(ps[2 + g // 2][:, (g % 2) * T:(g % 2 + 1) * T], w[:, g * P:(g + 1) * P], dT[:, g, :], True, True)
                last.then_inc(p3.sem, 1)
                self.give_back(46)
                pe.wait_ge(*p4.at(4))
                self.rows_product(pe, G, 47, mT, 4, (4, 5, 6, 7), p5)
                self.flush(pe, p5.at(1))

            @block.scalar
            def _(act):
                act.wait_ge(*p1.at(1))
                for b in range(2):
                    ins = s_.activation(dT[:, 2 * b:2 * b + 2, :], ps[b][:, :].rearrange("p (g t) -> p g t", g=2), ACT.Copy)
                ins.then_inc(p2.sem, 1)
                act.wait_ge(*p3.at(1))
                for g in range(4):
                    s_.activation(mT[:, g, :], ps[2 + g // 2][:, (g % 2) * T:(g % 2 + 1) * T], ACT.Copy,
                                  scale=pscale[:, g:g + 1]).then_inc(p4.sem, 1)

            @block.vector
            def _(dve):
                link = Chain(dve, self.dve_chain)
                for t in range(TT):
                    cos, sin = (rope[:, s, t, :].unsqueeze(1).to_broadcast([P, 8, 64]) for s in range(2))
                    lo, hi = qk5[:, t, :, 0, :], qk5[:, t, :, 1, :]
                    v_.tensor_tensor(ra, lo, cos, ALU.mult)
                    v_.tensor_tensor(rb, hi, sin, ALU.mult)
                    v_.tensor_tensor(rc_, lo, sin, ALU.mult)
                    link(v_.tensor_tensor(rd_, hi, cos, ALU.mult))
                    v_.tensor_tensor(lo, ra, rb, ALU.subtract)
                    link(v_.tensor_tensor(hi, rc_, rd_, ALU.add))
                dve.wait_ge(*p5.at(1))
                for t in range(TT):
                    for half in range(2):
                        o = gp[:, t, half * 512:(half + 1) * 512]
                        link(v_.tensor_tensor(o, o, ps[4 + 2 * t + half][:, :], ALU.mult))
        for s, n in ((here, 16), (p1, 1), (p2, 1), (p3, 1), (p4, 4), (p5, 1)):
            s.base += n

        qkT = Rh.rearrange("p (h t) -> p h t", h=8)
        kcw = R0.rearrange("p (s h t n) -> p s h t n", s=2, h=4, t=TT)
        S = R1.rearrange("p (s h e) -> p s h e", s=2, h=4)
        Dm = R2.rearrange("p (h m n) -> p h m n", h=4, m=TT)
        c1, c2_, c3_, c4_, c5_, c6_ = self.counters("cx_w", "cx_kw", "cx_S", "cx_Ss", "cx_turned", "cx_qk")
        with nc.Block() as block:
            block.sync(lambda sp: self.loads(sp, G + 49))
            block.gpsimd(lambda pool: self.make_lows(pool, G + 49))

            @block.scalar
            def _(act):
                for s in range(2):
                    for h in range(4):
                        s_.activation(wfb[:, s, h, :], rcol[:, :, s], ACT.Exp, scale=lg[:, 4 * s + h:4 * s + h + 1]
                                      ).then_inc(c1.sem, 1)
                for n in range(2):
                    act.wait_ge(*c5_.at(n + 1))
                    for b in range(2):
                        s_.activation(qkT[:, 4 * n + 2 * b:4 * n + 2 * b + 2, :],
                                      ps[4 + 2 * n + b][:, :].rearrange("p (h t) -> p h t", h=2), ACT.Copy).then_inc(c6_.sem, 1)
                act.wait_ge(*c3_.at(1))
                for b in range(4):
                    s_.activation(S[:, b // 2, 2 * (b % 2):2 * (b % 2) + 2, :], ps[b][:, :].rearrange("p (h e) -> p h e", h=2),
                                  ACT.Copy).then_inc(c4_.sem, 1)

            @block.vector
            def _(dve):
                dve.wait_ge(*c1.at(8))
                for s in range(2):
                    for h in range(4):
                        for t in range(TT):
                            v_.tensor_scalar(kcw[:, s, h, t, :], kc[:, t, h * P:(h + 1) * P], wfb[:, s, h, t:t + 1], None,
                                             ALU.mult).then_inc(c2_.sem, 1)

            @block.tensor
            def _(pe):
                for n in range(2):
                    for h in range(4):
                        for t in range(TT):
                            last = nc.tensor.transpose(ps[4 + 2 * n + h // 2][:, (h % 2) * T + t * P:(h % 2) * T + (t + 1) * P],
                                                       qkn[:, t, n * 512 + h * P:n * 512 + (h + 1) * P], self.ident)
                    last.then_inc(c5_.sem, 1)
                for s in range(2):
                    for h in range(4):
                        pe.wait_ge(*c2_.at(8 * s + 2 * h + 2))
                        for t in range(TT):
                            last = nc.tensor.matmul(ps[2 * s + h // 2][:, (h % 2) * T:(h % 2 + 1) * T], kcw[:, s, h, t, :],
                                                    vc[:, t, h * 256:(h + 1) * 256], start=t == 0, stop=t == 1)
                last.then_inc(c3_.sem, 1)
        for s, n in ((c1, 8), (c2_, 16), (c3_, 1), (c4_, 4), (c5_, 2), (c6_, 4)):
            s.base += n

        rel = kc.rearrange("p t n -> p (t n)").rearrange("p (s n) -> p s n", s=2)
        qd = qkn.rearrange("p t n -> p (t n)").rearrange("p (s h t) -> p s h t", s=2, h=4)
        PTb = pn.rearrange("p t n -> p (t n)").rearrange("p (b m n) -> p b m n", b=2, m=TT)
        yv = vc.rearrange("p t (h e) -> p t h e", h=4)
        rows_ = R0[:, 0:512].rearrange("p (s t) -> p s t", s=2)
        bn = R0[:, 512:512 + 48].rearrange("p (n s) -> p n s", n=8)
        mv = R0[:, 576:592].rearrange("p (n s) -> p n s", n=8)
        d1, d2, d3, d4, sc_, pt_, y_, ye, v1_, v2_, tn, te = self.counters(
            "rt_exp", "rt_D", "rt_dec", "rt_qd", "rt_scores", "rt_P", "rt_y", "rt_ys", "rt_var", "rt_root", "rt_turned", "rt_rT")
        here2, yn = self.counters("rt_here", "rt_yn")
        rT = self.xw
        with nc.Block() as block:
            @block.sync
            def _(sp):
                sp.dma_start(rel.rearrange("p s n -> p (s n)"), self.dram["ret"][:, 0:1024]).then_inc(here2.sem, 16)
                sp.dma_start(R0[:, 0:512], self.dram["ret_row"]).then_inc(here2.sem, 16)
                self.loads(sp, G + 49)

            @block.gpsimd
            def _(pool):
                self.make_lows(pool, G + 49)

            @block.scalar
            def _(act):
                act.wait_ge(*here2.at(32))
                for s in range(2):
                    for h in range(4):
                        s_.activation(qd[:, s, h, :], rows_[:, s, :], ACT.Exp, scale=lg[:, 4 * s + h:4 * s + h + 1]).then_inc(d3.sem, 1)
                for h in range(4):
                    act.wait_ge(*d1.at(h + 1))
                    o = Dm[:, h, :, :].rearrange("p m n -> p (m n)")
                    s_.activation(o, o, ACT.Exp).then_inc(d2.sem, 1)
                for h in range(4):
                    act.wait_ge(*y_.at(h + 1))
                    s_.activation(yv[:, :, h, :], ps[2 + h % 2][:, :].rearrange("p (t e) -> p t e", t=TT), ACT.Copy).then_inc(ye.sem, 1)
                act.wait_ge(*v1_.at(1))
                s_.activation(mv[:, :, 1], mv[:, :, 1], ACT.Sqrt).then_inc(v2_.sem, 1)
                for k in (2, 3, 6, 7):
                    act.wait_ge(*tn.at(k // 2 + 1))
                    s_.activation(rT[:, k, :], ps[4 + k // 2][:, (k % 2) * T:(k % 2 + 1) * T], ACT.Copy,
                                  scale=rnorm[:, k:k + 1]).then_inc(te.sem, 1)

            @block.vector
            def _(dve):
                link = Chain(dve, self.dve_chain)
                dve.wait_ge(*here2.at(32))
                for h in range(4):
                    o = Dm[:, h, :, :].rearrange("p m n -> p (m n)")
                    link(v_.tensor_scalar(o, rel[:, 0, :], lg[:, h:h + 1], None, ALU.mult))
                    v_.scalar_tensor_tensor(o, rel[:, 1, :], lg[:, 4 + h:5 + h], o, ALU.mult, ALU.add).then_inc(d1.sem, 1)
                dve.wait_ge(*d3.at(8))
                for s in range(2):
                    v_.tensor_tensor(qd[:, s, :, :], qd[:, s, :, :], qkT[:, 0:4, :], ALU.mult).then_inc(d4.sem, 1)
                for h in range(4):
                    dve.wait_ge(*sc_.at(h + 1))
                    dve.wait_ge(*d2.at(h + 1))
                    if h >= 2:
                        dve.wait_ge(*y_.at(h - 1))
                    v_.tensor_tensor(PTb[:, h % 2, :, :], ps[h % 2][:, :].rearrange("p (m n) -> p m n", m=TT), Dm[:, h, :, :],
                                     ALU.mult).then_inc(pt_.sem, 1)
                for h in range(4):
                    dve.wait_ge(*ye.at(h + 1))
                    for t in range(TT):
                        link(v_.bn_stats(bn[:, 4 * t + h, :], yv[:, t, h, :]))
                        link(v_.bn_aggr(mv[:, 4 * t + h, :], bn[:, 4 * t + h, :]))
                v_.tensor_scalar(mv[:, :, 1], mv[:, :, 1], EPS, None, ALU.add).then_inc(v1_.sem, 1)
                dve.wait_ge(*v2_.at(1))
                link(v_.reciprocal(mv[:, :, 1], mv[:, :, 1]))
                for t in range(TT):
                    for h in range(4):
                        n = 4 * t + h
                        last = v_.tensor_scalar(yv[:, t, h, :], yv[:, t, h, :], mv[:, n, 0:1], mv[:, n, 1:2], ALU.subtract, ALU.mult)
                link(last)
                for t in range(TT):
                    v_.tensor_tensor(vc[:, t, :], vc[:, t, :], gn[:, t, :], ALU.mult).then_inc(yn.sem, 1)
                for k in (0, 1, 4, 5):
                    dve.wait_ge(*tn.at(k // 2 + 1))
                    v_.tensor_scalar(rT[:, k, :], ps[4 + k // 2][:, (k % 2) * T:(k % 2 + 1) * T], rnorm[:, k:k + 1], None,
                                     ALU.mult).then_inc(te.sem, 1)

            @block.tensor
            def _(pe):
                def scores(h):
                    for m in range(TT):
                        last = nc.tensor.matmul(ps[h % 2][:, m * T:(m + 1) * T], qkT[:, 4 + h, m * P:(m + 1) * P], qkT[:, h, :],
                                                start=True, stop=True)
                    last.then_inc(sc_.sem, 1)
                scores(0)
                scores(1)
                pe.wait_ge(*d4.at(2))
                for h in range(4):
                    pe.wait_ge(*pt_.at(h + 1))
                    if h < 2:
                        scores(h + 2)
                    else:
                        pe.wait_ge(*ye.at(h - 1))
                    for t in range(TT):
                        o = ps[2 + h % 2][:, t * T:(t + 1) * T]
                        for m in range(TT):
                            nc.tensor.matmul(o, PTb[:, h % 2, m, t * P:(t + 1) * P], vn[:, m, h * 256:(h + 1) * 256],
                                             start=m == 0, stop=False)
                        for s in range(2):
                            last = nc.tensor.matmul(o, qd[:, s, h, t * P:(t + 1) * P], S[:, s, h, :], start=False, stop=s == 1)
                    last.then_inc(y_.sem, 1)
                pe.wait_ge(*yn.at(2))
                for k in range(KD):
                    for t in range(TT):
                        last = nc.tensor.transpose(ps[4 + k // 2][:, (k % 2) * T + t * P:(k % 2) * T + (t + 1) * P],
                                                   vc[:, t, k * P:(k + 1) * P], self.ident)
                    if k % 2:
                        last.then_inc(tn.sem, 1)
        for s, n in ((d1, 4), (d2, 4), (d3, 8), (d4, 2), (sc_, 4), (pt_, 4), (y_, 4), (ye, 4), (v1_, 1), (v2_, 1), (tn, 4),
                     (te, 8), (here2, 32), (yn, 2)):
            s.base += n

        o1, o2, o3, o4, o5, o6, o7 = self.counters("mo_ret", "mo_merged", "mo_turned", "mo_mT", "mo_g1", "mo_g1s", "mo_out")
        g1 = R0[:, 0:1024]
        mgT = Rh.rearrange("p (k t) -> p k t", k=KD)
        with nc.Block() as block:
            block.sync(lambda sp: self.loads(sp, G + 57))
            block.gpsimd(lambda pool: self.make_lows(pool, G + 57))

            @block.tensor
            def _(pe):
                self.gate_row(2, (4, 5)).then_inc(o5.sem, 1)
                self.rows_product(pe, G, 49, rT, KD, (0, 1, 2, 3), o1)
                pe.wait_ge(*o2.at(4))
                pe.wait_ge(*o6.at(2))
                for k in range(KD):
                    for t in range(TT):
                        last = nc.tensor.transpose(ps[4 + k // 2][:, (k % 2) * T + t * P:(k % 2) * T + (t + 1) * P],
                                                   gp[:, t, k * P:(k + 1) * P], self.ident)
                    if k % 2:
                        last.then_inc(o3.sem, 1)
                pe.wait_ge(*o4.at(8))
                self.rows_product(pe, G, 53, mgT, KD, (0, 1, 2, 3), o7)
                self.flush(pe, o7.at(1))

            @block.scalar
            def _(act):
                act.wait_ge(*o5.at(1))
                for b in range(2):
                    s_.activation(g1[:, b * 512:(b + 1) * 512], ps[4 + b][:, :], ACT.Copy).then_inc(o6.sem, 1)
                for k in (2, 3, 6, 7):
                    act.wait_ge(*o3.at(k // 2 + 1))
                    s_.activation(mgT[:, k, :], ps[4 + k // 2][:, (k % 2) * T:(k % 2 + 1) * T], ACT.Copy).then_inc(o4.sem, 1)

            @block.vector
            def _(dve):
                link = Chain(dve, self.dve_chain)
                dve.wait_ge(*o1.at(1))
                for t in range(TT):
                    for half in range(2):
                        sl = slice(half * 512, (half + 1) * 512)
                        link(v_.tensor_tensor(gr[:, t, sl], gr[:, t, sl], ps[2 * t + half][:, :], ALU.mult))
                        v_.tensor_tensor(gp[:, t, sl], gp[:, t, sl], gr[:, t, sl], ALU.add).then_inc(o2.sem, 1)
                for k in (0, 1, 4, 5):
                    dve.wait_ge(*o3.at(k // 2 + 1))
                    v_.tensor_copy(mgT[:, k, :], ps[4 + k // 2][:, (k % 2) * T:(k % 2 + 1) * T]).then_inc(o4.sem, 1)
                dve.wait_ge(*o7.at(1))
                for t in range(TT):
                    for half in range(2):
                        sl = slice(half * 512, (half + 1) * 512)
                        link(v_.tensor_tensor(gr[:, t, sl], ps[2 * t + half][:, :], g1[:, sl], ALU.mult))
                        link(v_.tensor_tensor(self.x[:, t, sl], self.x[:, t, sl], gr[:, t, sl], ALU.add))
        for s, n in ((o1, 1), (o2, 4), (o3, 4), (o4, 8), (o5, 1), (o6, 2), (o7, 1)):
            s.base += n

    def peer(self):
        nc, ps, G = self.nc, self.psum, G_SECOND
        v_, s_, g_ = nc.vector, nc.scalar, nc.gpsimd
        self.begin_stage()
        cursor = self.base

        def region(size):
            nonlocal cursor
            cursor += size
            return cursor - size, cursor

        raw_at, parts_at, ga_at, w_at = region(2 * TILE * 4), region(8 * D * 4), region(4 * T * 4), region(P * T * 4)
        assert w_at[1] <= self.keep
        xraw = Arena(nc, "peerX", *raw_at)("raw", 2 * TILE).rearrange("p (s m n) -> p s m n", s=2, m=2)
        split = Arena(nc, "peerS", *parts_at)
        U, V = ([split(f"{m}{n}", 2 * D, dt=F32R).rearrange("p (s n) -> p s n", s=2) for n in ("high", "low")]
                for m in "UV")
        weighted = Arena(nc, "peerG", *ga_at)
        GA = [weighted(f"GA{n}", 2 * T, dt=F32R).rearrange("p (b t) -> p b t", b=2) for n in ("high", "low")]
        Wt = Arena(nc, "peerW", *w_at)("W", P * T).rearrange("p (t i) -> p t i", t=T)
        g2 = Arena(nc, "peerG2", *ga_at)("g2", D)
        iota = Arena(nc, "peerI", *ga_at)("iota", P)
        stay = Arena(nc, "peerP", *parts_at)
        GT, I1T, I2T = (stay(n, T) for n in ("GT", "I1T", "I2T"))
        O1 = stay("O1", 8 * P).rearrange("p (q n) -> p q n", q=8)
        O2 = stay("O2", 8 * P).rearrange("p (q n) -> p q n", q=8)
        tmp = Arena(nc, "peerT", *w_at)
        xs = tmp("xs", TT * D).rearrange("p (t d) -> p t d", t=TT)
        xw = tmp("xw", KD * T).rearrange("p (k t) -> p k t", k=KD)
        qT = tmp("qT", 16 * T).rearrange("p (c t) -> p c t", c=16)
        sc = tmp("sc", 32 * P).rearrange("p (r n) -> p r n", r=32)
        val = tmp("val", 512).rearrange("p (r k) -> p r k", r=32)
        idx = tmp("idx", 512, dt=U32).rearrange("p (r k) -> p r k", r=32)
        best = tmp("best", 256).rearrange("p (r k) -> p r k", r=16)
        pos = tmp("pos", 256, dt=U32).rearrange("p (r k) -> p r k", r=16)
        posh = tmp("posh", 256, dt=U32).rearrange("p (r k) -> p r k", r=16)
        sm = tmp("sm", 16)

        done, freed, here, sdone, sfree, xhigh, xlow = self.counters("pr_done", "pr_freed", "pr_here", "pr_scores", "pr_sfreed",
                                                                "pr_xhigh", "pr_xlow")
        nact, ndve, npe, nend = self.norm_parts(self.x, xw, self.gA[:, 2, :], self.modT[:, 24:32, 0], "peer", xs)
        with nc.Block() as block:
            @block.sync
            def _(sp):
                sp.dma_start(iota, self.dram["iota"]).then_inc(here.sem, 16)
                self.loads(sp, G + 66)
                sp.wait_ge(*here.at(16))

            @block.gpsimd
            def _(pool):
                self.make_lows(pool, G + 66)

            @block.tensor
            def _(pe):
                npe(pe)
                for n in range(16):
                    if n >= 4:
                        pe.wait_ge(*freed.at(n - 3))
                    self.stationary_cols(ps[n % 4][:, 0:T], self.ring_tile(pe, G, 57 + n // 2), n % 2, xw
                                         ).then_inc(done.sem, 1)
                    if n % 2:
                        self.give_back(57 + n // 2)
                pe.wait_ge(*freed.at(16))
                keys = self.ring_tile(pe, G, 65)
                for t in range(TT):
                    for b in range(4):
                        if t:
                            pe.wait_ge(*sfree.at(b + 1))
                        for j in range(4):
                            c = 4 * b + j
                            last = self.mm(ps[4 + b][:, j * P:(j + 1) * P], qT[:, c, t * P:(t + 1) * P],
                                           keys[:, c * P:(c + 1) * P], True, True)
                        last.then_inc(sdone.sem, 1)
                self.give_back(65)
                self.flush(pe, sdone.at(8))

            @block.scalar
            def _(act):
                nact(act)
                act.wait_ge(self.counters("nrm_low")[0].sem, self.counters("nrm_low")[0].base + KD)
                s_.activation(self.xT[0], xw, ACT.Copy).then_inc(xhigh.sem, 1)
                for n in range(16):
                    act.wait_ge(*done.at(n + 1))
                    s_.activation(qT[:, n, :], ps[n % 4][:, 0:T], ACT.Copy).then_inc(freed.sem, 1)
                for t in range(TT):
                    for b in range(4):
                        act.wait_ge(*sdone.at(4 * t + b + 1))
                        s_.activation(sc[:, 16 * t + 4 * b:16 * t + 4 * b + 4, :], ps[4 + b][:, :].rearrange("p (r n) -> p r n", r=4),
                                      ACT.Copy).then_inc(sfree.sem, 1)

            @block.vector
            def _(dve):
                ndve(dve)
                dve.wait_ge(*xhigh.at(1))
                v_.tensor_tensor(self.xT[1], xw, self.xT[0].bitcast(F32), ALU.subtract).then_inc(xlow.sem, 1)
                dve.wait_ge(*xlow.at(1))
        nend()
        for s, n in ((done, 16), (freed, 16), (xhigh, 1), (xlow, 1), (here, 16), (sdone, 8), (sfree, 8)):
            s.base += n

        uloaded = self.counters("ex_u_loaded0", "ex_u_loaded1")
        vloaded = self.counters("ex_v_loaded0", "ex_v_loaded1")
        experts = self.dram["experts"]
        tk1, tk2, tk3, tk4 = self.counters("tk_sub", "tk_exp", "tk_ready", "tk_turned")
        (tk5,) = self.counters("tk_T")
        sw = qT.rearrange("p c t -> p (c t)").rearrange("p (r n) -> p r n", r=32)
        cand = sc.rearrange("p r n -> p (r n)").rearrange("p (r n) -> p r n", r=16)
        cw = sw.rearrange("p r n -> p (r n)").rearrange("p (r n) -> p r n", r=16)
        with nc.Block() as block:
            @block.sync
            def _(sp):
                for s in range(2):
                    sp.dma_start(xraw[:, s, 0, :], experts[s, :, 0:D]).then_inc(uloaded[s].sem, 16)
                    sp.dma_start(xraw[:, s, 1, :], experts[s, :, D:]).then_inc(vloaded[s].sem, 16)

            @block.vector
            def _(dve):
                link = Chain(dve, self.dve_chain)

                def top16(rows, src, spare, values, index):
                    for r in range(rows):
                        last = v_.max(values[:, r, 0:8], src[:, r, :])
                    link(last)
                    for r in range(rows):
                        last = v_.max_index(index[:, r, 0:8], values[:, r, 0:8], src[:, r, :])
                    for r in range(rows):
                        last = v_.match_replace(spare[:, r, :], values[:, r, 0:8], src[:, r, :], -3.0e38)
                    link(last)
                    for r in range(rows):
                        last = v_.max(values[:, r, 8:16], spare[:, r, :])
                    link(last)
                    for r in range(rows):
                        last = v_.max_index(index[:, r, 8:16], values[:, r, 8:16], spare[:, r, :])
                    link(last)

                top16(32, sc, sw, val, idx)
                v4 = val.rearrange("p (t h s) k -> p t h s k", t=TT, s=2)
                c4 = cand.rearrange("p (t h) n -> p t h n", t=TT)
                for t in range(TT):
                    last = v_.tensor_tensor(c4[:, t].rearrange("p h (a b) -> p h a b", a=16),
                                            v4[:, t, :, 0, :].unsqueeze(3).to_broadcast([P, 8, 16, 16]),
                                            v4[:, t, :, 1, :].unsqueeze(2).to_broadcast([P, 8, 16, 16]), ALU.add)
                link(last)
                top16(16, cand, cw, best, pos)
                link(v_.tensor_tensor(val[:, 0:16, :], best, best[:, :, 0:1].to_broadcast([P, 16, 16]), ALU.subtract))
                v_.tensor_scalar(posh, pos, 4, None, ALU.logical_shift_right).then_inc(tk1.sem, 1)
                dve.wait_ge(*tk1.at(1))
                link(v_.tensor_scalar(pos, pos, 15, None, ALU.bitwise_and))
                idf = sw.rearrange("p r n -> p (r n)")[:, 0:512].rearrange("p (r k) -> p r k", r=32)
                hf_, lf_ = (sw.rearrange("p r n -> p (r n)")[:, 512 + 256 * i:768 + 256 * i].rearrange("p (r k) -> p r k", r=16) for i in range(2))
                v_.tensor_copy(idf, idx)
                v_.tensor_copy(hf_, posh)
                link(v_.tensor_copy(lf_, pos))
                eq = sc.rearrange("p r n -> p (r n)").rearrange("p (r k j) -> p r k j", r=16, k=16)
                id2 = idf.rearrange("p (r s) k -> p r s k", s=2)
                jot = iota[:, 0:16].unsqueeze(1).unsqueeze(1).to_broadcast([P, 16, 16, 16])
                for part, (which, out) in enumerate(((hf_, xs[:, 0, 0:256]), (lf_, xs[:, 0, 256:512]))):
                    link(v_.tensor_tensor(eq, which.unsqueeze(3).to_broadcast([P, 16, 16, 16]), jot, ALU.is_equal))
                    link(v_.tensor_tensor(eq, eq, id2[:, :, part, :].unsqueeze(2).to_broadcast([P, 16, 16, 16]), ALU.mult))
                    link(v_.tensor_reduce(out.rearrange("p (r k) -> p r k", r=16), eq, AX.X, ALU.add))
                dve.wait_ge(*tk2.at(1))
                link(v_.tensor_reduce(sm, val[:, 0:16, :], AX.X, ALU.add))
                link(v_.reciprocal(sm, sm))
                v_.tensor_tensor(val[:, 0:16, :], val[:, 0:16, :], sm.unsqueeze(2).to_broadcast([P, 16, 16]), ALU.mult
                                 ).then_inc(tk3.sem, 1)
                dve.wait_ge(*tk4.at(1))
                for b, dst in enumerate((GT, I1T, I2T)):
                    v_.tensor_copy(dst, ps[b][:, 0:T]).then_inc(tk5.sem, 1)
                dve.wait_ge(*tk5.at(3))

            @block.scalar
            def _(act):
                act.wait_ge(*tk1.at(1))
                s_.activation(val[:, 0:16, :], val[:, 0:16, :], ACT.Exp).then_inc(tk2.sem, 1)

            @block.tensor
            def _(pe):
                pe.wait_ge(*tk3.at(1))
                v3 = val.rearrange("p r k -> p (r k)")
                for t in range(TT):
                    for b, src in enumerate((v3[:, t * P:(t + 1) * P], xs[:, 0, t * P:(t + 1) * P],
                                             xs[:, 0, 256 + t * P:256 + (t + 1) * P])):
                        last = nc.tensor.transpose(ps[b][:, t * P:(t + 1) * P], src, self.ident)
                last.then_inc(tk4.sem, 1)
        for s, n in ((tk1, 1), (tk2, 1), (tk3, 1), (tk4, 1), (tk5, 3)):
            s.base += n

        wo1, wo2, wmm, wev = self.counters("w_rows1", "w_rows2", "w_product", "w_written")
        QUADS = T // 4
        with nc.Block() as block:
            @block.vector
            def _(dve):
                def quad(q, b, first=False):
                    if not first:
                        dve.wait_ge(*wmm.at(q - 1))
                    for j in range(4):
                        t = q * 4 + j
                        last = v_.tensor_scalar(O1[:, 4 * b + j, :], iota, I1T[:, bass.ds(t, 1)], GT[:, bass.ds(t, 1)],
                                                ALU.is_equal, ALU.mult)
                    last.then_inc(wo1.sem, 1)
                quad(0, 0, True)
                quad(1, 1, True)
                with dve.Fori(1, QUADS // 2) as turn:
                    for b in range(2):
                        quad(turn * 2 + b, b)

            @block.gpsimd
            def _(pool):
                def quad(q, b, first=False):
                    if not first:
                        pool.wait_ge(*wmm.at(q - 1))
                    for j in range(4):
                        t = q * 4 + j
                        last = g_.tensor_scalar(O2[:, 4 * b + j, :], iota, I2T[:, bass.ds(t, 1)], None, ALU.is_equal)
                    last.then_inc(wo2.sem, 1)
                for q in range(QUADS):
                    quad(q, q % 2, q < 2)

            @block.tensor
            def _(pe):
                def quad(q, b, first=False):
                    pe.wait_ge(*wo1.at(q + 1))
                    pe.wait_ge(*wo2.at(q + 1))
                    if not first:
                        pe.wait_ge(*wev.at(q - 1))
                    for j in range(4):
                        last = nc.tensor.matmul(ps[b][:, j * P:(j + 1) * P], O1[:, 4 * b + j, :], O2[:, 4 * b + j, :],
                                                start=True, stop=True)
                    last.then_inc(wmm.sem, 1)
                quad(0, 0, True)
                quad(1, 1, True)
                with pe.Fori(1, QUADS // 2) as turn:
                    for b in range(2):
                        quad(turn * 2 + b, b)

            @block.scalar
            def _(act):
                with act.Fori(0, QUADS // 2) as turn:
                    for b in range(2):
                        act.wait_ge(*wmm.at(turn * 2 + (b + 1)))
                        s_.activation(Wt[:, bass.ds((turn * 2 + b) * 4, 4), :], ps[b][:, :].rearrange("p (t i) -> p t i", t=4),
                                      ACT.Copy).then_inc(wev.sem, 1)
        for s, n in ((wo1, QUADS), (wo2, QUADS), (wmm, QUADS), (wev, QUADS)):
            s.base += n

        xu, xd, xa, xp, xh, xg, uh, ul, vh, vl, gr, gc = self.counters(
            "ex_scores", "ex_sums", "ex_gelu", "ex_weighted", "ex_weighted_high", "ex_weighted_low",
            "ex_u_high", "ex_u_low", "ex_v_high", "ex_v_low", "ex_gate_row", "ex_gate")
        N = PEER_KEYS
        with nc.Block() as block:
            @block.sync
            def _(sp):
                with sp.Fori(1, N // 2) as turn:
                    for b in range(2):
                        row = experts[bass.ds(turn * 2 + b, 1)]
                        sp.wait_ge(*ul.at(turn * 2 + (b - 1)))
                        sp.dma_start(xraw[:, b, 0, :], row[:, :, 0:D].rearrange("a p n -> p (a n)")).then_inc(uloaded[b].sem, 16)
                        sp.wait_ge(*vl.at(turn * 2 + (b - 1)))
                        sp.dma_start(xraw[:, b, 1, :], row[:, :, D:].rearrange("a p n -> p (a n)")).then_inc(vloaded[b].sem, 16)

            @block.tensor
            def _(pe):
                def up(n, b, first=False):
                    pe.wait_ge(*ul.at(n + 1))
                    if not first:
                        pe.wait_ge(*xg.at(n - 1))
                    for k in range(KD):
                        last = self.product(ps[b][:, 0:T], [u[:, b, k * P:(k + 1) * P] for u in U],
                                            [x[:, k, :] for x in self.xT], k == 0, k == KD - 1)
                    last.then_inc(xu.sem, 1)

                def down(n, b, start=False, stop=False):
                    pe.wait_ge(*xg.at(n + 1))
                    pe.wait_ge(*vl.at(n + 1))
                    for t in range(TT):
                        for half in range(2):
                            last = self.product(ps[4 + 2 * t + half][:, :], [g[:, b, t * P:(t + 1) * P] for g in GA],
                                                [v[:, b, half * 512:(half + 1) * 512] for v in V], start, stop)
                    last.then_inc(xd.sem, 1)

                up(0, 0, first=True)
                up(1, 1, first=True)
                down(0, 0, start=True)
                with pe.Fori(1, N // 2) as turn:
                    for b in range(2):
                        up(turn * 2 + b, b)
                        down(turn * 2 + (b - 1), 1 - b)
                down(N - 1, 1, stop=True)
                self.gate_row(5, (0, 1)).then_inc(gr.sem, 1)

            @block.scalar
            def _(act):
                def u_high(n, b, turn):
                    act.wait_ge(*uloaded[b].at(turn * 16 + 16))
                    s_.activation(U[0][:, b, :], xraw[:, b, 0, :], ACT.Copy).then_inc(uh.sem, 1)

                def v_high(n, b, turn):
                    act.wait_ge(*vloaded[b].at(turn * 16 + 16))
                    s_.activation(V[0][:, b, :], xraw[:, b, 1, :], ACT.Copy).then_inc(vh.sem, 1)

                def step(n, b, turn, last=False):
                    act.wait_ge(*xu.at(n + 1))
                    s_.activation(ps[b][:, 0:T], ps[b][:, 0:T], ACT.Gelu).then_inc(xa.sem, 1)
                    if not last:
                        u_high(n + 2, b, turn + 1)
                    if last and b:
                        return
                    act.wait_ge(*xd.at(n))
                    v_high(n + 1, 1 - b, turn + b)

                u_high(0, 0, 0)
                u_high(1, 1, 0)
                v_high(0, 0, 0)
                act.wait_ge(*xu.at(1))
                s_.activation(ps[0][:, 0:T], ps[0][:, 0:T], ACT.Gelu).then_inc(xa.sem, 1)
                u_high(2, 0, 1)
                v_high(1, 1, 0)
                step(1, 1, 0)
                with act.Fori(1, N // 2 - 1) as turn:
                    for b in range(2):
                        step(turn * 2 + b, b, turn)
                step(N - 2, 0, N // 2 - 1, last=True)
                step(N - 1, 1, N // 2 - 1, last=True)
                act.wait_ge(*gr.at(1))
                for b in range(2):
                    s_.activation(g2[:, b * 512:(b + 1) * 512], ps[b][:, :], ACT.Copy).then_inc(gc.sem, 1)

            @block.gpsimd
            def _(pool):
                with pool.Fori(0, N // 2) as turn:
                    for b in range(2):
                        pool.wait_ge(*uh.at(turn * 2 + (b + 1)))
                        g_.tensor_tensor(U[1][:, b, :], xraw[:, b, 0, :], U[0][:, b, :].bitcast(F32), ALU.subtract
                                         ).then_inc(ul.sem, 1)

            @block.vector
            def _(dve):
                def v_low(n, b):
                    dve.wait_ge(*vh.at(n + 1))
                    v_.tensor_tensor(V[1][:, b, :], xraw[:, b, 1, :], V[0][:, b, :].bitcast(F32), ALU.subtract
                                     ).then_inc(vl.sem, 1)

                def step(n, b, first=False, last=False):
                    s = ps[b][:, 0:T]
                    dve.wait_ge(*xa.at(n + 1))
                    v_.tensor_tensor(s.unsqueeze(2), s.unsqueeze(2), Wt[:, :, bass.ds(n, 1)], ALU.mult).then_inc(xp.sem, 1)
                    dve.wait_ge(*xp.at(n + 1))
                    if not first:
                        dve.wait_ge(*xd.at(n - 1))
                    v_.tensor_copy(GA[0][:, b, :], s).then_inc(xh.sem, 1)
                    dve.wait_ge(*xh.at(n + 1))
                    v_.tensor_tensor(GA[1][:, b, :], s, GA[0][:, b, :].bitcast(F32), ALU.subtract).then_inc(xg.sem, 1)
                    if not last:
                        v_low(n + 1, 1 - b)

                v_low(0, 0)
                step(0, 0, first=True)
                step(1, 1, first=True)
                with dve.Fori(1, N // 2 - 1) as turn:
                    for b in range(2):
                        step(turn * 2 + b, b)
                step(N - 2, 0)
                step(N - 1, 1, last=True)
                dve.wait_ge(*gc.at(2))
                link = Chain(dve, self.dve_chain)
                for t in range(TT):
                    for half in range(2):
                        sl = slice(half * 512, (half + 1) * 512)
                        o = ps[4 + 2 * t + half][:, :]
                        link(v_.tensor_tensor(o, o, g2[:, sl], ALU.mult))
                        link(v_.tensor_tensor(self.x[:, t, sl], self.x[:, t, sl], o, ALU.add))
        for s, n in ((xu, N), (xd, N), (xa, N), (xp, N), (xh, N), (xg, N), (uh, N), (ul, N), (vh, N), (vl, N), (gr, 1), (gc, 2)):
            s.base += n
        for s in uloaded + vloaded:
            s.base += 8 * N


def build(nc, dram, out, stages=None, first=0, tiles=N_TILES):
    k = Kernel(nc, dram, out, stages)
    k.first = k.next_load = k.next_low = first
    k.tiles = tiles
    steps = [("ffn1a", lambda: k.ffn(G_FFN1A, 0)), ("ab", lambda: k.ab()),
             ("ffn2a", lambda: k.ffn(G_FFN2A, 2)), ("ffn1b", lambda: k.ffn(G_FFN1B, 3)),
             ("nsa", lambda: k.nsa()), ("ffn2b", lambda: k.ffn(G_FFN2B, 5)),
             ("final1", lambda: k.final_norm("final_norm")), ("mixed", lambda: k.second()),
             ("pre_final", lambda: k.peer()), ("out", lambda: k.final_norm("final_g"))]
    with k.ctx:
        k.start()
        k.end_stage()
        for name, step in steps:
            if stages is None or name in stages:
                step()
                k.end_stage()
        k.store(k.x)
        k.end_stage()


def cols_block(w, c0, n):
    return w[:, c0:c0 + n].reshape(KD, P, n).transpose(1, 0, 2).reshape(P, KD * n)


def rows_tiles(w):
    r = w.shape[0] // 256
    return [w[256 * i:256 * (i + 1)].reshape(2, P, D).transpose(1, 0, 2).reshape(P, TILE) for i in range(r)]


def tiles_of(block):
    return [block[:, i:i + TILE] for i in range(0, block.shape[1], TILE)]


def columns(v):
    return v.reshape(-1, P).T


def ffn_tiles(w_gu, w_down):
    tiles = []
    downs = rows_tiles(w_down)
    for i in range(FFN_GROUPS):
        both = np.concatenate([w_gu[:, 256 * i:256 * (i + 1)], w_gu[:, D_FF + 256 * i:D_FF + 256 * (i + 1)]], 1)
        tiles += tiles_of(cols_block(both, 0, 512))
        if i:
            tiles.append(downs[i - 1])
    return tiles + [downs[-1]]


def rg_tile(w_r, w_i):
    out = np.zeros((P, 16, P), np.float32)
    for m, w in enumerate((w_r, w_i)):
        for c in range(RG_CHUNKS):
            for b in range(2):
                out[64 * b:64 * b + 64, 4 * m + c, 64 * b:64 * b + 64] = w[2 * c + b]
    return out.reshape(P, TILE)


def nsa_q_order():
    order = []
    for c in range(8):
        for g in (2 * (c // 4), 2 * (c // 4) + 1):
            head = 4 * g + c % 4
            order += list(range(head * NSA_DH, (head + 1) * NSA_DH))
    return order


def layout(x, ffn1_norm, ffn1_w_gu, ffn1_w_down, mix_norm, ffn2_norm, ffn2_w_gu, ffn2_w_down, ab_w_in,
           rg_conv_w, rg_conv_b, rg_w_r, rg_b_r, rg_w_i, rg_b_i, rg_lambda, ml_conv_w, ml_conv_b,
           ml_b_i, ml_b_f, ml_norm, ab_w_out, nsa_w_in, nsa_pe_k, nsa_k_w1, nsa_k_b1, nsa_k_w2,
           nsa_pe_v, nsa_v_w1, nsa_v_b1, nsa_v_w2, nsa_b_gate, nsa_w_out, final_norm, c_2, ctx_2,
           c_ctx_2, ada_w_2, ada_b_2, norm_mix_g_2, norm_ffn_g_2, w_in_2, pool_w_2, pool_scale_2,
           pool_out_2, ret_decay_2, ret_norm_g_2, ret_out_2, w_out_2, peer_wq_2, peer_keys_2, peer_u_2,
           peer_v_2, final_g_2):
    tiles = ffn_tiles(ffn1_w_gu[0], ffn1_w_down[0])
    ab = ab_w_in[0]
    for c in range(0, 3072, 256):
        if c < 2048:
            tiles.append(cols_block(ab, c, 256))
        elif c % 512 == 0:
            tiles += tiles_of(cols_block(ab, c, 512))
    tiles += [rg_tile(rg_w_r[0], rg_w_i[0])] + rows_tiles(ab_w_out[0])
    tiles += ffn_tiles(ffn2_w_gu[0], ffn2_w_down[0])
    tiles += ffn_tiles(ffn1_w_gu[1], ffn1_w_down[1])
    nsa = nsa_w_in[0]
    part = lambda i: nsa[:, 1024 + 256 * i:1024 + 256 * (i + 1)]
    q = nsa[:, :1024][:, nsa_q_order()]
    n_tiles = [cols_block(q, c, 256) for c in range(0, 1024, 256)]
    n_tiles += [cols_block(part(2), 0, 256), cols_block(part(4), 0, 256)]
    for kv in (0, 1):
        w = part(kv).reshape(D, NSA_GROUPS, 1, NSA_DH)
        w = np.concatenate([w, w], 2).reshape(D, 512)
        n_tiles += [cols_block(w, 0, 256), cols_block(w, 256, 256)]
    n_tiles += tiles_of(cols_block(np.concatenate([part(3), part(5)], 1), 0, 512))
    for w1 in (nsa_k_w1[0], nsa_v_w1[0]):
        n_tiles += tiles_of(w1.reshape(16, P, 256).transpose(1, 0, 2).reshape(P, 4096))
    n_tiles += rows_tiles(nsa_w_out[0])
    tiles += n_tiles
    tiles += ffn_tiles(ffn2_w_gu[1], ffn2_w_down[1])
    w = w_in_2[0]
    s_tiles = [cols_block(ada_w_2[0], c, 256) for c in range(0, 6144, 256)]
    for c in range(0, 5632, 512):
        s_tiles += tiles_of(cols_block(w, c, 512))
    pw = np.zeros((P, TILE), np.float32)
    pw[:, :512] = pool_w_2[0].transpose(1, 0, 2).reshape(P, 512)
    s_tiles.append(pw)
    s_tiles += rows_tiles(pool_out_2[0]) + rows_tiles(ret_out_2[0]) + rows_tiles(w_out_2[0])
    s_tiles += [cols_block(peer_wq_2[0], c, 256) for c in range(0, 2048, 256)]
    s_tiles.append(peer_keys_2[0].transpose(3, 0, 1, 2).reshape(P, TILE))
    tiles += s_tiles
    stream = np.stack(tiles)
    assert stream.shape[0] == N_TILES, stream.shape

    u = peer_u_2[0].reshape(P, P, KD, P)
    v = peer_v_2[0].reshape(P, P, D)
    experts = np.concatenate([u.transpose(1, 3, 2, 0).reshape(P, P, D), v.transpose(1, 0, 2)], 2)

    gains = np.concatenate([columns(a) for a in (
        ffn1_norm[0], mix_norm[0], ffn2_norm[0], ffn1_norm[1], mix_norm[1], ffn2_norm[1],
        norm_mix_g_2[0], norm_ffn_g_2[0])], 1)
    conv_w = np.concatenate([rg_conv_w[0], ml_conv_w[0]], 1)
    conv_b = np.concatenate([rg_conv_b[0], ml_conv_b[0]], 0)
    taps = np.stack([columns(a) for a in [*conv_w, conv_b]], 2).reshape(P, 60)
    rgb = np.concatenate([columns(rg_b_r[0]), columns(rg_b_i[0]), columns(rg_lambda[0]), columns(ml_norm[0])], 1)
    ml_if = cols_block(ab, 3072, 8)
    ml_b = np.stack([ml_b_i[0], ml_b_f[0]], 1)
    j = np.arange(P)
    causal = (j[None, :] >= j[:, None]).astype(np.float32)
    ones = np.ones((P, P), np.float32)
    ml_mask = np.concatenate([causal, ones, causal], 1) * np.float32(ML_DH ** -0.5)
    ml_sel = np.repeat(np.eye(4, dtype=np.float32), P, 1)
    nsa_small = dict(
        w2=np.concatenate([nsa_k_w2[0].reshape(2, P, 64), nsa_k_w2[0].reshape(2, P, 64), nsa_v_w2[0].reshape(2, P, 64)], 2
                          ).transpose(1, 0, 2).reshape(P, 384),
        pe=np.concatenate([nsa_pe_k[0].reshape(16, P).T, nsa_pe_v[0].reshape(16, P).T], 1),
        b1=np.concatenate([columns(nsa_k_b1[0]), columns(nsa_v_b1[0])], 1),
        gw=cols_block(nsa, 2560, 48), gb=nsa_b_gate[0][None])
    t = np.arange(T)
    n = np.arange(16)
    cmask = ((n[None, :] * CMP_STRIDE + CMP_BLOCK - 1 <= t[:, None]) & (n[None, :] < N_CMP)).astype(np.float32)
    head_blocks = np.repeat(np.eye(8, dtype=np.float32), 16, 0)
    nmask = dict(causal_add=np.where(causal.T > 0, np.float32(0), np.float32(NEG)).astype(np.float32),
                 cmp=cmask.reshape(2, P, 16).transpose(1, 0, 2).reshape(P, 32), blocks=head_blocks)
    rows = T // 64
    row, col = np.repeat(np.arange(rows, dtype=np.float32), 64), np.tile(np.arange(64, dtype=np.float32), rows)
    inv = np.float32(10000.0) ** (-np.arange(32, dtype=np.float32) / 32)
    ang = np.concatenate([row[:, None] * inv, col[:, None] * inv], 1).astype(np.float32)
    rope = np.stack([np.cos(ang), np.sin(ang)], 0).astype(np.float32)
    rope = rope.reshape(2, 2, P, 64).transpose(2, 0, 1, 3).reshape(P, 256)
    band = np.zeros((4, T, T), np.float32)
    for g, wd in enumerate((2, 4, 8, 16)):
        lo, hi = np.clip(t - wd // 2, 0, T), np.clip(t + wd - wd // 2, 0, T)
        inside = (t[:, None] >= lo[None]) & (t[:, None] < hi[None])
        band[g] = inside / (hi - lo)[None].astype(np.float32) - np.eye(T, dtype=np.float32)
    band = band.reshape(4, 2, P, T).transpose(2, 0, 1, 3).reshape(P, 2048)
    rel = (t[None, :] - t[:, None]).astype(np.float32)
    ret = np.stack([np.maximum(rel, 0), np.maximum(-rel, 0), (rel >= 0).astype(np.float32), (rel < 0).astype(np.float32)])
    ret = ret.reshape(4, 2, P, T).transpose(2, 0, 1, 3).reshape(P, 2048)
    ret_row = np.concatenate([np.tile(t + 1, (P, 1)), np.tile(T - t, (P, 1))], 1).astype(np.float32)
    ret_col = np.stack([T - 1 - t, t], 1).reshape(2, P, 2).transpose(1, 0, 2).reshape(P, 4).astype(np.float32)
    iota = np.tile(np.arange(P, dtype=np.float32), (P, 1))
    return dict(
        x=x[0], stream=stream, experts=experts, ident=np.eye(P, dtype=np.float32), gains=gains,
        ab_taps=taps, ab_cols=rgb, ab_if=ml_if, ab_b=ml_b, ab_mask=ml_mask, ab_sel=ml_sel,
        nsa_w2=nsa_small["w2"], nsa_pe=nsa_small["pe"], nsa_b1=nsa_small["b1"], nsa_gw=nsa_small["gw"],
        nsa_gb=nsa_small["gb"], nsa_causal=nmask["causal_add"], nsa_cmp=nmask["cmp"], nsa_blocks=nmask["blocks"],
        final_norm=final_norm[None], final_g=final_g_2[None], ctx=ctx_2[0],
        cond=np.stack([columns(c_2[0]), columns(c_ctx_2)], 2).reshape(P, 16), ada_b=columns(ada_b_2[0]),
        rope=rope, band=band, pool_scale=columns(pool_scale_2[0]), decay=ret_decay_2[0].reshape(1, 8),
        ret=ret, ret_row=ret_row, ret_col=ret_col, ret_norm=columns(ret_norm_g_2[0]), iota=iota)


OUT_SHAPE = (1, T, D)


def kernel(**inputs):
    import concourse.bacc as bacc
    from concourse.bass_utils import run_bass_kernel_spmd
    arrays = layout(**{k: np.asarray(v) for k, v in inputs.items()})
    nc = bacc.Bacc("TRN2", target_bir_lowering=False, num_devices=1)
    dram, given = {}, {}
    for name, a in arrays.items():
        a = np.ascontiguousarray(a)
        given[f"in_{name}"] = a
        dram[name] = nc.dram_tensor(f"in_{name}", a.shape, mybir.dt.from_np(a.dtype), kind="ExternalInput").ap()
    out = nc.dram_tensor("out_0", OUT_SHAPE, F32, kind="ExternalOutput").ap()
    build(nc, dram, out)
    result = run_bass_kernel_spmd(nc, [given], core_ids=[0])
    return result.results[0]["out_0"]
```

```python
import concourse.bass as bass
from concourse import mybir
import numpy as np
from contextlib import ExitStack

F32 = mybir.dt.float32
F32R = mybir.dt.float32r
U32 = mybir.dt.uint32
ALU = mybir.AluOpType
ACT = mybir.ActivationFunctionType
AX = mybir.AxisListType

P = 128
T = 256
TT = T // P
D = 1024
KD = D // P
EPS = 1e-6
NEG = -1e30
D_FF = 2816
FFN_GROUPS = D_FF // 256
TILE = 2048
RAW, SPLIT = 6, 3
RG_CHUNKS = 4
CONV = 4
ML_HEADS, ML_DH = 4, 128
NSA_HEADS, NSA_GROUPS, NSA_DH = 16, 4, 64
CMP_BLOCK, CMP_STRIDE = 32, 16
N_CMP = (T - CMP_BLOCK) // CMP_STRIDE + 1
RET_HEADS, RET_DK, RET_DV = 4, 128, 256
PEER_HEADS, PEER_KEYS, PEER_TOPK = 8, 128, 16

FFN_TILES = 3 * FFN_GROUPS
G_FFN1A = 0
G_AB = G_FFN1A + FFN_TILES
G_FFN2A = G_AB + 17
G_FFN1B = G_FFN2A + FFN_TILES
G_NSA = G_FFN1B + FFN_TILES
G_FFN2B = G_NSA + 20
G_SECOND = G_FFN2B + FFN_TILES
G_PEER = G_SECOND + 57
N_TILES = G_SECOND + 65
WHOLE = {G_AB + 12, *range(G_NSA + 12, G_NSA + 16), *range(G_SECOND, G_SECOND + 24),
         *range(G_SECOND + 46, N_TILES)}


class Signal:

    def __init__(self, sem):
        self.sem, self.base = sem, 0

    def at(self, n):
        return self.sem, n + self.base


class Chain:

    def __init__(self, eng, signal):
        self.eng, self.counter = eng, signal

    def __call__(self, ins):
        self.counter.base += 1
        ins.then_inc(self.counter.sem, 1)
        self.eng.wait_ge(self.counter.sem, self.counter.base)


class Arena:

    def __init__(self, nc, tag, start, end):
        self.nc, self.tag, self.at, self.end = nc, tag, start, end

    def __call__(self, name, cols, parts=P, dt=F32):
        size = (cols * 4 + 31) // 32 * 32
        t = self.nc.alloc_sbuf_tensor_at(f"{self.tag}_{name}", [parts, cols], dt, offset=self.at)
        self.at += size
        assert self.at <= self.end, (self.tag, name, self.at, self.end)
        return t[:, :]


def sbuf_plan(nc):
    base = (nc.sbuf_base + 31) // 32 * 32
    end = nc.sbuf_usable_end // 32 * 32
    ring_end = base + (RAW + 2 * SPLIT) * TILE * 4
    keep = end - (3 * 8192 + 3200)
    return base, ring_end, keep, end


class Kernel:
    def __init__(self, nc, dram, out, stages):
        self.nc, self.dram, self.out, self.stages = nc, dram, out, stages
        self.ctx = ExitStack()
        self.base, self.ring_end, self.keep, self.end = sbuf_plan(nc)
        rings = Arena(nc, "ring", self.base, self.ring_end)
        self.raw = rings("raw", RAW * TILE)
        self.high = rings("high", SPLIT * TILE, dt=F32R)
        self.low = rings("low", SPLIT * TILE, dt=F32R)
        keep = Arena(nc, "keep", self.keep, self.end)
        self.x = keep("x", TT * D).rearrange("p (t d) -> p t d", t=TT)
        self.xw = Arena(nc, "alias", keep.at, keep.at + 8192)("xT", KD * T).rearrange("p (k t) -> p k t", k=KD)
        self.spare_at = keep.at + 8192
        self.xT = tuple(keep(f"xT{n}", KD * T, dt=F32R).rearrange("p (k t) -> p k t", k=KD) for n in ("high", "low"))
        self.ident = keep("ident", P)
        self.gains = keep("gains", 8 * KD).rearrange("p (n k) -> p n k", n=8)
        self.stat = keep("stat", 64)
        self.power = self.stat[:, 62:64]
        self.modT = keep("modT", 48 * 2).rearrange("p (c s) -> p c s", s=2)
        self.gA = keep("gA", 4 * KD).rearrange("p (n k) -> p n k", n=4)
        self.psum = [self.ctx.enter_context(nc.psum_tensor(f"bank{i}", [P, 512], F32)) for i in range(8)]
        self.sems, self.own, self.keeping = {}, [], True
        self.next_load = self.next_high = self.next_low = 0
        self.first, self.tiles = 0, 0
        self.loaded = [self.counter(f"raw_loaded{s}") for s in range(RAW)]
        self.high_done, self.low_done, self.released = self.counters("high_made", "low_made", "tile_released")
        self.act_chain = self.counter("act_chain")
        self.dve_chain = self.counter("dve_chain")
        self.keeping = False

    def counter(self, name):
        if name not in self.sems:
            if self.keeping or name.startswith(("nrm_", "ffn_", "add_", "fn_")):
                sem = self.ctx.enter_context(self.nc.semaphore(name))
            else:
                sem = self.nc.alloc_semaphore(name)
                self.own.append((name, sem))
            self.sems[name] = Signal(sem)
        return self.sems[name]

    def end_stage(self):
        for name, _ in self.own:
            self.sems.pop(name)
        self.nc.clear_and_free_semaphores([sem for _, sem in self.own])
        self.nc.all_engine_barrier()
        self.own = []

    def counters(self, *names):
        return [self.counter(n) for n in names]

    def arena(self, tag, whole=False):
        return Arena(self.nc, tag, self.base + RAW * TILE * 4 if whole else self.ring_end, self.keep)

    def raw_slot(self, n):
        at = (n - self.first) % RAW * TILE
        return self.raw[:, at:at + TILE]

    def parts(self, n):
        at = (n - self.first) % SPLIT * TILE
        return self.high[:, at:at + TILE], self.low[:, at:at + TILE]

    def highs(self, n):
        return sum(i not in WHOLE for i in range(self.first, n + 1))

    def released_at(self, n, loop=0):
        return self.released.sem, loop + (n - self.first + 1)

    def need(self, pe, n, loop=0):
        i = n - self.first
        if n in WHOLE:
            pe.wait_ge(self.loaded[i % RAW].sem, 16 * (i // RAW + 1))
        else:
            pe.wait_ge(self.low_done.sem, loop + (i + 1))

    def make_high(self, act, n, loop=0):
        i = n - self.first
        if n in WHOLE or i >= self.tiles:
            return
        act.wait_ge(self.loaded[i % RAW].sem, (loop * 16) + 16 * (i // RAW + 1))
        if i >= SPLIT:
            act.wait_ge(self.released.sem, loop * RAW + (i - SPLIT + 1))
        self.nc.scalar.activation(self.parts(n)[0], self.raw_slot(n), ACT.Copy).then_inc(self.high_done.sem, 1)

    def make_lows(self, pool, used_end):
        end = min(used_end + SPLIT, self.first + self.tiles)

        def low(n, loop=0):
            high, low_ = self.parts(n)
            if n in WHOLE:
                if n > self.first and n - 1 not in WHOLE:
                    pool.wait_ge(self.low_done.sem, n - self.first)
                pool.sem_inc(self.low_done.sem, 1)
                return
            pool.wait_ge(self.high_done.sem, loop + self.highs(n))
            self.nc.gpsimd.tensor_tensor(low_, self.raw_slot(n), high.bitcast(F32), ALU.subtract
                                         ).then_inc(self.low_done.sem, 1)

        n = self.next_low
        while n < end:
            turns = (end - n) // RAW
            if turns >= 2 and not any(n <= i < n + turns * RAW for i in WHOLE):
                with pool.Fori(0, turns) as turn:
                    for s in range(RAW):
                        low(n + s, turn * RAW)
                n += turns * RAW
            else:
                low(n)
                n += 1
        self.next_low = end

    def loads(self, sp, used_end, end=None):
        end = end or min([used_end + SPLIT + RAW, self.first + self.tiles] + [w + RAW for w in WHOLE if w >= used_end])
        stream = self.dram["stream"]

        def load(n, index, loop=0):
            i = n - self.first
            if i >= RAW:
                sp.wait_ge(self.low_done.sem, loop + (i - RAW + 1))
                if n - RAW in WHOLE:
                    sp.wait_ge(*self.released_at(n - RAW))
            sp.dma_start(self.raw_slot(n), stream[bass.ds(index, 1)].rearrange("a p n -> p (a n)")
                         ).then_inc(self.loaded[i % RAW].sem, 16)

        n = self.next_load
        while n < end:
            turns = (end - n) // RAW
            if n - self.first >= RAW and turns >= 2 and not any(n - RAW <= i < n + turns * RAW for i in WHOLE):
                with sp.Fori(0, turns) as turn:
                    for s in range(RAW):
                        load(n + s, turn * RAW + (n + s), turn * RAW)
                n += turns * RAW
            else:
                load(n, n)
                n += 1
        self.next_load = max(end, self.next_load)

    def product(self, out, stationary, moving, start, stop):
        (sh, sl), (mh, ml) = stationary, moving
        mm = self.nc.tensor.matmul
        mm(out, sh, mh, start=start, stop=False)
        mm(out, sh, ml, start=False, stop=False)
        return mm(out, sl, mh, start=False, stop=stop)

    def highs_from_psum(self, act, b0, out, filled, made, scale=None, bias=None):
        s_ = self.nc.scalar
        for b in range(KD // 2):
            act.wait_ge(*filled.at(b + 1))
            for k in (2 * b, 2 * b + 1):
                v = self.psum[b0 + b][:, (k % 2) * T:(k % 2 + 1) * T]
                if bias is not None:
                    s_.activation(v, v, ACT.Identity, scale=scale[:, k:k + 1], bias=bias[:, k:k + 1]).then_inc(made.sem, 1)
            if bias is not None:
                act.wait_ge(*made.at(4 * b + 2))
            for k in (2 * b, 2 * b + 1):
                v = self.psum[b0 + b][:, (k % 2) * T:(k % 2 + 1) * T]
                if bias is None and scale is not None:
                    ins = s_.activation(out[0][:, k, :], v, ACT.Copy, scale=scale[:, k:k + 1])
                else:
                    ins = s_.activation(out[0][:, k, :], v, ACT.Copy)
                ins.then_inc(made.sem, 1)

    def lows_from_psum(self, dve, b0, out, made, low, scale=None, bias=None):
        v_ = self.nc.vector
        step = 2 if bias is None else 4
        for b in range(KD // 2):
            dve.wait_ge(*made.at(step * (b + 1)))
            for k in (2 * b, 2 * b + 1):
                v = self.psum[b0 + b][:, (k % 2) * T:(k % 2 + 1) * T]
                h = out[0][:, k, :].bitcast(F32)
                if bias is None and scale is not None:
                    ins = v_.scalar_tensor_tensor(out[1][:, k, :], v, scale[:, k:k + 1], h, ALU.mult, ALU.subtract)
                else:
                    ins = v_.tensor_tensor(out[1][:, k, :], v, h, ALU.subtract)
                ins.then_inc(low.sem, 1)

    def norm_parts(self, src, outT, scale, bias, work, b0=0, names="nrm"):
        nc, stat, ps = self.nc, self.stat, self.psum
        at = 0 if names == "nrm" else 2 * TT
        ss, rstd = stat[:, at:at + TT], stat[:, at + TT:at + 2 * TT]
        xs, split = work, isinstance(outT, tuple)
        squared, mean, root, scaled, turned, high, evac = self.counters(*(f"{names}_{n}" for n in (
            "squared", "mean", "root", "scaled", "turned", "high", "low")))

        def on_act(act, rows=True, columns=True):
            for t in range(TT) if rows else ():
                nc.scalar.activation(xs[:, t, :], src[:, t, :], ACT.Square,
                                     accum_out=ss[:, t:t + 1]).then_inc(squared.sem, 1)
            if rows:
                act.wait_ge(*root.at(1))
                nc.scalar.activation(xs[:, 1, :], src[:, 1, :], ACT.Copy, scale=rstd[:, 1:2]).then_inc(scaled.sem, 1)
            if not columns:
                return
            if split:
                self.highs_from_psum(act, b0, outT, turned, high, scale, bias)
                return
            for k in (2, 3, 6, 7):
                act.wait_ge(*turned.at(k // 2 + 1))
                nc.scalar.activation(outT[:, k, :], ps[k // 2][:, (k % 2) * T:(k % 2 + 1) * T], ACT.Identity,
                                     scale=scale[:, k:k + 1],
                                     bias=bias[:, k:k + 1] if bias is not None else 0.0).then_inc(evac.sem, 1)


        def on_dve(dve):
            link = Chain(dve, self.dve_chain)
            dve.wait_ge(*squared.at(TT))
            nc.vector.tensor_scalar(ss, ss, 1.0 / D, EPS, ALU.mult, ALU.add).then_inc(mean.sem, 1)
            dve.wait_ge(*root.at(1))
            nc.vector.tensor_scalar(xs[:, 0, :], src[:, 0, :], rstd[:, 0:1], None, ALU.mult).then_inc(scaled.sem, 1)
            if split:
                self.lows_from_psum(dve, b0, outT, high, evac, scale, bias)
                return
            for k in (0, 1, 4, 5):
                dve.wait_ge(*turned.at(k // 2 + 1))
                if bias is not None:
                    nc.vector.tensor_scalar(outT[:, k, :], ps[k // 2][:, (k % 2) * T:(k % 2 + 1) * T], scale[:, k:k + 1],
                                            bias[:, k:k + 1], ALU.mult, ALU.add).then_inc(evac.sem, 1)
                else:
                    nc.vector.tensor_scalar(outT[:, k, :], ps[k // 2][:, (k % 2) * T:(k % 2 + 1) * T], scale[:, k:k + 1],
                                            None, ALU.mult).then_inc(evac.sem, 1)


        def on_pool(pool):
            pool.wait_ge(*mean.at(1))
            nc.gpsimd.tensor_tensor(rstd, ss, self.power, ALU.pow).then_inc(root.sem, 1)

        def on_pe(pe, chunks=KD):
            pe.wait_ge(*scaled.at(TT))
            for b in range(KD // 2):
                for k in (2 * b, 2 * b + 1):
                    for t in range(TT):
                        last = nc.tensor.transpose(ps[b0 + b][:, (k % 2) * T + t * P:(k % 2) * T + (t + 1) * P],
                                                   xs[:, t, k * P:(k + 1) * P], self.ident)
                last.then_inc(turned.sem, 1)
            if chunks:
                pe.wait_ge(*evac.at(chunks))

        def end():
            squared.base += TT
            mean.base += 1
            root.base += 1
            scaled.base += TT
            turned.base += KD // 2
            evac.base += KD
            if split:
                high.base += KD if bias is None else 2 * KD
        return on_act, on_dve, on_pool, on_pe, end

    def start(self):
        nc = self.nc
        here, filled = self.counters("start_loaded", "start_filled")
        with nc.Block() as block:
            @block.sync
            def _(sp):
                sp.dma_start(self.x, self.dram["x"].rearrange("(t p) d -> p t d", p=P)).then_inc(here.sem, 16)
                sp.dma_start(self.ident, self.dram["ident"]).then_inc(here.sem, 16)
                sp.dma_start(self.gains, self.dram["gains"].rearrange("p (n k) -> p n k", k=KD)).then_inc(here.sem, 16)
                self.loads(sp, self.first)
                sp.wait_ge(*here.at(48))

            @block.scalar
            def _(act):
                for n in range(SPLIT):
                    self.make_high(act, self.first + n)

            @block.gpsimd
            def _(pool):
                nc.gpsimd.memset(self.power, -0.5).then_inc(filled.sem, 1)
                pool.wait_ge(*filled.at(1))
                self.make_lows(pool, self.first)
        here.base += 48
        filled.base += 1

    def ffn(self, g0, gain):
        nc, ps = self.nc, self.psum
        work = self.arena(f"ffn{g0}")
        xs = work("xs", TT * D).rearrange("p (t d) -> p t d", t=TT)
        sg = [work(f"silu{t}", 256) for t in range(TT)]
        h = [work(f"h{t}", 256) for t in range(TT)]
        hT = [[work(f"hT{t}{n}", 256, dt=F32R) for n in range(2)] for t in range(TT)]
        norm_act, norm_dve, norm_pool, norm_pe, norm_end = self.norm_parts(
            self.x, self.xT, self.gains[:, gain, :], None, xs)
        silu = self.counters("ffn_silu0", "ffn_silu1")
        made = self.counters("ffn_h0", "ffn_h1")
        turned = self.counters("ffn_turned0", "ffn_turned1")
        hready = self.counters("ffn_hT0", "ffn_hT1")
        hhigh, acc = self.counters("ffn_hThigh", "ffn_acc")
        N = FFN_GROUPS
        TURNS = (N - 3) // 2
        tile_a = lambda i: g0 + (3 * i - 1 if i else 0)
        tile_b = lambda i: tile_a(i) + 1
        tile_d = lambda i: g0 + 3 * i + 4 if i < N - 1 else g0 + 3 * N - 1
        bank = lambda i, t: ps[2 * (i % 2) + t]

        with nc.Block() as block:
            @block.sync
            def _(sp):
                self.loads(sp, g0 + FFN_TILES)

            @block.gpsimd
            def _(pool):
                norm_pool(pool)
                self.make_lows(pool, g0 + FFN_TILES)

            @block.tensor
            def _(pe):
                norm_pe(pe, 4)

                def gate_up(i, second, loop):
                    n = tile_b(i) if second else tile_a(i)
                    self.need(pe, n, 3 * loop)
                    high, low = self.parts(n)
                    for k in range(4):
                        cut = slice(k * 512, (k + 1) * 512)
                        for t in range(TT):
                            kk = k + 4 * second
                            last = self.product(bank(i, t)[:, :], [x[:, kk, t * P:(t + 1) * P] for x in self.xT],
                                                (high[:, cut], low[:, cut]), kk == 0, kk == KD - 1)
                    last.then_inc(self.released.sem, 1)

                def turn(i, loop):
                    for t in range(TT):
                        pe.wait_ge(*made[t].at(loop + (i + 1)))
                        for f in range(2):
                            last = nc.tensor.transpose(bank(i, t)[:, f * P:(f + 1) * P],
                                                       h[t][:, f * P:(f + 1) * P], self.ident)
                        last.then_inc(turned[t].sem, 1)

                def down(i, loop, start, stop):
                    n = tile_d(i)
                    self.need(pe, n, 3 * loop)
                    high, low = self.parts(n)
                    for t in range(TT):
                        pe.wait_ge(*hready[t].at(loop + (i + 1)))
                        for f in range(2):
                            for half in range(2):
                                cut = slice(f * 1024 + half * 512, f * 1024 + (half + 1) * 512)
                                last = self.product(ps[4 + 2 * t + half][:, :], [x[:, f * P:(f + 1) * P] for x in hT[t]],
                                                    (high[:, cut], low[:, cut]), start and f == 0, stop and f == 1)
                    last.then_inc(self.released.sem, 1)

                def group(i, loop=0):
                    if i >= 2:
                        for t in range(TT):
                            pe.wait_ge(*hready[t].at(loop + (i - 1)))
                    gate_up(i, 0, loop)
                    if i == 0:
                        pe.wait_ge(*self.counter("nrm_low").at(KD))
                    else:
                        turn(i - 1, loop)
                    gate_up(i, 1, loop)
                    if i:
                        down(i - 1, loop, i == 1, False)

                group(0)
                group(1)
                with pe.Fori(0, TURNS) as turns:
                    for i in (2, 3):
                        group(i, turns * 2)
                group(N - 1)
                turn(N - 1, 0)
                down(N - 1, 0, False, True)

            @block.scalar
            def _(act):
                norm_act(act)

                def step(i, loop=0, tiles=0):
                    if i:
                        self.make_high(act, tile_a(i) + SPLIT, loop)
                    else:
                        self.make_high(act, g0 + SPLIT)
                    act.wait_ge(*self.released_at(tile_b(i), loop * RAW))
                    for t in range(TT):
                        if i:
                            act.wait_ge(*made[t].at(loop * 2 + i))
                        nc.scalar.activation(sg[t], bank(i, t)[:, 0:256], ACT.Silu).then_inc(silu[t].sem, 1)
                    self.make_high(act, tile_b(i) + SPLIT, loop)
                    if i:
                        self.make_high(act, tile_b(i) + 1 + SPLIT, loop)

                step(0)
                step(1)
                with act.Fori(0, TURNS) as turns:
                    for i in (2, 3):
                        step(i, turns)
                step(N - 1)
                self.make_high(act, g0 + FFN_TILES - 1 + SPLIT)

            @block.vector
            def _(dve):
                norm_dve(dve)

                def step(i, loop=0):
                    for t in range(TT):
                        dve.wait_ge(*silu[t].at(loop + (i + 1)))
                        if i:
                            dve.wait_ge(*turned[t].at(loop + i))
                        nc.vector.tensor_tensor(h[t], sg[t], bank(i, t)[:, 256:512], ALU.mult
                                                ).then_inc(made[t].sem, 1)
                    if i:
                        dve.wait_ge(*self.released_at(tile_d(i - 1), loop * 3))
                    for t in range(TT):
                        dve.wait_ge(*turned[t].at(loop + (i + 1)))
                        v = bank(i, t)[:, 0:256]
                        nc.vector.tensor_copy(hT[t][0], v).then_inc(hhigh.sem, 1)
                        dve.wait_ge(*hhigh.at(loop * 2 + (2 * i + t + 1)))
                        nc.vector.tensor_tensor(hT[t][1], v, hT[t][0].bitcast(F32), ALU.subtract
                                                ).then_inc(hready[t].sem, 1)

                step(0)
                step(1)
                with dve.Fori(0, TURNS) as turns:
                    for i in (2, 3):
                        step(i, turns * 2)
                step(N - 1)
                dve.wait_ge(*self.released_at(tile_d(N - 1)))
                for t in range(TT):
                    for half in range(2):
                        xv = self.x[:, t, half * 512:(half + 1) * 512]
                        last = nc.vector.scalar_tensor_tensor(xv, ps[4 + 2 * t + half][:, :], 0.5, xv,
                                                              ALU.mult, ALU.add)
                last.then_inc(acc.sem, 1)
                dve.wait_ge(*acc.at(1))
        norm_end()
        for s in silu + made + turned + hready:
            s.base += N
        hhigh.base += 2 * N
        acc.base += 1

    def store(self, src):
        nc = self.nc
        (stored,) = self.counters("stored")
        with nc.Block() as block:
            @block.sync
            def _(sp):
                sp.dma_start(self.out[0].rearrange("(t p) d -> p t d", p=P), src).then_inc(stored.sem, 16)
                sp.wait_ge(*stored.at(16))
        stored.base += 16

    def ring_tile(self, pe, g0, t):
        if g0 + t not in self.waited:
            self.waited.add(g0 + t)
            self.need(pe, g0 + t)
        return self.raw_slot(g0 + t) if g0 + t in WHOLE else self.parts(g0 + t)

    def mm(self, out, lhsT, rhs, start, stop):
        if isinstance(lhsT, (tuple, list)):
            ins = self.product(out, lhsT, rhs, start, stop)
        else:
            ins = self.nc.tensor.matmul(out, lhsT, rhs, start=start, stop=stop)
        if self.owed:
            self.owed -= 1
            ins.then_inc(self.released.sem, 1)
        return ins

    @staticmethod
    def cut(a, *at):
        return [x[at] for x in a] if isinstance(a, tuple) else a[at]

    def give_back(self, t):
        self.owed += 1

    def flush(self, pe, done):
        pe.wait_ge(*done)
        while self.owed:
            self.owed -= 1
            pe.sem_inc(self.released.sem, 1)

    def stationary_cols(self, out, w, c, actT):
        for k in range(KD):
            last = self.mm(out, self.cut(w, slice(None), slice(k * 256 + c * P, k * 256 + (c + 1) * P)),
                           self.cut(actT, slice(None), k), k == 0, k == KD - 1)
        return last

    def moving_cols(self, pe, outs, g0, tile, actT, done, last_use=True):
        for k in range(KD):
            w = self.cut(self.ring_tile(pe, g0, tile + k // 4), slice(None), slice((k % 4) * 512, (k % 4 + 1) * 512))
            for t in range(TT):
                last = self.mm(outs[t], self.cut(actT, slice(None), k, slice(t * P, (t + 1) * P)), w, k == 0, k == KD - 1)
                if k == KD - 1:
                    last.then_inc(done.sem, 1)
            if k % 4 == 3 and last_use:
                self.give_back(tile + k // 4)

    def rows_product(self, pe, g0, tile, actT, kn, banks, done):
        for k in range(kn):
            w = self.ring_tile(pe, g0, tile + k // 2)
            for t in range(TT):
                for half in range(2):
                    at = (k % 2) * D + half * 512
                    last = self.mm(self.psum[banks[2 * t + half]][:, :],
                                   self.cut(actT, slice(None), k, slice(t * P, (t + 1) * P)),
                                   self.cut(w, slice(None), slice(at, at + 512)), k == 0, k == kn - 1)
            if k % 2 == 1:
                self.give_back(tile + k // 2)
        last.then_inc(done.sem, 1)

    def begin_stage(self):
        self.waited, self.owed = set(), 0

    def ab(self):
        nc, ps, G = self.nc, self.psum, G_AB
        v_, s_ = nc.vector, nc.scalar
        self.begin_stage()
        work = self.arena("ab")
        taps = work("taps", 60).rearrange("p (m k) -> p m k", k=5)
        cols = work("cols", 16).rearrange("p (n c) -> p n c", c=4)
        wif = work("wif", 64).rearrange("p (k f) -> p k f", f=8)
        bif = work("bif", 2, parts=4)
        mask = work("mask", 384)
        sel = work("sel", 512, parts=4)
        xs = work("xs", TT * D).rearrange("p (t d) -> p t d", t=TT)
        xa = work("xa", 4 * (T + 3)).rearrange("p (c t) -> p c t", c=4)
        qk = work("qk", 8 * (T + 3)).rearrange("p (c t) -> p c t", c=8)
        ga = work("ga", 4 * T).rearrange("p (c t) -> p c t", c=4)
        v1 = work("v1", TT * 4 * 129).rearrange("p (t h d) -> p t h d", t=TT, h=4)
        so = work("so", TT * 512).rearrange("p (t d) -> p t d", t=TT)
        xc = work("xc", 4 * T).rearrange("p (c t) -> p c t", c=4)
        qc = work("qc", 8 * T).rearrange("p (c t) -> p c t", c=8)
        r = work("r", 4 * T).rearrange("p (c t) -> p c t", c=4)
        ig = work("ig", 4 * T).rearrange("p (c t) -> p c t", c=4)
        a = work("a", 4 * T).rearrange("p (c t) -> p c t", c=4)
        u = work("u", 4 * T).rearrange("p (c t) -> p c t", c=4)
        row = [work(f"row{i}", T, parts=4) for i in range(7)]
        ir, fr, mn, ex, cumf, al, ones = row
        big = work("E", 4 * 384).rearrange("p (h n) -> p h n", h=4)
        tiny = work("tiny", 96)
        Hn = work("Hn", TT * 4 * 129).rearrange("p (t h d) -> p t h d", t=TT, h=4)
        yT = self.xT
        wif_parts = tuple(work(f"wif{n}", 64, dt=F32R).rearrange("p (k f) -> p k f", f=8) for n in ("high", "low"))
        ifn = work("ifn", 16)
        wsplit, ifs, silus = self.counters("ab_wif", "ab_if", "ab_silu")
        small, done, freed, conv, z = self.counters("ab_small", "ab_done", "ab_freed", "ab_conv", "ab_padded")
        norm_act, norm_dve, norm_pool, norm_pe, norm_end = self.norm_parts(
            self.x, self.xT, self.gains[:, 1, :], None, xs)

        with nc.Block() as block:
            @block.sync
            def _(sp):
                for dst, name in ((taps.rearrange("p m k -> p (m k)"), "ab_taps"), (cols.rearrange("p n c -> p (n c)"), "ab_cols"),
                                  (wif.rearrange("p k f -> p (k f)"), "ab_if"), (bif, "ab_b"),
                                  (mask, "ab_mask"), (sel, "ab_sel")):
                    sp.dma_start(dst, self.dram[name]).then_inc(small.sem, 16)
                self.loads(sp, G + 12)

            @block.gpsimd
            def _(pool):
                nc.gpsimd.memset(xa[:, :, 0:3], 0.0).then_inc(z.sem, 1)
                nc.gpsimd.memset(qk[:, :, 0:3], 0.0).then_inc(z.sem, 1)
                nc.gpsimd.memset(v1[:, :, :, 128:129], 1.0).then_inc(z.sem, 1)
                nc.gpsimd.memset(ones, 1.0).then_inc(z.sem, 1)
                norm_pool(pool)
                self.make_lows(pool, G + 10)

            @block.tensor
            def _(pe):
                norm_pe(pe)
                for n in range(16):
                    if n >= 4:
                        pe.wait_ge(*freed.at(n - 3))
                    w = self.ring_tile(pe, G, n // 2)
                    self.stationary_cols(ps[n % 4][:, 0:T], w, n % 2, self.xT).then_inc(done.sem, 1)
                    if n % 2:
                        self.give_back(n // 2)
                for n in (16, 18):
                    pe.wait_ge(*freed.at(n - 2))
                    self.moving_cols(pe, [ps[(n + t) % 4][:, :] for t in range(TT)], G, 8 + (n - 16), self.xT, done)
                pe.wait_ge(*freed.at(18))
                pe.wait_ge(*wsplit.at(2))
                for t in range(TT):
                    for k in range(KD):
                        last = self.mm(ps[0][:, 8 * t:8 * t + 8], self.cut(self.xT, slice(None), k, slice(t * P, (t + 1) * P)),
                                       self.cut(wif_parts, slice(None), k), k == 0, k == KD - 1)
                last.then_inc(ifs.sem, 1)
                pe.wait_ge(*ifs.at(2))
                for t in range(TT):
                    for f in range(2):
                        last = nc.tensor.transpose(ps[1][0:4, f * T + t * P:f * T + (t + 1) * P],
                                                   ifn[:, 8 * t + 4 * f:8 * t + 4 * f + 4], self.ident)
                last.then_inc(done.sem, 1)
                self.flush(pe, done.at(21))

            @block.scalar
            def _(act):
                norm_act(act)
                act.wait_ge(*small.at(96))
                s_.activation(wif_parts[0], wif, ACT.Copy).then_inc(wsplit.sem, 1)
                for n in range(20):
                    if n in (2, 4, 6, 8, 10, 12, 14, 16):
                        self.make_high(act, G + n // 2 - 1 + SPLIT)
                    act.wait_ge(*done.at(n + 1))
                    src = ps[n % 4]
                    if n < 4:
                        ins = s_.activation(xa[:, n, 3:], src[:, 0:T], ACT.Copy)
                    elif n < 8:
                        ins = s_.activation(ga[:, n - 4, :], src[:, 0:T], ACT.Gelu_apprx_tanh)
                    elif n < 16:
                        ins = s_.activation(qk[:, n - 8, 3:], src[:, 0:T], ACT.Copy)
                    elif n < 18:
                        ins = s_.activation(v1[:, n - 16, :, 0:128], src[:, :].rearrange("p (h d) -> p h d", h=4), ACT.Copy)
                    else:
                        ins = s_.activation(so[:, n - 18, :], src[:, :], ACT.Sigmoid)
                    ins.then_inc(freed.sem, 1)
                    if n in (16, 17):
                        self.make_high(act, G + n - 8 + SPLIT)
                for c in range(8):
                    act.wait_ge(*conv.at(5 + c))
                    s_.activation(qc[:, c, :], qc[:, c, :], ACT.Silu).then_inc(silus.sem, 1)
                act.wait_ge(*ifs.at(1))
                s_.activation(ifn, ps[0][:, 0:16], ACT.Copy).then_inc(ifs.sem, 1)
                act.wait_ge(*done.at(21))
                s_.activation(ir, ps[1][0:4, 0:T], ACT.Identity, bias=bif[:, 0:1]).then_inc(freed.sem, 1)
                s_.activation(fr, ps[1][0:4, T:2 * T], ACT.Identity, bias=bif[:, 1:2]).then_inc(freed.sem, 1)

            @block.vector
            def _(dve):
                norm_dve(dve)
                link = Chain(dve, self.dve_chain)
                dve.wait_ge(*small.at(96))
                dve.wait_ge(*wsplit.at(1))
                v_.tensor_tensor(wif_parts[1], wif, wif_parts[0].bitcast(F32), ALU.subtract).then_inc(wsplit.sem, 1)
                dve.wait_ge(*z.at(4))
                for m in range(12):
                    src, dst = (xa[:, m, :], xc[:, m, :]) if m < 4 else (qk[:, m - 4, :], qc[:, m - 4, :])
                    dve.wait_ge(*freed.at(m + 1 if m < 4 else m + 5))
                    link(v_.tensor_scalar(dst, src[:, 0:T], taps[:, m, 0:1], taps[:, m, 4:5], ALU.mult, ALU.add))
                    for j in range(1, CONV):
                        ins = v_.scalar_tensor_tensor(dst, src[:, j:j + T], taps[:, m, j:j + 1], dst, ALU.mult, ALU.add)
                        if j < CONV - 1:
                            link(ins)
                    ins.then_inc(conv.sem, 1)
        norm_end()
        done.base += 21
        freed.base += 22
        silus.base += 8
        conv.base += 12
        z.base += 4
        wsplit.base += 2
        ifs.base += 2

        lam = tiny[:, 0:4]
        y, s1, s2, q_, negc, posc, mx = (tiny[:, 4 * i:4 * i + 4] for i in range(1, 8))
        aCol = tiny[:, 32:40]
        em = tiny[:, 40:48]
        dn, rc, ss, rt = (tiny[:, 48 + 8 * i:56 + 8 * i] for i in range(4))
        gates, sig, lamy, lamc, decays, u2, root, hs, ydone = self.counters(
            "ab_gates", "ab_sig", "ab_lamy", "ab_lamc", "ab_decays", "ab_u2", "ab_root", "ab_hs", "ab_y")
        r1, r3, r4, turned, colsr, mrow, sdone, e1, e2, pready, pv, hn, n1, n2, n3, turn2, yb = self.counters(
            "ml_arg", "ml_ln", "ml_rows", "ml_turned", "ml_cols", "ml_bcast", "ml_scores", "ml_e1",
            "ml_e2", "ml_p", "ml_pv", "ml_hn", "ml_ss", "ml_rt", "ml_yb", "ml_turn2", "ml_yT")
        ln_ = row[3]
        with nc.Block() as block:
            @block.sync
            def _(sp):
                self.loads(sp, G + 13)

            @block.gpsimd
            def _(pool):
                self.make_lows(pool, G + 13)

            @block.tensor
            def _(pe):
                w = self.ring_tile(pe, G, 12)
                for m in range(2):
                    for c in range(4):
                        last = self.mm(ps[2 * m + c // 2][:, (c % 2) * T:(c % 2 + 1) * T],
                                       w[:, (4 * m + c) * P:(4 * m + c + 1) * P], xc[:, c, :], True, True)
                    last.then_inc(gates.sem, 1)
                self.give_back(12)
                self.flush(pe, gates.at(2))
                pe.wait_ge(*sig.at(4))
                def scores(h):
                    b = ps[6 + h % 2]
                    nc.tensor.matmul(b[:, 0:256], qc[:, 4 + h, 0:P], qc[:, h, :], start=True, stop=True)
                    nc.tensor.matmul(b[:, 256:384], qc[:, 4 + h, P:T], qc[:, h, P:T], start=True, stop=True
                                     ).then_inc(sdone.sem, 1)
                scores(0)
                scores(1)
                pe.wait_ge(*r4.at(1))
                for n, rw in enumerate((al, mn)):
                    for t in range(TT):
                        last = nc.tensor.transpose(ps[3][:, 8 * n + 4 * t:8 * n + 4 * t + 4],
                                                   rw[:, t * P:(t + 1) * P], self.ident[0:4, 0:4])
                last.then_inc(turned.sem, 1)
                for h in range(4):
                    last = nc.tensor.matmul(ps[4 + h // 2][:, (h % 2) * T:(h % 2 + 1) * T],
                                            sel[:, h * P:(h + 1) * P], ex, start=True, stop=True)
                last.then_inc(mrow.sem, 1)
                for h in range(4):
                    pe.wait_ge(*pready.at(h + 1))
                    if h < 2:
                        scores(h + 2)
                    else:
                        pe.wait_ge(*hn.at(h - 1))
                    b = ps[h % 2]
                    nc.tensor.matmul(b[:, 0:129], big[:, h, 0:P], v1[:, 0, h, :], start=True, stop=True)
                    nc.tensor.matmul(b[:, 256:385], big[:, h, P:T], v1[:, 0, h, :], start=True, stop=False)
                    nc.tensor.matmul(b[:, 256:385], big[:, h, T:T + P], v1[:, 1, h, :], start=False, stop=True
                                     ).then_inc(pv.sem, 1)
                pe.wait_ge(*n3.at(1))
                for c in range(4):
                    for t in range(TT):
                        last = nc.tensor.transpose(ps[4 + c // 2][:, (c % 2) * T + t * P:(c % 2) * T + (t + 1) * P],
                                                   xs[:, t, c * P:(c + 1) * P], self.ident)
                last.then_inc(turn2.sem, 1)

            @block.scalar
            def _(act):
                link = Chain(act, self.act_chain)
                act.wait_ge(*r1.at(1))
                s_.activation(y, y, ACT.Exp).then_inc(lamy.sem, 1)
                link(s_.activation(ex, ex, ACT.Exp))
                s_.activation(ln_, ex, ACT.Ln, bias=1.0).then_inc(r3.sem, 1)
                act.wait_ge(*gates.at(2))
                for m, dst in enumerate((r, ig)):
                    for c in range(4):
                        ins = s_.activation(dst[:, c, :], ps[2 * m + c // 2][:, (c % 2) * T:(c % 2 + 1) * T],
                                            ACT.Sigmoid, bias=cols[:, m, c:c + 1])
                        if c % 2:
                            ins.then_inc(sig.sem, 1)
                act.wait_ge(*sig.at(4))
                act.wait_ge(*lamc.at(1))
                for c in range(4):
                    s_.activation(a[:, c, :], r[:, c, :], ACT.Exp, scale=negc[:, c:c + 1])
                    s_.activation(u[:, c, :], r[:, c, :], ACT.Tanh, scale=posc[:, c:c + 1]).then_inc(decays.sem, 1)
                act.wait_ge(*turned.at(1))
                link(s_.activation(aCol, ps[3][:, 0:8], ACT.Copy))
                s_.activation(em, ps[3][:, 8:16], ACT.Exp, scale=-1.0).then_inc(colsr.sem, 1)
                self.make_high(act, G + 13)
                for h in range(4):
                    act.wait_ge(*e1.at(h + 1))
                    s_.activation(big[:, h, :], big[:, h, :], ACT.Exp).then_inc(e2.sem, 1)
                act.wait_ge(*u2.at(1))
                s_.activation(u.rearrange("p c t -> p (c t)"), u.rearrange("p c t -> p (c t)"), ACT.Sqrt
                              ).then_inc(root.sem, 1)
                for h in range(4):
                    act.wait_ge(*pv.at(h + 1))
                    s_.activation(Hn[:, :, h, :], ps[h % 2][:, :].rearrange("p (t n) -> p t n", t=2)[:, :, 0:129],
                                  ACT.Copy).then_inc(hn.sem, 1)
                self.make_high(act, G + 14)
                self.make_high(act, G + 15)
                act.wait_ge(*ydone.at(1))
                s_.activation(yT[0][:, 0:4, :], r, ACT.Copy).then_inc(ydone.sem, 1)
                act.wait_ge(*n1.at(1))
                s_.activation(rt, ss, ACT.Sqrt).then_inc(n2.sem, 1)
                act.wait_ge(*turn2.at(1))
                for c in range(4):
                    s_.activation(yT[0][:, 4 + c, :], ps[4 + c // 2][:, (c % 2) * T:(c % 2 + 1) * T], ACT.Copy,
                                  scale=cols[:, 3, c:c + 1]).then_inc(yb.sem, 1)

            @block.vector
            def _(dve):
                link = Chain(dve, self.dve_chain)
                lam_ = cols[:, 2, :]
                link(v_.tensor_scalar(mx, lam_, -1.0, 0.0, ALU.mult, ALU.max))
                link(v_.tensor_scalar(s1, lam_, 0.0, None, ALU.max))
                link(v_.scalar_tensor_tensor(y, s1, -1.0, mx, ALU.mult, ALU.subtract))
                link(v_.tensor_scalar(mn, fr, 0.0, None, ALU.min))
                v_.scalar_tensor_tensor(ex, mn, 2.0, fr, ALU.mult, ALU.subtract).then_inc(r1.sem, 1)
                dve.wait_ge(*lamy.at(1))
                link(v_.tensor_scalar(s1, y, 2.0, None, ALU.add))
                link(v_.reciprocal(s1, s1))
                link(v_.tensor_tensor(s1, s1, y, ALU.mult))
                link(v_.tensor_tensor(s2, s1, s1, ALU.mult))
                link(v_.tensor_scalar(q_, s2, 1.0 / 15, None, ALU.mult))
                for o in (13, 11, 9, 7, 5, 3):
                    link(v_.scalar_tensor_tensor(q_, q_, 1.0 / o, s2, ALU.add, ALU.mult))
                link(v_.scalar_tensor_tensor(q_, q_, 1.0, s1, ALU.add, ALU.mult))
                link(v_.scalar_tensor_tensor(q_, q_, 2.0, mx, ALU.mult, ALU.add))
                link(v_.tensor_scalar(posc, q_, 8.0, None, ALU.mult))
                v_.tensor_scalar(negc, q_, -8.0, None, ALU.mult).then_inc(lamc.sem, 1)
                dve.wait_ge(*r3.at(1))
                link(v_.tensor_tensor(fr, mn, ln_, ALU.subtract))
                link(v_.tensor_tensor_scan(cumf, ones, fr, 0.0, ALU.mult, ALU.add))
                link(v_.tensor_tensor(al, ir, cumf, ALU.subtract))
                link(v_.tensor_tensor_scan(fr, al, al, NEG, ALU.max, ALU.max))
                link(v_.tensor_scalar(ex, fr, -1.0, None, ALU.mult))
                v_.tensor_tensor(mn, fr, cumf, ALU.add).then_inc(r4.sem, 1)
                dve.wait_ge(*colsr.at(1))
                dve.wait_ge(*mrow.at(1))
                for h in range(4):
                    mb = ps[4 + h // 2][:, (h % 2) * T:(h % 2 + 1) * T]
                    v_.tensor_scalar(big[:, h, 0:T], mb, aCol[:, h:h + 1], 0.0, ALU.add, ALU.min)
                    v_.tensor_scalar(big[:, h, T:], mb[:, P:T], aCol[:, 4 + h:5 + h], 0.0, ALU.add, ALU.min
                                     ).then_inc(e1.sem, 1)
                dve.wait_ge(*decays.at(4))
                link(v_.tensor_tensor(r, a, a, ALU.mult))
                v_.scalar_tensor_tensor(u.rearrange("p c t -> p (c t)"), r.rearrange("p c t -> p (c t)"), 1.0,
                                        u.rearrange("p c t -> p (c t)"), ALU.add, ALU.mult).then_inc(u2.sem, 1)
                for h in range(4):
                    dve.wait_ge(*e2.at(h + 1))
                    link(v_.tensor_tensor(big[:, h, :], big[:, h, :], mask, ALU.mult))
                    dve.wait_ge(*sdone.at(h + 1))
                    v_.tensor_tensor(big[:, h, :], big[:, h, :], ps[6 + h % 2][:, 0:384], ALU.mult
                                     ).then_inc(pready.sem, 1)
                link(v_.tensor_tensor(ig, ig, xc, ALU.mult))
                dve.wait_ge(*root.at(1))
                link(v_.tensor_tensor(u, u, ig, ALU.mult))
                for c in range(4):
                    v_.tensor_tensor_scan(r[:, c, :], a[:, c, :], u[:, c, :], 0.0, ALU.mult, ALU.add).then_inc(hs.sem, 1)
                dve.wait_ge(*hs.at(4))
                v_.tensor_tensor(r, ga, r, ALU.mult).then_inc(ydone.sem, 1)
                dve.wait_ge(*hn.at(4))
                heads = Hn.rearrange("p t h d -> p (t h) d")
                link(v_.tensor_copy(rc.unsqueeze(2), heads[:, :, 128:129]))
                link(v_.scalar_tensor_tensor(dn, rc, -1.0, rc, ALU.mult, ALU.max))
                link(v_.tensor_tensor(dn, dn, em, ALU.max))
                link(v_.reciprocal(rc, dn))
                link(v_.tensor_tensor(heads[:, :, 0:128], heads[:, :, 0:128],
                                      rc.unsqueeze(2).to_broadcast([P, 8, 128]), ALU.mult))
                sq = xs.rearrange("p t (h d) -> p (t h) d", d=128)[:, 0:8, :]
                link(v_.tensor_tensor(sq, heads[:, :, 0:128], heads[:, :, 0:128], ALU.mult))
                link(v_.tensor_reduce(ss, sq, AX.X, ALU.add))
                v_.tensor_scalar(ss, ss, 1.0 / ML_DH, EPS, ALU.mult, ALU.add).then_inc(n1.sem, 1)
                dve.wait_ge(*n2.at(1))
                link(v_.reciprocal(rt, rt))
                link(v_.tensor_tensor(heads[:, :, 0:128], heads[:, :, 0:128],
                                      rt.unsqueeze(2).to_broadcast([P, 8, 128]), ALU.mult))
                for t in range(TT):
                    ins = v_.tensor_tensor(xs[:, t, 0:512].rearrange("p (h d) -> p h d", h=4), Hn[:, t, :, 0:128],
                                           so[:, t, :].rearrange("p (h d) -> p h d", h=4), ALU.mult)
                    if t == 0:
                        link(ins)
                ins.then_inc(n3.sem, 1)
                dve.wait_ge(*ydone.at(2))
                v_.tensor_tensor(yT[1][:, 0:4, :], r, yT[0][:, 0:4, :].bitcast(F32), ALU.subtract).then_inc(ydone.sem, 1)
                dve.wait_ge(*yb.at(4))
                for c in range(4):
                    v_.scalar_tensor_tensor(yT[1][:, 4 + c, :], ps[4 + c // 2][:, (c % 2) * T:(c % 2 + 1) * T],
                                            cols[:, 3, c:c + 1], yT[0][:, 4 + c, :].bitcast(F32), ALU.mult, ALU.subtract
                                            ).then_inc(yb.sem, 1)
                dve.wait_ge(*yb.at(8))
        for s, n in ((gates, 2), (sig, 4), (lamy, 1), (lamc, 1), (decays, 4), (u2, 1), (root, 1), (hs, 4), (ydone, 3),
                     (r1, 1), (r3, 1), (r4, 1), (turned, 1), (colsr, 1), (mrow, 1), (sdone, 4), (e1, 4), (e2, 4),
                     (pready, 4), (pv, 4), (hn, 4), (n1, 1), (n2, 1), (n3, 1), (turn2, 1), (yb, 8)):
            s.base += n
        small.base += 96
        self.add_rows_product(G, 13, yT, KD, G + 17)

    def add_rows_product(self, g0, tile, actT, kn, end, scale=None):
        nc, ps = self.nc, self.psum
        done, added = self.counters("add_done", "add_added")
        with nc.Block() as block:
            @block.sync
            def _(sp):
                self.loads(sp, end)

            @block.tensor
            def _(pe):
                self.rows_product(pe, g0, tile, actT, kn, (0, 1, 2, 3), done)
                self.flush(pe, done.at(1))

            @block.scalar
            def _(act):
                for n in range(g0 + tile + SPLIT, end + SPLIT):
                    self.make_high(act, n)

            @block.gpsimd
            def _(pool):
                self.make_lows(pool, end)

            @block.vector
            def _(dve):
                dve.wait_ge(*done.at(1))
                for t in range(TT):
                    for half in range(2):
                        xv = self.x[:, t, half * 512:(half + 1) * 512]
                        if scale is None:
                            nc.vector.tensor_tensor(xv, ps[2 * t + half][:, :], xv, ALU.add).then_inc(added.sem, 1)
                dve.wait_ge(*added.at(4))
        done.base += 1
        added.base += 4

    def final_norm(self, name):
        nc = self.nc
        work = self.arena(name)
        gain = work("gain", D)
        sq = work("sq", TT * D).rearrange("p (t d) -> p t d", t=TT)
        ss = self.stat[:, 0:2]
        here, a_, b_, c_, d_ = self.counters("fn_here", "fn_sq", "fn_mean", "fn_root", "fn_x")
        with nc.Block() as block:
            @block.sync
            def _(sp):
                sp.dma_start(gain, self.dram[name].partition_broadcast(P).rearrange("p a d -> p (a d)")).then_inc(here.sem, 16)

            @block.scalar
            def _(act):
                for t in range(TT):
                    nc.scalar.activation(sq[:, t, :], self.x[:, t, :], ACT.Square, accum_out=ss[:, t:t + 1]).then_inc(a_.sem, 1)
                act.wait_ge(*b_.at(1))
                nc.scalar.activation(ss, ss, ACT.Sqrt).then_inc(c_.sem, 1)

            @block.vector
            def _(dve):
                link = Chain(dve, self.dve_chain)
                dve.wait_ge(*a_.at(2))
                nc.vector.tensor_scalar(ss, ss, 1.0 / D, EPS, ALU.mult, ALU.add).then_inc(b_.sem, 1)
                dve.wait_ge(*c_.at(1))
                link(nc.vector.reciprocal(ss, ss))
                dve.wait_ge(*here.at(16))
                for t in range(TT):
                    nc.vector.scalar_tensor_tensor(self.x[:, t, :], self.x[:, t, :], ss[:, t:t + 1], gain,
                                                   ALU.mult, ALU.mult).then_inc(d_.sem, 1)
                dve.wait_ge(*d_.at(2))
        here.base += 16
        a_.base += 2
        b_.base += 1
        c_.base += 1
        d_.base += 2

    def nsa(self):
        nc, ps, G = self.nc, self.psum, G_NSA
        v_, s_ = nc.vector, nc.scalar
        self.begin_stage()
        SC = NSA_DH ** -0.5
        work = self.arena("nsa")
        w2 = work("w2", 384).rearrange("p (k n) -> p k n", k=2)
        pe_ = work("pe", 32)
        b1 = work("b1", 4)
        gw = work("gw", 384).rearrange("p (k n) -> p k n", k=KD)
        gb = work("gb", 48)
        causal = work("causal", 384)
        cm = work("cm", 32).rearrange("p (t n) -> p t n", t=TT)
        cneg = work("cneg", 32).rearrange("p (t n) -> p t n", t=TT)
        blocks = work("blocks", 8)
        xs = work("xs", TT * D).rearrange("p (t d) -> p t d", t=TT)
        qT = work("qT", 8 * T).rearrange("p (c t) -> p c t", c=8)
        kT = [work(f"kT{i}", 2 * T).rearrange("p (c t) -> p c t", c=2) for i in range(2)]
        X = [work(f"cmpX{i}", 5 * T).rearrange("p (g t) -> p g t", g=5) for i in range(2)]
        vv = work("vv", TT * 512).rearrange("p (t n) -> p t n", t=TT)
        gates = work("gates", TT * 48).rearrange("p (t h b) -> p t h b", t=TT, b=3)
        hid = [work(f"hid{i}", 2 * 64).rearrange("p (c g n) -> p c g n", c=2, g=4) for i in range(2)]
        bcol = work("bcol", 4)
        hidR = work("hidR", 4 * P).rearrange("p (a c n) -> p a c n", a=2, c=2)
        kcT = work("kcT", 64)
        R = work("R", 128).rearrange("p (a d) -> p a d", a=2)
        Vbd = work("Vbd", 2 * 512).rearrange("p (a h d) -> p a h d", a=2, h=8)
        Sc = work("Sc", TT * 256).rearrange("p (t h n) -> p t h n", t=TT, h=16)
        cs = work("cs", 96)
        cPT = work("cPT", 512)
        SB = [work(f"SB{i}", 384) for i in range(4)]
        PT = [work(f"PT{i}", 384) for i in range(4)]
        m3 = [work(f"m3_{i}", 4) for i in range(4)]
        nm = [work(f"nm{i}", 2) for i in range(4)]
        sums = [work(f"sums{i}", 2) for i in range(4)]
        coef = [work(f"coef{i}", 2) for i in range(4)]
        gw_parts = tuple(work(f"gw{n}", 384, dt=F32R).rearrange("p (k n) -> p k n", k=KD) for n in ("high", "low"))
        (gsplit,) = self.counters("nsa_gw")
        small, done, fa, fd, z, gsum = self.counters("nsa_small", "nsa_done", "nsa_freed_act", "nsa_freed_dve",
                                                    "nsa_zero", "nsa_gates")
        norm_act, norm_dve, norm_pool, norm_pe, norm_end = self.norm_parts(
            self.x, self.xT, self.gains[:, 4, :], None, xs)
        UNITS = 23

        with nc.Block() as block:
            @block.sync
            def _(sp):
                for dst, name in ((w2.rearrange("p k n -> p (k n)"), "nsa_w2"), (pe_, "nsa_pe"), (b1, "nsa_b1"),
                                  (gw.rearrange("p k n -> p (k n)"), "nsa_gw"), (causal[:, 0:P], "nsa_causal"),
                                  (causal[:, T:], "nsa_causal"), (cm.rearrange("p t n -> p (t n)"), "nsa_cmp"),
                                  (blocks, "nsa_blocks")):
                    sp.dma_start(dst, self.dram[name]).then_inc(small.sem, 16)
                sp.dma_start(gb, self.dram["nsa_gb"].partition_broadcast(P).rearrange("p a d -> p (a d)")).then_inc(small.sem, 16)
                self.loads(sp, G + 12)

            @block.gpsimd
            def _(pool):
                g_ = nc.gpsimd
                g_.memset(causal[:, P:T], 0.0).then_inc(z.sem, 1)
                for i in range(2):
                    g_.memset(X[i][:, 4, :], 0.0).then_inc(z.sem, 1)
                    g_.memset(hid[i].rearrange("p c g n -> p (c g n)"), 0.0).then_inc(z.sem, 1)
                g_.memset(kcT, 0.0).then_inc(z.sem, 1)
                norm_pool(pool)
                self.make_lows(pool, G + 12)

            @block.tensor
            def _(pe):
                norm_pe(pe)
                for n in range(20):
                    if n >= 4:
                        pe.wait_ge(*(fd if n % 2 else fa).at((n - 4) // 2 + 1))
                    w = self.ring_tile(pe, G, n // 2)
                    self.stationary_cols(ps[n % 4][:, 0:T], w, n % 2, self.xT).then_inc(done.sem, 1)
                    if n % 2:
                        self.give_back(n // 2)
                pe.wait_ge(*fa.at(9))
                pe.wait_ge(*fd.at(9))
                self.moving_cols(pe, [ps[t][:, :] for t in range(TT)], G, 10, self.xT, done)
                pe.wait_ge(*fa.at(10))
                pe.wait_ge(*gsplit.at(2))
                for t in range(TT):
                    for k in range(KD):
                        last = self.mm(ps[2][:, t * 48:(t + 1) * 48], self.cut(self.xT, slice(None), k, slice(t * P, (t + 1) * P)),
                                       self.cut(gw_parts, slice(None), k), k == 0, k == KD - 1)
                last.then_inc(done.sem, 1)
                self.flush(pe, done.at(UNITS))

            def unit(n, copy):
                b = ps[n % 4]
                if n < 8:
                    return [copy(qT[:, n, :], b[:, 0:T])]
                if n < 12:
                    return [copy(kT[(n - 8) // 2][:, n % 2, :], b[:, 0:T])]
                if n < 20:
                    x_, g = X[(n - 12) // 4], n % 4
                    return [copy(x_[0:64, g, :], b[0:64, 0:T]), copy(x_[64:P, g, 0:T - 1], b[64:P, 1:T])]
                if n < 22:
                    return [copy(vv[:, n - 20, :], b[:, :])]

            @block.scalar
            def _(act):
                norm_act(act)
                act.wait_ge(*small.at(16 * 9))
                s_.activation(gw_parts[0], gw, ACT.Copy).then_inc(gsplit.sem, 1)
                for n in range(0, 22, 2):
                    if n:
                        self.make_high(act, G + n // 2 - 1 + SPLIT)
                    act.wait_ge(*done.at(n + 1))
                    unit(n, lambda o, i: s_.activation(o, i, ACT.Copy))[-1].then_inc(fa.sem, 1)
                act.wait_ge(*gsum.at(1))
                g2 = gates.rearrange("p t h b -> p (t h b)")
                s_.activation(g2, g2, ACT.Sigmoid).then_inc(fa.sem, 1)

            @block.vector
            def _(dve):
                norm_dve(dve)
                dve.wait_ge(*gsplit.at(1))
                v_.tensor_tensor(gw_parts[1], gw, gw_parts[0].bitcast(F32), ALU.subtract).then_inc(gsplit.sem, 1)
                for n in range(1, 22, 2):
                    dve.wait_ge(*done.at(n + 1))
                    unit(n, lambda o, i: v_.tensor_copy(o, i))[-1].then_inc(fd.sem, 1)
                dve.wait_ge(*small.at(16 * 9))
                dve.wait_ge(*done.at(23))
                v_.tensor_tensor(gates.rearrange("p t h b -> p t (h b)"),
                                 ps[2][:, 0:96].rearrange("p (t n) -> p t n", t=TT),
                                 gb.unsqueeze(1).to_broadcast([P, TT, 48]), ALU.add).then_inc(gsum.sem, 1)
                dve.wait_ge(*z.at(6))
                for i in range(2):
                    v_.tensor_copy(X[i][:, 4, 0:32].rearrange("p (j s) -> p j s", s=2)[:, :, 0],
                                   pe_[:, 16 * i:16 * i + 16]).then_inc(fd.sem, 1)
                v_.tensor_scalar(cneg, cm, -1.0, -NEG, ALU.add, ALU.mult).then_inc(fd.sem, 1)
        norm_end()
        done.base += UNITS
        fa.base += 12
        fd.base += 14
        z.base += 6
        gsum.base += 1
        gsplit.base += 2
        small.base += 16 * 9

        (hdone, hb, hready, c2, kready, repl, c4, rready, vbd, cscore, cexp, cpt, cpte, cdone, mxs, csum) = self.counters(
            "cm_hidden", "cm_bias", "cm_gelu", "cm_k2", "cm_kT", "cm_repl", "cm_R", "cm_Rs", "cm_vbd",
            "cm_scores", "cm_exp", "cm_turned", "cm_PT", "cm_out", "cm_max", "cm_scaled")
        with nc.Block() as block:
            @block.sync
            def _(sp):
                self.loads(sp, G + 13)

            @block.gpsimd
            def _(pool):
                self.make_lows(pool, G + 13)

            @block.tensor
            def _(pe):
                for i in range(2):
                    for hc in range(2):
                        for jj in range(16):
                            w = self.ring_tile(pe, G, 12 + 2 * i + jj // 8)
                            at = (jj % 8) * 256 + hc * P
                            rhs = X[i][:, :, 2 * jj:2 * jj + 225].rearrange("p g t -> p g t")[:, :, 0:225:16]
                            last = self.mm(ps[4 + i][:, 128 * hc:128 * hc + 75], w[:, at:at + P], rhs, jj == 0, jj == 15)
                            if hc and jj == 7:
                                self.give_back(12 + 2 * i)
                    last.then_inc(hdone.sem, 1)
                    self.give_back(13 + 2 * i)
                pe.wait_ge(*hready.at(1))
                for hc in range(2):
                    last = self.mm(ps[6][:, 0:64], w2[:, hc, 0:128], hid[0][:, hc, :, :].rearrange("p g n -> p (g n)"),
                                   hc == 0, hc == 1)
                last.then_inc(c2.sem, 1)
                pe.wait_ge(*repl.at(1))
                for a in range(2):
                    for hc in range(2):
                        last = self.mm(ps[7][:, a * 64:(a + 1) * 64], hidR[:, a, hc, :], w2[:, hc, 128:192], hc == 0, hc == 1)
                last.then_inc(c4.sem, 1)
                pe.wait_ge(*kready.at(1))
                for t in range(TT):
                    for g in range(4):
                        b = ps[4 + g % 2]
                        lo = 64 * (g % 2)
                        for r in range(4):
                            at = t * P + (g // 2) * 64 + r * 16
                            last = self.mm(b[:, at:at + 16], qT[lo:lo + 64, 4 * (g // 2) + r, t * P:(t + 1) * P],
                                           kcT[lo:lo + 64, g * 16:(g + 1) * 16], True, True)
                last.then_inc(cscore.sem, 1)
                pe.wait_ge(*csum.at(1))
                for t in range(TT):
                    for a in range(2):
                        n = 2 * t + a
                        last = nc.tensor.transpose(ps[6][:, n * P:(n + 1) * P],
                                                   Sc[:, t, 8 * a:8 * a + 8, :].rearrange("p h n -> p (h n)"), self.ident)
                last.then_inc(cpt.sem, 1)
                pe.wait_ge(*cpte.at(1))
                pe.wait_ge(*vbd.at(2))
                for t in range(TT):
                    for a in range(2):
                        n = 2 * t + a
                        last = self.mm(ps[n][:, :], cPT[:, n * P:(n + 1) * P], Vbd[:, a, :, :].rearrange("p h d -> p (h d)"),
                                       True, True)
                last.then_inc(cdone.sem, 1)
                self.flush(pe, cdone.at(1))

            @block.scalar
            def _(act):
                for i in range(2):
                    act.wait_ge(*hb.at(i + 1))
                    for hc in range(2):
                        ins = s_.activation(hid[i][:, hc, :, 0:N_CMP],
                                            ps[4 + i][:, 128 * hc:128 * hc + 60].rearrange("p (g n) -> p g n", g=4),
                                            ACT.Gelu_apprx_tanh, bias=bcol[:, 2 * i + hc:2 * i + hc + 1])
                    ins.then_inc(hready.sem, 1)
                act.wait_ge(*c2.at(1))
                s_.activation(kcT, ps[6][:, 0:64], ACT.Copy).then_inc(kready.sem, 1)
                act.wait_ge(*c4.at(1))
                s_.activation(R.rearrange("p a d -> p (a d)"), ps[7][:, 0:128], ACT.Copy).then_inc(rready.sem, 1)
                act.wait_ge(*mxs.at(1))
                s2 = Sc.rearrange("p t h n -> p (t h n)")
                s_.activation(s2, s2, ACT.Exp, scale=SC).then_inc(cexp.sem, 1)
                act.wait_ge(*cpt.at(1))
                s_.activation(cPT, ps[6][:, :], ACT.Copy).then_inc(cpte.sem, 1)

            @block.vector
            def _(dve):
                link = Chain(dve, self.dve_chain)
                for i in range(2):
                    dve.wait_ge(*hdone.at(i + 1))
                    v_.tensor_tensor(bcol[:, 2 * i:2 * i + 2].unsqueeze(2),
                                     ps[4 + i][:, 0:256].rearrange("p (c n) -> p c n", c=2)[:, :, 60:61],
                                     b1[:, 2 * i:2 * i + 2].unsqueeze(2), ALU.add).then_inc(hb.sem, 1)
                dve.wait_ge(*hready.at(2))
                for a in range(2):
                    for hc in range(2):
                        for g in range(2):
                            last = v_.tensor_copy(hidR[:, a, hc, g * 64:(g + 1) * 64].rearrange("p (r n) -> p r n", r=4),
                                                  hid[1][:, hc, 2 * a + g, :].unsqueeze(1).to_broadcast([P, 4, 16]))
                last.then_inc(repl.sem, 1)
                dve.wait_ge(*rready.at(1))
                for a in range(2):
                    v_.tensor_tensor(Vbd[:, a, :, :], R[:, a, :].unsqueeze(1).to_broadcast([P, 8, 64]),
                                     blocks.unsqueeze(2).to_broadcast([P, 8, 64]), ALU.mult).then_inc(vbd.sem, 1)
                dve.wait_ge(*cscore.at(1))
                mx, sm, co = cs[:, 0:32], cs[:, 32:64], cs[:, 64:96]
                for t in range(TT):
                    for b in range(2):
                        o = Sc[:, t, :, :].rearrange("p (a b r) n -> p a b r n", a=2, b=2)[:, :, b, :, :]
                        i_ = ps[4 + b][:, t * P:(t + 1) * P].rearrange("p (a r n) -> p a r n", a=2, r=4)
                        for a in range(2):
                            last = v_.tensor_tensor(o[:, a], i_[:, a], cm[:, t, :].unsqueeze(1).to_broadcast([P, 4, 16]), ALU.mult)
                link(last)
                for t in range(TT):
                    last = v_.tensor_tensor(Sc[:, t, :, :], Sc[:, t, :, :],
                                            cneg[:, t, :].unsqueeze(1).to_broadcast([P, 16, 16]), ALU.add)
                link(last)
                flat = Sc.rearrange("p t h n -> p (t h) n")
                link(v_.tensor_reduce(mx, flat, AX.X, ALU.max))
                v_.tensor_tensor(flat, flat, mx.unsqueeze(2).to_broadcast([P, 32, 16]), ALU.subtract).then_inc(mxs.sem, 1)
                dve.wait_ge(*cexp.at(1))
                link(v_.tensor_reduce(sm, flat, AX.X, ALU.add))
                link(v_.reciprocal(sm, sm))
                link(v_.tensor_tensor(co.rearrange("p (t h) -> p t h", t=TT), sm.rearrange("p (t h) -> p t h", t=TT),
                                      gates[:, :, :, 0], ALU.mult))
                for t in range(TT):
                    last = v_.tensor_tensor(Sc[:, t, :, :], Sc[:, t, :, :],
                                            cm[:, t, :].unsqueeze(1).to_broadcast([P, 16, 16]), ALU.mult)
                link(last)
                v_.tensor_tensor(flat, flat, co.unsqueeze(2).to_broadcast([P, 32, 16]), ALU.mult).then_inc(csum.sem, 1)
        for s, n in ((hdone, 2), (hb, 2), (hready, 2), (c2, 1), (kready, 1), (repl, 1), (c4, 1), (rready, 1), (vbd, 2),
                     (cscore, 1), (cexp, 1), (cpt, 1), (cpte, 1), (cdone, 1), (mxs, 1), (csum, 1)):
            s.base += n

        units = [(c, br, b) for c in range(8) for br in range(2) for b in range(2)]
        NU = len(units)
        TURN_LAG, PT_LAG = 3, 2
        head = lambda c, b: 4 * (2 * (c // 4) + b) + c % 4
        sco, sadd, smax, sexp, scoef, sscale, stn, spt, spv, ofin = self.counters(
            "at_scores", "at_masked", "at_max", "at_exp", "at_coef", "at_scaled", "at_turned", "at_PT", "at_pv", "at_o")
        oT_done, oT_high, oT_ev = self.counters("at_oT", "at_oThigh", "at_oTlow")
        with nc.Block() as block:
            @block.sync
            def _(sp):
                self.loads(sp, G + 16)

            @block.tensor
            def _(pe):
                def scores(n):
                    c, br, b = units[n]
                    if n >= 2:
                        pe.wait_ge(*sadd.at(n - 1))
                    lo = 64 * b
                    q, k, o = qT[lo:lo + 64, c, :], kT[br][lo:lo + 64, c // 4, :], ps[4 + b]
                    nc.tensor.matmul(o[:, 0:P], q[:, 0:P], k[:, 0:P], start=True, stop=True)
                    nc.tensor.matmul(o[:, P:384], q[:, P:T], k, start=True, stop=True).then_inc(sco.sem, 1)

                def turn(n):
                    b = units[n][2]
                    pe.wait_ge(*sscale.at(n + 1))
                    if n >= 2:
                        pe.wait_ge(*spt.at(n - 1))
                    for j in range(3):
                        last = nc.tensor.transpose(ps[6 + b][:, j * P:(j + 1) * P], SB[n % 4][:, j * P:(j + 1) * P], self.ident)
                    last.then_inc(stn.sem, 1)

                def values(n):
                    c, br, b = units[n]
                    h = head(c, b)
                    g, a, at = h // 4, h // 8, (h % 8) * 64
                    pe.wait_ge(*spt.at(n + 1))
                    col = br * 256 + g * 64
                    w = PT[n % 4]
                    nc.tensor.matmul(ps[a][:, at:at + 64], w[:, 0:P], vv[:, 0, col:col + 64], start=False, stop=True,
                                     skip_group_check=True)
                    nc.tensor.matmul(ps[2 + a][:, at:at + 64], w[:, P:T], vv[:, 0, col:col + 64], start=False, stop=True,
                                     skip_group_check=True)
                    nc.tensor.matmul(ps[2 + a][:, at:at + 64], w[:, T:384], vv[:, 1, col:col + 64], start=False, stop=True,
                                     skip_group_check=True).then_inc(spv.sem, 1)

                for n in range(NU + TURN_LAG + 1):
                    if n < NU:
                        scores(n)
                    if TURN_LAG <= n < NU + TURN_LAG:
                        turn(n - TURN_LAG)
                    if n > TURN_LAG:
                        values(n - TURN_LAG - 1)
                pe.wait_ge(*ofin.at(4))
                for k in range(KD):
                    for t in range(TT):
                        last = nc.tensor.transpose(ps[4 + k // 2][:, (k % 2) * T + t * P:(k % 2) * T + (t + 1) * P],
                                                   xs[:, t, k * P:(k + 1) * P], self.ident)
                    if k % 2:
                        last.then_inc(oT_done.sem, 1)

            @block.scalar
            def _(act):
                def pt(n):
                    act.wait_ge(*stn.at(n + 1))
                    if n >= 4:
                        act.wait_ge(*spv.at(n - 3))
                    s_.activation(PT[n % 4], ps[6 + units[n][2]][:, 0:384], ACT.Copy).then_inc(spt.sem, 1)

                for n in range(NU + PT_LAG):
                    if n in (6, 14, 22):
                        self.make_high(act, G + 16 + n // 8)
                    if n < NU:
                        act.wait_ge(*smax.at(n + 1))
                        if n >= 4:
                            act.wait_ge(*scoef.at(n - 3))
                        for t in range(TT):
                            w = SB[n % 4][:, t * P:(2 * t + 1) * P + t * 0] if t == 0 else SB[n % 4][:, P:384]
                            s_.activation(w, w, ACT.Exp, scale=SC, bias=nm[n % 4][:, t:t + 1],
                                          accum_out=sums[n % 4][:, t:t + 1]).then_inc(sexp.sem, 1)
                    if n >= PT_LAG:
                        pt(n - PT_LAG)
                self.highs_from_psum(act, 4, self.xT, oT_done, oT_high)

            @block.vector
            def _(dve):
                link = Chain(dve, self.dve_chain)

                def coefs(n):
                    c, br, b = units[n]
                    dve.wait_ge(*sexp.at(2 * n + 2))
                    if n >= 4:
                        dve.wait_ge(*sscale.at(n - 3))
                    link(v_.reciprocal(coef[n % 4], sums[n % 4]))
                    v_.tensor_tensor(coef[n % 4], coef[n % 4], gates[:, :, head(c, b), 1 + br], ALU.mult).then_inc(scoef.sem, 1)

                for n in range(NU + 1):
                    if n < NU:
                        dve.wait_ge(*sco.at(n + 1))
                        if n >= 4:
                            dve.wait_ge(*stn.at(n - 3))
                            dve.wait_ge(*sexp.at(2 * n - 6))
                        v_.tensor_tensor(SB[n % 4], ps[4 + units[n][2]][:, 0:384], causal, ALU.add).then_inc(sadd.sem, 1)
                        dve.wait_ge(*sadd.at(n + 1))
                        link(v_.tensor_reduce(m3[n % 4][:, 0:3], SB[n % 4].rearrange("p (j k) -> p j k", j=3), AX.X, ALU.max))
                        link(v_.tensor_tensor(m3[n % 4][:, 1:2], m3[n % 4][:, 1:2], m3[n % 4][:, 2:3], ALU.max))
                        v_.tensor_scalar(nm[n % 4], m3[n % 4][:, 0:2], -SC, None, ALU.mult).then_inc(smax.sem, 1)
                    if n >= 1:
                        coefs(n - 1)
                dve.wait_ge(*spv.at(NU))
                for t in range(TT):
                    for a in range(2):
                        v_.tensor_copy(xs[:, t, a * 512:(a + 1) * 512], ps[2 * t + a][:, :]).then_inc(ofin.sem, 1)
                self.lows_from_psum(dve, 4, self.xT, oT_high, oT_ev)
                dve.wait_ge(*oT_ev.at(8))

            @block.gpsimd
            def _(pool):
                for n in range(NU):
                    if n in (8, 16, 24):
                        self.make_lows(pool, G + 13 + n // 8)
                    pool.wait_ge(*scoef.at(n + 1))
                    nc.gpsimd.tensor_scalar(SB[n % 4][:, 0:P], SB[n % 4][:, 0:P], coef[n % 4][:, 0:1], 1.0, ALU.mult, ALU.mult)
                    nc.gpsimd.tensor_scalar(SB[n % 4][:, P:384], SB[n % 4][:, P:384], coef[n % 4][:, 1:2], 1.0,
                                            ALU.mult, ALU.mult).then_inc(sscale.sem, 1)
        for s, n in ((sco, NU), (sadd, NU), (smax, NU), (sexp, 2 * NU), (scoef, NU), (sscale, NU), (stn, NU), (spt, NU),
                     (spv, NU), (ofin, 4), (oT_done, 4), (oT_high, 8), (oT_ev, 8)):
            s.base += n
        self.add_rows_product(G, 16, self.xT, KD, G + 20)

    def softplus_tail(self, link, y, mx, s1, s2, q_):
        v_ = self.nc.vector
        link(v_.tensor_scalar(s1, y, 2.0, None, ALU.add))
        link(v_.reciprocal(s1, s1))
        link(v_.tensor_tensor(s1, s1, y, ALU.mult))
        link(v_.tensor_tensor(s2, s1, s1, ALU.mult))
        link(v_.tensor_scalar(q_, s2, 1.0 / 15, None, ALU.mult))
        for o in (13, 11, 9, 7, 5, 3):
            link(v_.scalar_tensor_tensor(q_, q_, 1.0 / o, s2, ALU.add, ALU.mult))
        link(v_.scalar_tensor_tensor(q_, q_, 1.0, s1, ALU.add, ALU.mult))
        link(v_.scalar_tensor_tensor(q_, q_, 2.0, mx, ALU.mult, ALU.add))

    def gate_row(self, part, banks):
        for k in range(KD):
            last = self.nc.tensor.matmul(self.psum[banks[k // 4]][:, (k % 4) * P:(k % 4 + 1) * P],
                                         self.modT[:, 8 * part + k, 0:1].to_broadcast([P, P]), self.ident,
                                         start=True, stop=True)
        return last

    def second(self):
        nc, ps, G = self.nc, self.psum, G_SECOND
        v_, s_ = nc.vector, nc.scalar
        self.begin_stage()
        KS = RET_DK ** -0.5
        work = self.arena("mix2")
        hcT = tuple(work(f"hcT{n}", 2048, dt=F32R).rearrange("p (k t) -> p k t", k=KD) for n in ("high", "low"))
        qkn = work("qkn", TT * 1024).rearrange("p (t n) -> p t n", t=TT)
        vn = work("vn", TT * 1024).rearrange("p (t n) -> p t n", t=TT)
        gn = work("gn", TT * 1024).rearrange("p (t n) -> p t n", t=TT)
        early = Arena(nc, "mix2early", work.at, self.keep)
        ctx_in, xs, xs_ctx = (early(n, TT * D).rearrange("p (t d) -> p t d", t=TT) for n in ("ctx", "xs", "xs_ctx"))
        gp = work("gp", TT * 1024).rearrange("p (t n) -> p t n", t=TT)
        gr = work("gr", TT * 1024).rearrange("p (t n) -> p t n", t=TT)
        vc = work("vc", TT * 1024).rearrange("p (t n) -> p t n", t=TT)
        kc = work("kc", TT * 512).rearrange("p (t n) -> p t n", t=TT)
        pn = work("pn", TT * 512).rearrange("p (t n) -> p t n", t=TT)
        late = Arena(nc, "mix2late", self.base + RAW * TILE * 4, self.ring_end)
        R0, R1, R2, Rh = (late(f"R{i}", 2048) for i in range(4))
        cond = work("cond", 16).rearrange("p (k s) -> p k s", s=2)
        adab = work("adab", 48)
        rope = work("rope", 256).rearrange("p (s t n) -> p s t n", s=2, t=TT)
        pscale = work("pscale", 4)
        rnorm = work("rnorm", 8)
        rcol = work("rcol", 4).rearrange("p (t s) -> p t s", s=2)
        lg = work("lg", 8)
        tiny = work("tiny", 5 * 8)
        adarow = [work(f"adarow{i}", 512, parts=2) for i in range(2)]
        rowed, turned = self.counters("s2_rowed", "s2_turned")
        wfb = work("wfb", 16).rearrange("p (s h t) -> p s h t", s=2, h=4)
        small, silu, ada, mods, sfirst, slast = self.counters("s2_small", "s2_silu", "s2_ada", "s2_mods", "s2_lgy", "s2_lg")

        with nc.Block() as block:
            @block.sync
            def _(sp):
                for dst, name in ((cond.rearrange("p k s -> p (k s)"), "cond"), (adab, "ada_b"),
                                  (rope.rearrange("p s t n -> p (s t n)"), "rope"), (pscale, "pool_scale"),
                                  (rnorm, "ret_norm"), (rcol.rearrange("p t s -> p (t s)"), "ret_col")):
                    sp.dma_start(dst, self.dram[name]).then_inc(small.sem, 16)
                sp.dma_start(lg, self.dram["decay"].partition_broadcast(P).rearrange("p a d -> p (a d)")).then_inc(small.sem, 16)
                sp.dma_start(ctx_in, self.dram["ctx"].rearrange("(t p) d -> p t d", p=P)).then_inc(small.sem, 16)
                self.loads(sp, G + 24, end=G + 30)

            @block.gpsimd
            def _(pool):
                self.make_lows(pool, G + 22)

            @block.scalar
            def _(act):
                act.wait_ge(*small.at(16 * 8))
                c2 = cond.rearrange("p k s -> p (k s)")
                s_.activation(c2, c2, ACT.Silu).then_inc(silu.sem, 1)
                act.wait_ge(*sfirst.at(1))
                s_.activation(tiny[:, 0:8], tiny[:, 0:8], ACT.Exp).then_inc(slast.sem, 1)
                for j in range(12):
                    act.wait_ge(*ada.at(j + 1))
                    if j >= 2:
                        act.wait_ge(*turned.at(j - 1))
                    s_.activation(adarow[j % 2], ps[j % 2][0:2, :], ACT.Copy).then_inc(rowed.sem, 1)
                    if j == 10:
                        self.make_high(act, G + 24)
                        self.make_high(act, G + 25)
                self.make_high(act, G + 26)

            @block.tensor
            def _(pe):
                pe.wait_ge(*silu.at(1))
                def columns(j):
                    pe.wait_ge(*rowed.at(j + 1))
                    for c in range(4):
                        last = nc.tensor.transpose(ps[4][:, 8 * j + 2 * c:8 * j + 2 * c + 2],
                                                   adarow[j % 2][:, c * P:(c + 1) * P], self.ident[0:2, 0:2])
                    return last.then_inc(turned.sem, 1)

                for j in range(12):
                    if j >= 2:
                        pe.wait_ge(*rowed.at(j - 1))
                    for k in range(KD):
                        w = self.ring_tile(pe, G, 2 * j + k // 4)[:, (k % 4) * 512:(k % 4 + 1) * 512]
                        last = self.mm(ps[j % 2][0:2, :], cond[:, k, :], w, k == 0, k == KD - 1)
                        if k == 3:
                            self.give_back(2 * j)
                    last.then_inc(ada.sem, 1)
                    self.give_back(2 * j + 1)
                    if j:
                        columns(j - 1)
                self.flush(pe, ada.at(12))
                columns(11)

            @block.vector
            def _(dve):
                link = Chain(dve, self.dve_chain)
                dve.wait_ge(*small.at(16 * 8))
                y, mx, s1, s2, q_ = (tiny[:, 8 * i:8 * i + 8] for i in range(5))
                link(v_.tensor_scalar(mx, lg, -1.0, 0.0, ALU.mult, ALU.max))
                link(v_.tensor_scalar(s1, lg, 0.0, None, ALU.max))
                v_.scalar_tensor_tensor(y, s1, -1.0, mx, ALU.mult, ALU.subtract).then_inc(sfirst.sem, 1)
                dve.wait_ge(*slast.at(1))
                self.softplus_tail(link, y, mx, s1, s2, q_)
                link(v_.tensor_scalar(lg, q_, -1.0, None, ALU.mult))
                dve.wait_ge(*turned.at(12))
                link(v_.tensor_tensor(self.modT, ps[4][:, 0:96].rearrange("p (c s) -> p c s", s=2),
                                      adab.unsqueeze(2).to_broadcast([P, 48, 2]), ALU.add))
                for n, (part, s, g) in enumerate(((1, 0, 6), (1, 1, 6), (4, 0, 7))):
                    v_.scalar_tensor_tensor(self.gA[:, n, :], self.modT[:, 8 * part:8 * part + 8, s], 1.0,
                                            self.gains[:, g, :], ALU.add, ALU.mult).then_inc(mods.sem, 1)
        for s, n in ((silu, 1), (ada, 12), (rowed, 12), (turned, 12), (mods, 3), (sfirst, 1), (slast, 1), (small, 16 * 8)):
            s.base += n

        nact, ndve, npool, npe, nend = self.norm_parts(self.x, self.xT, self.gA[:, 0, :], self.modT[:, 0:8, 0], xs)
        cact, cdve, cpool, cpe, cend = self.norm_parts(ctx_in, hcT, self.gA[:, 1, :], self.modT[:, 0:8, 1], xs_ctx,
                                                      4, "ctx")
        units = [(b, c, t) for b in range(11) for c in ((0, 1) if b in (2, 3, 4) else (0,)) for t in range(TT)]
        NU = len(units)
        done, freed = self.counters("s2_done", "s2_freed")
        with nc.Block() as block:
            @block.sync
            def _(sp):
                self.loads(sp, G + 46)

            @block.gpsimd
            def _(pool):
                npool(pool)
                self.make_lows(pool, G + 24)
                cpool(pool)
                self.make_lows(pool, G + 46)

            @block.tensor
            def _(pe):
                npe(pe)
                pairs = units[::2]
                for n, (b, c, _) in enumerate(pairs):
                    if n == 1:
                        cpe(pe, 0)
                    if c and not pairs[n - 1][1]:
                        pe.wait_ge(*self.counter("ctx_low").at(KD))
                    if n >= 2:
                        pe.wait_ge(*freed.at(2 * n - 2))
                    self.moving_cols(pe, [ps[(2 * n + t) % 4][:, :] for t in range(TT)], G, 24 + 2 * b, hcT if c else self.xT,
                                     done, n + 1 == len(pairs) or pairs[n + 1][0] != b)
                self.flush(pe, done.at(NU))

            @block.scalar
            def _(act):
                nact(act)
                cact(act, columns=False)
                for n, (b, c, t) in enumerate(units):
                    if t == 0:
                        if n and units[n - 1][0] != b:
                            self.make_high(act, G + 23 + 2 * b + SPLIT)
                        if n + 2 >= NU or units[n + 2][0] != b:
                            self.make_high(act, G + 24 + 2 * b + SPLIT)
                    if n == 2:
                        cact(act, rows=False)
                    act.wait_ge(*done.at(n + 1))
                    src, half = ps[n % 4][:, :], slice(((b + 1) % 2) * 512, ((b + 1) % 2) * 512 + 512)
                    if b == 0:
                        ins = s_.activation(pn[:, t, :], src, ACT.Copy)
                    elif b == 1:
                        ins = s_.activation(qkn[:, t, 0:512], src, ACT.Copy)
                    elif b == 2:
                        ins = s_.activation(kc[:, t, :] if c else qkn[:, t, 512:], src, ACT.Copy, scale=KS)
                    elif b < 5:
                        ins = s_.activation((vc if c else vn)[:, t, half], src, ACT.Copy)
                    elif b < 7:
                        ins = s_.activation(gn[:, t, half], src, ACT.Silu)
                    elif b < 9:
                        ins = s_.activation(gp[:, t, half], src, ACT.Sigmoid)
                    else:
                        ins = s_.activation(gr[:, t, half], src, ACT.Sigmoid)
                    ins.then_inc(freed.sem, 1)

            @block.vector
            def _(dve):
                ndve(dve)
                cdve(dve)
        nend()
        cend()
        done.base += NU
        freed.base += NU

        band = R0.rearrange("p (g s t) -> p g s t", g=4, s=TT)
        dT, mT = R1[:, 0:1024].rearrange("p (g t) -> p g t", g=4), R1[:, 1024:2048].rearrange("p (g t) -> p g t", g=4)
        here, p1, p2, p3, p4, p5 = self.counters("pl_here", "pl_d", "pl_ds", "pl_m", "pl_ms", "pl_out")
        qk5 = qkn.rearrange("p t (h s n) -> p t h s n", h=8, s=2)
        ra = R2[:, 0:512].rearrange("p (h n) -> p h n", h=8)
        rb = R2[:, 512:1024].rearrange("p (h n) -> p h n", h=8)
        rc_ = R2[:, 1024:1536].rearrange("p (h n) -> p h n", h=8)
        rd_ = R2[:, 1536:2048].rearrange("p (h n) -> p h n", h=8)
        with nc.Block() as block:
            @block.sync
            def _(sp):
                sp.dma_start(R0, self.dram["band"]).then_inc(here.sem, 16)
                self.loads(sp, G + 49)

            @block.gpsimd
            def _(pool):
                self.make_lows(pool, G + 49)

            @block.tensor
            def _(pe):
                pe.wait_ge(*here.at(16))
                for g in range(4):
                    for s in range(TT):
                        last = self.mm(ps[g // 2][:, (g % 2) * T:(g % 2 + 1) * T], pn[:, s, g * P:(g + 1) * P],
                                       band[:, g, s, :], s == 0, s == 1)
                last.then_inc(p1.sem, 1)
                w = self.ring_tile(pe, G, 46)
                pe.wait_ge(*p2.at(1))
                for g in range(4):
                    last = self.mm(ps[2 + g // 2][:, (g % 2) * T:(g % 2 + 1) * T], w[:, g * P:(g + 1) * P], dT[:, g, :], True, True)
                last.then_inc(p3.sem, 1)
                self.give_back(46)
                pe.wait_ge(*p4.at(4))
                self.rows_product(pe, G, 47, mT, 4, (4, 5, 6, 7), p5)
                self.flush(pe, p5.at(1))

            @block.scalar
            def _(act):
                act.wait_ge(*p1.at(1))
                for b in range(2):
                    ins = s_.activation(dT[:, 2 * b:2 * b + 2, :], ps[b][:, :].rearrange("p (g t) -> p g t", g=2), ACT.Copy)
                ins.then_inc(p2.sem, 1)
                act.wait_ge(*p3.at(1))
                for g in range(4):
                    s_.activation(mT[:, g, :], ps[2 + g // 2][:, (g % 2) * T:(g % 2 + 1) * T], ACT.Copy,
                                  scale=pscale[:, g:g + 1]).then_inc(p4.sem, 1)

            @block.vector
            def _(dve):
                link = Chain(dve, self.dve_chain)
                for t in range(TT):
                    cos, sin = (rope[:, s, t, :].unsqueeze(1).to_broadcast([P, 8, 64]) for s in range(2))
                    lo, hi = qk5[:, t, :, 0, :], qk5[:, t, :, 1, :]
                    v_.tensor_tensor(ra, lo, cos, ALU.mult)
                    v_.tensor_tensor(rb, hi, sin, ALU.mult)
                    v_.tensor_tensor(rc_, lo, sin, ALU.mult)
                    link(v_.tensor_tensor(rd_, hi, cos, ALU.mult))
                    v_.tensor_tensor(lo, ra, rb, ALU.subtract)
                    link(v_.tensor_tensor(hi, rc_, rd_, ALU.add))
                dve.wait_ge(*p5.at(1))
                for t in range(TT):
                    for half in range(2):
                        o = gp[:, t, half * 512:(half + 1) * 512]
                        link(v_.tensor_tensor(o, o, ps[4 + 2 * t + half][:, :], ALU.mult))
        for s, n in ((here, 16), (p1, 1), (p2, 1), (p3, 1), (p4, 4), (p5, 1)):
            s.base += n

        qkT = Rh.rearrange("p (h t) -> p h t", h=8)
        kcw = R0.rearrange("p (s h t n) -> p s h t n", s=2, h=4, t=TT)
        S = R1.rearrange("p (s h e) -> p s h e", s=2, h=4)
        Dm = R2.rearrange("p (h m n) -> p h m n", h=4, m=TT)
        c1, c2_, c3_, c4_, c5_, c6_ = self.counters("cx_w", "cx_kw", "cx_S", "cx_Ss", "cx_turned", "cx_qk")
        with nc.Block() as block:
            block.sync(lambda sp: self.loads(sp, G + 49))
            block.gpsimd(lambda pool: self.make_lows(pool, G + 49))

            @block.scalar
            def _(act):
                for s in range(2):
                    for h in range(4):
                        s_.activation(wfb[:, s, h, :], rcol[:, :, s], ACT.Exp, scale=lg[:, 4 * s + h:4 * s + h + 1]
                                      ).then_inc(c1.sem, 1)
                for n in range(2):
                    act.wait_ge(*c5_.at(n + 1))
                    for b in range(2):
                        s_.activation(qkT[:, 4 * n + 2 * b:4 * n + 2 * b + 2, :],
                                      ps[4 + 2 * n + b][:, :].rearrange("p (h t) -> p h t", h=2), ACT.Copy).then_inc(c6_.sem, 1)
                act.wait_ge(*c3_.at(1))
                for b in range(4):
                    s_.activation(S[:, b // 2, 2 * (b % 2):2 * (b % 2) + 2, :], ps[b][:, :].rearrange("p (h e) -> p h e", h=2),
                                  ACT.Copy).then_inc(c4_.sem, 1)

            @block.vector
            def _(dve):
                dve.wait_ge(*c1.at(8))
                for s in range(2):
                    for h in range(4):
                        for t in range(TT):
                            v_.tensor_scalar(kcw[:, s, h, t, :], kc[:, t, h * P:(h + 1) * P], wfb[:, s, h, t:t + 1], None,
                                             ALU.mult).then_inc(c2_.sem, 1)

            @block.tensor
            def _(pe):
                for n in range(2):
                    for h in range(4):
                        for t in range(TT):
                            last = nc.tensor.transpose(ps[4 + 2 * n + h // 2][:, (h % 2) * T + t * P:(h % 2) * T + (t + 1) * P],
                                                       qkn[:, t, n * 512 + h * P:n * 512 + (h + 1) * P], self.ident)
                    last.then_inc(c5_.sem, 1)
                for s in range(2):
                    for h in range(4):
                        pe.wait_ge(*c2_.at(8 * s + 2 * h + 2))
                        for t in range(TT):
                            last = nc.tensor.matmul(ps[2 * s + h // 2][:, (h % 2) * T:(h % 2 + 1) * T], kcw[:, s, h, t, :],
                                                    vc[:, t, h * 256:(h + 1) * 256], start=t == 0, stop=t == 1)
                last.then_inc(c3_.sem, 1)
        for s, n in ((c1, 8), (c2_, 16), (c3_, 1), (c4_, 4), (c5_, 2), (c6_, 4)):
            s.base += n

        rel = kc.rearrange("p t n -> p (t n)").rearrange("p (s n) -> p s n", s=2)
        qd = qkn.rearrange("p t n -> p (t n)").rearrange("p (s h t) -> p s h t", s=2, h=4)
        PTb = pn.rearrange("p t n -> p (t n)").rearrange("p (b m n) -> p b m n", b=2, m=TT)
        yv = vc.rearrange("p t (h e) -> p t h e", h=4)
        rows_ = R0[:, 0:512].rearrange("p (s t) -> p s t", s=2)
        bn = R0[:, 512:512 + 48].rearrange("p (n s) -> p n s", n=8)
        mv = R0[:, 576:592].rearrange("p (n s) -> p n s", n=8)
        d1, d2, d3, d4, sc_, pt_, y_, ye, v1_, v2_, tn, te = self.counters(
            "rt_exp", "rt_D", "rt_dec", "rt_qd", "rt_scores", "rt_P", "rt_y", "rt_ys", "rt_var", "rt_root", "rt_turned", "rt_rT")
        here2, yn = self.counters("rt_here", "rt_yn")
        rT = self.xw
        with nc.Block() as block:
            @block.sync
            def _(sp):
                sp.dma_start(rel.rearrange("p s n -> p (s n)"), self.dram["ret"][:, 0:1024]).then_inc(here2.sem, 16)
                sp.dma_start(R0[:, 0:512], self.dram["ret_row"]).then_inc(here2.sem, 16)
                self.loads(sp, G + 49)

            @block.gpsimd
            def _(pool):
                self.make_lows(pool, G + 49)

            @block.scalar
            def _(act):
                act.wait_ge(*here2.at(32))
                for s in range(2):
                    for h in range(4):
                        s_.activation(qd[:, s, h, :], rows_[:, s, :], ACT.Exp, scale=lg[:, 4 * s + h:4 * s + h + 1]).then_inc(d3.sem, 1)
                for h in range(4):
                    act.wait_ge(*d1.at(h + 1))
                    o = Dm[:, h, :, :].rearrange("p m n -> p (m n)")
                    s_.activation(o, o, ACT.Exp).then_inc(d2.sem, 1)
                for h in range(4):
                    act.wait_ge(*y_.at(h + 1))
                    s_.activation(yv[:, :, h, :], ps[2 + h % 2][:, :].rearrange("p (t e) -> p t e", t=TT), ACT.Copy).then_inc(ye.sem, 1)
                act.wait_ge(*v1_.at(1))
                s_.activation(mv[:, :, 1], mv[:, :, 1], ACT.Sqrt).then_inc(v2_.sem, 1)
                for k in (2, 3, 6, 7):
                    act.wait_ge(*tn.at(k // 2 + 1))
                    s_.activation(rT[:, k, :], ps[4 + k // 2][:, (k % 2) * T:(k % 2 + 1) * T], ACT.Copy,
                                  scale=rnorm[:, k:k + 1]).then_inc(te.sem, 1)

            @block.vector
            def _(dve):
                link = Chain(dve, self.dve_chain)
                dve.wait_ge(*here2.at(32))
                for h in range(4):
                    o = Dm[:, h, :, :].rearrange("p m n -> p (m n)")
                    link(v_.tensor_scalar(o, rel[:, 0, :], lg[:, h:h + 1], None, ALU.mult))
                    v_.scalar_tensor_tensor(o, rel[:, 1, :], lg[:, 4 + h:5 + h], o, ALU.mult, ALU.add).then_inc(d1.sem, 1)
                dve.wait_ge(*d3.at(8))
                for s in range(2):
                    v_.tensor_tensor(qd[:, s, :, :], qd[:, s, :, :], qkT[:, 0:4, :], ALU.mult).then_inc(d4.sem, 1)
                for h in range(4):
                    dve.wait_ge(*sc_.at(h + 1))
                    dve.wait_ge(*d2.at(h + 1))
                    if h >= 2:
                        dve.wait_ge(*y_.at(h - 1))
                    v_.tensor_tensor(PTb[:, h % 2, :, :], ps[h % 2][:, :].rearrange("p (m n) -> p m n", m=TT), Dm[:, h, :, :],
                                     ALU.mult).then_inc(pt_.sem, 1)
                for h in range(4):
                    dve.wait_ge(*ye.at(h + 1))
                    for t in range(TT):
                        link(v_.bn_stats(bn[:, 4 * t + h, :], yv[:, t, h, :]))
                        link(v_.bn_aggr(mv[:, 4 * t + h, :], bn[:, 4 * t + h, :]))
                v_.tensor_scalar(mv[:, :, 1], mv[:, :, 1], EPS, None, ALU.add).then_inc(v1_.sem, 1)
                dve.wait_ge(*v2_.at(1))
                link(v_.reciprocal(mv[:, :, 1], mv[:, :, 1]))
                for t in range(TT):
                    for h in range(4):
                        n = 4 * t + h
                        last = v_.tensor_scalar(yv[:, t, h, :], yv[:, t, h, :], mv[:, n, 0:1], mv[:, n, 1:2], ALU.subtract, ALU.mult)
                link(last)
                for t in range(TT):
                    v_.tensor_tensor(vc[:, t, :], vc[:, t, :], gn[:, t, :], ALU.mult).then_inc(yn.sem, 1)
                for k in (0, 1, 4, 5):
                    dve.wait_ge(*tn.at(k // 2 + 1))
                    v_.tensor_scalar(rT[:, k, :], ps[4 + k // 2][:, (k % 2) * T:(k % 2 + 1) * T], rnorm[:, k:k + 1], None,
                                     ALU.mult).then_inc(te.sem, 1)

            @block.tensor
            def _(pe):
                def scores(h):
                    for m in range(TT):
                        last = nc.tensor.matmul(ps[h % 2][:, m * T:(m + 1) * T], qkT[:, 4 + h, m * P:(m + 1) * P], qkT[:, h, :],
                                                start=True, stop=True)
                    last.then_inc(sc_.sem, 1)
                scores(0)
                scores(1)
                pe.wait_ge(*d4.at(2))
                for h in range(4):
                    pe.wait_ge(*pt_.at(h + 1))
                    if h < 2:
                        scores(h + 2)
                    else:
                        pe.wait_ge(*ye.at(h - 1))
                    for t in range(TT):
                        o = ps[2 + h % 2][:, t * T:(t + 1) * T]
                        for m in range(TT):
                            nc.tensor.matmul(o, PTb[:, h % 2, m, t * P:(t + 1) * P], vn[:, m, h * 256:(h + 1) * 256],
                                             start=m == 0, stop=False)
                        for s in range(2):
                            last = nc.tensor.matmul(o, qd[:, s, h, t * P:(t + 1) * P], S[:, s, h, :], start=False, stop=s == 1)
                    last.then_inc(y_.sem, 1)
                pe.wait_ge(*yn.at(2))
                for k in range(KD):
                    for t in range(TT):
                        last = nc.tensor.transpose(ps[4 + k // 2][:, (k % 2) * T + t * P:(k % 2) * T + (t + 1) * P],
                                                   vc[:, t, k * P:(k + 1) * P], self.ident)
                    if k % 2:
                        last.then_inc(tn.sem, 1)
        for s, n in ((d1, 4), (d2, 4), (d3, 8), (d4, 2), (sc_, 4), (pt_, 4), (y_, 4), (ye, 4), (v1_, 1), (v2_, 1), (tn, 4),
                     (te, 8), (here2, 32), (yn, 2)):
            s.base += n

        o1, o2, o3, o4, o5, o6, o7 = self.counters("mo_ret", "mo_merged", "mo_turned", "mo_mT", "mo_g1", "mo_g1s", "mo_out")
        g1 = R0[:, 0:1024]
        mgT = Rh.rearrange("p (k t) -> p k t", k=KD)
        with nc.Block() as block:
            block.sync(lambda sp: self.loads(sp, G + 57))
            block.gpsimd(lambda pool: self.make_lows(pool, G + 57))

            @block.tensor
            def _(pe):
                self.gate_row(2, (4, 5)).then_inc(o5.sem, 1)
                self.rows_product(pe, G, 49, rT, KD, (0, 1, 2, 3), o1)
                pe.wait_ge(*o2.at(4))
                pe.wait_ge(*o6.at(2))
                for k in range(KD):
                    for t in range(TT):
                        last = nc.tensor.transpose(ps[4 + k // 2][:, (k % 2) * T + t * P:(k % 2) * T + (t + 1) * P],
                                                   gp[:, t, k * P:(k + 1) * P], self.ident)
                    if k % 2:
                        last.then_inc(o3.sem, 1)
                pe.wait_ge(*o4.at(8))
                self.rows_product(pe, G, 53, mgT, KD, (0, 1, 2, 3), o7)
                self.flush(pe, o7.at(1))

            @block.scalar
            def _(act):
                act.wait_ge(*o5.at(1))
                for b in range(2):
                    s_.activation(g1[:, b * 512:(b + 1) * 512], ps[4 + b][:, :], ACT.Copy).then_inc(o6.sem, 1)
                for k in (2, 3, 6, 7):
                    act.wait_ge(*o3.at(k // 2 + 1))
                    s_.activation(mgT[:, k, :], ps[4 + k // 2][:, (k % 2) * T:(k % 2 + 1) * T], ACT.Copy).then_inc(o4.sem, 1)

            @block.vector
            def _(dve):
                link = Chain(dve, self.dve_chain)
                dve.wait_ge(*o1.at(1))
                for t in range(TT):
                    for half in range(2):
                        sl = slice(half * 512, (half + 1) * 512)
                        link(v_.tensor_tensor(gr[:, t, sl], gr[:, t, sl], ps[2 * t + half][:, :], ALU.mult))
                        v_.tensor_tensor(gp[:, t, sl], gp[:, t, sl], gr[:, t, sl], ALU.add).then_inc(o2.sem, 1)
                for k in (0, 1, 4, 5):
                    dve.wait_ge(*o3.at(k // 2 + 1))
                    v_.tensor_copy(mgT[:, k, :], ps[4 + k // 2][:, (k % 2) * T:(k % 2 + 1) * T]).then_inc(o4.sem, 1)
                dve.wait_ge(*o7.at(1))
                for t in range(TT):
                    for half in range(2):
                        sl = slice(half * 512, (half + 1) * 512)
                        link(v_.tensor_tensor(gr[:, t, sl], ps[2 * t + half][:, :], g1[:, sl], ALU.mult))
                        link(v_.tensor_tensor(self.x[:, t, sl], self.x[:, t, sl], gr[:, t, sl], ALU.add))
        for s, n in ((o1, 1), (o2, 4), (o3, 4), (o4, 8), (o5, 1), (o6, 2), (o7, 1)):
            s.base += n

    def peer(self):
        nc, ps, G = self.nc, self.psum, G_SECOND
        v_, s_, g_ = nc.vector, nc.scalar, nc.gpsimd
        self.begin_stage()
        cursor = self.base

        def region(size):
            nonlocal cursor
            cursor += size
            return cursor - size, cursor

        raw_at, parts_at, ga_at, w_at = region(2 * TILE * 4), region(8 * D * 4), region(4 * T * 4), region(P * T * 4)
        assert w_at[1] <= self.keep
        xraw = Arena(nc, "peerX", *raw_at)("raw", 2 * TILE).rearrange("p (s m n) -> p s m n", s=2, m=2)
        split = Arena(nc, "peerS", *parts_at)
        U, V = ([split(f"{m}{n}", 2 * D, dt=F32R).rearrange("p (s n) -> p s n", s=2) for n in ("high", "low")]
                for m in "UV")
        weighted = Arena(nc, "peerG", *ga_at)
        GA = [weighted(f"GA{n}", 2 * T, dt=F32R).rearrange("p (b t) -> p b t", b=2) for n in ("high", "low")]
        Wt = Arena(nc, "peerW", *w_at)("W", P * T).rearrange("p (t i) -> p t i", t=T)
        g2 = Arena(nc, "peerG2", *ga_at)("g2", D)
        iota = Arena(nc, "peerI", *ga_at)("iota", P)
        stay = Arena(nc, "peerP", *parts_at)
        GT, I1T, I2T, minus_I2T = (stay(n, T) for n in ("GT", "I1T", "I2T", "minus_I2T"))
        O1 = stay("O1", 16 * P).rearrange("p (q n) -> p q n", q=16)
        O2 = stay("O2", 16 * P).rearrange("p (q n) -> p q n", q=16)
        tmp = Arena(nc, "peerT", *w_at)
        xs = tmp("xs", TT * D).rearrange("p (t d) -> p t d", t=TT)
        xw = tmp("xw", KD * T).rearrange("p (k t) -> p k t", k=KD)
        qT = tmp("qT", 16 * T).rearrange("p (c t) -> p c t", c=16)
        keys = tmp("keys", TILE)
        sc = tmp("sc", 32 * P).rearrange("p (r n) -> p r n", r=32)
        spare = tmp("spare", 8 * P).rearrange("p (r n) -> p r n", r=8)
        cand = tmp("cand", 4 * 256).rearrange("p (r n) -> p r n", r=4)
        cspare = tmp("cspare", 4 * 256).rearrange("p (r n) -> p r n", r=4)
        eq = tmp("eq", 4 * 256).rearrange("p (r k j) -> p r k j", r=4, k=16)
        val = tmp("val", 512).rearrange("p (r k) -> p r k", r=32)
        idx = tmp("idx", 512, dt=U32).rearrange("p (r k) -> p r k", r=32)
        idf = tmp("idf", 512).rearrange("p (r k) -> p r k", r=32)
        rank_arrays = [tmp(n, 256).rearrange("p (r k) -> p r k", r=16) for n in ("best", "weight", "i1", "i2", "hi", "lo")]
        best, weight, i1, i2, hi, lo = rank_arrays
        pos = tmp("pos", 256, dt=U32).rearrange("p (r k) -> p r k", r=16)
        posh = tmp("posh", 256, dt=U32).rearrange("p (r k) -> p r k", r=16)
        sm = tmp("sm", 16)
        experts = self.dram["experts"]

        done, freed, here, sdone, sfree, xhigh, xlow = self.counters("pr_done", "pr_freed", "pr_here", "pr_scores", "pr_sfreed",
                                                                    "pr_xhigh", "pr_xlow")
        tk1, tk2, tk3, tk4, tk5, shifted = self.counters("tk_sub", "tk_exp", "tk_ready", "tk_turned", "tk_T", "tk_shifted")
        uloaded = self.counters("ex_u_loaded0", "ex_u_loaded1")
        vloaded = self.counters("ex_v_loaded0", "ex_v_loaded1")
        nact, ndve, npool, npe, nend = self.norm_parts(self.x, xw, self.gA[:, 2, :], self.modT[:, 24:32, 0], xs)
        with nc.Block() as block:
            @block.sync
            def _(sp):
                sp.dma_start(iota, self.dram["iota"]).then_inc(here.sem, 16)
                sp.dma_start(keys, self.dram["stream"][N_TILES]).then_inc(here.sem, 16)
                self.loads(sp, N_TILES)
                sp.wait_ge(*self.released_at(N_TILES - 1))
                for s in range(2):
                    sp.dma_start(xraw[:, s, 0, :], experts[s, :, 0:D]).then_inc(uloaded[s].sem, 16)
                    sp.dma_start(xraw[:, s, 1, :], experts[s, :, D:]).then_inc(vloaded[s].sem, 16)

            @block.gpsimd
            def _(pool):
                npool(pool)
                self.make_lows(pool, N_TILES)
                pool.wait_ge(*xhigh.at(1))
                g_.tensor_tensor(self.xT[1], xw, self.xT[0].bitcast(F32), ALU.subtract).then_inc(xlow.sem, 1)
                pool.wait_ge(*xlow.at(1))

            @block.tensor
            def _(pe):
                def scores(b):
                    pe.wait_ge(*freed.at(4 * b + 4))
                    if b >= 2:
                        pe.wait_ge(*sfree.at(2 * b - 2))
                    for t in range(TT):
                        for j in range(4):
                            c = 4 * b + j
                            last = self.mm(ps[4 + 2 * (b % 2) + t][:, j * P:(j + 1) * P], qT[:, c, t * P:(t + 1) * P],
                                           keys[:, c * P:(c + 1) * P], True, True)
                        last.then_inc(sdone.sem, 1)

                npe(pe)
                pe.wait_ge(*here.at(32))
                for n in range(16):
                    if n >= 4:
                        pe.wait_ge(*freed.at(n - 3))
                    self.stationary_cols(ps[n % 4][:, 0:T], self.ring_tile(pe, G, 57 + n // 2), n % 2, xw
                                         ).then_inc(done.sem, 1)
                    if n % 2:
                        self.give_back(57 + n // 2)
                    if n % 4 == 0 and n:
                        scores(n // 4 - 1)
                scores(3)
                self.flush(pe, sdone.at(8))
                pe.wait_ge(*tk3.at(1))
                for t in range(TT):
                    for b, src in enumerate((weight, i1, i2)):
                        rows = src.rearrange("p (t r) k -> p t (r k)", t=TT)[:, t]
                        last = nc.tensor.transpose(ps[b][:, t * P:(t + 1) * P], rows, self.ident)
                last.then_inc(tk4.sem, 1)

            @block.scalar
            def _(act):
                def scores_out(b):
                    for t in range(TT):
                        act.wait_ge(*sdone.at(2 * b + t + 1))
                        s_.activation(sc[:, 8 * b + 4 * t:8 * b + 4 * t + 4, :],
                                      ps[4 + 2 * (b % 2) + t][:, :].rearrange("p (r n) -> p r n", r=4),
                                      ACT.Copy).then_inc(sfree.sem, 1)

                nact(act)
                act.wait_ge(self.counters("nrm_low")[0].sem, self.counters("nrm_low")[0].base + KD)
                s_.activation(self.xT[0], xw, ACT.Copy).then_inc(xhigh.sem, 1)
                for n in range(16):
                    act.wait_ge(*done.at(n + 1))
                    s_.activation(qT[:, n, :], ps[n % 4][:, 0:T], ACT.Copy).then_inc(freed.sem, 1)
                    if n % 4 == 0 and n:
                        scores_out(n // 4 - 1)
                scores_out(3)
                act.wait_ge(*tk1.at(2))
                s_.activation(weight, weight, ACT.Exp).then_inc(tk2.sem, 1)

            @block.vector
            def _(dve):
                link = Chain(dve, self.dve_chain)

                def top16(rows, src, spare, values, index):
                    n0 = rows[0]
                    for r in rows:
                        last = v_.max(values[:, r, 0:8], src[:, r - n0, :])
                    link(last)
                    for r in rows:
                        last = v_.max_index(index[:, r, 0:8], values[:, r, 0:8], src[:, r - n0, :])
                    for r in rows:
                        last = v_.match_replace(spare[:, r - n0, :], values[:, r, 0:8], src[:, r - n0, :], -3.0e38)
                    link(last)
                    for r in rows:
                        last = v_.max(values[:, r, 8:16], spare[:, r - n0, :])
                    link(last)
                    for r in rows:
                        last = v_.max_index(index[:, r, 8:16], values[:, r, 8:16], spare[:, r - n0, :])
                    link(last)

                ndve(dve)
                dve.wait_ge(*here.at(32))
                jot = iota[:, 0:16].unsqueeze(1).unsqueeze(1).to_broadcast([P, 4, 16, 16])
                pairs = val.rearrange("p (r s) k -> p r s k", s=2)
                ids = idf.rearrange("p (r s) k -> p r s k", s=2)
                for b in range(4):
                    r = slice(4 * b, 4 * b + 4)
                    dve.wait_ge(*sfree.at(2 * b + 2))
                    top16(range(8 * b, 8 * b + 8), sc[:, 8 * b:8 * b + 8], spare, val, idx)
                    link(v_.tensor_tensor(cand.rearrange("p r (i j) -> p r i j", i=16),
                                          pairs[:, r, 0, :].unsqueeze(3).to_broadcast([P, 4, 16, 16]),
                                          pairs[:, r, 1, :].unsqueeze(2).to_broadcast([P, 4, 16, 16]), ALU.add))
                    top16(range(4 * b, 4 * b + 4), cand, cspare, best, pos)
                    if b == 3:
                        for t in range(TT):
                            sums = best.rearrange("p (b t h) k -> p t b h k", b=4, t=TT)[:, t]
                            v_.tensor_tensor(weight[:, 8 * t:8 * t + 8].rearrange("p (b h) k -> p b h k", b=4), sums,
                                             sums[:, :, :, 0:1].to_broadcast([P, 4, 2, 16]), ALU.subtract).then_inc(tk1.sem, 1)
                    v_.tensor_scalar(posh[:, r], pos[:, r], 4, None, ALU.logical_shift_right).then_inc(shifted.sem, 1)
                    v_.tensor_copy(idf[:, 8 * b:8 * b + 8], idx[:, 8 * b:8 * b + 8])
                    dve.wait_ge(*shifted.at(b + 1))
                    v_.tensor_copy(hi[:, r], posh[:, r])
                    link(v_.tensor_scalar(pos[:, r], pos[:, r], 15, None, ALU.bitwise_and))
                    link(v_.tensor_copy(lo[:, r], pos[:, r]))
                    for part, (which, out) in enumerate(((hi, i1), (lo, i2))):
                        link(v_.tensor_tensor(eq, which[:, r].unsqueeze(3).to_broadcast([P, 4, 16, 16]), jot, ALU.is_equal))
                        link(v_.tensor_tensor(eq, eq, ids[:, r, part, :].unsqueeze(2).to_broadcast([P, 4, 16, 16]), ALU.mult))
                        link(v_.tensor_reduce(out.rearrange("p (t b h) k -> p t b (h k)", t=TT, b=4)[:, :, b],
                                              eq.rearrange("p (t h) k j -> p t (h k) j", t=TT), AX.X, ALU.add))
                dve.wait_ge(*tk2.at(1))
                link(v_.tensor_reduce(sm, weight, AX.X, ALU.add))
                link(v_.reciprocal(sm, sm))
                v_.tensor_tensor(weight, weight, sm.unsqueeze(2).to_broadcast([P, 16, 16]), ALU.mult).then_inc(tk3.sem, 1)
                dve.wait_ge(*tk4.at(1))
                for b, dst in enumerate((GT, I1T, I2T)):
                    v_.tensor_copy(dst, ps[b][:, 0:T]).then_inc(tk5.sem, 1)
                v_.tensor_scalar(minus_I2T, ps[2][:, 0:T], -1.0, None, ALU.mult).then_inc(tk5.sem, 1)
                dve.wait_ge(*tk5.at(4))
        nend()
        for s, n in ((done, 16), (freed, 16), (xhigh, 1), (xlow, 1), (here, 32), (sdone, 8), (sfree, 8), (tk1, 2), (tk2, 1),
                     (tk3, 1), (tk4, 1), (tk5, 4), (shifted, 4)):
            s.base += n

        wo1, wo2, wo3, wabs, wmm, wev = self.counters("w_rows1", "w_rows2", "w_rows3", "w_distance", "w_product", "w_written")
        QUADS = T // 4
        with nc.Block() as block:
            @block.vector
            def _(dve):
                def quad(q, b, first=False):
                    if not first:
                        dve.wait_ge(*wmm.at(q - 3))
                    v_.tensor_scalar(O2[:, 4 * b + 2, :], iota, I2T[:, bass.ds(q * 4 + 2, 1)], None, ALU.is_equal)
                    for j in range(4):
                        t = q * 4 + j
                        last = v_.tensor_scalar(O1[:, 4 * b + j, :], iota, I1T[:, bass.ds(t, 1)], GT[:, bass.ds(t, 1)],
                                                ALU.is_equal, ALU.mult)
                    last.then_inc(wo1.sem, 1)
                for b in range(4):
                    quad(b, b, True)
                with dve.Fori(1, QUADS // 4) as turn:
                    for b in range(4):
                        quad(turn * 4 + b, b)

            @block.gpsimd
            def _(pool):
                def quad(q, b, first=False):
                    if not first:
                        pool.wait_ge(*wmm.at(q - 3))
                    for j in range(2):
                        t = q * 4 + j
                        last = g_.tensor_scalar(O2[:, 4 * b + j, :], iota, I2T[:, bass.ds(t, 1)], None, ALU.is_equal)
                    last.then_inc(wo2.sem, 1)
                for q in range(QUADS):
                    quad(q, q % 4, q < 4)

            @block.tensor
            def _(pe):
                def quad(q, b, first=False):
                    pe.wait_ge(*wo1.at(q + 1))
                    pe.wait_ge(*wo2.at(q + 1))
                    pe.wait_ge(*wo3.at(q + 1))
                    if not first:
                        pe.wait_ge(*wev.at(q - 3))
                    for j in range(4):
                        last = nc.tensor.matmul(ps[b][:, j * P:(j + 1) * P], O1[:, 4 * b + j, :], O2[:, 4 * b + j, :],
                                                start=True, stop=True)
                    last.then_inc(wmm.sem, 1)
                for b in range(4):
                    quad(b, b, True)
                with pe.Fori(1, QUADS // 4) as turn:
                    for b in range(4):
                        quad(turn * 4 + b, b)

            @block.scalar
            def _(act):
                def unit_row(q, b):
                    o = O2[:, 4 * b + 3, :]
                    s_.activation(o, iota, ACT.Abs, bias=minus_I2T[:, bass.ds(q * 4 + 3, 1)]).then_inc(wabs.sem, 1)
                    act.wait_ge(*wabs.at(q + 1))
                    s_.activation(o, o, ACT.Relu, scale=-1.0, bias=1.0).then_inc(wo3.sem, 1)

                def out(q, b):
                    act.wait_ge(*wmm.at(q + 1))
                    s_.activation(Wt[:, bass.ds(q * 4, 4), :], ps[b][:, :].rearrange("p (t i) -> p t i", t=4),
                                  ACT.Copy).then_inc(wev.sem, 1)

                for b in range(4):
                    unit_row(b, b)
                with act.Fori(0, QUADS // 4 - 1) as turn:
                    for b in range(4):
                        out(turn * 4 + b, b)
                        unit_row(turn * 4 + (b + 4), b)
                for b in range(4):
                    out(QUADS - 4 + b, b)
        for s, n in ((wo1, QUADS), (wo2, QUADS), (wo3, QUADS), (wabs, QUADS), (wmm, QUADS), (wev, QUADS)):
            s.base += n

        xu, xd, xa, xp, xh, xg, uh, ul, vh, vl, gr, gc = self.counters(
            "ex_scores", "ex_sums", "ex_gelu", "ex_weighted", "ex_weighted_high", "ex_weighted_low",
            "ex_u_high", "ex_u_low", "ex_v_high", "ex_v_low", "ex_gate_row", "ex_gate")
        N = PEER_KEYS
        with nc.Block() as block:
            @block.sync
            def _(sp):
                with sp.Fori(1, N // 2) as turn:
                    for b in range(2):
                        row = experts[bass.ds(turn * 2 + b, 1)]
                        sp.wait_ge(*ul.at(turn * 2 + (b - 1)))
                        sp.dma_start(xraw[:, b, 0, :], row[:, :, 0:D].rearrange("a p n -> p (a n)")).then_inc(uloaded[b].sem, 16)
                        sp.wait_ge(*vl.at(turn * 2 + (b - 1)))
                        sp.dma_start(xraw[:, b, 1, :], row[:, :, D:].rearrange("a p n -> p (a n)")).then_inc(vloaded[b].sem, 16)

            @block.tensor
            def _(pe):
                def up(n, b, first=False):
                    pe.wait_ge(*ul.at(n + 1))
                    if not first:
                        pe.wait_ge(*xg.at(n - 1))
                    for k in range(KD):
                        last = self.product(ps[b][:, 0:T], [u[:, b, k * P:(k + 1) * P] for u in U],
                                            [x[:, k, :] for x in self.xT], k == 0, k == KD - 1)
                    last.then_inc(xu.sem, 1)

                def down(n, b, start=False, stop=False):
                    pe.wait_ge(*xg.at(n + 1))
                    pe.wait_ge(*vl.at(n + 1))
                    for t in range(TT):
                        for half in range(2):
                            last = self.product(ps[4 + 2 * t + half][:, :], [g[:, b, t * P:(t + 1) * P] for g in GA],
                                                [v[:, b, half * 512:(half + 1) * 512] for v in V], start, stop)
                    last.then_inc(xd.sem, 1)

                up(0, 0, first=True)
                up(1, 1, first=True)
                down(0, 0, start=True)
                with pe.Fori(1, N // 2) as turn:
                    for b in range(2):
                        up(turn * 2 + b, b)
                        down(turn * 2 + (b - 1), 1 - b)
                down(N - 1, 1, stop=True)
                self.gate_row(5, (0, 1)).then_inc(gr.sem, 1)

            @block.scalar
            def _(act):
                def u_high(n, b, turn):
                    act.wait_ge(*uloaded[b].at(turn * 16 + 16))
                    s_.activation(U[0][:, b, :], xraw[:, b, 0, :], ACT.Copy).then_inc(uh.sem, 1)

                def v_high(n, b, turn):
                    act.wait_ge(*vloaded[b].at(turn * 16 + 16))
                    s_.activation(V[0][:, b, :], xraw[:, b, 1, :], ACT.Copy).then_inc(vh.sem, 1)

                def step(n, b, turn, last=False):
                    act.wait_ge(*xu.at(n + 1))
                    s_.activation(ps[b][:, 0:T], ps[b][:, 0:T], ACT.Gelu).then_inc(xa.sem, 1)
                    if not last:
                        u_high(n + 2, b, turn + 1)
                    if last and b:
                        return
                    act.wait_ge(*xd.at(n))
                    v_high(n + 1, 1 - b, turn + b)

                u_high(0, 0, 0)
                u_high(1, 1, 0)
                v_high(0, 0, 0)
                act.wait_ge(*xu.at(1))
                s_.activation(ps[0][:, 0:T], ps[0][:, 0:T], ACT.Gelu).then_inc(xa.sem, 1)
                u_high(2, 0, 1)
                v_high(1, 1, 0)
                step(1, 1, 0)
                with act.Fori(1, N // 2 - 1) as turn:
                    for b in range(2):
                        step(turn * 2 + b, b, turn)
                step(N - 2, 0, N // 2 - 1, last=True)
                step(N - 1, 1, N // 2 - 1, last=True)
                act.wait_ge(*gr.at(1))
                for b in range(2):
                    s_.activation(g2[:, b * 512:(b + 1) * 512], ps[b][:, :], ACT.Copy).then_inc(gc.sem, 1)

            @block.gpsimd
            def _(pool):
                with pool.Fori(0, N // 2) as turn:
                    for b in range(2):
                        pool.wait_ge(*uh.at(turn * 2 + (b + 1)))
                        g_.tensor_tensor(U[1][:, b, :], xraw[:, b, 0, :], U[0][:, b, :].bitcast(F32), ALU.subtract
                                         ).then_inc(ul.sem, 1)

            @block.vector
            def _(dve):
                def v_low(n, b):
                    dve.wait_ge(*vh.at(n + 1))
                    v_.tensor_tensor(V[1][:, b, :], xraw[:, b, 1, :], V[0][:, b, :].bitcast(F32), ALU.subtract
                                     ).then_inc(vl.sem, 1)

                def step(n, b, first=False, last=False):
                    s = ps[b][:, 0:T]
                    dve.wait_ge(*xa.at(n + 1))
                    v_.tensor_tensor(s.unsqueeze(2), s.unsqueeze(2), Wt[:, :, bass.ds(n, 1)], ALU.mult).then_inc(xp.sem, 1)
                    dve.wait_ge(*xp.at(n + 1))
                    if not first:
                        dve.wait_ge(*xd.at(n - 1))
                    v_.tensor_copy(GA[0][:, b, :], s).then_inc(xh.sem, 1)
                    dve.wait_ge(*xh.at(n + 1))
                    v_.tensor_tensor(GA[1][:, b, :], s, GA[0][:, b, :].bitcast(F32), ALU.subtract).then_inc(xg.sem, 1)
                    if not last:
                        v_low(n + 1, 1 - b)

                v_low(0, 0)
                step(0, 0, first=True)
                step(1, 1, first=True)
                with dve.Fori(1, N // 2 - 1) as turn:
                    for b in range(2):
                        step(turn * 2 + b, b)
                step(N - 2, 0)
                step(N - 1, 1, last=True)
                dve.wait_ge(*gc.at(2))
                link = Chain(dve, self.dve_chain)
                for t in range(TT):
                    for half in range(2):
                        sl = slice(half * 512, (half + 1) * 512)
                        o = ps[4 + 2 * t + half][:, :]
                        link(v_.tensor_tensor(o, o, g2[:, sl], ALU.mult))
                        link(v_.tensor_tensor(self.x[:, t, sl], self.x[:, t, sl], o, ALU.add))
        for s, n in ((xu, N), (xd, N), (xa, N), (xp, N), (xh, N), (xg, N), (uh, N), (ul, N), (vh, N), (vl, N), (gr, 1), (gc, 2)):
            s.base += n
        for s in uloaded + vloaded:
            s.base += 8 * N


def build(nc, dram, out, stages=None, first=0, tiles=N_TILES):
    k = Kernel(nc, dram, out, stages)
    k.first = k.next_load = k.next_low = first
    k.tiles = tiles
    steps = [("ffn1a", lambda: k.ffn(G_FFN1A, 0)), ("ab", lambda: k.ab()),
             ("ffn2a", lambda: k.ffn(G_FFN2A, 2)), ("ffn1b", lambda: k.ffn(G_FFN1B, 3)),
             ("nsa", lambda: k.nsa()), ("ffn2b", lambda: k.ffn(G_FFN2B, 5)),
             ("final1", lambda: k.final_norm("final_norm")), ("mixed", lambda: k.second()),
             ("pre_final", lambda: k.peer()), ("out", lambda: k.final_norm("final_g"))]
    with k.ctx:
        k.start()
        k.end_stage()
        for name, step in steps:
            if stages is None or name in stages:
                step()
                k.end_stage()
        k.store(k.x)
        k.end_stage()


def cols_block(w, c0, n):
    return w[:, c0:c0 + n].reshape(KD, P, n).transpose(1, 0, 2).reshape(P, KD * n)


def rows_tiles(w):
    r = w.shape[0] // 256
    return [w[256 * i:256 * (i + 1)].reshape(2, P, D).transpose(1, 0, 2).reshape(P, TILE) for i in range(r)]


def tiles_of(block):
    return [block[:, i:i + TILE] for i in range(0, block.shape[1], TILE)]


def columns(v):
    return v.reshape(-1, P).T


def ffn_tiles(w_gu, w_down):
    tiles = []
    downs = rows_tiles(w_down)
    for i in range(FFN_GROUPS):
        both = np.concatenate([w_gu[:, 256 * i:256 * (i + 1)], w_gu[:, D_FF + 256 * i:D_FF + 256 * (i + 1)]], 1)
        tiles += tiles_of(cols_block(both, 0, 512))
        if i:
            tiles.append(downs[i - 1])
    return tiles + [downs[-1]]


def rg_tile(w_r, w_i):
    out = np.zeros((P, 16, P), np.float32)
    for m, w in enumerate((w_r, w_i)):
        for c in range(RG_CHUNKS):
            for b in range(2):
                out[64 * b:64 * b + 64, 4 * m + c, 64 * b:64 * b + 64] = w[2 * c + b]
    return out.reshape(P, TILE)


def nsa_q_order():
    order = []
    for c in range(8):
        for g in (2 * (c // 4), 2 * (c // 4) + 1):
            head = 4 * g + c % 4
            order += list(range(head * NSA_DH, (head + 1) * NSA_DH))
    return order


def layout(x, ffn1_norm, ffn1_w_gu, ffn1_w_down, mix_norm, ffn2_norm, ffn2_w_gu, ffn2_w_down, ab_w_in,
           rg_conv_w, rg_conv_b, rg_w_r, rg_b_r, rg_w_i, rg_b_i, rg_lambda, ml_conv_w, ml_conv_b,
           ml_b_i, ml_b_f, ml_norm, ab_w_out, nsa_w_in, nsa_pe_k, nsa_k_w1, nsa_k_b1, nsa_k_w2,
           nsa_pe_v, nsa_v_w1, nsa_v_b1, nsa_v_w2, nsa_b_gate, nsa_w_out, final_norm, c_2, ctx_2,
           c_ctx_2, ada_w_2, ada_b_2, norm_mix_g_2, norm_ffn_g_2, w_in_2, pool_w_2, pool_scale_2,
           pool_out_2, ret_decay_2, ret_norm_g_2, ret_out_2, w_out_2, peer_wq_2, peer_keys_2, peer_u_2,
           peer_v_2, final_g_2):
    tiles = ffn_tiles(ffn1_w_gu[0], ffn1_w_down[0])
    ab = ab_w_in[0]
    for c in range(0, 3072, 256):
        if c < 2048:
            tiles.append(cols_block(ab, c, 256))
        elif c % 512 == 0:
            tiles += tiles_of(cols_block(ab, c, 512))
    tiles += [rg_tile(rg_w_r[0], rg_w_i[0])] + rows_tiles(ab_w_out[0])
    tiles += ffn_tiles(ffn2_w_gu[0], ffn2_w_down[0])
    tiles += ffn_tiles(ffn1_w_gu[1], ffn1_w_down[1])
    nsa = nsa_w_in[0]
    part = lambda i: nsa[:, 1024 + 256 * i:1024 + 256 * (i + 1)]
    q = nsa[:, :1024][:, nsa_q_order()]
    n_tiles = [cols_block(q, c, 256) for c in range(0, 1024, 256)]
    n_tiles += [cols_block(part(2), 0, 256), cols_block(part(4), 0, 256)]
    for kv in (0, 1):
        w = part(kv).reshape(D, NSA_GROUPS, 1, NSA_DH)
        w = np.concatenate([w, w], 2).reshape(D, 512)
        n_tiles += [cols_block(w, 0, 256), cols_block(w, 256, 256)]
    n_tiles += tiles_of(cols_block(np.concatenate([part(3), part(5)], 1), 0, 512))
    for w1 in (nsa_k_w1[0], nsa_v_w1[0]):
        n_tiles += tiles_of(w1.reshape(16, P, 256).transpose(1, 0, 2).reshape(P, 4096))
    n_tiles += rows_tiles(nsa_w_out[0])
    tiles += n_tiles
    tiles += ffn_tiles(ffn2_w_gu[1], ffn2_w_down[1])
    w = w_in_2[0]
    s_tiles = []
    for c in range(0, 6144, 512):
        s_tiles += tiles_of(cols_block(ada_w_2[0], c, 512))
    for c in range(0, 5632, 512):
        s_tiles += tiles_of(cols_block(w, c, 512))
    pw = np.zeros((P, TILE), np.float32)
    pw[:, :512] = pool_w_2[0].transpose(1, 0, 2).reshape(P, 512)
    s_tiles.append(pw)
    s_tiles += rows_tiles(pool_out_2[0]) + rows_tiles(ret_out_2[0]) + rows_tiles(w_out_2[0])
    s_tiles += [cols_block(peer_wq_2[0], c, 256) for c in range(0, 2048, 256)]
    s_tiles.append(peer_keys_2[0].transpose(3, 0, 1, 2).reshape(P, TILE))
    tiles += s_tiles
    stream = np.stack(tiles)
    assert stream.shape[0] == N_TILES + 1, stream.shape

    u = peer_u_2[0].reshape(P, P, KD, P)
    v = peer_v_2[0].reshape(P, P, D)
    experts = np.concatenate([u.transpose(1, 3, 2, 0).reshape(P, P, D), v.transpose(1, 0, 2)], 2)

    gains = np.concatenate([columns(a) for a in (
        ffn1_norm[0], mix_norm[0], ffn2_norm[0], ffn1_norm[1], mix_norm[1], ffn2_norm[1],
        norm_mix_g_2[0], norm_ffn_g_2[0])], 1)
    conv_w = np.concatenate([rg_conv_w[0], ml_conv_w[0]], 1)
    conv_b = np.concatenate([rg_conv_b[0], ml_conv_b[0]], 0)
    taps = np.stack([columns(a) for a in [*conv_w, conv_b]], 2).reshape(P, 60)
    rgb = np.concatenate([columns(rg_b_r[0]), columns(rg_b_i[0]), columns(rg_lambda[0]), columns(ml_norm[0])], 1)
    ml_if = cols_block(ab, 3072, 8)
    ml_b = np.stack([ml_b_i[0], ml_b_f[0]], 1)
    j = np.arange(P)
    causal = (j[None, :] >= j[:, None]).astype(np.float32)
    ones = np.ones((P, P), np.float32)
    ml_mask = np.concatenate([causal, ones, causal], 1) * np.float32(ML_DH ** -0.5)
    ml_sel = np.repeat(np.eye(4, dtype=np.float32), P, 1)
    nsa_small = dict(
        w2=np.concatenate([nsa_k_w2[0].reshape(2, P, 64), nsa_k_w2[0].reshape(2, P, 64), nsa_v_w2[0].reshape(2, P, 64)], 2
                          ).transpose(1, 0, 2).reshape(P, 384),
        pe=np.concatenate([nsa_pe_k[0].reshape(16, P).T, nsa_pe_v[0].reshape(16, P).T], 1),
        b1=np.concatenate([columns(nsa_k_b1[0]), columns(nsa_v_b1[0])], 1),
        gw=cols_block(nsa, 2560, 48), gb=nsa_b_gate[0][None])
    t = np.arange(T)
    n = np.arange(16)
    cmask = ((n[None, :] * CMP_STRIDE + CMP_BLOCK - 1 <= t[:, None]) & (n[None, :] < N_CMP)).astype(np.float32)
    head_blocks = np.repeat(np.eye(8, dtype=np.float32), 16, 0)
    nmask = dict(causal_add=np.where(causal.T > 0, np.float32(0), np.float32(NEG)).astype(np.float32),
                 cmp=cmask.reshape(2, P, 16).transpose(1, 0, 2).reshape(P, 32), blocks=head_blocks)
    rows = T // 64
    row, col = np.repeat(np.arange(rows, dtype=np.float32), 64), np.tile(np.arange(64, dtype=np.float32), rows)
    inv = np.float32(10000.0) ** (-np.arange(32, dtype=np.float32) / 32)
    ang = np.concatenate([row[:, None] * inv, col[:, None] * inv], 1).astype(np.float32)
    rope = np.stack([np.cos(ang), np.sin(ang)], 0).astype(np.float32)
    rope = rope.reshape(2, 2, P, 64).transpose(2, 0, 1, 3).reshape(P, 256)
    band = np.zeros((4, T, T), np.float32)
    for g, wd in enumerate((2, 4, 8, 16)):
        lo, hi = np.clip(t - wd // 2, 0, T), np.clip(t + wd - wd // 2, 0, T)
        inside = (t[:, None] >= lo[None]) & (t[:, None] < hi[None])
        band[g] = inside / (hi - lo)[None].astype(np.float32) - np.eye(T, dtype=np.float32)
    band = band.reshape(4, 2, P, T).transpose(2, 0, 1, 3).reshape(P, 2048)
    rel = (t[None, :] - t[:, None]).astype(np.float32)
    ret = np.stack([np.maximum(rel, 0), np.maximum(-rel, 0), (rel >= 0).astype(np.float32), (rel < 0).astype(np.float32)])
    ret = ret.reshape(4, 2, P, T).transpose(2, 0, 1, 3).reshape(P, 2048)
    ret_row = np.concatenate([np.tile(t + 1, (P, 1)), np.tile(T - t, (P, 1))], 1).astype(np.float32)
    ret_col = np.stack([T - 1 - t, t], 1).reshape(2, P, 2).transpose(1, 0, 2).reshape(P, 4).astype(np.float32)
    iota = np.tile(np.arange(P, dtype=np.float32), (P, 1))
    return dict(
        x=x[0], stream=stream, experts=experts, ident=np.eye(P, dtype=np.float32), gains=gains,
        ab_taps=taps, ab_cols=rgb, ab_if=ml_if, ab_b=ml_b, ab_mask=ml_mask, ab_sel=ml_sel,
        nsa_w2=nsa_small["w2"], nsa_pe=nsa_small["pe"], nsa_b1=nsa_small["b1"], nsa_gw=nsa_small["gw"],
        nsa_gb=nsa_small["gb"], nsa_causal=nmask["causal_add"], nsa_cmp=nmask["cmp"], nsa_blocks=nmask["blocks"],
        final_norm=final_norm[None], final_g=final_g_2[None], ctx=ctx_2[0],
        cond=np.stack([columns(c_2[0]), columns(c_ctx_2)], 2).reshape(P, 16), ada_b=columns(ada_b_2[0]),
        rope=rope, band=band, pool_scale=columns(pool_scale_2[0]), decay=ret_decay_2[0].reshape(1, 8),
        ret=ret, ret_row=ret_row, ret_col=ret_col, ret_norm=columns(ret_norm_g_2[0]), iota=iota)


OUT_SHAPE = (1, T, D)


def kernel(**inputs):
    import concourse.bacc as bacc
    from concourse.bass_utils import run_bass_kernel_spmd
    arrays = layout(**{k: np.asarray(v) for k, v in inputs.items()})
    nc = bacc.Bacc("TRN2", target_bir_lowering=False, num_devices=1)
    dram, given = {}, {}
    for name, a in arrays.items():
        a = np.ascontiguousarray(a)
        given[f"in_{name}"] = a
        dram[name] = nc.dram_tensor(f"in_{name}", a.shape, mybir.dt.from_np(a.dtype), kind="ExternalInput").ap()
    out = nc.dram_tensor("out_0", OUT_SHAPE, F32, kind="ExternalOutput").ap()
    build(nc, dram, out)
    result = run_bass_kernel_spmd(nc, [given], core_ids=[0])
    return result.results[0]["out_0"]
```
